# Optimizing a Trainium2 kernel written in Bass

```python
import math
import jax
import jax.numpy as jnp
from jax import lax
import numpy as np

D_MODEL = 1024
BATCH = 1
SEQ = 1024
DEPTH = 1
DEC_BATCH = 8
DEC_SEQ = 1
PAST_LEN = 1024
PAGE_SIZE = 128

NSA_HEADS = 8
NSA_KV = 2
NSA_GROUP = NSA_HEADS // NSA_KV
NSA_DH = 64
BRANCH_WIDTH = 512
CMP_STRIDE = 16
CMP_BLOCK = 2 * CMP_STRIDE
CMP_HID = 128
SEL_BLOCK = 64
N_SELECT = 16
WINDOW = 512
Q_BLOCK = 128
N_KV_STREAMS = 6
N_CACHE_STREAMS = 4
N_BUCKETS = 32
MAX_DISTANCE = 128
DN_HEADS = 4
DN_DK = 128
DN_DV = 128
DN_CONV = 4
DN_CHUNK = 64
DN_CONV_DIM = DN_HEADS * (2 * DN_DK + DN_DV)
HG_HEADS = 4
HG_DK = 128
HG_DV = 128
HG_CHUNK = 64
N_EXPERTS = 16
N_EXPERT_GROUPS = 4
EXPERTS_PER_GROUP = N_EXPERTS // N_EXPERT_GROUPS
TOP_K = 2
D_EXPERT = 512
MOE_ROW_BLOCK = 128
D_PLE = 256
DEEPNORM_ALPHA = (2 * DEPTH) ** 0.25
DEEPNORM_BETA = (8 * DEPTH) ** -0.25
EPS = 1e-6
NEG = -1e30
IN_SPLITS = (NSA_HEADS * NSA_DH, N_KV_STREAMS * NSA_KV * NSA_DH, 3 * NSA_HEADS,
             DN_CONV_DIM, DN_HEADS, DN_HEADS, DN_HEADS * DN_DV,
             HG_HEADS * HG_DK, HG_HEADS * HG_DK, HG_HEADS * HG_DV, HG_HEADS * HG_DV,
             3 * D_MODEL)
D_IN = sum(IN_SPLITS)

kernel_name = 'nsa_deltanet_hgrn2_moe_decoder_step'

def _split(z, sizes):
    return jnp.split(z, np.cumsum(sizes)[:-1].tolist(), axis=-1)

def _layer_norm(x, g, b):
    x32 = x.astype(jnp.float32)
    mu = x32.mean(-1, keepdims=True)
    var = jnp.square(x32 - mu).mean(-1, keepdims=True)
    return ((x32 - mu) * lax.rsqrt(var + EPS) * g + b).astype(x.dtype)

def _masked_softmax(logits, mask):
    z = jnp.where(mask, logits.astype(jnp.float32), NEG)
    e = jnp.exp(z - z.max(-1, keepdims=True)) * mask
    s = e.sum(-1, keepdims=True)
    return e / jnp.where(s > 0, s, 1.0)

def _l2norm(a):
    a32 = a.astype(jnp.float32)
    return (a32 * lax.rsqrt(jnp.sum(a32 * a32, -1, keepdims=True) + EPS)).astype(a.dtype)

def _gated_rmsnorm(o, gate, w):
    B, L, H, dv = o.shape
    o32 = o.astype(jnp.float32)
    o32 = o32 * lax.rsqrt(jnp.mean(o32 * o32, -1, keepdims=True) + EPS) * w
    return (o32.reshape(B, L, H * dv) * jax.nn.silu(gate.astype(jnp.float32))).astype(gate.dtype)

def _t5_bucket(dist):
    n = jnp.maximum(dist, 0)
    exact = N_BUCKETS // 2
    rel = jnp.log(jnp.maximum(n, 1).astype(jnp.float32) / exact) / math.log(MAX_DISTANCE / exact)
    large = jnp.minimum(exact + (rel * (N_BUCKETS - exact)).astype(jnp.int32), N_BUCKETS - 1)
    return jnp.where(n < exact, n, large)

def _head_bias(dist, rel_bias):
    Q, K = dist.shape
    bias = rel_bias[_t5_bucket(dist)]
    return bias.reshape(Q, K, NSA_KV, NSA_GROUP).transpose(2, 3, 0, 1).astype(jnp.float32)

def _compress(rows, w1, w2, pe):
    B, T, G, dh = rows.shape
    n_chunk = T // CMP_STRIDE
    r = rows[:, :n_chunk * CMP_STRIDE].reshape(B, n_chunk, CMP_STRIDE, G, dh)
    w1h = w1.reshape(2, CMP_STRIDE, dh, CMP_HID)
    lo = jnp.einsum('bcsgd,sdh->bcgh', r, w1h[0])
    hi = jnp.einsum('bcsgd,sdh->bcgh', r, w1h[1])
    h = lo[:, :-1] + hi[:, 1:] + pe.reshape(-1) @ w1
    return jax.nn.silu(h) @ w2

def _importance_map(n_cmp, n_sb):
    c0 = jnp.arange(n_cmp) * CMP_STRIDE
    c1 = c0 + CMP_BLOCK - 1
    b0 = jnp.arange(n_sb) * SEL_BLOCK
    b1 = b0 + SEL_BLOCK - 1
    return ((c0[:, None] <= b1[None, :]) & (c1[:, None] >= b0[None, :])).astype(jnp.float32)

def _nsa_core(q, gates, t, kc, vc, cmp_end, imp_map, ks_blk, vs_blk, kw, vw, w_pos, rel_bias):
    f32 = jnp.float32
    B, Q = q.shape[:2]
    lg = jnp.einsum('bqgjd,bcgd->bgjqc', q, kc).astype(f32) + _head_bias(t[:, None] - cmp_end[None, :], rel_bias)
    p_cmp = _masked_softmax(lg, cmp_end[None, :] <= t[:, None])
    o_cmp = jnp.einsum('bgjqc,bcgd->bqgjd', p_cmp.astype(vc.dtype), vc)
    n_sb = ks_blk.shape[2]
    n_top = min(N_SELECT, n_sb)
    imp = jnp.einsum('bgjqc,cn->bgqn', p_cmp, imp_map)
    blk = jnp.arange(n_sb)[None, :]
    cur = (t // SEL_BLOCK)[:, None]
    forced = (blk == 0) | (blk == cur) | (blk == cur - 1)
    score = jnp.where(blk * SEL_BLOCK <= t[:, None], jnp.where(forced, jnp.inf, imp), -jnp.inf)
    top_s, top_i = lax.top_k(score, n_top)
    b_ix = jnp.arange(B)[:, None, None, None]
    g_ix = jnp.arange(NSA_KV)[None, :, None, None]
    n_keys = n_top * SEL_BLOCK
    ks = ks_blk[b_ix, g_ix, top_i].reshape(B, NSA_KV, Q, n_keys, NSA_DH)
    vs = vs_blk[b_ix, g_ix, top_i].reshape(B, NSA_KV, Q, n_keys, NSA_DH)
    s_pos = (top_i[..., None] * SEL_BLOCK + jnp.arange(SEL_BLOCK)).reshape(B, NSA_KV, Q, n_keys)
    s_ok = jnp.repeat(top_s > -jnp.inf, SEL_BLOCK, axis=-1) & (s_pos <= t[:, None])
    table = rel_bias.reshape(N_BUCKETS, NSA_KV, NSA_GROUP).transpose(1, 2, 0)
    bucket = _t5_bucket(t[:, None] - s_pos)
    s_bias = table[jnp.arange(NSA_KV)[None, :, None, None, None],
                   jnp.arange(NSA_GROUP)[None, None, :, None, None],
                   bucket[:, :, None]].astype(f32)
    lg = jnp.einsum('bqgjd,bgqmd->bgjqm', q, ks).astype(f32) + s_bias
    p_sel = _masked_softmax(lg, s_ok[:, :, None])
    o_sel = jnp.einsum('bgjqm,bgqmd->bqgjd', p_sel.astype(vs.dtype), vs)
    w_ok = (w_pos[None, :] <= t[:, None]) & (w_pos[None, :] > t[:, None] - WINDOW) & (w_pos[None, :] >= 0)
    lg = jnp.einsum('bqgjd,bkgd->bgjqk', q, kw).astype(f32) + _head_bias(t[:, None] - w_pos[None, :], rel_bias)
    p_win = _masked_softmax(lg, w_ok)
    o_win = jnp.einsum('bgjqk,bkgd->bqgjd', p_win.astype(vw.dtype), vw)
    o = gates[..., 0:1] * o_cmp + gates[..., 1:2] * o_sel + gates[..., 2:3] * o_win
    return o.reshape(B, Q, NSA_HEADS * NSA_DH)

def _nsa_mixer(q_raw, kv_raw, gate_raw, past_rows, win_buf, w_cmp1, w_cmp2, pe_cmp, rel_bias):
    B, L, _ = q_raw.shape
    q = (q_raw * NSA_DH ** -0.5).reshape(B, L, NSA_KV, NSA_GROUP, NSA_DH)
    gates = jax.nn.sigmoid(gate_raw).reshape(B, L, NSA_KV, NSA_GROUP, 3)
    kv = kv_raw.reshape(B, L, N_KV_STREAMS, NSA_KV, NSA_DH)
    new_rows, new_win = kv[:, :, :N_CACHE_STREAMS], kv[:, :, N_CACHE_STREAMS:]
    pos0 = 0 if past_rows is None else past_rows.shape[1]
    rows = new_rows if past_rows is None else jnp.concatenate([past_rows, new_rows], 1)
    T = rows.shape[1]
    kc = _compress(rows[:, :, 0], w_cmp1[0], w_cmp2[0], pe_cmp[0])
    vc = _compress(rows[:, :, 1], w_cmp1[1], w_cmp2[1], pe_cmp[1])
    n_cmp = kc.shape[1]
    cmp_end = jnp.arange(n_cmp) * CMP_STRIDE + CMP_BLOCK - 1
    n_sb = -(-T // SEL_BLOCK)
    sel = jnp.pad(rows[:, :, 2:4], ((0, 0), (0, n_sb * SEL_BLOCK - T), (0, 0), (0, 0), (0, 0)))
    sel = sel.reshape(B, n_sb, SEL_BLOCK, 2, NSA_KV, NSA_DH).transpose(3, 0, 4, 1, 2, 5)
    imp_map = _importance_map(n_cmp, n_sb)
    wrows = new_win if win_buf is None else jnp.concatenate([win_buf, new_win], 1)
    n_buf = wrows.shape[1] - L

    def attend(q_b, g_b, t, kw, w_pos):
        return _nsa_core(q_b, g_b, t, kc, vc, cmp_end, imp_map, sel[0], sel[1],
                         kw[:, :, 0], kw[:, :, 1], w_pos, rel_bias)

    if past_rows is None:
        qb = min(Q_BLOCK, L)
        wpad = jnp.pad(wrows, ((0, 0), (WINDOW, 0), (0, 0), (0, 0), (0, 0)))

        def block(i):
            s0 = i * qb
            return attend(lax.dynamic_slice_in_dim(q, s0, qb, 1),
                          lax.dynamic_slice_in_dim(gates, s0, qb, 1),
                          s0 + jnp.arange(qb),
                          lax.dynamic_slice_in_dim(wpad, s0, WINDOW + qb, 1),
                          s0 - WINDOW + jnp.arange(WINDOW + qb))

        o = lax.map(block, jnp.arange(L // qb))
        o = jnp.moveaxis(o, 0, 1).reshape(B, L, NSA_HEADS * NSA_DH)
    else:
        o = attend(q, gates, pos0 + jnp.arange(L), wrows, pos0 - n_buf + jnp.arange(n_buf + L))
    keep = min(WINDOW, pos0 + L)
    return o, new_rows, wrows[:, -keep:]

def _chunk(a, c):
    B, L = a.shape[:2]
    n = -(-L // c)
    a = jnp.pad(a, [(0, 0), (0, n * c - L)] + [(0, 0)] * (a.ndim - 2))
    a = a.reshape((B, n, c) + a.shape[2:])
    return jnp.moveaxis(a, (1, 2), (0, 3))

def _unchunk(o, L):
    n, B, H, c, d = o.shape
    return jnp.moveaxis(o, (0, 3), (1, 2)).reshape(B, n * c, H, d)[:, :L]

def _gated_delta(q, k, v, beta, g, s0):
    f32 = jnp.float32
    L = k.shape[1]
    c = min(DN_CHUNK, L)
    qs, ks, vs = (_chunk(a.astype(f32), c) for a in (q, k, v))
    bs, gs = _chunk(beta.astype(f32), c), _chunk(g.astype(f32), c)
    incl = jnp.tril(jnp.ones((c, c), bool))
    strict = jnp.tril(jnp.ones((c, c), bool), -1)
    eye = jnp.eye(c, dtype=f32)

    def step(S, xs):
        qc, kc, vc, bc, gc = xs
        G = jnp.cumsum(gc, -1)
        dec = jnp.where(incl, jnp.exp(jnp.where(incl, G[..., :, None] - G[..., None, :], 0.0)), 0.0)
        kb = kc * bc[..., None]
        A = jnp.where(strict, jnp.einsum('bhtk,bhsk->bhts', kb, kc) * dec, 0.0)
        Tm = lax.linalg.triangular_solve(eye + A, jnp.broadcast_to(eye, A.shape), left_side=True, lower=True)
        u = Tm @ (vc * bc[..., None])
        w = Tm @ (kb * jnp.exp(G)[..., None])
        v_new = u - w @ S
        attn = jnp.einsum('bhtk,bhsk->bhts', qc, kc) * dec
        o = (qc * jnp.exp(G)[..., None]) @ S + attn @ v_new
        S = S * jnp.exp(G[..., -1])[..., None, None] + jnp.einsum(
            'bhtk,bhtv->bhkv', kc * jnp.exp(G[..., -1:] - G)[..., None], v_new)
        return S, o

    S, o = lax.scan(step, s0.astype(f32), (qs, ks, vs, bs, gs))
    return _unchunk(o, L).astype(v.dtype), S.astype(s0.dtype)

def _gla_scan(q, k, v, logf, s0):
    f32 = jnp.float32
    L = k.shape[1]
    c = min(HG_CHUNK, L)
    qs, ks, vs, fs = (_chunk(a.astype(f32), c) for a in (q, k, v, logf))
    incl = jnp.tril(jnp.ones((c, c), bool))[:, :, None]

    def step(S, xs):
        qc, kc, vc, fc = xs
        G = jnp.cumsum(fc, axis=-2)
        diff = G[:, :, :, None, :] - G[:, :, None, :, :]
        dec = jnp.where(incl, jnp.exp(jnp.where(incl, diff, 0.0)), 0.0)
        attn = jnp.einsum('bhtk,bhsk,bhtsk->bhts', qc, kc, dec)
        o = jnp.einsum('bhtk,bhkv->bhtv', qc * jnp.exp(G), S) + jnp.einsum('bhts,bhsv->bhtv', attn, vc)
        S = S * jnp.exp(G[:, :, -1])[..., None] + jnp.einsum(
            'bhsk,bhsv->bhkv', kc * jnp.exp(G[:, :, -1:] - G), vc)
        return S, o

    S, o = lax.scan(step, s0.astype(f32), (qs, ks, vs, fs))
    return _unchunk(o, L).astype(v.dtype), S.astype(s0.dtype)

def _short_conv(u, buf, w):
    L = u.shape[1]
    xc = jnp.concatenate([buf, u], 1)
    y = sum(xc[:, j:j + L] * w[j] for j in range(DN_CONV))
    return jax.nn.silu(y), xc[:, -(DN_CONV - 1):]

def _deltanet_mixer(qkv_raw, a_raw, b_raw, gate_raw, conv_buf, s0, conv_w, a_log, dt_bias, norm_w):
    f32 = jnp.float32
    B, L, _ = qkv_raw.shape
    if conv_buf is None:
        conv_buf = jnp.zeros((B, DN_CONV - 1, DN_CONV_DIM), qkv_raw.dtype)
    if s0 is None:
        s0 = jnp.zeros((B, DN_HEADS, DN_DK, DN_DV), qkv_raw.dtype)
    u, new_buf = _short_conv(qkv_raw, conv_buf, conv_w)
    q, k, v = _split(u, (DN_HEADS * DN_DK, DN_HEADS * DN_DK, DN_HEADS * DN_DV))
    q = _l2norm(q.reshape(B, L, DN_HEADS, DN_DK)) * DN_DK ** -0.5
    k = _l2norm(k.reshape(B, L, DN_HEADS, DN_DK))
    v = v.reshape(B, L, DN_HEADS, DN_DV)
    beta = jax.nn.sigmoid(b_raw.astype(f32))
    g = -jnp.exp(a_log.astype(f32)) * jax.nn.softplus(a_raw.astype(f32) + dt_bias.astype(f32))
    o, s_new = _gated_delta(q, k, v, beta, g, s0)
    return _gated_rmsnorm(o, gate_raw, norm_w), new_buf, s_new

def _hgrn2_mixer(q_raw, f_raw, i_raw, gate_raw, s0, lb, norm_w):
    B, L, _ = q_raw.shape
    if s0 is None:
        s0 = jnp.zeros((B, HG_HEADS, HG_DK, HG_DV), q_raw.dtype)
    q = q_raw.reshape(B, L, HG_HEADS, HG_DK) * HG_DK ** -0.5
    f = lb + (1.0 - lb) * jax.nn.sigmoid(f_raw.astype(jnp.float32))
    logf = jnp.log(f).reshape(B, L, HG_HEADS, HG_DK)
    k = (1.0 - f).reshape(B, L, HG_HEADS, HG_DK)
    v = i_raw.reshape(B, L, HG_HEADS, HG_DV)
    o, s_new = _gla_scan(q, k, v, logf, s0)
    return _gated_rmsnorm(o, gate_raw, norm_w), s_new

def _moe(x, w_router, router_bias, wg, wu, wd):
    f32 = jnp.float32
    N, D = x.shape
    scores = jax.nn.sigmoid((x @ w_router).astype(f32))
    biased = scores + router_bias.astype(f32)
    grp = lax.top_k(biased.reshape(N, N_EXPERT_GROUPS, EXPERTS_PER_GROUP), TOP_K)[0].sum(-1)
    gsel = jnp.argmax(grp, -1)
    in_grp = (jnp.arange(N_EXPERTS) // EXPERTS_PER_GROUP)[None, :] == gsel[:, None]
    _, eidx = lax.top_k(jnp.where(in_grp, biased, -jnp.inf), TOP_K)
    gw = jnp.take_along_axis(scores, eidx, -1)
    gw = gw / gw.sum(-1, keepdims=True)
    n_assign = N * TOP_K
    e_flat = eidx.reshape(-1)
    order = jnp.argsort(e_flat)
    e_sorted = e_flat[order]
    counts = jnp.bincount(e_flat, length=N_EXPERTS)
    padded = (counts + MOE_ROW_BLOCK - 1) // MOE_ROW_BLOCK * MOE_ROW_BLOCK
    pad_end = jnp.cumsum(padded)
    dest = (pad_end - padded)[e_sorted] + jnp.arange(n_assign) - (jnp.cumsum(counts) - counts)[e_sorted]
    n_blocks = -(-n_assign // MOE_ROW_BLOCK) + N_EXPERTS
    n_rows = n_blocks * MOE_ROW_BLOCK
    tok = jnp.full((n_rows,), N, jnp.int32).at[dest].set((order // TOP_K).astype(jnp.int32))
    wt = jnp.zeros((n_rows,), f32).at[dest].set(gw.reshape(-1)[order])
    blk_exp = jnp.minimum(jnp.searchsorted(pad_end, jnp.arange(n_blocks) * MOE_ROW_BLOCK, side='right'),
                          N_EXPERTS - 1)
    x_pad = jnp.concatenate([x, jnp.zeros((1, D), x.dtype)])

    def expert_block(args):
        e, tk, w = args
        h = x_pad[tk]
        a = jax.nn.silu(h @ wg[e]) * (h @ wu[e])
        return ((a @ wd[e]) * w[:, None]).astype(x.dtype)

    out = lax.map(expert_block, (blk_exp, tok.reshape(n_blocks, MOE_ROW_BLOCK),
                                 wt.reshape(n_blocks, MOE_ROW_BLOCK)))
    y = jnp.zeros((N + 1, D), x.dtype).at[tok].add(out.reshape(n_rows, D))
    return y[:N]

def _trunk_layer(x, ple, lb, past, w_in, w_cmp1, w_cmp2, pe_cmp, dn_conv_w, dn_a_log, dn_dt_bias,
                 dn_norm_w, hg_norm_w, w_branch, w_out, ln1_g, ln1_b, ln2_g, ln2_b, w_router,
                 router_bias, w_exp_gate, w_exp_up, w_exp_down, w_ple, w_ple_gate, rel_bias):
    past_rows, win_buf, conv_buf, dn_state, hg_state = past
    B, L, D = x.shape
    (nsa_q, nsa_kv, nsa_g, dn_qkv, dn_a, dn_b, dn_g,
     hg_q, hg_f, hg_i, hg_g, merge) = _split(x @ w_in, IN_SPLITS)
    o_a, rows_new, win_new = _nsa_mixer(nsa_q, nsa_kv, nsa_g, past_rows, win_buf, w_cmp1, w_cmp2, pe_cmp, rel_bias)
    o_b, conv_new, dn_new = _deltanet_mixer(dn_qkv, dn_a, dn_b, dn_g, conv_buf, dn_state, dn_conv_w,
                                            dn_a_log, dn_dt_bias, dn_norm_w)
    o_c, hg_new = _hgrn2_mixer(hg_q, hg_f, hg_i, hg_g, hg_state, lb, hg_norm_w)
    g = jax.nn.sigmoid(merge).reshape(B, L, 3, D)
    m = (g[:, :, 0] * (o_a @ w_branch[0]) + g[:, :, 1] * (o_b @ w_branch[1])
         + g[:, :, 2] * (o_c @ w_branch[2]))
    x = _layer_norm(DEEPNORM_ALPHA * x + m @ w_out, ln1_g, ln1_b)
    ffn = _moe(x.reshape(B * L, D), w_router, router_bias, w_exp_gate, w_exp_up, w_exp_down).reshape(B, L, D)
    ple_term = (ple @ w_ple) * jax.nn.sigmoid(x @ w_ple_gate)
    x = _layer_norm(DEEPNORM_ALPHA * x + ffn + ple_term, ln2_g, ln2_b)
    return x, (rows_new, win_new, conv_new, dn_new, hg_new)

def _stack_layers(states, i):
    return jnp.stack([s[i] for s in states])

def setup_inputs(seed: int = 0) -> dict:
    key = jax.random.key(seed)
    k = jax.random.split(key, 40)
    f32 = jnp.float32

    def nrm(i, shape, scale):
        return jax.random.normal(k[i], shape, f32) * scale

    n_pages = PAST_LEN // PAGE_SIZE
    n_used = DEC_BATCH * n_pages
    n_pool = n_used + max(n_used // 4, 1)
    win_len = min(WINDOW, PAST_LEN)
    page_table = jax.random.permutation(k[7], n_pool)[:n_used].reshape(DEC_BATCH, n_pages).astype(jnp.int32)
    a_log = jnp.log(jax.random.uniform(k[14], (DEPTH, DN_HEADS), f32, 1.0, 16.0))
    dt = jnp.exp(jax.random.uniform(k[15], (DEPTH, DN_HEADS), f32, math.log(1e-3), math.log(1e-1)))
    dt_bias = dt + jnp.log(-jnp.expm1(-dt))
    return {
        'x_prompt': nrm(0, (BATCH, SEQ, D_MODEL), 1.0),
        'x_sample': nrm(1, (DEC_BATCH, DEC_SEQ, D_MODEL), 1.0),
        'cache_nsa': nrm(2, (DEPTH, n_pool, PAGE_SIZE, N_CACHE_STREAMS, NSA_KV, NSA_DH), 1.0),
        'state_win': nrm(3, (DEPTH, DEC_BATCH, win_len, 2, NSA_KV, NSA_DH), 1.0),
        'state_dn_conv': nrm(4, (DEPTH, DEC_BATCH, DN_CONV - 1, DN_CONV_DIM), 1.0),
        'state_dn': nrm(5, (DEPTH, DEC_BATCH, DN_HEADS, DN_DK, DN_DV), 0.3),
        'state_hg': nrm(6, (DEPTH, DEC_BATCH, HG_HEADS, HG_DK, HG_DV), 0.3),
        'page_table': page_table,
        'p_prompt': nrm(8, (DEPTH, BATCH, SEQ, D_PLE), 1.0),
        'p_sample': nrm(9, (DEPTH, DEC_BATCH, DEC_SEQ, D_PLE), 1.0),
        'w_in': nrm(10, (DEPTH, D_MODEL, D_IN), D_MODEL ** -0.5),
        'w_cmp1': nrm(11, (DEPTH, 2, CMP_BLOCK * NSA_DH, CMP_HID), (CMP_BLOCK * NSA_DH) ** -0.5),
        'w_cmp2': nrm(12, (DEPTH, 2, CMP_HID, NSA_DH), CMP_HID ** -0.5),
        'pe_cmp': nrm(13, (DEPTH, 2, CMP_BLOCK, NSA_DH), 0.1),
        'dn_conv_w': nrm(16, (DEPTH, DN_CONV, DN_CONV_DIM), 0.5),
        'dn_a_log': a_log,
        'dn_dt_bias': dt_bias,
        'dn_norm_w': 1.0 + nrm(17, (DEPTH, DN_DV), 0.01),
        'hg_lb_logits': nrm(18, (DEPTH, HG_HEADS * HG_DK), 0.3),
        'hg_norm_w': 1.0 + nrm(19, (DEPTH, HG_DV), 0.01),
        'w_branch': nrm(20, (DEPTH, 3, BRANCH_WIDTH, D_MODEL), BRANCH_WIDTH ** -0.5 * DEEPNORM_BETA),
        'w_out': nrm(21, (DEPTH, D_MODEL, D_MODEL), D_MODEL ** -0.5 * DEEPNORM_BETA),
        'ln1_g': 1.0 + nrm(22, (DEPTH, D_MODEL), 0.01),
        'ln1_b': nrm(23, (DEPTH, D_MODEL), 0.01),
        'ln2_g': 1.0 + nrm(24, (DEPTH, D_MODEL), 0.01),
        'ln2_b': nrm(25, (DEPTH, D_MODEL), 0.01),
        'w_router': nrm(26, (D_MODEL, N_EXPERTS), D_MODEL ** -0.5),
        'router_bias': nrm(27, (N_EXPERTS,), 0.01),
        'w_exp_gate': nrm(28, (DEPTH, N_EXPERTS, D_MODEL, D_EXPERT), D_MODEL ** -0.5),
        'w_exp_up': nrm(29, (DEPTH, N_EXPERTS, D_MODEL, D_EXPERT), D_MODEL ** -0.5),
        'w_exp_down': nrm(30, (DEPTH, N_EXPERTS, D_EXPERT, D_MODEL), D_EXPERT ** -0.5 * DEEPNORM_BETA),
        'w_ple': nrm(31, (DEPTH, D_PLE, D_MODEL), D_PLE ** -0.5 * DEEPNORM_BETA),
        'w_ple_gate': nrm(32, (DEPTH, D_MODEL, D_MODEL), D_MODEL ** -0.5),
        'rel_bias': nrm(33, (N_BUCKETS, NSA_HEADS), 0.5),
    }

def reference(x_prompt, x_sample, cache_nsa, state_win, state_dn_conv, state_dn, state_hg, page_table,
              p_prompt, p_sample, w_in, w_cmp1, w_cmp2, pe_cmp, dn_conv_w, dn_a_log, dn_dt_bias, dn_norm_w,
              hg_lb_logits, hg_norm_w, w_branch, w_out, ln1_g, ln1_b, ln2_g, ln2_b, w_router, router_bias,
              w_exp_gate, w_exp_up, w_exp_down, w_ple, w_ple_gate, rel_bias):
    lb = jnp.cumsum(jax.nn.softmax(hg_lb_logits.astype(jnp.float32), axis=0), axis=0)
    lb = lb - lb[0:1]
    n_dec = page_table.shape[0]
    y_prompt, y_sample = x_prompt, x_sample
    st_p, st_s = [], []
    for l in range(DEPTH):
        lw = (w_in[l], w_cmp1[l], w_cmp2[l], pe_cmp[l], dn_conv_w[l], dn_a_log[l], dn_dt_bias[l],
              dn_norm_w[l], hg_norm_w[l], w_branch[l], w_out[l], ln1_g[l], ln1_b[l], ln2_g[l], ln2_b[l],
              w_router, router_bias, w_exp_gate[l], w_exp_up[l], w_exp_down[l], w_ple[l], w_ple_gate[l],
              rel_bias)
        y_prompt, s = _trunk_layer(y_prompt, p_prompt[l], lb[l], (None, None, None, None, None), *lw)
        st_p.append(s)
        past_rows = cache_nsa[l][page_table].reshape(n_dec, -1, N_CACHE_STREAMS, NSA_KV, NSA_DH)
        y_sample, s = _trunk_layer(y_sample, p_sample[l], lb[l],
                                   (past_rows, state_win[l], state_dn_conv[l], state_dn[l], state_hg[l]), *lw)
        st_s.append(s)
    nsa_rows_prompt = _stack_layers(st_p, 0)
    nsa_rows_sample = _stack_layers(st_s, 0)
    win_prompt = _stack_layers(st_p, 1)
    win_sample = _stack_layers(st_s, 1)
    conv_prompt = _stack_layers(st_p, 2)
    conv_sample = _stack_layers(st_s, 2)
    dn_prompt = _stack_layers(st_p, 3)
    dn_sample = _stack_layers(st_s, 3)
    hg_prompt = _stack_layers(st_p, 4)
    hg_sample = _stack_layers(st_s, 4)
    return (y_prompt, y_sample, nsa_rows_prompt, nsa_rows_sample, win_prompt, win_sample,
            conv_prompt, conv_sample, dn_prompt, dn_sample, hg_prompt, hg_sample)


_drawn_inputs = setup_inputs


def setup_inputs(seed=0):
    import zlib

    import numpy as np

    out = dict(_drawn_inputs(seed))
    spreads = {}
    factors = {'cache_nsa': 6.632,
     'pe_cmp': 4.183,
     'dn_norm_w': 4.735,
     'hg_norm_w': 5.037,
     'ln2_g': 5.644,
     'ln2_b': 5.61}
    for name, (base, spread) in spreads.items():
        noise = np.random.default_rng([zlib.crc32(name.encode()), seed]).standard_normal(out[name].shape)
        drawn = base * np.exp(spread * noise) if base else spread * noise
        out[name] = jnp.asarray(drawn.astype(out[name].dtype))
    for name, factor in factors.items():
        out[name] = (out[name] * factor).astype(out[name].dtype)
    return out
```

```python
from contextlib import ExitStack

import concourse.bass as bass
import numpy as np
from concourse import mybir

F32 = mybir.dt.float32
I32 = mybir.dt.int32
U32 = mybir.dt.uint32
ALU = mybir.AluOpType
ACT = mybir.ActivationFunctionType
AX = mybir.AxisListType

P = 128
D = 1024
KT = D // P
TP = 1024
NB = 8
T = TP + NB
NW = 3
W = T // NW
BLK = 128
NBLK = TP // BLK
DH = 64
GR = 4
G = 2
NH = G * GR
PAST = 1024
PAGES = PAST // P
NPOOL = 80
WIN = 512
STR = 16
NCMP = TP // STR - 1
SELB = 64
NSB = 17
NBUCK = 32
LSEL = 1280
LWIN = 768
NEG = -1e30
H4 = 4
LEV = 7
NE = 16
TOPK = 2
EB = (TOPK * T + NE * (P - 1)) // P
DE = 512
ALPHA = 2 ** 0.25
EPS = 1e-6
NTT = NBLK + 1


def mid(ap, n):
    return ap.unsqueeze(1).to_broadcast([ap.shape[0], n, ap.shape[1]])


def last(ap, n):
    return ap.unsqueeze(2).to_broadcast([ap.shape[0], ap.shape[1], n])


class Link:

    def __init__(self, eng, sem):
        self.eng, self.sem, self.n = eng, sem, 0

    def __call__(self, ins):
        self.n += 1
        ins.then_inc(self.sem, 1)
        self.eng.wait_ge(self.sem, self.n)


class Semaphores(dict):

    def __init__(self, core, stage):
        self.core, self.stage = core, stage

    def __missing__(self, name):
        self[name] = self.core.sem(f"{self.stage}_{name}")
        return self[name]


class Core:

    def __init__(self, nc, dram):
        self.nc = nc
        self.dram = dram
        self.ps = nc.alloc_psum_tensor("ps", [P, 8, 512], F32)

        self.held = []

    def sem(self, name):
        self.held.append(self.nc.alloc_semaphore(name))
        return self.held[-1]

    def retire(self):
        self.nc.all_engine_barrier()
        self.nc.clear_and_free_semaphores(self.held)
        self.nc.all_engine_barrier()
        self.held = []


class Routing:

    def __init__(self, nc):
        self.dest = nc.alloc_sbuf_tensor("rt_dest", [P, TOPK, NTT], U32)
        self.wt = nc.alloc_sbuf_tensor("rt_wt", [P, TOPK, NTT], F32)
        self.plan = nc.alloc_sbuf_tensor("rt_plan", [1, EB + 1], I32)


def project(c, name, wt, ntiles, dst):
    nc, ps, xT = c.nc, c.ps, c.xT
    w_here = [c.sem(f"{name}_w_here{j}") for j in range(2)]
    z_ready = c.sem(f"{name}_z_ready")
    z_copied = c.sem(f"{name}_z_copied")
    assert ntiles % 2 == 0
    with nc.sbuf_tensor(f"{name}_w", [P, 2, KT, P], F32) as wb, nc.Block() as block:
        @block.sync
        def _(sp):
            with sp.Fori(0, ntiles // 2) as i:
                for j in range(2):
                    sp.wait_ge(z_ready, 2 * i + j + 1)
                    sp.dma_start(wb[:, j], wt[2 * i + j]).then_inc(w_here[j], 16)

        @block.tensor
        def _(pe):
            pe.sem_inc(z_ready, 2)
            with pe.Fori(0, ntiles // 2) as i:
                for j in range(2):
                    pe.wait_ge(w_here[j], 16 * i + 16)
                    pe.wait_ge(z_copied, 2 * i + j + 1)
                    for n in range(NW):
                        for k in range(KT):
                            mm = pe.matmul(ps[:, 3 * j + n, 0:W], wb[:, j, k, :], xT[:, k, n * W:(n + 1) * W],
                                           start=(k == 0), stop=(k == KT - 1))
                    mm.then_inc(z_ready, 1)

        @block.scalar
        def _(act):
            act.sem_inc(z_copied, 2)
            with act.Fori(0, ntiles // 2) as i:
                for j in range(2):
                    act.wait_ge(z_ready, 2 * i + j + 3)
                    act.activation(dst[:, 2 * i + j, :].rearrange("p (n w) -> p n w", n=NW),
                                   ps[:, 3 * j:3 * j + NW, 0:W], ACT.Copy).then_inc(z_copied, 1)


def load_shared(c):
    nc, dr = c.nc, c.dram
    loaded = c.sem("shared_loaded")
    with nc.Block() as block:
        @block.sync
        def _(sp):
            sp.dma_start(c.xT[:], dr["xT"]).then_inc(loaded, 16)
            sp.dma_start(c.ident[:], dr["ident"]).then_inc(loaded, 16)
            sp.wait_ge(loaded, 32)

        @block.vector
        def _(dve):
            dve.memset(c.ones[:], 1.0)
            dve.memset(c.eps[:], EPS)


def small_projection(c, name, dst):
    nc, ps, xT = c.nc, c.ps, c.xT
    w_here, z_ready = c.sem(f"{name}_w_here"), c.sem(f"{name}_z_ready")
    with nc.sbuf_tensor(f"{name}_w", [P, KT, 96], F32) as wb, nc.Block() as block:
        @block.sync
        def _(sp):
            sp.dma_start(wb[:], c.dram["w_small"]).then_inc(w_here, 16)

        @block.tensor
        def _(pe):
            pe.wait_ge(w_here, 16)
            for n in range(NW):
                for k in range(KT):
                    mm = pe.matmul(ps[0:96, n, 0:W], wb[:, k, :], xT[:, k, n * W:(n + 1) * W],
                                   start=(k == 0), stop=(k == KT - 1))
            mm.then_inc(z_ready, 1)

        @block.scalar
        def _(act):
            act.wait_ge(z_ready, 1)
            act.activation(dst[:].rearrange("p (n w) -> p n w", n=NW), ps[0:96, 0:NW, 0:W], ACT.Copy)


def nsa_prepare(c, q, kv, small):
    nc, ps, dr = c.nc, c.ps, c.dram
    s = Semaphores(c, "prep")
    with ExitStack() as ctx:
        rb = ctx.enter_context(nc.sbuf_tensor("prep_rb", [33, NH], F32))
        hot = ctx.enter_context(nc.sbuf_tensor("prep_hot", [33, LSEL + LWIN], F32))
        bv = ctx.enter_context(nc.sbuf_tensor("prep_bv", [NH, LSEL + LWIN], F32))
        block = ctx.enter_context(nc.Block())

        @block.sync
        def _(sp):
            sp.dma_start(rb[:], dr["rb_aug"]).then_inc(s["in"], 16)
            sp.dma_start(hot[:], dr["hot"]).then_inc(s["in"], 16)
            sp.dma_start(dr["o_kvT"], kv).then_inc(s["out"], 16)
            sp.wait_ge(s["gate"], 1)
            sp.dma_start(dr["s_gate"], small[0:24, TP:T]).then_inc(s["out"], 16)
            sp.wait_ge(s["biasc"], 1)
            sp.dma_start(dr["s_bias"], bv[:].unsqueeze(1).to_broadcast([NH, P, LSEL + LWIN])).then_inc(s["out"], 16)
            sp.wait_ge(s["out"], 48)

        @block.tensor
        def _(pe):
            pe.wait_ge(s["gate"], 1)
            for i in range(NBLK):
                t = pe.transpose(ps[:, 4, 32 * i:32 * i + 24], small[0:24, i * BLK:(i + 1) * BLK], c.ident[0:24, 0:24])
            t.then_inc(s["gt"], 1)
            pe.wait_ge(s["in"], 32)
            for n in range(4):
                mm = pe.matmul(ps[0:NH, n, :], rb[:], hot[:, 512 * n:512 * n + 512], start=True, stop=True)
            mm.then_inc(s["bias"], 1)

        @block.scalar
        def _(act):
            act.activation(small[0:24, :], small[0:24, :], ACT.Sigmoid).then_inc(s["gate"], 1)

        @block.vector
        def _(dve):
            dve.tensor_scalar(q, q, DH ** -0.5, None, ALU.mult)
            dve.wait_ge(s["gt"], 1)
            dve.tensor_copy(c.gtok[:], ps[:, 4, 0:256].rearrange("p (i h) -> p i h", h=32)[:, :, 0:24])
            dve.wait_ge(s["bias"], 1)
            dve.tensor_copy(bv[:].rearrange("p (n w) -> p n w", n=4), ps[0:NH, 0:4, :]).then_inc(s["biasc"], 1)


def nsa_samples_scores(c, q, kv, Ss, kc, vc):
    nc, ps, dr = c.nc, c.ps, c.dram
    s = Semaphores(c, "ns")
    HB = NB // 2
    with ExitStack() as ctx:
        sb = lambda n, sh, dt=F32: ctx.enter_context(nc.sbuf_tensor(f"ns_{n}", sh, dt))
        tab = sb("tab", [1, NB * PAGES], I32)
        w1 = sb("w1", [P, 2, 32, P])
        w2 = sb("w2", [P, 2, DH])
        pe_ = sb("pe", [DH, 2, 32])
        peb = sb("peb", [P, 2])
        cmpT = c.outs[:].rearrange("p m t -> p (m t)")[:, GR * T:GR * T + 2 * HB * PAST].rearrange("p (s b t) -> p s b t", s=2, b=HB)
        pg = sb("pg", [P, 4, 3 * P])
        kT = sb("kT", [P, 2, PAST])
        hid = sb("hid", [P, 2, HB * NCMP])
        qz = sb("qz", [P, NB * (SELB + NB)])
        block = ctx.enter_context(nc.Block())
        cache = dr["cache"]
        tiles = [(b, p) for b in range(NB) for p in range(PAGES)]
        WT = 4

        @block.sync
        def _(sp):
            sp.dma_start(tab[:], dr["table"]).then_inc(s["tab"], 16)
            for h in range(2):
                sp.dma_start(w1[h * DH:(h + 1) * DH], dr["w_cmp1"]).then_inc(s["w"], 16)
            sp.dma_start(w2[:], dr["w_cmp2"]).then_inc(s["w"], 16)
            sp.dma_start(pe_[:], dr["pe_cmp"]).then_inc(s["w"], 16)
            sp.wait_ge(s["tab"], 16)
            n = 0
            for b in range(NB):
                for p in range(PAGES):
                    if n >= 4:
                        sp.wait_ge(s["turned"], n - 3)
                    v = sp.value_load(tab[0:1, b * PAGES + p:b * PAGES + p + 1], min_val=0, max_val=NPOOL - 1)
                    sp.dma_start(pg[:, n % 4, :], cache[bass.ds(v, 1), :, 0:3 * P].rearrange("o t f -> t (o f)")).then_inc(s[f"pg{n % 4}"], 16)
                    n += 1

        @block.tensor
        def _(pe):
            pe.wait_ge(s["w"], 64)
            for st in range(2):
                for t in range(32):
                    mm = pe.matmul(ps[:, 7, st:st + 1], w1[0:DH, st, t, :], pe_[:, st, t:t + 1], start=(t == 0), stop=(t == 31))
            mm.then_inc(s["peb"], 1)

            def compress(st, g, src, nseq, dst_bank):
                r = slice(g * DH, (g + 1) * DH)
                for t in range(32):
                    lo = t // STR
                    mv = src[r].rearrange("p b (k s) -> p b k s", s=STR)[:, :, lo:lo + NCMP, t % STR]
                    mm = pe.matmul(ps[:, dst_bank, 0:nseq * NCMP], w1[r, st, t, :], mv, start=(t == 0), stop=(t == 31))
                mm.then_inc(s["lo"], 1)

            def second(n, st, g, q0, nseq):
                pe.wait_ge(s["hid"], n + 1)
                if n >= 1:
                    pe.wait_ge(s["h2c"], n)
                if st == 0:
                    mm = pe.matmul(ps[g * DH:(g + 1) * DH, 6, 0:nseq * NCMP], w2[:, 0, :], hid[:, n % 2, 0:nseq * NCMP], start=True, stop=True)
                else:
                    for b in range(nseq):
                        mm = pe.matmul(ps[0:NCMP, 6, b * DH:(b + 1) * DH], hid[:, n % 2, b * NCMP:(b + 1) * NCMP], w2[:, 1, :], start=True, stop=True)
                mm.then_inc(s["h2"], 1)

            n = 0
            pe.wait_ge(s["pebc"], 1)
            for st in range(2):
                for g in range(G):
                    if n >= 2:
                        pe.wait_ge(s["hid"], n - 1)
                    compress(st, g, kv[:, st:st + 1, 0:TP], 1, 4 + n % 2)
                    second(n, st, g, NB, 1)
                    n += 1
            tn = 0
            for b in range(NB):
                if b >= 1:
                    pe.wait_ge(s["scored"], b)
                for p in range(PAGES):
                    pe.wait_ge(s[f"pg{tn % 4}"], 16 * (tn // 4 + 1))
                    if tn >= 2:
                        pe.wait_ge(s["turncopied"], tn - 1)
                    if p == 0 and b % HB == 0 and b > 0:
                        pe.wait_ge(s["h2"], 8)
                    for st in range(3):
                        t = pe.transpose(ps[:, 4 + tn % 2, st * P:(st + 1) * P], pg[:, tn % 4, st * P:(st + 1) * P], c.ident[:])
                    t.then_inc(s["turned"], 1)
                    tn += 1
                pe.wait_ge(s["qz"], 1)
                pe.wait_ge(s["turncopied"], tn)
                for h in range(2):
                    mm = pe.matmul(ps[0:64, h, :], qz[:, b * 64:(b + 1) * 64], kT[:, b % 2, h * 512:(h + 1) * 512], start=(b == 0), stop=(b == NB - 1))
                mm.then_inc(s["scored"], 1)
                if b % HB == HB - 1:
                    for st in range(2):
                        for g in range(G):
                            pe.wait_ge(s["hid"], n - 1)
                            compress(st, g, cmpT[:, st], HB, 4 + n % 2)
                            second(n, st, g, b - HB + 1, HB)
                            n += 1

        @block.scalar
        def _(act):
            act.wait_ge(s["pebc"], 1)

            def hidden(n, nseq):
                act.wait_ge(s["lo"], n + 1)
                if n >= 2:
                    act.wait_ge(s["h2"], n - 1)
                st = (n // 2) % 2
                act.activation(hid[:, n % 2, 0:nseq * NCMP], ps[:, 4 + n % 2, 0:nseq * NCMP], ACT.Silu, bias=peb[:, st:st + 1]).then_inc(s["hid"], 1)

            for n in range(4):
                hidden(n, 1)
            for b in range(NB):
                if b % HB == HB - 1:
                    for k in range(4):
                        hidden(4 + (b // HB) * 4 + k, HB)

        @block.vector
        def _(dve):
            link = Link(dve, s["link"])
            link(dve.memset(qz[:], 0.0))
            for g in range(G):
                r = slice(g * DH, (g + 1) * DH)
                z = dve.tensor_copy(qz[r].rearrange("p (b x) -> p b x", x=SELB + NB)[:, :, g * GR:(g + 1) * GR],
                                    q[r, :, TP:T].rearrange("p j b -> p b j"))
            z.then_inc(s["qz"], 1)
            dve.wait_ge(s["peb"], 1)
            dve.tensor_copy(peb[:], ps[:, 7, 0:2]).then_inc(s["pebc"], 1)

            def second(n, st, g, q0, nseq):
                dve.wait_ge(s["h2"], n + 1)
                r = slice(g * DH, (g + 1) * DH)
                if st == 0:
                    o = dve.tensor_copy(kc[r, q0:q0 + nseq, :], ps[r, 6, 0:nseq * NCMP].rearrange("p (b k) -> p b k", b=nseq))
                else:
                    o = dve.tensor_copy(vc[:, q0:q0 + nseq, r], ps[0:NCMP, 6, 0:nseq * DH].rearrange("p (b k) -> p b k", b=nseq))
                o.then_inc(s["h2c"], 1)

            n = 0
            for st in range(2):
                for g in range(G):
                    second(n, st, g, NB, 1)
                    n += 1
            tn = 0
            for b in range(NB):
                for p in range(PAGES):
                    dve.wait_ge(s["turned"], tn + 1)
                    if p == 0 and b >= 2:
                        dve.wait_ge(s["scored"], b - 1)
                    dve.tensor_copy(cmpT[:, :, b % HB, p * P:(p + 1) * P], ps[:, 4 + tn % 2, 0:2 * P].rearrange("p (s t) -> p s t", s=2))
                    dve.tensor_copy(kT[:, b % 2, p * P:(p + 1) * P], ps[:, 4 + tn % 2, 2 * P:3 * P]).then_inc(s["turncopied"], 1)
                    tn += 1
                if b % HB == HB - 1:
                    for st in range(2):
                        for g in range(G):
                            second(n, st, g, b - HB + 1, HB)
                            n += 1
            dve.wait_ge(s["scored"], NB)
            dve.tensor_copy(Ss[:, 0:PAST].rearrange("p (h k) -> p h k", h=2), ps[0:64, 0:2, :])
    
    s2 = Semaphores(c, "nw")
    with ExitStack() as ctx:
        sb = lambda n, sh, dt=F32: ctx.enter_context(nc.sbuf_tensor(f"nw_{n}", sh, dt))
        wk = sb("wk", [P, 2, 4, P])
        wT = sb("wT", [P, 2, WIN])
        qz = sb("qz", [P, NB * (SELB + NB)])
        block = ctx.enter_context(nc.Block())

        @block.sync
        def _(sp):
            for b in range(NB):
                if b >= 2:
                    sp.wait_ge(s2["turned"], b - 1)
                sp.dma_start(wk[:, b % 2], dr["state_win"][b].rearrange("(n p) f -> p n f", p=P)[:, :, 0:P]).then_inc(s2[f"in{b % 2}"], 16)

        @block.tensor
        def _(pe):
            pe.wait_ge(s2["qz"], 1)
            for b in range(NB):
                pe.wait_ge(s2[f"in{b % 2}"], 16 * (b // 2 + 1))
                if b >= 2:
                    pe.wait_ge(s2["copied"], b - 1)
                for n in range(4):
                    t = pe.transpose(ps[:, 4 + b % 2, n * P:(n + 1) * P], wk[:, b % 2, n, :], c.ident[:])
                t.then_inc(s2["turned"], 1)
                pe.wait_ge(s2["copied"], b + 1)
                pe.matmul(ps[0:64, 2, :], qz[:, b * 64:(b + 1) * 64], wT[:, b % 2, :], start=(b == 0), stop=(b == NB - 1)).then_inc(s2["scored"], 1)
            for b in range(NB):
                pe.matmul(ps[0:64, 3, 0:NCMP], qz[:, b * 64:(b + 1) * 64], kc[:, b, :], start=(b == 0), stop=(b == NB - 1))
            for k, st in enumerate((2, 4)):
                for b in range(NB):
                    mm = pe.matmul(ps[0:64, 3, 64 + 8 * k:72 + 8 * k], qz[:, b * 64:(b + 1) * 64], kv[:, st, TP:T], start=(b == 0), stop=(b == NB - 1))
            mm.then_inc(s2["cmp"], 1)

        @block.vector
        def _(dve):
            link = Link(dve, s2["link"])
            link(dve.memset(qz[:], 0.0))
            for g in range(G):
                r = slice(g * DH, (g + 1) * DH)
                z = dve.tensor_copy(qz[r].rearrange("p (b x) -> p b x", x=SELB + NB)[:, :, g * GR:(g + 1) * GR],
                                    q[r, :, TP:T].rearrange("p j b -> p b j"))
            z.then_inc(s2["qz"], 1)
            for b in range(NB):
                dve.wait_ge(s2["turned"], b + 1)
                if b >= 2:
                    dve.wait_ge(s2["scored"], b - 1)
                dve.tensor_copy(wT[:, b % 2, :], ps[:, 4 + b % 2, :]).then_inc(s2["copied"], 1)
            dve.wait_ge(s2["scored"], NB)
            dve.tensor_copy(Ss[:, SO_WIN:SO_WIN + WIN], ps[0:64, 2, :])
            dve.wait_ge(s2["cmp"], 1)
            dve.tensor_copy(Ss[:, SO_NSEL:SO_NSEL + NB], ps[0:64, 3, 64:72])
            dve.tensor_copy(Ss[:, SO_NWIN:SO_NWIN + NB], ps[0:64, 3, 72:80])
            dve.tensor_copy(Ss[:, SO_CMP:SO_CMP + NCMP], ps[0:64, 3, 0:NCMP])


SO_NSEL = PAST
SO_WIN = SO_NSEL + NB
SO_NWIN = SO_WIN + WIN
SO_CMP = SO_NWIN + NB
SO_END = SO_CMP + NCMP + 1


def nsa_samples_finish(c, kv, Ss, vc):
    nc, ps, dr = c.nc, c.ps, c.dram
    s = Semaphores(c, "nf")
    BR = ((0, SO_WIN), (SO_WIN, SO_CMP), (SO_CMP, SO_CMP + NCMP))
    with ExitStack() as ctx:
        sb = lambda n, sh, dt=F32: ctx.enter_context(nc.sbuf_tensor(f"nf_{n}", sh, dt))
        tab = sb("tab", [1, NB * PAGES], I32)
        vs = sb("vs", [P, NB * PAGES, P])
        vw = sb("vw", [P, NB, 4, P])
        vn = sb("vn", [NB, 2, P])
        bs = sb("bs", [64, PAST + 1])
        bw = sb("bw", [64, WIN + 1])
        own = sb("own", [64, NB])
        gs = sb("gs", [64, 3])
        imap = sb("imap", [NCMP, NSB])
        grp = sb("grp", [64, 64])
        idx = sb("idx", [64, NSB])
        sm = sb("sm", [64, 16])
        ec = sb("ec", [64, NCMP])
        ecT = sb("ecT", [NCMP, 64])
        imp = sb("imp", [64, NSB])
        eq = sb("eq", [64, NSB])
        dm = sb("dm", [64, 16])
        pt = sb("pt", [P, 15, 64])
        block = ctx.enter_context(nc.Block())

        @block.sync
        def _(sp):
            sp.dma_start(tab[:], dr["table"]).then_inc(s["tab"], 16)
            for b in range(NB):
                r = slice(b * NH, (b + 1) * NH)
                sp.dma_start(bs[r], dr["s_bias"][:, 0, P - 1:P + PAST]).then_inc(s["in"], 16)
                sp.dma_start(bw[r], dr["s_bias"][:, 0, LSEL + P - 1:LSEL + P + WIN]).then_inc(s["in"], 16)
                sp.dma_start(gs[r], dr["s_gate"].rearrange("(h r) b -> b h r", r=3)[b], allow_slow_non_contiguous=True).then_inc(s["in"], 16)
            for t, n in ((own, "own"), (imap, "imap"), (grp, "grp"), (idx, "idx")):
                sp.dma_start(t[:], dr[n]).then_inc(s["in"], 16)
            sp.wait_ge(s["tab"], 16)
            for n in range(NB * PAGES):
                v = sp.value_load(tab[0:1, n:n + 1], min_val=0, max_val=NPOOL - 1)
                sp.dma_start(vs[:, n, :], dr["cache"][bass.ds(v, 1), :, 3 * P:4 * P].rearrange("o t f -> t (o f)")).then_inc(s["v"], 16)
            for b in range(NB):
                sp.dma_start(vw[:, b], dr["state_win"][b].rearrange("(n p) f -> p n f", p=P)[:, :, P:2 * P]).then_inc(s["v"], 16)

        @block.vector
        def _(dve):
            link = Link(dve, s["link"])
            dve.wait_ge(s["in"], 16 * (3 * NB + 4))
            dve.tensor_tensor(Ss[:, 0:PAST], Ss[:, 0:PAST], bs[:, 0:PAST], ALU.add)
            dve.tensor_tensor(Ss[:, SO_WIN:SO_NWIN], Ss[:, SO_WIN:SO_NWIN], bw[:, 0:WIN], ALU.add)
            dve.scalar_tensor_tensor(Ss[:, SO_NSEL:SO_WIN], Ss[:, SO_NSEL:SO_WIN], bs[:, PAST:PAST + 1], own[:], ALU.add, ALU.add)
            dve.scalar_tensor_tensor(Ss[:, SO_NWIN:SO_CMP], Ss[:, SO_NWIN:SO_CMP], bw[:, WIN:WIN + 1], own[:], ALU.add, ALU.add)
            cs = slice(*BR[2])
            link(dve.tensor_tensor(Ss[:, cs], Ss[:, cs], bs[:, 31:31 + STR * (NCMP - 1) + 1:STR], ALU.add))
            link(dve.tensor_reduce(sm[:, 0:1], Ss[:, cs], AX.X, ALU.max))
            dve.tensor_scalar(sm[:, 1:2], sm[:, 0:1], -1.0, None, ALU.mult).then_inc(s["zc"], 1)
            dve.wait_ge(s["ec"], 1)
            link(dve.reciprocal(sm[:, 3:4], sm[:, 2:3]))
            dve.tensor_scalar(ec[:], ec[:], sm[:, 3:4], None, ALU.mult).then_inc(s["impt"], 1)
            dve.wait_ge(s["imptc"], 1)
            dve.tensor_copy(ecT[:], ps[0:NCMP, 0, 0:64]).then_inc(s["imp"], 1)
            dve.wait_ge(s["impc"], 1)
            dve.tensor_copy(imp[:], ps[0:64, 1, 0:NSB]).then_inc(s["imp"], 1)
            dve.wait_ge(s["grp"], 1)
            link(dve.tensor_copy(imp[:], ps[0:64, 2, 0:NSB]))
            n = slice(1, NSB - 2)
            link(dve.tensor_reduce(sm[:, 4:5], imp[:, n], AX.X, ALU.min))
            link(dve.tensor_scalar(eq[:, n], imp[:, n], sm[:, 4:5], None, ALU.is_equal))
            link(dve.tensor_tensor(eq[:, n], eq[:, n], idx[:, n], ALU.mult))
            link(dve.tensor_reduce(sm[:, 5:6], eq[:, n], AX.X, ALU.max))
            link(dve.tensor_scalar(dm[:], idx[:, 0:16], sm[:, 5:6], NEG, ALU.is_equal, ALU.mult))
            sel = Ss[:, 0:PAST].rearrange("p (n k) -> p n k", k=SELB)
            link(dve.tensor_tensor(sel, sel, last(dm[:], SELB), ALU.add))
            for k, (a, b) in enumerate(BR):
                link(dve.tensor_reduce(sm[:, 6 + k:7 + k], Ss[:, a:b], AX.X, ALU.max))
            dve.tensor_scalar(sm[:, 6:9], sm[:, 6:9], -1.0, None, ALU.mult).then_inc(s["z3"], 1)
            dve.wait_ge(s["e3"], 1)
            link(dve.reciprocal(sm[:, 12:15], sm[:, 9:12]))
            link(dve.tensor_tensor(sm[:, 12:14], sm[:, 12:14], gs[:, 1:3], ALU.mult))
            link(dve.tensor_tensor(sm[:, 14:15], sm[:, 14:15], gs[:, 0:1], ALU.mult))
            for k, (a, b) in enumerate(BR):
                o = dve.tensor_scalar(Ss[:, a:b], Ss[:, a:b], sm[:, 12 + k:13 + k], None, ALU.mult)
            o.then_inc(s["p3"], 1)
            dve.wait_ge(s["pt"], 1)
            dve.tensor_copy(pt[:, 0:8, :], ps[:, 0, :].rearrange("p (n q) -> p n q", q=64))
            dve.tensor_copy(pt[:, 8:12, :], ps[:, 1, 0:256].rearrange("p (n q) -> p n q", q=64))
            dve.tensor_copy(pt[0:NB, 12:14, :], ps[0:NB, 1, 256:384].rearrange("p (n q) -> p n q", q=64))
            dve.tensor_copy(pt[0:NCMP, 14, :], ps[0:NCMP, 1, 384:448])
            dve.tensor_copy(vn[:], ps[0:NB, 2, 0:2 * P].rearrange("p (n q) -> p n q", q=P)).then_inc(s["ptc"], 1)
            dve.wait_ge(s["pv"], 1)
            for g in range(G):
                r = slice(g * DH, (g + 1) * DH)
                dve.tensor_copy(c.oT[0][r, :, TP:T], ps[r, 3, 0:64].rearrange("p (b g j) -> p g j b", g=G, j=GR)[:, g])

        @block.scalar
        def _(act):
            act.wait_ge(s["zc"], 1)
            act.activation(ec[:], Ss[:, SO_CMP:SO_CMP + NCMP], ACT.Exp, bias=sm[:, 1:2], accum_out=sm[:, 2:3]).then_inc(s["ec"], 1)
            act.wait_ge(s["z3"], 1)
            for k, (a, b) in enumerate(BR):
                o = act.activation(Ss[:, a:b], Ss[:, a:b], ACT.Exp, bias=sm[:, 6 + k:7 + k], accum_out=sm[:, 9 + k:10 + k])
            o.then_inc(s["e3"], 1)

        @block.tensor
        def _(pe):
            pe.wait_ge(s["impt"], 1)
            pe.transpose(ps[0:NCMP, 0, 0:64], ec[:], c.ident[0:64, 0:64]).then_inc(s["imptc"], 1)
            pe.wait_ge(s["imp"], 1)
            pe.matmul(ps[0:64, 1, 0:NSB], ecT[:], imap[:], start=True, stop=True).then_inc(s["impc"], 1)
            pe.wait_ge(s["imp"], 2)
            pe.matmul(ps[0:64, 2, 0:NSB], grp[:], imp[:], start=True, stop=True).then_inc(s["grp"], 1)
            pe.wait_ge(s["p3"], 1)
            idt = c.ident[0:64, 0:64]
            for n in range(8):
                pe.transpose(ps[:, 0, n * 64:n * 64 + 64], Ss[:, n * P:(n + 1) * P], idt)
            for n in range(4):
                pe.transpose(ps[:, 1, n * 64:n * 64 + 64], Ss[:, SO_WIN + n * P:SO_WIN + (n + 1) * P], idt)
            pe.transpose(ps[0:NB, 1, 256:320], Ss[:, SO_NSEL:SO_NSEL + NB], idt)
            pe.transpose(ps[0:NB, 1, 320:384], Ss[:, SO_NWIN:SO_NWIN + NB], idt)
            pe.transpose(ps[0:NCMP, 1, 384:448], Ss[:, SO_CMP:SO_CMP + NCMP], idt)
            for k in range(2):
                t = pe.transpose(ps[0:NB, 2, k * P:(k + 1) * P], kv[:, 3 + 2 * k, TP:T], c.ident[:])
            t.then_inc(s["pt"], 1)
            pe.wait_ge(s["ptc"], 1)
            pe.wait_ge(s["v"], 16 * (NB * PAGES + NB))
            for b in range(NB):
                q = slice(b * NH, (b + 1) * NH)
                out = ps[:, 3, q]
                for n in range(8):
                    pe.matmul(out, vs[:, b * PAGES + n, :], pt[:, n, q], start=(n == 0), stop=False)
                for n in range(4):
                    pe.matmul(out, vw[:, b, n, :], pt[:, 8 + n, q], start=False, stop=False)
                for n in range(2):
                    pe.matmul(out, vn[:, n, :], pt[0:NB, 12 + n, q], start=False, stop=False)
                mm = pe.matmul(out, vc[:, b, :], pt[0:NCMP, 14, q], start=False, stop=True)
            mm.then_inc(s["pv"], 1)


def nsa_prompt(c, q, kv, kc, vc):
    nc, ps, dr = c.nc, c.ps, c.dram
    s = Semaphores(c, "np")
    NSL = 4
    LM = PAST + P
    with ExitStack() as ctx:
        sb = lambda n, sh, dt=F32: ctx.enter_context(nc.sbuf_tensor(f"np_{n}", sh, dt))
        mt = sb("mt", [P, GR, LM])
        mw = sb("mw", [P, GR, 5 * P])
        vt = sb("vt", [P, 2, NBLK, P])
        z = sb("z", [P, 2, 14 * P])
        sm = sb("sm", [P, 2, 12])
        ptb = sb("ptb", [P, NSL, 512])
        block = ctx.enter_context(nc.Block())
        steps = [(g, i, j) for g in range(G) for i in range(NBLK) for j in range(GR)]

        def widths(i):
            return (i + 1) * P, min(i + 1, 5) * P, 8 * i + 7

        def blocks(i):
            ws, ww, wc = widths(i)
            out = [(n * P, P, 0, n) for n in range(i + 1)]
            out += [(ws + n * P, P, 1, max(0, i - 4) + n) for n in range(ww // P)]
            return out + [(ws + ww, wc, 2, 0)]

        def groups(i):
            b = blocks(i)
            return [b[k:k + 4] for k in range(0, len(b), 4)]

        @block.sync
        def _(sp):
            for g in range(G):
                if g:
                    sp.wait_ge(s["zdone"], NBLK * GR)
                for j in range(GR):
                    h = g * GR + j
                    v, pitch = dr["s_bias"][h:h + 1, 0:1, :], LSEL + LWIN - 1
                    sp.dma_start(mt[:, j, :], bass.AP(v.tensor, v.offset + P - 1, [[pitch, P], [1, LM]])).then_inc(s[f"in{g}"], 16)
                    sp.dma_start(mw[:, j, :], bass.AP(v.tensor, v.offset + LSEL + P - 1, [[pitch, P], [1, 5 * P]])).then_inc(s[f"in{g}"], 16)

        @block.tensor
        def _(pe):
            for k in range(2):
                for i in range(NBLK):
                    t = pe.transpose(ps[:, 2 * k + i // 4, (i % 4) * P:(i % 4 + 1) * P], kv[:, 3 + 2 * k, i * P:(i + 1) * P], c.ident[:])
            t.then_inc(s["vt"], 1)
            pe.wait_ge(s["vtc"], 1)

            def scores(n):
                g, i, j = steps[n]
                r = slice(g * DH, (g + 1) * DH)
                qq = q[r, j, i * P:(i + 1) * P]
                ws, ww, wc = widths(i)
                if n:
                    pe.wait_ge(s["zdone"], n)
                for a in range(0, ws, 512):
                    e = min(ws, a + 512)
                    pe.matmul(ps[:, a // 512, 0:e - a], qq, kv[r, 2, a:e], start=True, stop=True)
                k0 = max(0, i - 4) * P
                a = min(ww, 512)
                pe.matmul(ps[:, 2, 0:a], qq, kv[r, 4, k0:k0 + a], start=True, stop=True)
                if ww > a:
                    pe.matmul(ps[:, 3, 0:ww - a], qq, kv[r, 4, k0 + a:k0 + ww], start=True, stop=True)
                pe.matmul(ps[:, 3, 256:256 + wc], qq, kc[r, NB, 0:wc], start=True, stop=True).then_inc(s["scored"], 1)

            cnt = [0, 0]

            def turn(n, grp):
                k = cnt[0]
                if k >= 2:
                    pe.wait_ge(s["ptc"], k - 1)
                for m, (col, w, _, _) in enumerate(grp):
                    t = pe.transpose(ps[0:w, 4 + k % 2, m * P:(m + 1) * P], z[:, n % 2, col:col + w], c.ident[:])
                t.then_inc(s["pt"], 1)
                cnt[0] += 1

            def values(n, grp, first, final):
                g, i, j = steps[n]
                r = slice(g * DH, (g + 1) * DH)
                k = cnt[1]
                pe.wait_ge(s["ptc"], k + 1)
                if first and n >= 2:
                    pe.wait_ge(s["oc"], n - 1)
                for m, (_, w, br, kb) in enumerate(grp):
                    v = vt[:, br, kb, r] if br < 2 else vc[0:w, NB, r]
                    mm = pe.matmul(ps[r, 6 + n % 2, 0:P], v, ptb[0:w, k % NSL, m * P:(m + 1) * P],
                                   start=(first and m == 0), stop=(final and m == len(grp) - 1))
                mm.then_inc(s["pv"], 1)
                cnt[1] += 1

            def finish(n):
                gr = groups(steps[n][1])
                pe.wait_ge(s["p"], n + 1)
                turn(n, gr[0])
                for k in range(len(gr)):
                    if k + 1 < len(gr):
                        turn(n, gr[k + 1])
                    values(n, gr[k], k == 0, k == len(gr) - 1)

            for n in range(len(steps)):
                scores(n)
                if n:
                    finish(n - 1)
            finish(len(steps) - 1)

        @block.vector
        def _(dve):
            link = Link(dve, s["link"])
            dve.wait_ge(s["vt"], 1)
            dve.tensor_copy(vt[:].rearrange("p k (a b) t -> p (k a) (b t)", a=2), ps[:, 0:4, :]).then_inc(s["vtc"], 1)
            turned = np.cumsum([0] + [len(groups(i)) for _, i, _ in steps]).tolist()

            def bias(n):
                g, i, j = steps[n]
                ws, ww, wc = widths(i)
                if j == 0 and i == 0:
                    dve.wait_ge(s[f"in{g}"], 16 * 2 * GR)
                dve.wait_ge(s["scored"], n + 1)
                if n >= 2:
                    dve.wait_ge(s["pt"], turned[n - 1])
                zz = z[:, n % 2]
                m0 = PAST - i * P
                mx = sm[:, n % 2, 0:4]
                if ws <= 512:
                    dve.tensor_tensor_reduce(zz[:, 0:ws], ps[:, 0, 0:ws], mt[:, j, m0:m0 + ws], 1.0, NEG, ALU.add, ALU.max, mx[:, 0:1])
                else:
                    dve.tensor_tensor_reduce(zz[:, 0:512], ps[:, 0, :], mt[:, j, m0:m0 + 512], 1.0, NEG, ALU.add, ALU.max, mx[:, 3:4])
                    link(dve.tensor_tensor_reduce(zz[:, 512:ws], ps[:, 1, 0:ws - 512], mt[:, j, m0 + 512:m0 + ws], 1.0, NEG, ALU.add, ALU.max, mx[:, 0:1]))
                    dve.tensor_tensor(mx[:, 0:1], mx[:, 0:1], mx[:, 3:4], ALU.max)
                w0 = 5 * P - ww
                a = min(ww, 512)
                dve.tensor_tensor_reduce(zz[:, ws:ws + a], ps[:, 2, 0:a], mw[:, j, w0:w0 + a], 1.0, NEG, ALU.add, ALU.max, mx[:, 1:2])
                if ww > a:
                    link(dve.tensor_tensor_reduce(zz[:, ws + a:ws + ww], ps[:, 3, 0:ww - a], mw[:, j, w0 + a:w0 + ww], 1.0, NEG, ALU.add, ALU.max, sm[:, n % 2, 7:8]))
                    dve.tensor_tensor(mx[:, 1:2], mx[:, 1:2], sm[:, n % 2, 7:8], ALU.max)
                c0 = m0 + 31
                o = dve.tensor_tensor_reduce(zz[:, ws + ww:ws + ww + wc], ps[:, 3, 256:256 + wc], mt[:, j, c0:c0 + STR * (wc - 1) + 1:STR],
                                             1.0, NEG, ALU.add, ALU.max, mx[:, 2:3])
                link(o)
                dve.tensor_scalar(sm[:, n % 2, 4:7], mx[:, 0:3], -1e29, -1.0, ALU.max, ALU.mult).then_inc(s["zdone"], 1)

            def scale(n):
                g, i, j = steps[n]
                ws, ww, wc = widths(i)
                dve.wait_ge(s["exp"], n + 1)
                h = g * GR + j
                su = sm[:, n % 2, 8:11]
                link(dve.tensor_scalar(su, su, 0.5, None, ALU.max))
                link(dve.reciprocal(su, su))
                dve.tensor_tensor(su[:, 0:2], su[:, 0:2], c.gtok[:, i, 3 * h + 1:3 * h + 3], ALU.mult)
                link(dve.tensor_tensor(su[:, 2:3], su[:, 2:3], c.gtok[:, i, 3 * h:3 * h + 1], ALU.mult))
                zz = z[:, n % 2]
                for k, (a, e) in enumerate(((0, ws), (ws, ws + ww), (ws + ww, ws + ww + wc))):
                    o = dve.tensor_scalar(zz[:, a:e], zz[:, a:e], su[:, k:k + 1], None, ALU.mult)
                o.then_inc(s["p"], 1)

            def output(n):
                g, i, j = steps[n]
                r = slice(g * DH, (g + 1) * DH)
                dve.wait_ge(s["pv"], turned[n + 1])
                dve.tensor_copy(c.oT[0][r, j, i * P:(i + 1) * P], ps[r, 6 + n % 2, 0:P]).then_inc(s["oc"], 1)

            N = len(steps)
            for n in range(N + 2):
                if n < N:
                    bias(n)
                if 1 <= n <= N:
                    scale(n - 1)
                if n >= 2:
                    output(n - 2)

        @block.scalar
        def _(act):
            cnt = [0]

            def exps(n):
                g, i, j = steps[n]
                ws, ww, wc = widths(i)
                act.wait_ge(s["zdone"], n + 1)
                zz = z[:, n % 2]
                for k, (a, e) in enumerate(((0, ws), (ws, ws + ww), (ws + ww, ws + ww + wc))):
                    o = act.activation(zz[:, a:e], zz[:, a:e], ACT.Exp, bias=sm[:, n % 2, 4 + k:5 + k], accum_out=sm[:, n % 2, 8 + k:9 + k])
                o.then_inc(s["exp"], 1)

            def copies(n):
                for grp in groups(steps[n][1]):
                    k = cnt[0]
                    act.wait_ge(s["pt"], k + 1)
                    if k >= NSL:
                        act.wait_ge(s["pv"], k - NSL + 1)
                    full = [m for m in grp if m[1] == P]
                    o = None
                    if full:
                        o = act.activation(ptb[:, k % NSL, 0:len(full) * P], ps[:, 4 + k % 2, 0:len(full) * P], ACT.Copy)
                    if len(full) < len(grp):
                        w, m = grp[-1][1], len(full) * P
                        o = act.activation(ptb[0:w, k % NSL, m:m + P], ps[0:w, 4 + k % 2, m:m + P], ACT.Copy)
                    o.then_inc(s["ptc"], 1)
                    cnt[0] += 1

            for n in range(len(steps)):
                exps(n)
                if n:
                    copies(n - 1)
            copies(len(steps) - 1)


def inverse_norm(c, name, x, ntiles, mean, post):
    nc, ps = c.nc, c.ps
    s = Semaphores(c, name)
    with nc.sbuf_tensor(f"{name}_sq", [P, 2, T], F32) as sq, nc.sbuf_tensor(f"{name}_r", [P, 2, T], F32) as rr, nc.Block() as block:
        @block.gpsimd
        def _(pool):
            for m in range(ntiles):
                if m >= 2:
                    pool.wait_ge(s["ss"], m - 1)
                pool.tensor_tensor(sq[:, m % 2], x[:, m], x[:, m], ALU.mult).then_inc(s["sq"], 1)

        @block.tensor
        def _(pe):
            for m in range(ntiles):
                pe.wait_ge(s["sq"], m + 1)
                if m >= 2:
                    pe.wait_ge(s["ln"], m - 1)
                for n in range(NW):
                    mm = pe.matmul(ps[:, 3 * (m % 2) + n, 0:W], c.ones[:], sq[:, m % 2, n * W:(n + 1) * W], start=True, stop=True)
                mm.then_inc(s["ss"], 1)

        @block.scalar
        def _(act):
            for m in range(ntiles):
                act.wait_ge(s["ss"], m + 1)
                if m >= 2:
                    act.wait_ge(s["done"], m - 1)
                act.activation(rr[:, m % 2].rearrange("p (n w) -> p n w", n=NW), ps[:, 3 * (m % 2):3 * (m % 2) + NW, 0:W],
                               ACT.Ln, bias=c.eps[:], scale=mean).then_inc(s["ln"], 1)
                act.wait_ge(s["ln"], m + 1)
                act.activation(rr[:, m % 2], rr[:, m % 2], ACT.Exp, scale=-0.5).then_inc(s["r"], 1)

        @block.vector
        def _(dve):
            for m in range(ntiles):
                dve.wait_ge(s["r"], m + 1)
                post(dve, m, rr[:, m % 2]).then_inc(s["done"], 1)


def gated_norm(c, name, o, gate, w_in):
    nc = c.nc
    s = Semaphores(c, name)
    with nc.sbuf_tensor(f"{name}_w", [P, 1], F32) as w:
        with nc.Block() as block:
            @block.sync
            def _(sp):
                sp.dma_start(w[:], w_in).then_inc(s["in"], 16)
                sp.wait_ge(s["in"], 16)

            @block.scalar
            def _(act):
                for m in range(H4):
                    act.activation(gate[:, m], gate[:, m], ACT.Silu)

        inverse_norm(c, f"{name}_in", o, H4, 1.0 / P,
                     lambda dve, m, r: dve.scalar_tensor_tensor(o[:, m], o[:, m], w[:], r, ALU.mult, ALU.mult))
        with nc.Block() as block:
            @block.vector
            def _(dve):
                for m in range(2):
                    dve.tensor_tensor(o[:, m], o[:, m], gate[:, m], ALU.mult)

            @block.gpsimd
            def _(pool):
                for m in range(2, 4):
                    pool.tensor_tensor(o[:, m], o[:, m], gate[:, m], ALU.mult)


def deltanet_conv(c, z):
    nc, dr = c.nc, c.dram
    NT = 12
    s = Semaphores(c, "cv")
    with ExitStack() as ctx:
        sb = lambda n, sh: ctx.enter_context(nc.sbuf_tensor(f"cv_{n}", sh, F32))
        cw = sb("cw", [P, NT, 4])
        hist = sb("hist", [P, NT, NB, 3])
        y = sb("y", [P, 2, T])
        st = sb("st", [P, NT, 3 + 3 * NB])
        block = ctx.enter_context(nc.Block())

        @block.sync
        def _(sp):
            sp.dma_start(cw[:], dr["conv_w"]).then_inc(s["in"], 16)
            sp.dma_start(hist[:], dr["conv_state"]).then_inc(s["in"], 16)
            sp.wait_ge(s["st"], 2)
            sp.dma_start(dr["o_conv"], st[:]).then_inc(s["out"], 16)
            sp.wait_ge(s["out"], 16)

        @block.gpsimd
        def _(pool):
            pool.wait_ge(s["in"], 32)
            pool.tensor_copy(st[:, :, 0:3], z[:, 0:NT, TP - 3:TP])
            sv = st[:, :, 3:3 + 3 * NB].rearrange("p m (b t) -> p m b t", t=3)
            pool.tensor_copy(sv[:, :, :, 0:2], hist[:, :, :, 1:3]).then_inc(s["st"], 1)
            pool.tensor_copy(sv[:, :, :, 2], z[:, 0:NT, TP:T]).then_inc(s["st"], 1)

        @block.vector
        def _(dve):
            link = Link(dve, s["link"])
            dve.wait_ge(s["in"], 32)
            dve.wait_ge(s["st"], 2)
            for m in range(NT):
                if m >= 2:
                    dve.wait_ge(s["silu"], m - 1)
                yy = y[:, m % 2]
                link(dve.tensor_scalar(yy, z[:, m], cw[:, m, 3:4], None, ALU.mult))
                for k in range(1, 4):
                    w = cw[:, m, 3 - k:4 - k]
                    dve.scalar_tensor_tensor(yy[:, TP:T], hist[:, m, :, 3 - k], w, yy[:, TP:T], ALU.mult, ALU.add)
                    o = dve.scalar_tensor_tensor(yy[:, k:TP], z[:, m, 0:TP - k], w, yy[:, k:TP], ALU.mult, ALU.add)
                    if k < 3:
                        link(o)
                o.then_inc(s["y"], 1)

        @block.scalar
        def _(act):
            for m in range(NT):
                act.wait_ge(s["y"], m + 1)
                act.activation(z[:, m], y[:, m % 2], ACT.Silu).then_inc(s["silu"], 1)


def deltanet_scalars(c, small, reset, gcol, bcol, egcol, sel):
    nc, ps, dr = c.nc, c.ps, c.dram
    s = Semaphores(c, "ds")
    with ExitStack() as ctx:
        sb = lambda n, sh: ctx.enter_context(nc.sbuf_tensor(f"ds_{n}", sh, F32))
        par = sb("par", [P, 2])
        tmp = sb("tmp", [P, 2, T])
        one = sb("one", [P, TP])
        block = ctx.enter_context(nc.Block())
        a, A = slice(32, 36), small[32:36, :]

        @block.sync
        def _(sp):
            sp.dma_start(par[a], dr["dn_par"]).then_inc(s["in"], 16)

        @block.scalar
        def _(act):
            act.wait_ge(s["in"], 16)
            act.activation(par[a, 0:1], par[a, 0:1], ACT.Exp).then_inc(s["ea"], 1)
            act.wait_ge(s["x"], 1)
            act.activation(tmp[a, 0], A, ACT.Abs).then_inc(s["alink"], 1)
            act.wait_ge(s["alink"], 1)
            act.activation(tmp[a, 0], tmp[a, 0], ACT.Exp, scale=-1.0).then_inc(s["alink"], 1)
            act.wait_ge(s["alink"], 2)
            act.activation(tmp[a, 0], tmp[a, 0], ACT.Ln, bias=c.ones[a, 0:1]).then_inc(s["l"], 1)
            act.activation(small[64:68, :], small[64:68, :], ACT.Sigmoid).then_inc(s["b"], 1)
            act.wait_ge(s["gc"], 1)
            act.activation(egcol[:], gcol[:], ACT.Exp).then_inc(s["alink"], 1)
            act.activation(small[a, TP:T], small[a, TP:T], ACT.Exp)

        @block.vector
        def _(dve):
            link = Link(dve, s["link"])
            for r in (32, 64):
                dve.tensor_copy(sel[r:r + 4], c.ident[r:r + 4, r:r + 4].unsqueeze(2).to_broadcast([4, 4, P]))
            link(dve.memset(one[a], 1.0))
            dve.wait_ge(s["in"], 16)
            dve.tensor_scalar(A, A, par[a, 1:2], None, ALU.add).then_inc(s["x"], 1)
            link(dve.memset(one[a].rearrange("p (i t) -> p i t", t=BLK)[:, :, 0:1], 0.0))
            dve.wait_ge(s["l"], 1)
            link(dve.tensor_scalar(tmp[a, 1], A, 0.0, None, ALU.max))
            link(dve.tensor_tensor(tmp[a, 1], tmp[a, 1], tmp[a, 0], ALU.add))
            dve.wait_ge(s["ea"], 1)
            link(dve.tensor_scalar(tmp[a, 1], tmp[a, 1], par[a, 0:1], -1.0, ALU.mult, ALU.mult))
            dve.tensor_copy(small[a, TP:T], tmp[a, 1, TP:T])
            dve.tensor_tensor_scan(small[a, 0:TP], one[a], tmp[a, 1, 0:TP], 0.0, ALU.mult, ALU.add).then_inc(s["g"], 1)
            dve.wait_ge(s["t"], 1)
            dve.tensor_copy(gcol[:].rearrange("p i h -> p (i h)"), ps[:, 0, 0:32])
            dve.tensor_copy(bcol[:].rearrange("p i h -> p (i h)"), ps[:, 1, 0:32]).then_inc(s["gc"], 1)
            dve.wait_ge(s["alink"], 3)
            dve.tensor_scalar(egcol[:], egcol[:], -1.0, None, ALU.mult)

        @block.tensor
        def _(pe):
            pe.wait_ge(s["g"], 1)
            pe.wait_ge(s["b"], 1)
            for k, r in enumerate((slice(32, 36), slice(64, 68))):
                for i in range(NBLK):
                    t = pe.transpose(ps[:, k, 4 * i:4 * i + 4], small[r, i * BLK:(i + 1) * BLK], c.ident[r, r])
            t.then_inc(s["t"], 1)


def deltanet_prompt(c, z, small, gcol, bcol, egcol, sel, S, o):
    nc, ps, dr = c.nc, c.ps, c.dram
    s = Semaphores(c, "dp")
    C = H4 * P
    with ExitStack() as ctx:
        sb = lambda n, sh: ctx.enter_context(nc.sbuf_tensor(f"dp_{n}", sh, F32))
        up = sb("up", [P, LEV, P])
        lo = sb("lo", [P, 3, P])
        egb, kt, vt, dec, A, AT, at, X, Y, Wm, vn, qg, kd, rhs, qks = (sb(n, [P, C]) for n in (
            "egb", "kt", "vt", "dec", "A", "AT", "at", "X", "Y", "Wm", "vn", "qg", "kd", "rhs", "qks"))
        atm = sb("atm", [P, 2, C])
        dcol = sb("dcol", [P, 2, H4])
        block = ctx.enter_context(nc.Block())
        hd = lambda h: slice(h * P, (h + 1) * P)
        as4 = lambda t: t.rearrange("p (h x) -> p h x", h=H4)
        R = LEV - 1

        @block.sync
        def _(sp):
            sp.dma_start(up[:], dr["up"]).then_inc(s["in"], 16)
            sp.dma_start(lo[:], dr["lo"]).then_inc(s["in"], 16)

        @block.tensor
        def _(pe):
            for i in range(NBLK):
                t = slice(i * BLK, (i + 1) * BLK)
                if i:
                    pe.wait_ge(s["Su"], i)
                    pe.wait_ge(s["oc"], i)
                for h in range(H4):
                    q, k = z[:, h, t], z[:, 4 + h, t]
                    pe.matmul(ps[:, 0, hd(h)], k, k, start=True, stop=True)
                    pe.matmul(ps[:, 1, hd(h)], q, k, start=True, stop=True)
                    pe.matmul(ps[:, 2, hd(h)], sel[32:36, h, :], small[32:36, t], start=True, stop=True)
                    pe.transpose(ps[:, 3, hd(h)], k, c.ident[:])
                    mm = pe.transpose(ps[:, 4, hd(h)], z[:, 8 + h, t], c.ident[:])
                mm.then_inc(s["raw"], 1)
                pe.wait_ge(s["A"], i + 1)
                for h in range(H4):
                    pe.transpose(ps[:, 5, hd(h)], A[:, hd(h)], c.ident[:])
                    mm = pe.transpose(ps[:, 6, hd(h)], qks[:, hd(h)], c.ident[:])
                mm.then_inc(s["turned"], 1)
                pe.wait_ge(s["X0"], i + 1)
                for l in range(1, LEV):
                    n = i * R + l
                    pe.wait_ge(s["atm"], n)
                    if l > 1:
                        pe.wait_ge(s["XYs"], n - 1)
                    for h in range(H4):
                        mm = pe.matmul(ps[:, 0, hd(h)], atm[:, l % 2, hd(h)], X[:, hd(h)], start=True, stop=True)
                    mm.then_inc(s["Wm"], 1)
                    pe.wait_ge(s["Wc"], n)
                    for h in range(H4):
                        if l < LEV - 1:
                            pe.matmul(ps[:, 1, hd(h)], Y[:, hd(h)], Wm[:, hd(h)], start=True, stop=True)
                        mm = pe.matmul(ps[:, 2, hd(h)], Wm[:, hd(h)], Y[:, hd(h)], start=True, stop=True)
                    mm.then_inc(s["XY"], 1)
                for h in range(H4):
                    mm = pe.matmul(ps[:, 3, hd(h)], z[:, 4 + h, t], S[:, hd(h)], start=True, stop=True)
                mm.then_inc(s["ks"], 1)
                pe.wait_ge(s["rhs"], i + 1)
                for h in range(H4):
                    mm = pe.matmul(ps[:, 4, hd(h)], Y[:, hd(h)], rhs[:, hd(h)], start=True, stop=True)
                mm.then_inc(s["vn"], 1)
                pe.wait_ge(s["vnc"], i + 1)
                pe.wait_ge(s["qg"], i + 1)
                for h in range(H4):
                    pe.matmul(ps[:, 7, hd(h)], kd[:, hd(h)], vn[:, hd(h)], start=True, stop=True)
                for h in range(H4):
                    pe.matmul(ps[:, 6, hd(h)], S[:, hd(h)], qg[:, hd(h)], start=True, stop=False)
                    mm = pe.matmul(ps[:, 6, hd(h)], vn[:, hd(h)], at[:, hd(h)], start=False, stop=True)
                mm.then_inc(s["ou"], 1)

        @block.scalar
        def _(act):
            for i in range(NBLK):
                t = slice(i * BLK, (i + 1) * BLK)
                act.wait_ge(s["raw"], i + 1)
                act.activation(egb[:], ps[:, 2, :], ACT.Exp).then_inc(s["egb"], 1)
                act.activation(kt[:], ps[:, 3, :], ACT.Copy)
                act.activation(vt[:], ps[:, 4, :], ACT.Copy).then_inc(s["tok"], 1)
                act.wait_ge(s["diff"], i + 1)
                act.activation(dec[:], dec[:], ACT.Exp, scale=-1.0).then_inc(s["dec"], 1)
                act.activation(dcol[:, 1], dcol[:, 0], ACT.Exp).then_inc(s["dcx"], 1)
                act.wait_ge(s["turned"], i + 1)
                act.activation(AT[:], ps[:, 5, :], ACT.Copy)
                act.activation(at[:], ps[:, 6, :], ACT.Copy).then_inc(s["AT"], 1)
                for l in range(1, LEV):
                    n = i * R + l
                    act.wait_ge(s["Wm"], n)
                    act.activation(Wm[:], ps[:, 0, :], ACT.Copy).then_inc(s["Wc"], 1)
                act.wait_ge(s["vn"], i + 1)
                act.activation(vn[:], ps[:, 4, :], ACT.Copy).then_inc(s["vnc"], 1)
                act.wait_ge(s["ou"], i + 1)
                act.activation(o[:, :, t], as4(ps[:, 6, :]), ACT.Copy).then_inc(s["oc"], 1)

        @block.gpsimd
        def _(pool):
            pool.wait_ge(s["in"], 32)
            for i in range(NBLK):
                pool.wait_ge(s["AT"], i + 1)
                for l in range(1, LEV):
                    n = i * R + l
                    if l >= 3:
                        pool.wait_ge(s["Wm"], n - 2)
                    pool.tensor_tensor(as4(atm[:, l % 2]), as4(AT[:]), mid(up[:, l, :], H4), ALU.mult).then_inc(s["atm"], 1)

        @block.vector
        def _(dve):
            link = Link(dve, s["link"])
            link(dve.memset(S[:], 0.0))
            dve.wait_ge(s["in"], 32)
            for i in range(NBLK):
                dve.wait_ge(s["raw"], i + 1)
                dve.wait_ge(s["egb"], i + 1)
                for h in range(H4):
                    dve.tensor_scalar(dec[:, hd(h)], ps[:, 2, hd(h)], gcol[:, i, h:h + 1], 0.0, ALU.subtract, ALU.max)
                dve.tensor_tensor(dcol[:, 0], ps[:, 2, P - 1:C:P], gcol[:, i, :], ALU.subtract).then_inc(s["diff"], 1)
                dve.wait_ge(s["dec"], i + 1)
                link(dve.tensor_tensor(as4(dec[:]), as4(dec[:]), mid(lo[:, 0, :], H4), ALU.mult))
                for h in range(H4):
                    dve.scalar_tensor_tensor(A[:, hd(h)], ps[:, 0, hd(h)], bcol[:, i, h:h + 1], dec[:, hd(h)], ALU.mult, ALU.mult)
                link(dve.tensor_tensor(qks[:], ps[:, 1, :], dec[:], ALU.mult))
                dve.tensor_tensor(as4(A[:]), as4(A[:]), mid(lo[:, 1, :], H4), ALU.mult).then_inc(s["A"], 1)
                dve.wait_ge(s["A"], i + 1)
                link(dve.tensor_tensor(as4(X[:]), as4(A[:]), mid(lo[:, 2, :], H4), ALU.mult))
                dve.tensor_tensor(as4(X[:]), mid(c.ident[:], H4), as4(X[:]), ALU.subtract)
                dve.wait_ge(s["AT"], i + 1)
                link(dve.tensor_tensor(as4(Y[:]), as4(AT[:]), mid(up[:, 0, :], H4), ALU.mult))
                dve.tensor_tensor(as4(Y[:]), mid(c.ident[:], H4), as4(Y[:]), ALU.subtract).then_inc(s["X0"], 1)
                dve.tensor_tensor(as4(qg[:]), z[:, 0:4, i * BLK:(i + 1) * BLK], as4(egb[:]), ALU.mult)
                dve.wait_ge(s["tok"], i + 1)
                dve.wait_ge(s["dcx"], i + 1)
                dve.tensor_tensor(as4(kd[:]), as4(kt[:]), last(dcol[:, 1], P), ALU.mult).then_inc(s["qg"], 1)
                for l in range(1, LEV):
                    n = i * R + l
                    dve.wait_ge(s["XY"], n)
                    if l < LEV - 1:
                        dve.tensor_tensor(X[:], X[:], ps[:, 1, :], ALU.subtract)
                    dve.tensor_tensor(Y[:], Y[:], ps[:, 2, :], ALU.subtract).then_inc(s["XYs"], 1)
                dve.wait_ge(s["ks"], i + 1)
                link(dve.tensor_tensor(as4(rhs[:]), as4(ps[:, 3, :]), last(egcol[:, i, :], P), ALU.mult))
                link(dve.tensor_tensor(rhs[:], rhs[:], vt[:], ALU.add))
                dve.wait_ge(s["XYs"], (i + 1) * R)
                dve.tensor_tensor(as4(rhs[:]), as4(rhs[:]), last(bcol[:, i, :], P), ALU.mult).then_inc(s["rhs"], 1)
                dve.wait_ge(s["ou"], i + 1)
                link(dve.tensor_tensor(as4(S[:]), as4(S[:]), last(egb[:, P - 1:C:P], P), ALU.mult))
                dve.tensor_tensor(S[:], S[:], ps[:, 7, :], ALU.add).then_inc(s["Su"], 1)


def store_states(c, name, S, out):
    nc = c.nc
    sem = c.sem(f"{name}_stored")
    with nc.Block() as block:
        @block.sync
        def _(sp):
            sp.dma_start(out, S).then_inc(sem, 16)
            sp.wait_ge(sem, 16)


def recurrent_samples(c, name, state_in, state_out, o, q, k, vT, decay, beta=None):
    nc, ps, dr = c.nc, c.ps, c.dram
    s = Semaphores(c, name)
    NPR = H4 * NB
    N = 4
    with ExitStack() as ctx:
        sb = lambda n, sh: ctx.enter_context(nc.sbuf_tensor(f"{name}_{n}", sh, F32))
        S = sb("S", [P, NPR, P])
        pr = sb("pr", [P, N, P])
        dg = sb("dg", [P, N, P])
        u = sb("u", [P, N, P])
        qc = sb("qc", [P, NPR])
        block = ctx.enter_context(nc.Block())

        @block.sync
        def _(sp):
            sp.dma_start(S[:], state_in).then_inc(s["in"], 16)
            sp.wait_ge(s["u"], NPR // N)
            sp.dma_start(state_out, S[:]).then_inc(s["out"], 16)
            sp.wait_ge(s["out"], 16)

        @block.vector
        def _(dve):
            link = Link(dve, s["link"])
            dve.tensor_copy(qc[:].rearrange("p (h b) -> p h b", b=NB), q).then_inc(s["q"], 1)
            dve.wait_ge(s["in"], 16)
            for n in range(NPR // N):
                h, b0 = n * N // NB, n * N % NB
                sl = slice(n * N, (n + 1) * N)
                kk, vv = k[:, h, b0:b0 + N], vT[:, h, b0:b0 + N]
                d = decay(h, b0, N)
                if beta is not None:
                    dve.tensor_tensor(pr[:], S[:, sl], last(kk, P), ALU.mult)
                dve.tensor_tensor(dg[:], mid(c.ident[:], N), last(vv, P), ALU.mult).then_inc(s["p"], 1)
                link(dve.tensor_tensor(S[:, sl], S[:, sl], last(d, P), ALU.mult))
                dve.wait_ge(s["mm"], n + 1)
                vb = ps[:, 1, :].rearrange("p (n v) -> p n v", n=N)
                if beta is not None:
                    link(dve.tensor_tensor(u[:], ps[:, 0, :].rearrange("p (n v) -> p n v", n=N), last(d, P), ALU.mult))
                    link(dve.tensor_tensor(u[:], vb, u[:], ALU.subtract))
                    link(dve.tensor_tensor(u[:], u[:], last(beta(h, b0, N), P), ALU.mult))
                    link(dve.tensor_tensor(u[:], u[:], last(kk, P), ALU.mult))
                else:
                    link(dve.tensor_tensor(u[:], vb, last(kk, P), ALU.mult))
                dve.tensor_tensor(S[:, sl], S[:, sl], u[:], ALU.add).then_inc(s["u"], 1)
            dve.wait_ge(s["omm"], 1)
            dve.tensor_copy(o[:, :, TP:T], ps[:, 2, 0:NPR].rearrange("p (h b) -> p h b", b=NB))

        @block.tensor
        def _(pe):
            for n in range(NPR // N):
                pe.wait_ge(s["p"], n + 1)
                if n:
                    pe.wait_ge(s["u"], n)
                if beta is not None:
                    pe.matmul(ps[:, 0, :], c.ones[:], pr[:].rearrange("p n v -> p (n v)"), start=True, stop=True)
                pe.matmul(ps[:, 1, :], c.ones[:], dg[:].rearrange("p n v -> p (n v)"), start=True, stop=True).then_inc(s["mm"], 1)
            pe.wait_ge(s["u"], NPR // N)
            pe.wait_ge(s["q"], 1)
            for n in range(NPR):
                mm = pe.matmul(ps[:, 2, n:n + 1], S[:, n, :], qc[:, n:n + 1], start=True, stop=True)
            mm.then_inc(s["omm"], 1)


def spread_rows(c, name, sel, small, rows, dst):
    nc, ps = c.nc, c.ps
    mmd = c.sem(f"{name}_spread")
    with nc.Block() as block:
        @block.tensor
        def _(pe):
            for k, r in enumerate(rows):
                for h in range(H4):
                    mm = pe.matmul(ps[:, k, h * NB:(h + 1) * NB], sel[r:r + 4, h, :], small[r:r + 4, TP:T], start=True, stop=True)
            mm.then_inc(mmd, 1)

        @block.vector
        def _(dve):
            dve.wait_ge(mmd, 1)
            dve.tensor_copy(dst[:].rearrange("p k h b -> p k (h b)"), ps[:, 0:len(rows), 0:H4 * NB])


def deltanet(c, small):
    nc, dr = c.nc, c.dram
    o = c.oT[1]
    with ExitStack() as ctx:
        sb = lambda n, sh: ctx.enter_context(nc.sbuf_tensor(f"dn_{n}", sh, F32))
        z = sb("z", [P, 16, T])
        gcol, bcol, egcol = sb("gcol", [P, NBLK, H4]), sb("bcol", [P, NBLK, H4]), sb("egcol", [P, NBLK, H4])
        sel = sb("sel", [P, H4, P])
        dbs = sb("dbs", [P, 2, H4, NB])
        S = sb("S", [P, H4 * P])
        project(c, "dnp", dr["w_dn"], 16, z)
        deltanet_conv(c, z)
        inverse_norm(c, "l2", z, 8, 1.0,
                     lambda dve, m, r: dve.scalar_tensor_tensor(z[:, m], z[:, m], P ** -0.5 if m < 4 else 1.0, r, ALU.mult, ALU.mult))
        deltanet_scalars(c, small, None, gcol, bcol, egcol, sel)
        spread_rows(c, "dn", sel, small, (32, 64), dbs)
        recurrent_samples(c, "dns", dr["state_dn"], dr["o_dn_s"], o, z[:, 0:4, TP:T], z[:, 4:8, TP:T], z[:, 8:12, TP:T],
                          lambda h, b, n: dbs[:, 0, h, b:b + n], lambda h, b, n: dbs[:, 1, h, b:b + n])
        deltanet_prompt(c, z, small, gcol, bcol, egcol, sel, S, o)
        store_states(c, "dn", S[:], dr["o_dn_p"])
        gated_norm(c, "dng", o, z[:, 12:16], dr["dn_norm"])


def hgrn2(c):
    nc, ps, dr = c.nc, c.ps, c.dram
    o = c.oT[2]
    with ExitStack() as ctx:
        sb = lambda n, sh: ctx.enter_context(nc.sbuf_tensor(f"hg_{n}", sh, F32))
        z = sb("z", [P, 16, T])
        project(c, "hgp", dr["w_hg"], 16, z)
        f = sb("f", [P, H4, NB])
        Gs = sb("Gs", [P, 2, T])
        s = Semaphores(c, "hg")
        with ExitStack() as c2:
            s2 = lambda n, sh: c2.enter_context(nc.sbuf_tensor(f"hg_{n}", sh, F32))
            up = s2("up", [P, LEV, P])
            one = s2("one", [P, TP])
            lf = s2("lf", [P, T])
            E = s2("E", [P, TP])
            Z = s2("Z", [P, TP])
            tmp = s2("tmp", [P, 512])
            at = s2("at", [P, NBLK, P])
            vt = s2("vt", [P, NBLK, P])
            qg = s2("qg", [P, TP])
            kd = s2("kd", [P, TP])
            kt = s2("kt", [P, NBLK, P])
            S = s2("S", [P, H4, P])
            block = c2.enter_context(nc.Block())
            NL = LEV + 1

            @block.sync
            def _(sp):
                sp.dma_start(up[:], dr["up"]).then_inc(s["in"], 16)
                sp.wait_ge(s["Su"], H4 * NBLK)
                sp.dma_start(dr["o_hg_p"], S[:]).then_inc(s["out"], 16)
                sp.wait_ge(s["out"], 16)

            @block.scalar
            def _(act):
                for h in range(H4):
                    k = z[:, 4 + h]
                    if h:
                        act.wait_ge(s["G"], h)
                    act.activation(lf[:], k, ACT.Abs).then_inc(s["alink"], 1)
                    act.wait_ge(s["alink"], 2 * h + 1)
                    act.activation(lf[:], lf[:], ACT.Exp, scale=-1.0).then_inc(s["alink"], 1)
                    act.wait_ge(s["alink"], 2 * h + 2)
                    act.activation(lf[:], lf[:], ACT.Ln, bias=c.ones[:, 0:1]).then_inc(s["l"], 1)
                    act.wait_ge(s["a"], h + 1)
                    act.activation(k, k, ACT.Sigmoid, scale=-1.0).then_inc(s["k"], 1)
                    act.wait_ge(s["G"], h + 1)
                    act.activation(f[:, h, :], Gs[:, h % 2, TP:T], ACT.Exp)
                    if h:
                        act.wait_ge(s["Su"], NBLK * h)
                    act.activation(qg[:], Gs[:, h % 2, 0:TP], ACT.Exp).then_inc(s["fs"], 1)
                    for l in range(LEV):
                        n = h * LEV + l
                        act.wait_ge(s["D"], n + 1)
                        act.activation(E[:], E[:], ACT.Exp).then_inc(s["E"], 1)
                    act.wait_ge(s["kd"], 2 * h + 1)
                    act.activation(kd[:], kd[:], ACT.Exp).then_inc(s["kt"], 1)
                    act.wait_ge(s["vt"], h + 1)
                    act.activation(vt[:].rearrange("p (a b) t -> p a (b t)", a=2), ps[:, 4:6, :], ACT.Copy).then_inc(s["vtc"], 1)
                    for i in range(NBLK):
                        n = h * NBLK + i
                        act.wait_ge(s["ou"], n + 1)
                        act.activation(o[:, h, i * BLK:(i + 1) * BLK], ps[:, 2 + n % 2, 0:P], ACT.Copy).then_inc(s["oc"], 1)

            @block.vector
            def _(dve):
                link = Link(dve, s["link"])
                link(dve.memset(one[:], 1.0))
                dve.memset(S[:], 0.0)
                link(dve.memset(one[:].rearrange("p (i t) -> p i t", t=BLK)[:, :, 0:1], 0.0))
                dve.tensor_scalar(z[:, 0:4], z[:, 0:4], P ** -0.5, None, ALU.mult).then_inc(s["q"], 1)
                dve.wait_ge(s["in"], 16)
                dve.wait_ge(s["q"], 1)
                for h in range(H4):
                    q, k = z[:, h, 0:TP], z[:, 4 + h, 0:TP]
                    G = Gs[:, h % 2]
                    dve.wait_ge(s["l"], h + 1)
                    dve.tensor_scalar(G, z[:, 4 + h], 0.0, None, ALU.min).then_inc(s["a"], 1)
                    dve.wait_ge(s["a"], h + 1)
                    link(dve.tensor_tensor(lf[:], G, lf[:], ALU.subtract))
                    dve.tensor_copy(G[:, TP:T], lf[:, TP:T])
                    dve.tensor_tensor_scan(G[:, 0:TP], one[:], lf[:, 0:TP], 0.0, ALU.mult, ALU.add).then_inc(s["G"], 1)
                    dve.wait_ge(s["G"], h + 1)
                    dve.wait_ge(s["k"], h + 1)
                    for l in range(-1, LEV):
                        m = h * NL + l + 1
                        if l >= 0:
                            n = h * LEV + l
                            hs = 1 << l
                            v = lambda t: t.rearrange("p (i u x) -> p i u x", u=2, x=hs)
                            Gv = v(G[:, 0:TP])
                            anchor = Gv[:, :, 0, hs - 1:hs].to_broadcast([P, TP // (2 * hs), hs])
                            dve.wait_ge(s["mm"], 2 * m)
                            dve.tensor_tensor(v(E[:])[:, :, 1], Gv[:, :, 1], anchor, ALU.subtract)
                            dve.tensor_tensor(v(E[:])[:, :, 0], anchor, Gv[:, :, 0], ALU.subtract).then_inc(s["D"], 1)
                            dve.wait_ge(s["E"], n + 1)
                            dve.tensor_tensor(v(Z[:])[:, :, 1], v(q)[:, :, 1], v(E[:])[:, :, 1], ALU.mult)
                            dve.tensor_tensor(v(Z[:])[:, :, 0], v(k)[:, :, 0], v(E[:])[:, :, 0], ALU.mult).then_inc(s["Z"], 1)
                        elif h:
                            dve.wait_ge(s["Su"], NBLK * h)
                        for a in range(2):
                            dve.wait_ge(s["mm"], 2 * m + a + 1)
                            src = ps[:, a, :].rearrange("p (i t) -> p i t", t=P)
                            dst = at[:, 4 * a:4 * a + 4, :]
                            if l < 0:
                                link(dve.tensor_tensor(dst, src, mid(c.ident[:], 4), ALU.mult))
                            else:
                                t4 = tmp[:].rearrange("p (i t) -> p i t", t=P)
                                link(dve.tensor_tensor(t4, src, mid(up[:, l, :], 4), ALU.mult))
                                link(dve.tensor_tensor(dst, dst, t4, ALU.add))
                        dve.sem_inc(s["mk"], 1)
                    Gc = G[:, 0:TP].rearrange("p (i t) -> p i t", t=BLK)
                    kc_ = kd[:].rearrange("p (i t) -> p i t", t=BLK)
                    dve.tensor_tensor(kc_, Gc[:, :, BLK - 1:BLK].to_broadcast([P, NBLK, BLK]), Gc, ALU.subtract).then_inc(s["kd"], 1)
                    dve.wait_ge(s["kt"], h + 1)
                    dve.tensor_tensor(kd[:], kd[:], k, ALU.mult).then_inc(s["kd"], 1)
                    dve.wait_ge(s["fs"], h + 1)
                    link(dve.tensor_copy(tmp[:, 0:NBLK], qg[:, BLK - 1:TP:BLK]))
                    dve.tensor_tensor(qg[:], qg[:], q, ALU.mult).then_inc(s["qg"], 1)
                    dve.wait_ge(s["ktc"], h + 1)
                    dve.tensor_copy(kt[:].rearrange("p (a b) t -> p a (b t)", a=2), ps[:, 6:8, :]).then_inc(s["at"], 1)
                    for i in range(NBLK):
                        n = h * NBLK + i
                        dve.wait_ge(s["ou"], n + 1)
                        link(dve.tensor_scalar(S[:, h, :], S[:, h, :], tmp[:, i:i + 1], None, ALU.mult))
                        dve.tensor_tensor(S[:, h, :], S[:, h, :], ps[:, n % 2, 0:P], ALU.add).then_inc(s["Su"], 1)

            @block.tensor
            def _(pe):
                pe.wait_ge(s["q"], 1)
                for h in range(H4):
                    pe.wait_ge(s["k"], h + 1)
                    for l in range(-1, LEV):
                        m = h * NL + l + 1
                        if l >= 0:
                            pe.wait_ge(s["Z"], h * LEV + l + 1)
                        if m:
                            pe.wait_ge(s["mk"], m)
                        if l < 0 and h:
                            pe.wait_ge(s["Su"], NBLK * h)
                        for a in range(2):
                            for i in range(4 * a, 4 * a + 4):
                                t = slice(i * BLK, (i + 1) * BLK)
                                x, y = (Z[:, t], Z[:, t]) if l >= 0 else (z[:, 4 + h, t], z[:, h, t])
                                mm = pe.matmul(ps[:, a, (i - 4 * a) * P:(i - 4 * a + 1) * P], x, y, start=True, stop=True)
                            mm.then_inc(s["mm"], 1)
                    if h:
                        pe.wait_ge(s["oc"], NBLK * h)
                    for i in range(NBLK):
                        t_ = pe.transpose(ps[:, 4 + i // 4, (i % 4) * P:(i % 4 + 1) * P], z[:, 8 + h, i * BLK:(i + 1) * BLK], c.ident[:])
                    t_.then_inc(s["vt"], 1)
                    pe.wait_ge(s["kd"], 2 * h + 2)
                    for i in range(NBLK):
                        t_ = pe.transpose(ps[:, 6 + i // 4, (i % 4) * P:(i % 4 + 1) * P], kd[:, i * BLK:(i + 1) * BLK], c.ident[:])
                    t_.then_inc(s["ktc"], 1)
                    pe.wait_ge(s["at"], h + 1)
                    pe.wait_ge(s["vtc"], h + 1)
                    pe.wait_ge(s["qg"], h + 1)
                    pe.wait_ge(s["mk"], NL * (h + 1))
                    for i in range(NBLK):
                        n = h * NBLK + i
                        t = slice(i * BLK, (i + 1) * BLK)
                        if n:
                            pe.wait_ge(s["Su"], n)
                        if n >= 2:
                            pe.wait_ge(s["oc"], n - 1)
                        pe.matmul(ps[:, n % 2, 0:P], kt[:, i, :], vt[:, i, :], start=True, stop=True)
                        pe.matmul(ps[:, 2 + n % 2, 0:P], S[:, h, :], qg[:, t], start=True, stop=False)
                        pe.matmul(ps[:, 2 + n % 2, 0:P], vt[:, i, :], at[:, i, :], start=False, stop=True).then_inc(s["ou"], 1)

        recurrent_samples(c, "hgs", dr["state_hg"], dr["o_hg_s"], o, z[:, 0:4, TP:T], z[:, 4:8, TP:T], z[:, 8:12, TP:T],
                          lambda h, b, n: f[:, h, b:b + n])
        gated_norm(c, "hgg", o, z[:, 12:16], dr["hg_norm"])


def merge(c, mT):
    nc, ps, dr = c.nc, c.ps, c.dram
    wg_here = [c.sem(f"mg_gate_w{b}") for b in range(3)]
    wb_here = [c.sem(f"mg_branch_w{b}") for b in range(3)]
    s = Semaphores(c, "mg")
    with ExitStack() as ctx:
        sb = lambda n, sh: ctx.enter_context(nc.sbuf_tensor(f"mg_{n}", sh, F32))
        wg = sb("wg", [P, 3, KT, P])
        wb = sb("wb", [P, 3, H4, P])
        sg = sb("sg", [P, T])
        tmp = sb("tmp", [P, T])
        block = ctx.enter_context(nc.Block())
        win = lambda t: t.rearrange("p (n w) -> p n w", n=NW)

        @block.sync
        def _(sp):
            with sp.Fori(0, KT) as m:
                for b in range(3):
                    sp.wait_ge(s["wfree"], 3 * m + b + 1)
                    sp.dma_start(wg[:, b], dr["w_mg"][3 * m + b]).then_inc(wg_here[b], 16)
                    sp.dma_start(wb[:, b], dr["w_br"][3 * m + b]).then_inc(wb_here[b], 16)

        @block.tensor
        def _(pe):
            pe.sem_inc(s["wfree"], 3)
            with pe.Fori(0, KT) as m:
                for b in range(3):
                    pe.wait_ge(wg_here[b], 16 * m + 16)
                    pe.wait_ge(s["gate_read"], 3 * m + b + 1)
                    for n in range(NW):
                        for k in range(KT):
                            mm = pe.matmul(ps[:, n, 0:W], wg[:, b, k, :], c.xT[:, k, n * W:(n + 1) * W], start=(k == 0), stop=(k == KT - 1))
                    mm.then_inc(s["gate"], 1)
                    pe.wait_ge(wb_here[b], 16 * m + 16)
                    pe.wait_ge(s["br_read"], 3 * m + b + 1)
                    for n in range(NW):
                        for k in range(H4):
                            mm = pe.matmul(ps[:, 3 + n, 0:W], wb[:, b, k, :], c.oT[b][:, k, n * W:(n + 1) * W], start=(k == 0), stop=(k == H4 - 1))
                    mm.then_inc(s["br"], 1)
                    pe.wait_ge(s["br"], 3 * m + b + 1)
                    pe.sem_inc(s["wfree"], 1)

        @block.scalar
        def _(act):
            act.sem_inc(s["gate_read"], 1)
            with act.Fori(0, KT) as m:
                for b in range(3):
                    act.wait_ge(s["gate"], 3 * m + b + 1)
                    act.wait_ge(s["sg_used"], 3 * m + b + 1)
                    act.activation(win(sg[:]), ps[:, 0:NW, 0:W], ACT.Sigmoid).then_inc(s["gate_read"], 1)

        @block.vector
        def _(dve):
            dve.sem_inc(s["br_read"], 1)
            dve.sem_inc(s["sg_used"], 1)
            with dve.Fori(0, KT) as m:
                for b in range(3):
                    dve.wait_ge(s["br"], 3 * m + b + 1)
                    dve.wait_ge(s["gate_read"], 3 * m + b + 2)
                    if b == 0:
                        dve.tensor_tensor(win(mT[:, m, :]), win(sg[:]), ps[:, 3:3 + NW, 0:W], ALU.mult).then_inc(s["br_read"], 1)
                    else:
                        dve.tensor_tensor(win(tmp[:]), win(sg[:]), ps[:, 3:3 + NW, 0:W], ALU.mult).then_inc(s["br_read"], 1)
                    dve.wait_ge(s["br_read"], 3 * m + b + 2)
                    dve.sem_inc(s["sg_used"], 1)
                    if b:
                        dve.tensor_tensor(mT[:, m, :], mT[:, m, :], tmp[:], ALU.add).then_inc(s["link"], 1)
                        dve.wait_ge(s["link"], 2 * m + b)


def rows(t):
    return BLK if t < NBLK else NB


def norm_rows(dve, act_sems, link, y, r, st, gb, n):
    asked, given = act_sems
    for h in range(2):
        dve.bn_stats(st[0:r, 6 * h:6 * h + 6], y[:, h * 512:(h + 1) * 512])
    link(dve.engine_nop())
    link(dve.bn_aggr(st[0:r, 12:14], st[0:r, 0:12]))
    dve.engine_nop().then_inc(asked, 1)
    dve.wait_ge(given, n + 1)
    link(dve.tensor_scalar(y, y, st[0:r, 12:13], st[0:r, 14:15], ALU.subtract, ALU.mult))
    link(dve.tensor_tensor(y, y, gb[0:r, 0], ALU.mult))
    return dve.tensor_tensor(y, y, gb[0:r, 1], ALU.add)


def inverse_root(act, eps, st, r, asked, given, own, n):
    act.wait_ge(asked, n + 1)
    act.activation(st[0:r, 14:15], st[0:r, 13:14], ACT.Ln, bias=eps[0:r]).then_inc(own, 1)
    act.wait_ge(own, n + 1)
    act.activation(st[0:r, 14:15], st[0:r, 14:15], ACT.Exp, scale=-0.5).then_inc(given, 1)


def mix_out(c, mT, y, x1T):
    nc, ps, dr = c.nc, c.ps, c.dram
    s = Semaphores(c, "mo")
    with ExitStack() as ctx:
        sb = lambda n, sh: ctx.enter_context(nc.sbuf_tensor(f"mo_{n}", sh, F32))
        w = sb("w", [P, KT, D])
        gb = sb("gb", [P, 2, D])
        xt = sb("xt", [P, 2, D])
        st = sb("st", [P, 16])
        block = ctx.enter_context(nc.Block())

        @block.sync
        def _(sp):
            sp.dma_start(w[:], dr["w_out"]).then_inc(s["w"], 16)
            for k in range(2):
                sp.dma_start(gb[:, k, :], dr["ln1"][k:k + 1, :].to_broadcast([P, D])).then_inc(s["gb"], 16)
            for t in range(NTT):
                if t >= 2:
                    sp.wait_ge(s["read"], t - 1)
                sp.dma_start(xt[0:rows(t), t % 2], dr["x"][t * BLK:t * BLK + rows(t)]).then_inc(s["x"], 16)
                sp.wait_ge(s["x"], 16 * (t + 1))
            for t in range(NTT):
                sp.wait_ge(s["y"], t + 1)
                sp.dma_start(dr["s_x1"][t * BLK:t * BLK + rows(t)], y[0:rows(t), t, :]).then_inc(s["stored"], 16)
            sp.wait_ge(s["stored"], 16 * NTT)

        @block.tensor
        def _(pe):
            pe.wait_ge(s["w"], 16)

            def turn(t):
                r = rows(t)
                pe.wait_ge(s["y"], t + 1)
                if t:
                    pe.wait_ge(s["trc"], t)
                for k in range(KT):
                    tr = pe.transpose(ps[:, 4 + k // 4, (k % 4) * P:(k % 4) * P + r], y[0:r, t, k * P:(k + 1) * P], c.ident[0:r, 0:r])
                tr.then_inc(s["tr"], 1)

            for t in range(NTT):
                r = rows(t)
                if t >= 2:
                    pe.wait_ge(s["read"], t - 1)
                for n in range(2):
                    for k in range(KT):
                        mm = pe.matmul(ps[0:r, 2 * (t % 2) + n, :], mT[:, k, t * BLK:t * BLK + r], w[:, k, n * 512:(n + 1) * 512], start=(k == 0), stop=(k == KT - 1))
                mm.then_inc(s["mm"], 1)
                if t:
                    turn(t - 1)
            turn(NTT - 1)

        @block.vector
        def _(dve):
            link = Link(dve, s["link"])
            dve.wait_ge(s["gb"], 32)
            for t in range(NTT):
                r = rows(t)
                dve.wait_ge(s["mm"], t + 1)
                dve.wait_ge(s["x"], 16 * (t + 1))
                yy = y[0:r, t, :]
                dve.scalar_tensor_tensor(yy.rearrange("p (n w) -> p n w", n=2), xt[0:r, t % 2].rearrange("p (n w) -> p n w", n=2), ALPHA,
                                         ps[0:r, 2 * (t % 2):2 * (t % 2) + 2, :], ALU.mult, ALU.add).then_inc(s["read"], 1)
                dve.wait_ge(s["read"], t + 1)
                norm_rows(dve, (s["asked"], s["given"]), link, yy, r, st, gb, t).then_inc(s["y"], 1)

        @block.scalar
        def _(act):
            def copy(t):
                r = rows(t)
                act.wait_ge(s["tr"], t + 1)
                act.activation(x1T[:, :, t * BLK:t * BLK + r].rearrange("p (a b) t -> p a b t", a=2),
                               ps[:, 4:6, :].rearrange("p a (b t) -> p a b t", b=4)[:, :, :, 0:r], ACT.Copy).then_inc(s["trc"], 1)

            for t in range(NTT):
                inverse_root(act, c.eps, st, rows(t), s["asked"], s["given"], s["own"], t)
                if t:
                    copy(t - 1)
            copy(NTT - 1)


def route(c, x1T, rt):
    nc, ps, dr = c.nc, c.ps, c.dram
    s = Semaphores(c, "rt")
    NG = 4
    FAR = 65536.0
    with ExitStack() as ctx:
        sb = lambda n, sh, dt=F32: ctx.enter_context(nc.sbuf_tensor(f"rt_{n}", sh, dt))
        w = sb("w", [P, KT, NE])
        rb = sb("rb", [P, NE])
        tri = sb("tri", [P, P])
        blk = sb("blk", [P, EB])
        tok = sb("tok", [P, NTT], U32)
        zero = sb("zero", [P, EB + 1], U32)
        sc = sb("sc", [P, NTT, NE])
        bi = sb("bi", [P, NTT * NG, 4])
        rank = sb("rank", [P, NTT * NG, 4])
        gs = sb("gs", [P, NTT, NG])
        grank = sb("grank", [P, NTT, NG])
        a = sb("a", [P, NTT * NG])
        b = sb("b", [P, NTT * NG])
        su = sb("su", [P, NTT])
        gw = sb("gw", [P, NTT, NE])
        at = sb("at", [P, NTT, NE])
        far = sb("far", [P, NTT, NE])
        eq = sb("eq", [P, NTT, NE])
        df = sb("df", [P, TOPK, NTT])
        cnt = sb("cnt", [P, NE])
        nb = sb("nb", [P, NE])
        cum = sb("cum", [P, NE])
        t16 = sb("t16", [P, NE])
        past = sb("past", [P, EB, NE])
        be = sb("be", [P, EB + 1])
        block = ctx.enter_context(nc.Block())
        sel = rank[:].rearrange("p (t g) e -> p t (g e)", g=NG)
        fl = lambda t: t.rearrange("p t e -> p (t e)")

        @block.sync
        def _(sp):
            sp.dma_start(w[:], dr["w_router"]).then_inc(s["in"], 16)
            sp.dma_start(rb[:], dr["router_bias"].to_broadcast([P, NE])).then_inc(s["in"], 16)
            sp.dma_start(tri[:], dr["tri"]).then_inc(s["in"], 16)
            sp.dma_start(blk[:], dr["blk"]).then_inc(s["in"], 16)
            sp.dma_start(tok[:], dr["tok"]).then_inc(s["in"], 16)
            sp.wait_ge(s["zero"], 1)
            sp.dma_start(dr["s_row"].rearrange("(p n) o -> p (n o)", p=P), zero[:]).then_inc(s["cleared"], 16)

        @block.gpsimd
        def _(pool):
            pool.wait_ge(s["in"], 80)
            pool.wait_ge(s["cleared"], 16)
            pool.wait_ge(s["dest"], 1)
            for k in range(TOPK):
                for t in range(NTT):
                    r = rows(t)
                    pool.indirect_dma_start(dr["s_row"], bass.IndirectOffsetOnAxis(rt.dest[0:r, k, t:t + 1], 0),
                                            tok[0:r, t:t + 1], None).then_inc(s["scattered"], 16)
            pool.wait_ge(s["scattered"], 16 * TOPK * NTT)

        @block.tensor
        def _(pe):
            pe.wait_ge(s["in"], 80)
            for t in range(NTT):
                r = rows(t)
                for k in range(KT):
                    mm = pe.matmul(ps[0:r, 0, t * NE:(t + 1) * NE], x1T[:, k, t * BLK:t * BLK + r], w[:, k, :], start=(k == 0), stop=(k == KT - 1))
            mm.then_inc(s["mm"], 1)
            pe.wait_ge(s["sel"], 1)
            for t in range(NTT):
                r = rows(t)
                out = ps[0:r, 1, t * NE:(t + 1) * NE]
                pe.matmul(out, tri[0:r, 0:r], sel[0:r, t, :], start=True, stop=(t == 0))
                for u in range(t):
                    pe.matmul(out, c.ones[:, 0:r], sel[:, u, :], start=False, stop=(u == t - 1))
            for t in range(NTT):
                mm = pe.matmul(ps[:, 2, 0:NE], c.ones[0:rows(t), :], sel[0:rows(t), t, :], start=(t == 0), stop=(t == NTT - 1))
            mm.then_inc(s["counts"], 1)

        @block.scalar
        def _(act):
            act.wait_ge(s["z"], 1)
            act.wait_ge(s["mm"], 1)
            act.activation(fl(sc[:, 0:NBLK, :]), ps[:, 0, 0:NBLK * NE], ACT.Sigmoid)
            act.activation(sc[0:NB, NBLK, :], ps[0:NB, 0, NBLK * NE:NTT * NE], ACT.Sigmoid).then_inc(s["sig"], 1)

        @block.vector
        def _(dve):
            link = Link(dve, s["link"])
            dve.memset(zero[:], 0).then_inc(s["zero"], 1)
            dve.memset(sc[:], 0.5).then_inc(s["z"], 1)
            dve.memset(rank[:], 0.0)
            dve.memset(grank[:], 0.0)
            dve.wait_ge(s["sig"], 1)
            dve.wait_ge(s["in"], 80)
            link(dve.tensor_tensor(bi[:].rearrange("p (t g) e -> p t (g e)", g=NG), sc[:], mid(rb[:], NTT), ALU.add))
            gsv = gs[:].rearrange("p t g -> p (t g)")
            pairs = [(i, j) for i in range(4) for j in range(i + 1, 4)]
            for n, (i, j) in enumerate(pairs):
                x, y = bi[:, :, i], bi[:, :, j]
                link(dve.tensor_tensor(a[:], x, y, ALU.add))
                link(dve.tensor_copy(gsv, a[:]) if n == 0 else dve.tensor_tensor(gsv, gsv, a[:], ALU.max))
                dve.tensor_tensor(a[:], y, x, ALU.is_gt)
                link(dve.tensor_tensor(b[:], x, y, ALU.is_ge))
                dve.tensor_tensor(rank[:, :, i], rank[:, :, i], a[:], ALU.add)
                link(dve.tensor_tensor(rank[:, :, j], rank[:, :, j], b[:], ALU.add))
            for i, j in pairs:
                x, y = gs[:, :, i], gs[:, :, j]
                dve.tensor_tensor(a[:, 0:NTT], y, x, ALU.is_gt)
                link(dve.tensor_tensor(b[:, 0:NTT], x, y, ALU.is_ge))
                dve.tensor_tensor(grank[:, :, i], grank[:, :, i], a[:, 0:NTT], ALU.add)
                link(dve.tensor_tensor(grank[:, :, j], grank[:, :, j], b[:, 0:NTT], ALU.add))
            rk, grk = fl(rank[:]), fl(grank[:])
            dve.tensor_scalar(rk, rk, 2.0, None, ALU.is_lt)
            link(dve.tensor_scalar(grk, grk, 1.0, None, ALU.is_lt))
            dve.tensor_tensor(rank[:], rank[:], last(grk, 4), ALU.mult).then_inc(s["sel"], 1)
            dve.wait_ge(s["sel"], 1)
            link(dve.tensor_tensor(fl(gw[:]), rk, fl(sc[:]), ALU.mult))
            link(dve.tensor_reduce(su[:], gw[:], AX.X, ALU.add))
            link(dve.reciprocal(su[:], su[:]))
            link(dve.tensor_tensor(gw[:], gw[:], last(su[:], NE), ALU.mult))
            dve.wait_ge(s["counts"], 1)
            link(dve.tensor_copy(cnt[:], ps[:, 2, 0:NE]))
            link(dve.tensor_scalar(nb[:], cnt[:], 0.0, None, ALU.is_gt))
            for k in range(1, NTT):
                link(dve.tensor_scalar(t16[:], cnt[:], float(k * P), None, ALU.is_gt))
                link(dve.tensor_tensor(nb[:], nb[:], t16[:], ALU.add))
            link(dve.tensor_tensor_scan(cum[:], c.ones[:, 0:NE], nb[:], 0.0, ALU.mult, ALU.add))
            link(dve.tensor_tensor(past[:], last(blk[:], NE), mid(cum[:], EB), ALU.is_ge))
            link(dve.tensor_reduce(be[:, 0:EB], past[:], AX.X, ALU.add))
            dve.tensor_scalar(be[:, 0:EB], be[:, 0:EB], NE - 1.0, None, ALU.min)
            link(dve.tensor_copy(be[:, EB:EB + 1], cum[:, NE - 1:NE]))
            dve.tensor_copy(rt.plan[:], be[0:1, :])
            link(dve.tensor_tensor(nb[:], cum[:], nb[:], ALU.subtract))
            link(dve.tensor_scalar(nb[:], nb[:], float(P), None, ALU.mult))
            dve.memset(at[:, NBLK, :], 0.0)
            link(dve.tensor_tensor(at[:, 0:NBLK, :], ps[:, 1, 0:NBLK * NE].rearrange("p (t e) -> p t e", e=NE), mid(nb[:], NBLK), ALU.add))
            link(dve.tensor_tensor(at[0:NB, NBLK, :], ps[0:NB, 1, NBLK * NE:NTT * NE], nb[0:NB], ALU.add))
            link(dve.tensor_scalar(fl(far[:]), rk, -FAR, FAR, ALU.mult, ALU.add))
            link(dve.tensor_tensor(at[:], at[:], far[:], ALU.add))
            link(dve.tensor_reduce(df[:, 0, :], at[:], AX.X, ALU.min))
            link(dve.tensor_tensor(eq[:], at[:], last(df[:, 0, :], NE), ALU.is_equal))
            link(dve.tensor_tensor(eq[:], eq[:], gw[:], ALU.mult))
            link(dve.tensor_reduce(rt.wt[:, 0, :], eq[:], AX.X, ALU.add))
            link(dve.tensor_scalar(fl(far[:]), fl(far[:]), -2.0, None, ALU.mult))
            link(dve.tensor_tensor(at[:], at[:], far[:], ALU.add))
            link(dve.tensor_reduce(df[:, 1, :], at[:], AX.X, ALU.max))
            link(dve.tensor_tensor(eq[:], at[:], last(df[:, 1, :], NE), ALU.is_equal))
            link(dve.tensor_tensor(eq[:], eq[:], gw[:], ALU.mult))
            link(dve.tensor_reduce(rt.wt[:, 1, :], eq[:], AX.X, ALU.add))
            dve.tensor_copy(rt.dest[:], df[:]).then_inc(s["dest"], 1)


def ple(c, x1T, y):
    nc, ps, dr = c.nc, c.ps, c.dram
    s = Semaphores(c, "pl")
    with ExitStack() as ctx:
        sb = lambda n, sh: ctx.enter_context(nc.sbuf_tensor(f"pl_{n}", sh, F32))
        wg = sb("wg", [P, KT, D])
        wp = sb("wp", [P, 2, D])
        pT = sb("pT", [P, 2, T])
        sg = sb("sg", [P, 2, D])
        block = ctx.enter_context(nc.Block())

        @block.sync
        def _(sp):
            sp.dma_start(pT[:], dr["pT"]).then_inc(s["in"], 16)
            sp.dma_start(wp[:], dr["w_ple"]).then_inc(s["in"], 16)
            sp.dma_start(wg[:], dr["w_ple_gate"]).then_inc(s["in"], 16)

        @block.tensor
        def _(pe):
            pe.wait_ge(s["in"], 48)
            for t in range(NTT):
                r = rows(t)
                tk = slice(t * BLK, t * BLK + r)
                q = 4 * (t % 2)
                if t >= 2:
                    pe.wait_ge(s["read"], t - 1)
                for n in range(2):
                    for k in range(KT):
                        pe.matmul(ps[0:r, q + n, :], x1T[:, k, tk], wg[:, k, n * 512:(n + 1) * 512], start=(k == 0), stop=(k == KT - 1))
                    for k in range(2):
                        mm = pe.matmul(ps[0:r, q + 2 + n, :], pT[:, k, tk], wp[:, k, n * 512:(n + 1) * 512], start=(k == 0), stop=(k == 1))
                mm.then_inc(s["mm"], 1)

        @block.scalar
        def _(act):
            for t in range(NTT):
                r, q = rows(t), 4 * (t % 2)
                act.wait_ge(s["mm"], t + 1)
                if t >= 2:
                    act.wait_ge(s["used"], t - 1)
                act.activation(sg[0:r, t % 2].rearrange("p (n w) -> p n w", n=2), ps[0:r, q:q + 2, :], ACT.Sigmoid).then_inc(s["sig"], 1)

        @block.vector
        def _(dve):
            for t in range(NTT):
                r, q = rows(t), 4 * (t % 2)
                dve.wait_ge(s["sig"], t + 1)
                g = sg[0:r, t % 2].rearrange("p (n w) -> p n w", n=2)
                dve.tensor_tensor(g, g, ps[0:r, q + 2:q + 4, :], ALU.mult).then_inc(s["read"], 1)
                dve.wait_ge(s["read"], t + 1)
                dve.scalar_tensor_tensor(y[0:r, t, :], y[0:r, t, :], ALPHA, sg[0:r, t % 2], ALU.mult, ALU.add).then_inc(s["used"], 1)


def experts(c, rt):
    nc, ps, dr = c.nc, c.ps, c.dram
    HT = DE // P
    w_here = [c.sem(f"ex_w_here{j}") for j in range(2)]
    row_here = [c.sem(f"ex_row_here{j}") for j in range(2)]
    x_here = [c.sem(f"ex_x_here{j}") for j in range(2)]
    stored = [c.sem(f"ex_stored{j}") for j in range(2)]
    s = Semaphores(c, "ex")
    with ExitStack() as ctx:
        sb = lambda n, sh, dt=F32: ctx.enter_context(nc.sbuf_tensor(f"ex_{n}", sh, dt))
        wg = sb("wg", [P, 2, KT, DE])
        wu = sb("wu", [P, 2, KT, DE])
        wd = sb("wd", [P, 2, HT, D])
        row = sb("row", [P, 2], U32)
        xb = sb("xb", [P, 2, D])
        xT = sb("xT", [P, 2, KT, P])
        a = sb("a", [P, DE])
        aT = sb("aT", [P, HT, P])
        ob = sb("ob", [P, 2, D])
        zero = c.outs[:].rearrange("p m t -> p (m t)")[:, NTT * D:(NTT + 1) * D]
        block = ctx.enter_context(nc.Block())

        def blocks(eng):
            n = eng.value_load(rt.plan[0:1, EB:EB + 1], min_val=1, max_val=EB)
            with eng.Fori(0, EB // 2) as i:
                for j in range(2):
                    with eng.If(2 * i + j < n):
                        yield i, j

        @block.sync
        def _(sp):
            def rows_of(i, j):
                sp.dma_start(row[:, j:j + 1], dr["s_row"][bass.ds(i * P, P)]).then_inc(row_here[j], 16)

            rows_of(0, 0)
            for i, j in blocks(sp):
                n = 2 * i + j
                e = sp.value_load(rt.plan[0:1, bass.ds(n, 1)], min_val=0, max_val=NE - 1)
                sp.wait_ge(s["down"], n + 1)
                sp.dma_start(wg[:, j], dr["w_eg"][bass.ds(e, 1)].rearrange("o p k n -> p (o k) n")).then_inc(w_here[j], 16)
                sp.dma_start(wu[:, j], dr["w_eu"][bass.ds(e, 1)].rearrange("o p k n -> p (o k) n")).then_inc(w_here[j], 16)
                sp.dma_start(wd[:, j], dr["w_ed"][bass.ds(e, 1)].rearrange("o p k n -> p (o k) n")).then_inc(w_here[j], 16)
                sp.wait_ge(s["turned"], n + 1)
                rows_of(n + 1, 1 - j)
            sp.wait_ge(s["zero"], 1)
            n = sp.value_load(rt.plan[0:1, EB:EB + 1], min_val=1, max_val=EB)
            with sp.Fori(0, EB) as i:
                with sp.If(i >= n):
                    sp.dma_start(dr["s_rows"][bass.ds(i * P, P)], zero).then_inc(s["cleared"], 16)
                with sp.If(i < n):
                    sp.sem_inc(s["cleared"], 16)
            sp.wait_ge(s["cleared"], 16 * EB)

        @block.gpsimd
        def _(pool):
            def gather(j):
                pool.indirect_dma_start(xb[:, j, :], None, dr["s_x1"], bass.IndirectOffsetOnAxis(row[:, j:j + 1], 0)).then_inc(x_here[j], 16)

            pool.memset(zero, 0.0).then_inc(s["zero"], 1)
            pool.wait_ge(row_here[0], 16)
            gather(0)
            for i, j in blocks(pool):
                n = 2 * i + j
                pool.wait_ge(row_here[1 - j], 16 * i + 16 * (1 + j))
                pool.wait_ge(s["turned"], n + 1)
                pool.sem_inc(s["gathering"], 1)
                gather(1 - j)

        @block.tensor
        def _(pe):
            pe.sem_inc(s["down"], 2)

            def turn(i, j):
                for k in range(KT):
                    t = pe.transpose(ps[:, k // 4, (k % 4) * P:(k % 4 + 1) * P], xb[:, j, k * P:(k + 1) * P], c.ident[:])
                t.then_inc(s["turned"], 1)

            pe.wait_ge(x_here[0], 16)
            turn(0, 0)
            for i, j in blocks(pe):
                n = 2 * i + j
                pe.wait_ge(s["x_copied"], n + 1)
                pe.wait_ge(w_here[j], 48 * i + 48)
                for o, w in ((2, wg), (3, wu)):
                    for k in range(KT):
                        mm = pe.matmul(ps[:, o, :], xT[:, j, k, :], w[:, j, k, :], start=(k == 0), stop=(k == KT - 1))
                    mm.then_inc(s["gate" if o == 2 else "up"], 1)
                pe.wait_ge(x_here[1 - j], 16 * i + 16 * (1 + j))
                turn(n + 1, 1 - j)
                pe.wait_ge(s["a"], n + 1)
                for k in range(HT):
                    t = pe.transpose(ps[:, 4, k * P:(k + 1) * P], a[:, k * P:(k + 1) * P], c.ident[:])
                t.then_inc(s["a_turned"], 1)
                pe.wait_ge(s["a_copied"], n + 1)
                pe.wait_ge(s["o_copied"], 2 * n + 2)
                for o in range(2):
                    for k in range(HT):
                        mm = pe.matmul(ps[:, 5 + o, :], aT[:, k, :], wd[:, j, k, o * 512:(o + 1) * 512], start=(k == 0), stop=(k == HT - 1))
                mm.then_inc(s["down"], 1)

        @block.scalar
        def _(act):
            def x_copy(j):
                act.activation(xT[:, j].rearrange("p (a k) t -> p a (k t)", a=2), ps[:, 0:2, :], ACT.Copy).then_inc(s["x_copied"], 1)

            act.wait_ge(s["turned"], 1)
            x_copy(0)
            for i, j in blocks(act):
                n = 2 * i + j
                act.wait_ge(s["gate"], n + 1)
                act.activation(a[:], ps[:, 2, :], ACT.Silu).then_inc(s["silu"], 1)
                act.wait_ge(s["turned"], n + 2)
                x_copy(1 - j)
                act.wait_ge(s["down"], n + 3)
                act.wait_ge(stored[j], 16 * i + 16)
                act.activation(ob[:, j, 0:512], ps[:, 5, :], ACT.Copy).then_inc(s["o_copied"], 1)
                act.wait_ge(s["o_copied"], 2 * n + 4)
                act.dma_start(dr["s_rows"][bass.ds(n * P, P)], ob[:, j, :]).then_inc(stored[j], 16)
            n = act.value_load(rt.plan[0:1, EB:EB + 1], min_val=1, max_val=EB)
            act.wait_ge(stored[0], 16 * ((n + 1) // 2) + 16)
            act.wait_ge(stored[1], 16 * (n // 2) + 16)
            act.sem_inc(s["all_stored"], 1)

        @block.vector
        def _(dve):
            dve.sem_inc(s["o_copied"], 2)
            dve.sem_inc(stored[0], 16)
            dve.sem_inc(stored[1], 16)
            for i, j in blocks(dve):
                n = 2 * i + j
                dve.wait_ge(s["up"], n + 1)
                dve.wait_ge(s["silu"], n + 1)
                dve.tensor_tensor(a[:], a[:], ps[:, 3, :], ALU.mult).then_inc(s["a"], 1)
                dve.wait_ge(s["a_turned"], n + 1)
                dve.tensor_copy(aT[:].rearrange("p k t -> p (k t)"), ps[:, 4, :]).then_inc(s["a_copied"], 1)
                dve.wait_ge(s["down"], n + 3)
                dve.wait_ge(stored[j], 16 * i + 16)
                dve.tensor_copy(ob[:, j, 512:1024], ps[:, 6, :]).then_inc(s["o_copied"], 1)


def last_norm(c, y, rt):
    nc, dr = c.nc, c.dram
    s = Semaphores(c, "ln")
    with ExitStack() as ctx:
        sb = lambda n, sh: ctx.enter_context(nc.sbuf_tensor(f"ln_{n}", sh, F32))
        gb = sb("gb", [P, 2, D])
        st = sb("st", [P, 16])
        er = sb("er", [P, TOPK, 3, D])
        block = ctx.enter_context(nc.Block())

        @block.gpsimd
        def _(pool):
            for t in range(NTT):
                r = rows(t)
                if t >= 3:
                    pool.wait_ge(s["added"], t - 2)
                for k in range(TOPK):
                    pool.indirect_dma_start(er[0:r, k, t % 3, :], None, dr["s_rows"], bass.IndirectOffsetOnAxis(rt.dest[0:r, k, t:t + 1], 0))\
                        .then_inc(s[f"rows{t % 3}"], 16)

        @block.sync
        def _(sp):
            for k in range(2):
                sp.dma_start(gb[:, k, :], dr["ln2"][k:k + 1, :].to_broadcast([P, D])).then_inc(s["in"], 16)
            for t in range(NTT):
                sp.wait_ge(s["y"], t + 1)
                sp.dma_start(dr["o_y"][t * BLK:t * BLK + rows(t)], y[0:rows(t), t, :]).then_inc(s["out"], 16)
            sp.wait_ge(s["out"], 16 * NTT)

        @block.vector
        def _(dve):
            link = Link(dve, s["link"])
            dve.wait_ge(s["in"], 32)
            for t in range(NTT):
                r = rows(t)
                yy = y[0:r, t, :]
                dve.wait_ge(s[f"rows{t % 3}"], 32 * (t // 3 + 1))
                link(dve.scalar_tensor_tensor(yy, er[0:r, 0, t % 3, :], rt.wt[0:r, 0, t:t + 1], yy, ALU.mult, ALU.add))
                dve.scalar_tensor_tensor(yy, er[0:r, 1, t % 3, :], rt.wt[0:r, 1, t:t + 1], yy, ALU.mult, ALU.add).then_inc(s["added"], 1)
                dve.wait_ge(s["added"], t + 1)
                norm_rows(dve, (s["asked"], s["given"]), link, yy, r, st, gb, t).then_inc(s["y"], 1)

        @block.scalar
        def _(act):
            for t in range(NTT):
                inverse_root(act, c.eps, st, rows(t), s["asked"], s["given"], s["own"], t)


def attention(c):
    nc = c.nc
    with ExitStack() as ctx:
        sb = lambda n, sh: ctx.enter_context(nc.sbuf_tensor(f"at_{n}", sh, F32))
        z = sb("z", [P, 10, T])
        q, kv = z[:, 0:GR, :], z[:, GR:10, :]
        c.gtok = sb("gtok", [P, NBLK, 24])
        kc = sb("kc", [P, NB + 1, NCMP])
        vc = sb("vc", [NCMP, NB + 1, P])
        project(c, "nsa", c.dram["w_nsa"], 10, z)
        nsa_prepare(c, q, kv, c.small)
        with nc.sbuf_tensor("at_Ss", [64, SO_END], F32) as Ss:
            nsa_samples_scores(c, q, kv, Ss, kc, vc)
            nsa_samples_finish(c, kv, Ss, vc)
        nsa_prompt(c, q, kv, kc, vc)


def window_states(c):
    nc, dr = c.nc, c.dram
    sem = c.sem("window_moved")
    with nc.Block() as block:
        @block.sync
        def _(sp):
            sp.dma_start(dr["o_win"], dr["state_win"][:, 1:WIN, :]).then_inc(sem, 16)
            sp.wait_ge(sem, 16)


def layer(nc, dram):
    c = Core(nc, dram)
    c.ident = nc.alloc_sbuf_tensor("ident", [P, P], F32)
    c.ones = nc.alloc_sbuf_tensor("ones", [P, P], F32)
    c.eps = nc.alloc_sbuf_tensor("eps", [P, 1], F32)
    c.xT = nc.alloc_sbuf_tensor("xT", [P, KT, T], F32)
    outs = nc.alloc_sbuf_tensor("outs", [P, 3 * H4, T], F32)
    c.outs = outs
    c.oT = [outs[:, b * H4:(b + 1) * H4, :] for b in range(3)]
    x1T = c.xT
    y = outs[:].rearrange("p m t -> p (m t)")[:, 0:NTT * D].rearrange("p (t d) -> p t d", d=D)
    load_shared(c)
    window_states(c)
    with nc.sbuf_tensor("small", [96, T], F32) as small:
        c.small = small
        small_projection(c, "small", small)
        attention(c)
        c.retire()
        deltanet(c, small)
        c.retire()
    hgrn2(c)
    c.retire()
    with nc.sbuf_tensor("mT", [P, KT, T], F32) as mT:
        merge(c, mT)
        mix_out(c, mT, y, x1T)
    rt = Routing(nc)
    route(c, x1T, rt)
    ple(c, x1T, y)
    experts(c, rt)
    last_norm(c, y, rt)



def bucket(dist):
    n = np.maximum(dist, 0)
    exact = NBUCK // 2
    rel = np.log(np.maximum(n, 1).astype(np.float32) / np.float32(exact)) / np.float32(np.log(128 / exact))
    large = np.minimum(exact + (rel * np.float32(NBUCK - exact)).astype(np.int32), NBUCK - 1)
    return np.where(n < exact, n, large)


def constants():
    f = np.float32
    hot = np.zeros((33, LSEL + LWIN), f)
    for off, d, live in ((0, 1151 - np.arange(LSEL), lambda d: d >= 0), (LSEL, 639 - np.arange(LWIN), lambda d: (d >= 0) & (d < WIN))):
        ok = live(d)
        hot[bucket(d)[ok], off + np.where(ok)[0]] = 1
        hot[32, off + np.where(~ok)[0]] = NEG
    i = np.arange(P)
    up = np.zeros((P, LEV, P), f)
    for l in range(LEV):
        h = 1 << l
        same = (i[:, None] // (2 * h)) == (i[None, :] // (2 * h))
        up[:, l, :] = same & (i[:, None] % (2 * h) < h) & (i[None, :] % (2 * h) >= h)
    lo = np.stack([i[None, :] <= i[:, None], i[None, :] < i[:, None], up[:, 0, :].T > 0], 1).astype(f)
    r = np.arange(64)
    own = np.where(r[:, None] // NH == np.arange(NB)[None, :], 0, NEG).astype(f)
    grp = (r[:, None] // GR == r[None, :] // GR).astype(f)
    c0, b0 = np.arange(NCMP) * STR, np.arange(NSB) * SELB
    imap = ((c0[:, None] <= b0[None, :] + SELB - 1) & (c0[:, None] + 2 * STR - 1 >= b0[None, :])).astype(f)
    idx = np.broadcast_to(np.arange(NSB, dtype=f), (64, NSB)).copy()
    return {"ident": np.eye(P, dtype=f), "hot": hot, "up": up, "lo": lo, "own": own, "grp": grp, "imap": imap, "idx": idx,
            "tri": (i[:, None] < i[None, :]).astype(f), "blk": np.broadcast_to(np.arange(EB, dtype=f), (P, EB)).copy(),
            "tok": (np.arange(NTT)[None, :] * P + i[:, None]).astype(np.uint32)}


def tiles(w):
    k = w.shape[0] // P
    return np.ascontiguousarray(w.reshape(k, P, -1, P).transpose(2, 1, 0, 3))


def rows_by_partition(w):
    return np.ascontiguousarray(w.reshape(w.shape[0] // P, P, -1).transpose(1, 0, 2))


def lay_in(a):
    w = a["w_in"][0]
    at = np.cumsum([0, 512, 768, 24, 1536, 4, 4, 512, 512, 512, 512, 512, 3072])
    (nq, nkv, ng, dqkv, da, db, dg, hq, hf, hi, hg, mg) = (w[:, at[i]:at[i + 1]] for i in range(12))
    nq = nq.reshape(D, G, GR, DH).transpose(0, 2, 1, 3).reshape(D, 512)
    small = np.zeros((D, 96), w.dtype)
    small[:, 0:24], small[:, 32:36], small[:, 64:68] = ng, da, db
    x = np.concatenate([a["x_prompt"][0], a["x_sample"][:, 0]], 0)
    pl = np.concatenate([a["p_prompt"][0, 0], a["p_sample"][0, :, 0]], 0)
    wb = a["w_branch"][0].copy()
    wb[0] = wb[0].reshape(G, GR, DH, D).transpose(1, 0, 2, 3).reshape(512, D)
    state = lambda s: np.ascontiguousarray(s[0].transpose(2, 1, 0, 3).reshape(P, H4 * NB, P))
    out = {
        "xT": rows_by_partition(np.ascontiguousarray(x.T)), "x": x,
        "pT": rows_by_partition(np.ascontiguousarray(pl.T)),
        "w_nsa": tiles(np.concatenate([nq, nkv], 1)), "w_small": rows_by_partition(small),
        "w_dn": tiles(np.concatenate([dqkv, dg], 1)), "w_hg": tiles(np.concatenate([hq, hf, hi, hg], 1)),
        "w_mg": np.ascontiguousarray(tiles(mg).reshape(3, KT, P, KT, P).transpose(1, 0, 2, 3, 4).reshape(24, P, KT, P)),
        "w_br": np.ascontiguousarray(np.stack([tiles(wb[b]) for b in range(3)], 1).reshape(24, P, H4, P)),
        "w_out": rows_by_partition(a["w_out"][0]),
        "rb_aug": np.concatenate([a["rel_bias"], np.ones((1, NH), np.float32)], 0),
        "cache": np.ascontiguousarray(a["cache_nsa"][0].reshape(NPOOL, P, 512)),
        "table": np.ascontiguousarray(a["page_table"].reshape(1, NB * PAGES).astype(np.int32)),
        "state_win": np.ascontiguousarray(a["state_win"][0].reshape(NB, WIN, 2 * P)),
        "w_cmp1": np.ascontiguousarray(a["w_cmp1"][0].reshape(2, 32, DH, P).transpose(2, 0, 1, 3)),
        "w_cmp2": np.ascontiguousarray(a["w_cmp2"][0].transpose(1, 0, 2)),
        "pe_cmp": np.ascontiguousarray(a["pe_cmp"][0].transpose(2, 0, 1)),
        "conv_w": np.ascontiguousarray(a["dn_conv_w"][0].reshape(4, 12, P).transpose(2, 1, 0)),
        "conv_state": np.ascontiguousarray(a["state_dn_conv"][0].reshape(NB, 3, 12, P).transpose(3, 2, 0, 1)),
        "dn_par": np.stack([a["dn_a_log"][0], a["dn_dt_bias"][0]], 1),
        "dn_norm": np.ascontiguousarray(a["dn_norm_w"][0].reshape(P, 1)), "hg_norm": np.ascontiguousarray(a["hg_norm_w"][0].reshape(P, 1)),
        "state_dn": state(a["state_dn"]), "state_hg": state(a["state_hg"]),
        "ln1": np.concatenate([a["ln1_g"], a["ln1_b"]], 0), "ln2": np.concatenate([a["ln2_g"], a["ln2_b"]], 0),
        "w_router": rows_by_partition(a["w_router"]), "router_bias": a["router_bias"].reshape(1, NE),
        "w_eg": np.ascontiguousarray(a["w_exp_gate"][0].reshape(NE, KT, P, DE).transpose(0, 2, 1, 3)),
        "w_eu": np.ascontiguousarray(a["w_exp_up"][0].reshape(NE, KT, P, DE).transpose(0, 2, 1, 3)),
        "w_ed": np.ascontiguousarray(a["w_exp_down"][0].reshape(NE, DE // P, P, D).transpose(0, 2, 1, 3)),
        "w_ple": rows_by_partition(a["w_ple"][0]), "w_ple_gate": rows_by_partition(a["w_ple_gate"][0]),
    }
    return {**out, **constants()}


OUTS = {"o_y": (T, D), "o_kvT": (P, 6, T), "o_win": (NB, WIN - 1, 2 * P), "o_conv": (P, 12, 3 + 3 * NB),
        "o_dn_p": (P, H4 * P), "o_dn_s": (P, H4 * NB, P), "o_hg_p": (P, H4, P), "o_hg_s": (P, H4 * NB, P)}
SCRATCH = {"s_gate": ((24, NB), F32), "s_bias": ((NH, P, LSEL + LWIN), F32), "s_x1": ((T, D), F32),
           "s_row": (((EB + 1) * P, 1), U32), "s_rows": ((EB * P, D), F32)}


def lay_out(o):
    kv = np.ascontiguousarray(np.asarray(o["o_kvT"]).transpose(2, 1, 0)).reshape(T, 6, G, DH)
    rows_, win = kv[:, 0:4], kv[:, 4:6]
    st = np.asarray(o["o_conv"])
    cp = st[:, :, 0:3].transpose(2, 1, 0).reshape(3, 1536)
    cs = st[:, :, 3:].reshape(P, 12, NB, 3).transpose(2, 3, 1, 0).reshape(NB, 3, 1536)
    y = np.asarray(o["o_y"])
    ws = np.concatenate([np.asarray(o["o_win"]).reshape(NB, WIN - 1, 2, G, DH), win[TP:, None]], 1)
    state = lambda s: np.ascontiguousarray(np.asarray(s).reshape(P, H4, NB, P).transpose(2, 1, 0, 3))[None]
    pst = lambda s: np.ascontiguousarray(np.asarray(s).reshape(P, H4, P).transpose(1, 0, 2))[None, None]
    return (y[None, 0:TP], y[TP:, None], rows_[None, None, 0:TP], rows_[None, TP:, None],
            win[None, None, TP - WIN:TP], ws[None], cp[None, None], cs[None],
            pst(o["o_dn_p"]), state(o["o_dn_s"]), pst(o["o_hg_p"]), state(o["o_hg_s"]))


def kernel(**inputs):
    import concourse.bacc as bacc
    from concourse.bass_utils import run_bass_kernel_spmd

    nc = bacc.Bacc("TRN2", target_bir_lowering=False, num_devices=1)
    arrays = {f"in_{n}": np.ascontiguousarray(a) for n, a in lay_in({k: np.asarray(v) for k, v in inputs.items()}).items()}
    dram = {n[3:]: nc.dram_tensor(n, a.shape, mybir.dt.from_np(a.dtype), kind="ExternalInput").ap() for n, a in arrays.items()}
    for n, shape in OUTS.items():
        dram[n] = nc.dram_tensor(f"out_{n}", shape, F32, kind="ExternalOutput").ap()
    for n, (shape, dt) in SCRATCH.items():
        dram[n] = nc.dram_tensor(f"scratch_{n}", shape, dt, kind="Internal").ap()
    layer(nc, dram)
    r = run_bass_kernel_spmd(nc, [arrays], core_ids=[0])
    return lay_out({n: r.results[0][f"out_{n}"] for n in OUTS})
```

```python
from contextlib import ExitStack

import concourse.bass as bass
import numpy as np
from concourse import mybir

F32 = mybir.dt.float32
I32 = mybir.dt.int32
U32 = mybir.dt.uint32
ALU = mybir.AluOpType
ACT = mybir.ActivationFunctionType
AX = mybir.AxisListType

P = 128
D = 1024
KT = D // P
TP = 1024
NB = 8
T = TP + NB
NW = 3
W = T // NW
BLK = 128
NBLK = TP // BLK
DH = 64
GR = 4
G = 2
NH = G * GR
PAST = 1024
PAGES = PAST // P
NPOOL = 80
WIN = 512
STR = 16
NCMP = TP // STR - 1
SELB = 64
NSB = 17
NBUCK = 32
LSEL = 1280
LWIN = 768
NEG = -1e30
H4 = 4
LEV = 7
NE = 16
TOPK = 2
EB = (TOPK * T + NE * (P - 1)) // P
DE = 512
ALPHA = 2 ** 0.25
EPS = 1e-6
NTT = NBLK + 1


def mid(ap, n):
    return ap.unsqueeze(1).to_broadcast([ap.shape[0], n, ap.shape[1]])


def last(ap, n):
    return ap.unsqueeze(2).to_broadcast([ap.shape[0], ap.shape[1], n])


class Link:

    def __init__(self, eng, sem):
        self.eng, self.sem, self.n = eng, sem, 0

    def __call__(self, ins):
        self.n += 1
        ins.then_inc(self.sem, 1)
        self.eng.wait_ge(self.sem, self.n)


class Semaphores(dict):

    def __init__(self, core, stage):
        self.core, self.stage = core, stage

    def __missing__(self, name):
        self[name] = self.core.sem(f"{self.stage}_{name}")
        return self[name]


class Core:

    def __init__(self, nc, dram):
        self.nc = nc
        self.dram = dram
        self.ps = nc.alloc_psum_tensor("ps", [P, 8, 512], F32)

        self.held = []

    def sem(self, name):
        self.held.append(self.nc.alloc_semaphore(name))
        return self.held[-1]

    def retire(self):
        self.nc.all_engine_barrier()
        self.nc.clear_and_free_semaphores(self.held)
        self.nc.all_engine_barrier()
        self.held = []


class Routing:

    def __init__(self, nc):
        self.dest = nc.alloc_sbuf_tensor("rt_dest", [P, TOPK, NTT], U32)
        self.wt = nc.alloc_sbuf_tensor("rt_wt", [P, TOPK, NTT], F32)
        self.plan = nc.alloc_sbuf_tensor("rt_plan", [1, EB + 1], I32)


def project(c, name, wt, ntiles, dst, conv=None):
    nc, ps, xT = c.nc, c.ps, c.xT
    w_here = [c.sem(f"{name}_w_here{j}") for j in range(2)]
    z_ready = c.sem(f"{name}_z_ready")
    z_copied = c.sem(f"{name}_z_copied")
    assert ntiles % 2 == 0
    with nc.sbuf_tensor(f"{name}_w", [P, 2, KT, P], F32) as wb, nc.Block() as block:
        @block.sync
        def _(sp):
            with sp.Fori(0, ntiles // 2) as i:
                for j in range(2):
                    sp.wait_ge(z_ready, 2 * i + j + 1)
                    sp.dma_start(wb[:, j], wt[2 * i + j]).then_inc(w_here[j], 16)

        @block.tensor
        def _(pe):
            pe.sem_inc(z_ready, 2)
            with pe.Fori(0, ntiles // 2) as i:
                for j in range(2):
                    pe.wait_ge(w_here[j], 16 * i + 16)
                    pe.wait_ge(z_copied, 2 * i + j + 1)
                    for n in range(NW):
                        for k in range(KT):
                            mm = pe.matmul(ps[:, 3 * j + n, 0:W], wb[:, j, k, :], xT[:, k, n * W:(n + 1) * W],
                                           start=(k == 0), stop=(k == KT - 1))
                    mm.then_inc(z_ready, 1)

        @block.scalar
        def _(act):
            act.sem_inc(z_copied, 2)

            def copies(first, end, silu):
                with act.Fori(first // 2, end // 2) as i:
                    for j in range(2):
                        act.wait_ge(z_ready, 2 * i + j + 3)
                        act.activation(dst[:, 2 * i + j, :].rearrange("p (n w) -> p n w", n=NW),
                                       ps[:, 3 * j:3 * j + NW, 0:W], ACT.Copy).then_inc(z_copied, 1)
                        if silu:
                            conv.silu(act, i, j)

            if conv:
                copies(0, conv.NT, True)
            copies(conv.NT if conv else 0, ntiles, False)

        if conv:
            @block.vector
            def _(dve):
                conv.vector(dve, z_copied)

            @block.gpsimd
            def _(pool):
                conv.store(pool)


def load_shared(c, w_small):
    nc, dr = c.nc, c.dram
    loaded = c.sem("shared_loaded")
    with nc.Block() as block:
        @block.sync
        def _(sp):
            sp.dma_start(c.xT[:], dr["xT"]).then_inc(loaded, 16)
            sp.dma_start(c.ident[:], dr["ident"]).then_inc(loaded, 16)
            sp.dma_start(w_small, dr["w_small"]).then_inc(loaded, 16)
            sp.wait_ge(loaded, 48)

        @block.vector
        def _(dve):
            dve.memset(c.ones[:], 1.0)
            dve.memset(c.eps[:], EPS)


def small_projection(c, name, wb, dst):
    nc, ps, xT = c.nc, c.ps, c.xT
    z_ready = c.sem(f"{name}_z_ready")
    with nc.Block() as block:
        @block.tensor
        def _(pe):
            for n in range(NW):
                for k in range(KT):
                    mm = pe.matmul(ps[0:96, n, 0:W], wb[:, k, :], xT[:, k, n * W:(n + 1) * W],
                                   start=(k == 0), stop=(k == KT - 1))
            mm.then_inc(z_ready, 1)

        @block.scalar
        def _(act):
            act.wait_ge(z_ready, 1)
            act.activation(dst[:].rearrange("p (n w) -> p n w", n=NW), ps[0:96, 0:NW, 0:W], ACT.Copy)


def nsa_prepare(c, q, kv, small):
    nc, ps, dr = c.nc, c.ps, c.dram
    s = Semaphores(c, "prep")
    with ExitStack() as ctx:
        rb = ctx.enter_context(nc.sbuf_tensor("prep_rb", [33, NH], F32))
        hot = ctx.enter_context(nc.sbuf_tensor("prep_hot", [33, LSEL + LWIN], F32))
        bv = ctx.enter_context(nc.sbuf_tensor("prep_bv", [NH, LSEL + LWIN], F32))
        block = ctx.enter_context(nc.Block())

        @block.sync
        def _(sp):
            sp.dma_start(rb[:], dr["rb_aug"]).then_inc(s["in"], 16)
            sp.dma_start(hot[:], dr["hot"]).then_inc(s["in"], 16)
            sp.dma_start(dr["o_kvT"], kv).then_inc(s["out"], 16)
            sp.wait_ge(s["gate"], 1)
            sp.dma_start(dr["s_gate"], small[0:24, TP:T]).then_inc(s["out"], 16)
            sp.wait_ge(s["biasc"], 1)
            sp.dma_start(dr["s_bias"], bv[:].unsqueeze(1).to_broadcast([NH, P, LSEL + LWIN])).then_inc(s["out"], 16)
            sp.wait_ge(s["out"], 48)

        @block.tensor
        def _(pe):
            pe.wait_ge(s["gate"], 1)
            for i in range(NBLK):
                t = pe.transpose(ps[:, 4, 32 * i:32 * i + 24], small[0:24, i * BLK:(i + 1) * BLK], c.ident[0:24, 0:24])
            t.then_inc(s["gt"], 1)
            pe.wait_ge(s["in"], 32)
            for n in range(4):
                mm = pe.matmul(ps[0:NH, n, :], rb[:], hot[:, 512 * n:512 * n + 512], start=True, stop=True)
            mm.then_inc(s["bias"], 1)

        @block.scalar
        def _(act):
            act.activation(small[0:24, :], small[0:24, :], ACT.Sigmoid).then_inc(s["gate"], 1)

        @block.vector
        def _(dve):
            dve.tensor_scalar(q, q, DH ** -0.5, None, ALU.mult)
            dve.wait_ge(s["gt"], 1)
            dve.tensor_copy(c.gtok[:], ps[:, 4, 0:256].rearrange("p (i h) -> p i h", h=32)[:, :, 0:24])
            dve.wait_ge(s["bias"], 1)
            dve.tensor_copy(bv[:].rearrange("p (n w) -> p n w", n=4), ps[0:NH, 0:4, :]).then_inc(s["biasc"], 1)


def nsa_samples_scores(c, q, kv, Ss, kc, vc, vs, v_here):
    nc, ps, dr = c.nc, c.ps, c.dram
    s = Semaphores(c, "ns")
    HB = NB // 2
    with ExitStack() as ctx:
        sb = lambda n, sh, dt=F32: ctx.enter_context(nc.sbuf_tensor(f"ns_{n}", sh, dt))
        tab = sb("tab", [1, NB * PAGES], I32)
        w1 = sb("w1", [P, 2, 32, P])
        w2 = sb("w2", [P, 2, DH])
        pe_ = sb("pe", [DH, 2, 32])
        peb = sb("peb", [P, 2])
        cmpT = c.outs[:].rearrange("p m t -> p (m t)")[:, GR * T:GR * T + 2 * HB * PAST].rearrange("p (s b t) -> p s b t", s=2, b=HB)
        pg = sb("pg", [P, 4, 3 * P])
        kT = sb("kT", [P, 2, PAST])
        hid = sb("hid", [P, 2, HB * NCMP])
        qz = sb("qz", [P, NB * (SELB + NB)])
        block = ctx.enter_context(nc.Block())
        cache = dr["cache"]
        tiles = [(b, p) for b in range(NB) for p in range(PAGES)]
        WT = 4

        @block.sync
        def _(sp):
            sp.dma_start(tab[:], dr["table"]).then_inc(s["tab"], 16)
            for h in range(2):
                sp.dma_start(w1[h * DH:(h + 1) * DH], dr["w_cmp1"]).then_inc(s["w"], 16)
            sp.dma_start(w2[:], dr["w_cmp2"]).then_inc(s["w"], 16)
            sp.dma_start(pe_[:], dr["pe_cmp"]).then_inc(s["w"], 16)
            sp.wait_ge(s["tab"], 16)
            n = 0
            for b in range(NB):
                for p in range(PAGES):
                    if n >= 4:
                        sp.wait_ge(s["turned"], n - 3)
                    v = sp.value_load(tab[0:1, b * PAGES + p:b * PAGES + p + 1], min_val=0, max_val=NPOOL - 1)
                    sp.dma_start(pg[:, n % 4, :], cache[bass.ds(v, 1), :, 0:3 * P].rearrange("o t f -> t (o f)")).then_inc(s[f"pg{n % 4}"], 16)
                    n += 1

        @block.tensor
        def _(pe):
            pe.wait_ge(s["w"], 64)
            for st in range(2):
                for t in range(32):
                    mm = pe.matmul(ps[:, 7, st:st + 1], w1[0:DH, st, t, :], pe_[:, st, t:t + 1], start=(t == 0), stop=(t == 31))
            mm.then_inc(s["peb"], 1)

            def compress(st, src, nseq):
                for t in range(32):
                    lo = t // STR
                    for g in range(G):
                        r = slice(g * DH, (g + 1) * DH)
                        mv = src[r].rearrange("p b (k s) -> p b k s", s=STR)[:, :, lo:lo + NCMP, t % STR]
                        mm = pe.matmul(ps[:, 4 + g, 0:nseq * NCMP], w1[r, st, t, :], mv, start=(t == 0), stop=(t == 31))
                        if t == 31:
                            mm.then_inc(s["lo"], 1)

            def second(n, st, g, q0, nseq):
                pe.wait_ge(s["hid"], n + 1)
                if n >= 1:
                    pe.wait_ge(s["h2c"], n)
                if st == 0:
                    mm = pe.matmul(ps[g * DH:(g + 1) * DH, 6, 0:nseq * NCMP], w2[:, 0, :], hid[:, n % 2, 0:nseq * NCMP], start=True, stop=True)
                else:
                    for b in range(nseq):
                        mm = pe.matmul(ps[0:NCMP, 6, b * DH:(b + 1) * DH], hid[:, n % 2, b * NCMP:(b + 1) * NCMP], w2[:, 1, :], start=True, stop=True)
                mm.then_inc(s["h2"], 1)

            n = 0
            pe.wait_ge(s["pebc"], 1)
            for st in range(2):
                if n:
                    pe.wait_ge(s["hid"], n)
                compress(st, kv[:, st:st + 1, 0:TP], 1)
                for g in range(G):
                    second(n, st, g, NB, 1)
                    n += 1
            tn = 0
            for b in range(NB):
                if b >= 1:
                    pe.wait_ge(s["scored"], b)
                for p in range(PAGES):
                    pe.wait_ge(s[f"pg{tn % 4}"], 16 * (tn // 4 + 1))
                    if tn >= 2:
                        pe.wait_ge(s["turncopied"], tn - 1)
                    if p == 0 and b % HB == 0 and b > 0:
                        pe.wait_ge(s["h2"], 8)
                    for st in range(3):
                        t = pe.transpose(ps[:, 4 + tn % 2, st * P:(st + 1) * P], pg[:, tn % 4, st * P:(st + 1) * P], c.ident[:])
                    t.then_inc(s["turned"], 1)
                    tn += 1
                pe.wait_ge(s["qz"], 1)
                pe.wait_ge(s["turncopied"], tn)
                for h in range(2):
                    mm = pe.matmul(ps[0:64, h, :], qz[:, b * 64:(b + 1) * 64], kT[:, b % 2, h * 512:(h + 1) * 512], start=(b == 0), stop=(b == NB - 1))
                mm.then_inc(s["scored"], 1)
                if b % HB == HB - 1:
                    for st in range(2):
                        pe.wait_ge(s["hid"], n)
                        compress(st, cmpT[:, st], HB)
                        for g in range(G):
                            second(n, st, g, b - HB + 1, HB)
                            n += 1

        @block.gpsimd
        def _(pool):
            pool.wait_ge(s["tab"], 16)
            for n in range(NB * PAGES):
                v = pool.value_load(tab[0:1, n:n + 1], min_val=0, max_val=NPOOL - 1)
                pool.dma_start(vs[:, n, :], dr["cache"][bass.ds(v, 1), :, 3 * P:4 * P].rearrange("o t f -> t (o f)")).then_inc(v_here, 16)

        @block.scalar
        def _(act):
            act.wait_ge(s["pebc"], 1)

            def hidden(n, nseq):
                act.wait_ge(s["lo"], n + 1)
                if n >= 2:
                    act.wait_ge(s["h2"], n - 1)
                st = (n // 2) % 2
                act.activation(hid[:, n % 2, 0:nseq * NCMP], ps[:, 4 + n % 2, 0:nseq * NCMP], ACT.Silu, bias=peb[:, st:st + 1]).then_inc(s["hid"], 1)

            for n in range(4):
                hidden(n, 1)
            for b in range(NB):
                if b % HB == HB - 1:
                    for k in range(4):
                        hidden(4 + (b // HB) * 4 + k, HB)

        @block.vector
        def _(dve):
            link = Link(dve, s["link"])
            link(dve.memset(qz[:], 0.0))
            for g in range(G):
                r = slice(g * DH, (g + 1) * DH)
                z = dve.tensor_copy(qz[r].rearrange("p (b x) -> p b x", x=SELB + NB)[:, :, g * GR:(g + 1) * GR],
                                    q[r, :, TP:T].rearrange("p j b -> p b j"))
            z.then_inc(s["qz"], 1)
            dve.wait_ge(s["peb"], 1)
            dve.tensor_copy(peb[:], ps[:, 7, 0:2]).then_inc(s["pebc"], 1)

            def second(n, st, g, q0, nseq):
                dve.wait_ge(s["h2"], n + 1)
                r = slice(g * DH, (g + 1) * DH)
                if st == 0:
                    o = dve.tensor_copy(kc[r, q0:q0 + nseq, :], ps[r, 6, 0:nseq * NCMP].rearrange("p (b k) -> p b k", b=nseq))
                else:
                    o = dve.tensor_copy(vc[:, q0:q0 + nseq, r], ps[0:NCMP, 6, 0:nseq * DH].rearrange("p (b k) -> p b k", b=nseq))
                o.then_inc(s["h2c"], 1)

            n = 0
            for st in range(2):
                for g in range(G):
                    second(n, st, g, NB, 1)
                    n += 1
            tn = 0
            for b in range(NB):
                for p in range(PAGES):
                    dve.wait_ge(s["turned"], tn + 1)
                    if p == 0 and b >= 2:
                        dve.wait_ge(s["scored"], b - 1)
                    dve.tensor_copy(cmpT[:, :, b % HB, p * P:(p + 1) * P], ps[:, 4 + tn % 2, 0:2 * P].rearrange("p (s t) -> p s t", s=2))
                    dve.tensor_copy(kT[:, b % 2, p * P:(p + 1) * P], ps[:, 4 + tn % 2, 2 * P:3 * P]).then_inc(s["turncopied"], 1)
                    tn += 1
                if b % HB == HB - 1:
                    for st in range(2):
                        for g in range(G):
                            second(n, st, g, b - HB + 1, HB)
                            n += 1
            dve.wait_ge(s["scored"], NB)
            dve.tensor_copy(Ss[:, 0:PAST].rearrange("p (h k) -> p h k", h=2), ps[0:64, 0:2, :])
    
    s2 = Semaphores(c, "nw")
    with ExitStack() as ctx:
        sb = lambda n, sh, dt=F32: ctx.enter_context(nc.sbuf_tensor(f"nw_{n}", sh, dt))
        wk = sb("wk", [P, 2, 4, P])
        wT = sb("wT", [P, 2, WIN])
        qz = sb("qz", [P, NB * (SELB + NB)])
        block = ctx.enter_context(nc.Block())

        @block.sync
        def _(sp):
            for b in range(NB):
                if b >= 2:
                    sp.wait_ge(s2["turned"], b - 1)
                sp.dma_start(wk[:, b % 2], dr["state_win"][b].rearrange("(n p) f -> p n f", p=P)[:, :, 0:P]).then_inc(s2[f"in{b % 2}"], 16)

        @block.tensor
        def _(pe):
            pe.wait_ge(s2["qz"], 1)
            for b in range(NB):
                pe.wait_ge(s2[f"in{b % 2}"], 16 * (b // 2 + 1))
                if b >= 2:
                    pe.wait_ge(s2["copied"], b - 1)
                for n in range(4):
                    t = pe.transpose(ps[:, 4 + b % 2, n * P:(n + 1) * P], wk[:, b % 2, n, :], c.ident[:])
                t.then_inc(s2["turned"], 1)
                pe.wait_ge(s2["copied"], b + 1)
                pe.matmul(ps[0:64, 2, :], qz[:, b * 64:(b + 1) * 64], wT[:, b % 2, :], start=(b == 0), stop=(b == NB - 1)).then_inc(s2["scored"], 1)
            for b in range(NB):
                pe.matmul(ps[0:64, 3, 0:NCMP], qz[:, b * 64:(b + 1) * 64], kc[:, b, :], start=(b == 0), stop=(b == NB - 1))
            for k, st in enumerate((2, 4)):
                for b in range(NB):
                    mm = pe.matmul(ps[0:64, 3, 64 + 8 * k:72 + 8 * k], qz[:, b * 64:(b + 1) * 64], kv[:, st, TP:T], start=(b == 0), stop=(b == NB - 1))
            mm.then_inc(s2["cmp"], 1)

        @block.vector
        def _(dve):
            link = Link(dve, s2["link"])
            link(dve.memset(qz[:], 0.0))
            for g in range(G):
                r = slice(g * DH, (g + 1) * DH)
                z = dve.tensor_copy(qz[r].rearrange("p (b x) -> p b x", x=SELB + NB)[:, :, g * GR:(g + 1) * GR],
                                    q[r, :, TP:T].rearrange("p j b -> p b j"))
            z.then_inc(s2["qz"], 1)
            for b in range(NB):
                dve.wait_ge(s2["turned"], b + 1)
                if b >= 2:
                    dve.wait_ge(s2["scored"], b - 1)
                dve.tensor_copy(wT[:, b % 2, :], ps[:, 4 + b % 2, :]).then_inc(s2["copied"], 1)
            dve.wait_ge(s2["scored"], NB)
            dve.tensor_copy(Ss[:, SO_WIN:SO_WIN + WIN], ps[0:64, 2, :])
            dve.wait_ge(s2["cmp"], 1)
            dve.tensor_copy(Ss[:, SO_NSEL:SO_NSEL + NB], ps[0:64, 3, 64:72])
            dve.tensor_copy(Ss[:, SO_NWIN:SO_NWIN + NB], ps[0:64, 3, 72:80])
            dve.tensor_copy(Ss[:, SO_CMP:SO_CMP + NCMP], ps[0:64, 3, 0:NCMP])


SO_NSEL = PAST
SO_WIN = SO_NSEL + NB
SO_NWIN = SO_WIN + WIN
SO_CMP = SO_NWIN + NB
SO_END = SO_CMP + NCMP + 1


def nsa_samples_finish(c, kv, Ss, vc, vs, v_here):
    nc, ps, dr = c.nc, c.ps, c.dram
    s = Semaphores(c, "nf")
    BR = ((0, SO_WIN), (SO_WIN, SO_CMP), (SO_CMP, SO_CMP + NCMP))
    with ExitStack() as ctx:
        sb = lambda n, sh, dt=F32: ctx.enter_context(nc.sbuf_tensor(f"nf_{n}", sh, dt))
        vw = sb("vw", [P, NB, 4, P])
        vn = sb("vn", [NB, 2, P])
        bs = sb("bs", [64, PAST + 1])
        bw = sb("bw", [64, WIN + 1])
        own = sb("own", [64, NB])
        gs = sb("gs", [64, 3])
        imap = sb("imap", [NCMP, NSB])
        grp = sb("grp", [64, 64])
        idx = sb("idx", [64, NSB])
        sm = sb("sm", [64, 16])
        ec = sb("ec", [64, NCMP])
        ecT = sb("ecT", [NCMP, 64])
        imp = sb("imp", [64, NSB])
        eq = sb("eq", [64, NSB])
        dm = sb("dm", [64, 16])
        pt = sb("pt", [P, 15, 64])
        block = ctx.enter_context(nc.Block())

        @block.sync
        def _(sp):
            for t, src in ((bs, dr["s_bias"][:, 0, P - 1:P + PAST]), (bw, dr["s_bias"][:, 0, LSEL + P - 1:LSEL + P + WIN])):
                sp.dma_start(t[:], src.unsqueeze(0).to_broadcast([NB, *src.shape])).then_inc(s["in"], 16)
            sp.dma_start(gs[:], dr["s_gate"].rearrange("(h r) b -> b h r", r=3), allow_slow_non_contiguous=True).then_inc(s["in"], 16)
            for t, n in ((own, "own"), (imap, "imap"), (grp, "grp"), (idx, "idx")):
                sp.dma_start(t[:], dr[n]).then_inc(s["in"], 16)

        @block.vector
        def _(dve):
            link = Link(dve, s["link"])
            dve.wait_ge(s["in"], 16 * 7)
            dve.tensor_tensor(Ss[:, 0:PAST], Ss[:, 0:PAST], bs[:, 0:PAST], ALU.add)
            dve.tensor_tensor(Ss[:, SO_WIN:SO_NWIN], Ss[:, SO_WIN:SO_NWIN], bw[:, 0:WIN], ALU.add)
            dve.scalar_tensor_tensor(Ss[:, SO_NSEL:SO_WIN], Ss[:, SO_NSEL:SO_WIN], bs[:, PAST:PAST + 1], own[:], ALU.add, ALU.add)
            dve.scalar_tensor_tensor(Ss[:, SO_NWIN:SO_CMP], Ss[:, SO_NWIN:SO_CMP], bw[:, WIN:WIN + 1], own[:], ALU.add, ALU.add)
            cs = slice(*BR[2])
            link(dve.tensor_tensor(Ss[:, cs], Ss[:, cs], bs[:, 31:31 + STR * (NCMP - 1) + 1:STR], ALU.add))
            link(dve.tensor_reduce(sm[:, 0:1], Ss[:, cs], AX.X, ALU.max))
            dve.tensor_scalar(sm[:, 1:2], sm[:, 0:1], -1.0, None, ALU.mult).then_inc(s["zc"], 1)
            dve.wait_ge(s["ec"], 1)
            link(dve.reciprocal(sm[:, 3:4], sm[:, 2:3]))
            dve.tensor_scalar(ec[:], ec[:], sm[:, 3:4], None, ALU.mult).then_inc(s["impt"], 1)
            dve.wait_ge(s["imptc"], 1)
            dve.tensor_copy(ecT[:], ps[0:NCMP, 0, 0:64]).then_inc(s["imp"], 1)
            dve.wait_ge(s["impc"], 1)
            dve.tensor_copy(imp[:], ps[0:64, 1, 0:NSB]).then_inc(s["imp"], 1)
            dve.wait_ge(s["grp"], 1)
            link(dve.tensor_copy(imp[:], ps[0:64, 2, 0:NSB]))
            n = slice(1, NSB - 2)
            link(dve.tensor_reduce(sm[:, 4:5], imp[:, n], AX.X, ALU.min))
            link(dve.tensor_scalar(eq[:, n], imp[:, n], sm[:, 4:5], None, ALU.is_equal))
            link(dve.tensor_tensor(eq[:, n], eq[:, n], idx[:, n], ALU.mult))
            link(dve.tensor_reduce(sm[:, 5:6], eq[:, n], AX.X, ALU.max))
            link(dve.tensor_scalar(dm[:], idx[:, 0:16], sm[:, 5:6], NEG, ALU.is_equal, ALU.mult))
            sel = Ss[:, 0:PAST].rearrange("p (n k) -> p n k", k=SELB)
            link(dve.tensor_tensor(sel, sel, last(dm[:], SELB), ALU.add))
            for k, (a, b) in enumerate(BR):
                link(dve.tensor_reduce(sm[:, 6 + k:7 + k], Ss[:, a:b], AX.X, ALU.max))
            dve.tensor_scalar(sm[:, 6:9], sm[:, 6:9], -1.0, None, ALU.mult).then_inc(s["z3"], 1)
            dve.wait_ge(s["e3"], 1)
            link(dve.reciprocal(sm[:, 12:15], sm[:, 9:12]))
            link(dve.tensor_tensor(sm[:, 12:14], sm[:, 12:14], gs[:, 1:3], ALU.mult))
            link(dve.tensor_tensor(sm[:, 14:15], sm[:, 14:15], gs[:, 0:1], ALU.mult))
            for k, (a, b) in enumerate(BR):
                o = dve.tensor_scalar(Ss[:, a:b], Ss[:, a:b], sm[:, 12 + k:13 + k], None, ALU.mult)
            o.then_inc(s["p3"], 1)
            dve.wait_ge(s["pt"], 1)
            dve.tensor_copy(pt[:, 0:8, :], ps[:, 0, :].rearrange("p (n q) -> p n q", q=64))
            dve.tensor_copy(pt[:, 8:12, :], ps[:, 1, 0:256].rearrange("p (n q) -> p n q", q=64))
            dve.tensor_copy(pt[0:NB, 12:14, :], ps[0:NB, 1, 256:384].rearrange("p (n q) -> p n q", q=64))
            dve.tensor_copy(pt[0:NCMP, 14, :], ps[0:NCMP, 1, 384:448])
            dve.tensor_copy(vn[:], ps[0:NB, 2, 0:2 * P].rearrange("p (n q) -> p n q", q=P)).then_inc(s["ptc"], 1)
            dve.wait_ge(s["pv"], 1)
            for g in range(G):
                r = slice(g * DH, (g + 1) * DH)
                dve.tensor_copy(c.oT[0][r, :, TP:T], ps[r, 3, 0:64].rearrange("p (b g j) -> p g j b", g=G, j=GR)[:, g])

        @block.scalar
        def _(act):
            for b in range(NB):
                act.dma_start(vw[:, b], dr["state_win"][b].rearrange("(n p) f -> p n f", p=P)[:, :, P:2 * P]).then_inc(s["v"], 16)
            act.wait_ge(s["zc"], 1)
            act.activation(ec[:], Ss[:, SO_CMP:SO_CMP + NCMP], ACT.Exp, bias=sm[:, 1:2], accum_out=sm[:, 2:3]).then_inc(s["ec"], 1)
            act.wait_ge(s["z3"], 1)
            for k, (a, b) in enumerate(BR):
                o = act.activation(Ss[:, a:b], Ss[:, a:b], ACT.Exp, bias=sm[:, 6 + k:7 + k], accum_out=sm[:, 9 + k:10 + k])
            o.then_inc(s["e3"], 1)

        @block.tensor
        def _(pe):
            pe.wait_ge(s["impt"], 1)
            pe.transpose(ps[0:NCMP, 0, 0:64], ec[:], c.ident[0:64, 0:64]).then_inc(s["imptc"], 1)
            pe.wait_ge(s["imp"], 1)
            pe.matmul(ps[0:64, 1, 0:NSB], ecT[:], imap[:], start=True, stop=True).then_inc(s["impc"], 1)
            pe.wait_ge(s["imp"], 2)
            pe.matmul(ps[0:64, 2, 0:NSB], grp[:], imp[:], start=True, stop=True).then_inc(s["grp"], 1)
            pe.wait_ge(s["p3"], 1)
            idt = c.ident[0:64, 0:64]
            for n in range(8):
                pe.transpose(ps[:, 0, n * 64:n * 64 + 64], Ss[:, n * P:(n + 1) * P], idt)
            for n in range(4):
                pe.transpose(ps[:, 1, n * 64:n * 64 + 64], Ss[:, SO_WIN + n * P:SO_WIN + (n + 1) * P], idt)
            pe.transpose(ps[0:NB, 1, 256:320], Ss[:, SO_NSEL:SO_NSEL + NB], idt)
            pe.transpose(ps[0:NB, 1, 320:384], Ss[:, SO_NWIN:SO_NWIN + NB], idt)
            pe.transpose(ps[0:NCMP, 1, 384:448], Ss[:, SO_CMP:SO_CMP + NCMP], idt)
            for k in range(2):
                t = pe.transpose(ps[0:NB, 2, k * P:(k + 1) * P], kv[:, 3 + 2 * k, TP:T], c.ident[:])
            t.then_inc(s["pt"], 1)
            pe.wait_ge(s["ptc"], 1)
            pe.wait_ge(v_here, 16 * NB * PAGES)
            pe.wait_ge(s["v"], 16 * NB)
            for b in range(NB):
                q = slice(b * NH, (b + 1) * NH)
                out = ps[:, 3, q]
                for n in range(8):
                    pe.matmul(out, vs[:, b * PAGES + n, :], pt[:, n, q], start=(n == 0), stop=False)
                for n in range(4):
                    pe.matmul(out, vw[:, b, n, :], pt[:, 8 + n, q], start=False, stop=False)
                for n in range(2):
                    pe.matmul(out, vn[:, n, :], pt[0:NB, 12 + n, q], start=False, stop=False)
                mm = pe.matmul(out, vc[:, b, :], pt[0:NCMP, 14, q], start=False, stop=True)
            mm.then_inc(s["pv"], 1)


def nsa_prompt(c, q, kv, kc, vc):
    nc, ps, dr = c.nc, c.ps, c.dram
    s = Semaphores(c, "np")
    NSL = 4
    LAG = 2
    LM = PAST + P
    with ExitStack() as ctx:
        sb = lambda n, sh, dt=F32: ctx.enter_context(nc.sbuf_tensor(f"np_{n}", sh, dt))
        mt = sb("mt", [P, GR, LM])
        mw = sb("mw", [P, GR, 5 * P])
        vt = sb("vt", [P, 2, NBLK, P])
        z = sb("z", [P, LAG + 1, 14 * P])
        sm = sb("sm", [P, LAG + 1, 12])
        ptb = sb("ptb", [P, NSL, 512])
        block = ctx.enter_context(nc.Block())
        steps = [(g, i, j) for g in range(G) for i in range(NBLK) for j in range(GR)]

        def widths(i):
            return (i + 1) * P, min(i + 1, 5) * P, 8 * i + 7

        def blocks(i):
            ws, ww, wc = widths(i)
            out = [(n * P, P, 0, n) for n in range(i + 1)]
            out += [(ws + n * P, P, 1, max(0, i - 4) + n) for n in range(ww // P)]
            return out + [(ws + ww, wc, 2, 0)]

        def groups(i):
            b = blocks(i)
            return [b[k:k + 4] for k in range(0, len(b), 4)]

        @block.sync
        def _(sp):
            for g in range(G):
                if g:
                    sp.wait_ge(s["zdone"], NBLK * GR)
                for j in range(GR):
                    h = g * GR + j
                    v, pitch = dr["s_bias"][h:h + 1, 0:1, :], LSEL + LWIN - 1
                    sp.dma_start(mt[:, j, :], bass.AP(v.tensor, v.offset + P - 1, [[pitch, P], [1, LM]])).then_inc(s[f"in{g}"], 16)
                    sp.dma_start(mw[:, j, :], bass.AP(v.tensor, v.offset + LSEL + P - 1, [[pitch, P], [1, 5 * P]])).then_inc(s[f"in{g}"], 16)
                if not g:
                    sp.dma_start(c.xT[:], dr["xT"]).then_inc(s["x"], 16)
                    sp.dma_start(dr["o_win"], dr["state_win"][:, 1:WIN, :]).then_inc(s["window"], 16)
            sp.wait_ge(s["x"], 16)
            sp.wait_ge(s["window"], 16)

        @block.tensor
        def _(pe):
            for k in range(2):
                for i in range(NBLK):
                    t = pe.transpose(ps[:, 2 * k + i // 4, (i % 4) * P:(i % 4 + 1) * P], kv[:, 3 + 2 * k, i * P:(i + 1) * P], c.ident[:])
            t.then_inc(s["vt"], 1)
            pe.wait_ge(s["vtc"], 1)

            def scores(n):
                g, i, j = steps[n]
                r = slice(g * DH, (g + 1) * DH)
                qq = q[r, j, i * P:(i + 1) * P]
                ws, ww, wc = widths(i)
                if n:
                    pe.wait_ge(s["zdone"], n)
                for a in range(0, ws, 512):
                    e = min(ws, a + 512)
                    pe.matmul(ps[:, a // 512, 0:e - a], qq, kv[r, 2, a:e], start=True, stop=True)
                k0 = max(0, i - 4) * P
                a = min(ww, 512)
                pe.matmul(ps[:, 2, 0:a], qq, kv[r, 4, k0:k0 + a], start=True, stop=True)
                if ww > a:
                    pe.matmul(ps[:, 3, 0:ww - a], qq, kv[r, 4, k0 + a:k0 + ww], start=True, stop=True)
                pe.matmul(ps[:, 3, 256:256 + wc], qq, kc[r, NB, 0:wc], start=True, stop=True).then_inc(s["scored"], 1)

            cnt = [0, 0]

            def turn(n, grp):
                k = cnt[0]
                if k >= 2:
                    pe.wait_ge(s["ptc"], k - 1)
                for m, (col, w, _, _) in enumerate(grp):
                    t = pe.transpose(ps[0:w, 4 + k % 2, m * P:(m + 1) * P], z[:, n % (LAG + 1), col:col + w], c.ident[:])
                t.then_inc(s["pt"], 1)
                cnt[0] += 1

            def values(n, grp, first, final):
                g, i, j = steps[n]
                r = slice(g * DH, (g + 1) * DH)
                k = cnt[1]
                pe.wait_ge(s["ptc"], k + 1)
                if first and n >= 2:
                    pe.wait_ge(s["oc"], n - 1)
                for m, (_, w, br, kb) in enumerate(grp):
                    v = vt[:, br, kb, r] if br < 2 else vc[0:w, NB, r]
                    mm = pe.matmul(ps[r, 6 + n % 2, 0:P], v, ptb[0:w, k % NSL, m * P:(m + 1) * P],
                                   start=(first and m == 0), stop=(final and m == len(grp) - 1))
                mm.then_inc(s["pv"], 1)
                cnt[1] += 1

            def finish(n):
                gr = groups(steps[n][1])
                pe.wait_ge(s["p"], n + 1)
                turn(n, gr[0])
                for k in range(len(gr)):
                    if k + 1 < len(gr):
                        turn(n, gr[k + 1])
                    values(n, gr[k], k == 0, k == len(gr) - 1)

            for n in range(len(steps)):
                scores(n)
                if n >= LAG:
                    finish(n - LAG)
            for n in range(len(steps) - LAG, len(steps)):
                finish(n)

        @block.vector
        def _(dve):
            link = Link(dve, s["link"])
            dve.wait_ge(s["vt"], 1)
            dve.tensor_copy(vt[:].rearrange("p k (a b) t -> p (k a) (b t)", a=2), ps[:, 0:4, :]).then_inc(s["vtc"], 1)
            turned = np.cumsum([0] + [len(groups(i)) for _, i, _ in steps]).tolist()

            def bias(n):
                g, i, j = steps[n]
                ws, ww, wc = widths(i)
                if j == 0 and i == 0:
                    dve.wait_ge(s[f"in{g}"], 16 * 2 * GR)
                dve.wait_ge(s["scored"], n + 1)
                if n > LAG:
                    dve.wait_ge(s["pt"], turned[n - LAG])
                zz = z[:, n % (LAG + 1)]
                m0 = PAST - i * P
                mx = sm[:, n % (LAG + 1), 0:4]
                if ws <= 512:
                    dve.tensor_tensor_reduce(zz[:, 0:ws], ps[:, 0, 0:ws], mt[:, j, m0:m0 + ws], 1.0, NEG, ALU.add, ALU.max, mx[:, 0:1])
                else:
                    dve.tensor_tensor_reduce(zz[:, 0:512], ps[:, 0, :], mt[:, j, m0:m0 + 512], 1.0, NEG, ALU.add, ALU.max, mx[:, 3:4])
                    link(dve.tensor_tensor_reduce(zz[:, 512:ws], ps[:, 1, 0:ws - 512], mt[:, j, m0 + 512:m0 + ws], 1.0, NEG, ALU.add, ALU.max, mx[:, 0:1]))
                    dve.tensor_tensor(mx[:, 0:1], mx[:, 0:1], mx[:, 3:4], ALU.max)
                w0 = 5 * P - ww
                a = min(ww, 512)
                dve.tensor_tensor_reduce(zz[:, ws:ws + a], ps[:, 2, 0:a], mw[:, j, w0:w0 + a], 1.0, NEG, ALU.add, ALU.max, mx[:, 1:2])
                if ww > a:
                    link(dve.tensor_tensor_reduce(zz[:, ws + a:ws + ww], ps[:, 3, 0:ww - a], mw[:, j, w0 + a:w0 + ww], 1.0, NEG, ALU.add, ALU.max, sm[:, n % (LAG + 1), 7:8]))
                    dve.tensor_tensor(mx[:, 1:2], mx[:, 1:2], sm[:, n % (LAG + 1), 7:8], ALU.max)
                c0 = m0 + 31
                o = dve.tensor_tensor_reduce(zz[:, ws + ww:ws + ww + wc], ps[:, 3, 256:256 + wc], mt[:, j, c0:c0 + STR * (wc - 1) + 1:STR],
                                             1.0, NEG, ALU.add, ALU.max, mx[:, 2:3])
                link(o)
                dve.tensor_scalar(sm[:, n % (LAG + 1), 4:7], mx[:, 0:3], -1e29, -1.0, ALU.max, ALU.mult).then_inc(s["zdone"], 1)

            def scale(n):
                g, i, j = steps[n]
                ws, ww, wc = widths(i)
                dve.wait_ge(s["exp"], n + 1)
                h = g * GR + j
                su = sm[:, n % (LAG + 1), 8:11]
                link(dve.tensor_scalar(su, su, 0.5, None, ALU.max))
                link(dve.reciprocal(su, su))
                dve.tensor_tensor(su[:, 0:2], su[:, 0:2], c.gtok[:, i, 3 * h + 1:3 * h + 3], ALU.mult)
                link(dve.tensor_tensor(su[:, 2:3], su[:, 2:3], c.gtok[:, i, 3 * h:3 * h + 1], ALU.mult))
                zz = z[:, n % (LAG + 1)]
                for k, (a, e) in enumerate(((0, ws), (ws, ws + ww), (ws + ww, ws + ww + wc))):
                    o = dve.tensor_scalar(zz[:, a:e], zz[:, a:e], su[:, k:k + 1], None, ALU.mult)
                o.then_inc(s["p"], 1)

            def output(n):
                g, i, j = steps[n]
                r = slice(g * DH, (g + 1) * DH)
                dve.wait_ge(s["pv"], turned[n + 1])
                dve.tensor_copy(c.oT[0][r, j, i * P:(i + 1) * P], ps[r, 6 + n % 2, 0:P]).then_inc(s["oc"], 1)

            N = len(steps)
            for n in range(N + LAG + 1):
                if n < N:
                    bias(n)
                if 1 <= n <= N:
                    scale(n - 1)
                if n > LAG:
                    output(n - LAG - 1)

        @block.scalar
        def _(act):
            cnt = [0]

            def exps(n):
                g, i, j = steps[n]
                ws, ww, wc = widths(i)
                act.wait_ge(s["zdone"], n + 1)
                zz = z[:, n % (LAG + 1)]
                for k, (a, e) in enumerate(((0, ws), (ws, ws + ww), (ws + ww, ws + ww + wc))):
                    o = act.activation(zz[:, a:e], zz[:, a:e], ACT.Exp, bias=sm[:, n % (LAG + 1), 4 + k:5 + k], accum_out=sm[:, n % (LAG + 1), 8 + k:9 + k])
                o.then_inc(s["exp"], 1)

            def copies(n):
                for grp in groups(steps[n][1]):
                    k = cnt[0]
                    act.wait_ge(s["pt"], k + 1)
                    if k >= NSL:
                        act.wait_ge(s["pv"], k - NSL + 1)
                    full = [m for m in grp if m[1] == P]
                    o = None
                    if full:
                        o = act.activation(ptb[:, k % NSL, 0:len(full) * P], ps[:, 4 + k % 2, 0:len(full) * P], ACT.Copy)
                    if len(full) < len(grp):
                        w, m = grp[-1][1], len(full) * P
                        o = act.activation(ptb[0:w, k % NSL, m:m + P], ps[0:w, 4 + k % 2, m:m + P], ACT.Copy)
                    o.then_inc(s["ptc"], 1)
                    cnt[0] += 1

            for n in range(len(steps)):
                if n >= LAG:
                    copies(n - LAG)
                exps(n)
            for n in range(len(steps) - LAG, len(steps)):
                copies(n)


def inverse_norm(c, name, x, ntiles, mean, post):
    nc, ps = c.nc, c.ps
    s = Semaphores(c, name)
    with nc.sbuf_tensor(f"{name}_sq", [P, 2, T], F32) as sq, nc.sbuf_tensor(f"{name}_r", [P, 2, T], F32) as rr, nc.Block() as block:
        @block.gpsimd
        def _(pool):
            for m in range(ntiles):
                if m >= 2:
                    pool.wait_ge(s["ss"], m - 1)
                pool.tensor_tensor(sq[:, m % 2], x[:, m], x[:, m], ALU.mult).then_inc(s["sq"], 1)

        @block.tensor
        def _(pe):
            for m in range(ntiles):
                pe.wait_ge(s["sq"], m + 1)
                if m >= 2:
                    pe.wait_ge(s["ln"], m - 1)
                for n in range(NW):
                    mm = pe.matmul(ps[:, 3 * (m % 2) + n, 0:W], c.ones[:], sq[:, m % 2, n * W:(n + 1) * W], start=True, stop=True)
                mm.then_inc(s["ss"], 1)

        @block.scalar
        def _(act):
            for m in range(ntiles):
                act.wait_ge(s["ss"], m + 1)
                if m >= 2:
                    act.wait_ge(s["done"], m - 1)
                act.activation(rr[:, m % 2].rearrange("p (n w) -> p n w", n=NW), ps[:, 3 * (m % 2):3 * (m % 2) + NW, 0:W],
                               ACT.Ln, bias=c.eps[:], scale=mean).then_inc(s["ln"], 1)
                act.wait_ge(s["ln"], m + 1)
                act.activation(rr[:, m % 2], rr[:, m % 2], ACT.Exp, scale=-0.5).then_inc(s["r"], 1)

        @block.vector
        def _(dve):
            for m in range(ntiles):
                dve.wait_ge(s["r"], m + 1)
                post(dve, m, rr[:, m % 2]).then_inc(s["done"], 1)


def gated_norm(c, name, o, gate, w_in):
    nc = c.nc
    s = Semaphores(c, name)
    with nc.sbuf_tensor(f"{name}_w", [P, 1], F32) as w:
        with nc.Block() as block:
            @block.sync
            def _(sp):
                sp.dma_start(w[:], w_in).then_inc(s["in"], 16)
                sp.wait_ge(s["in"], 16)

            @block.scalar
            def _(act):
                for m in range(H4):
                    act.activation(gate[:, m], gate[:, m], ACT.Silu)

        inverse_norm(c, f"{name}_in", o, H4, 1.0 / P,
                     lambda dve, m, r: dve.scalar_tensor_tensor(o[:, m], o[:, m], w[:], r, ALU.mult, ALU.mult))
        with nc.Block() as block:
            @block.vector
            def _(dve):
                for m in range(2):
                    dve.tensor_tensor(o[:, m], o[:, m], gate[:, m], ALU.mult)

            @block.gpsimd
            def _(pool):
                for m in range(2, 4):
                    pool.tensor_tensor(o[:, m], o[:, m], gate[:, m], ALU.mult)


class Convolution:
    NT = 12

    def __init__(self, c, z, sb):
        self.c, self.z = c, z
        self.cw = sb("cw", [P, self.NT, 4])
        self.hist = sb("hist", [P, self.NT, NB, 3])
        self.y = sb("y", [P, 2, T])
        self.st = sb("st", [P, self.NT, 3 + 3 * NB])
        self.s = Semaphores(c, "cv")

    def vector(self, dve, z_copied):
        s, z, y, cw, hist, st = self.s, self.z, self.y, self.cw, self.hist, self.st
        dve.wait_ge(s["in"], 32)
        dve.sem_inc(s["silu"], 2)
        sv = st[:, :, 3:3 + 3 * NB].rearrange("p m (b t) -> p m b t", t=3)
        dve.tensor_copy(sv[:, :, :, 0:2], hist[:, :, :, 1:3])
        with dve.Fori(0, self.NT // 2) as i:
            for j in range(2):
                m = 2 * i + j
                zm, yy = z[:, m, :], y[:, j]
                dve.wait_ge(z_copied, m + 3)
                dve.tensor_copy(st[:, m, 0:3], zm[:, TP - 3:TP])
                dve.tensor_copy(st[:, m, 5:3 + 3 * NB:3], zm[:, TP:T])
                dve.wait_ge(s["silu"], m + 1)
                dve.tensor_scalar(yy, zm, cw[:, m, 3:4], None, ALU.mult).then_inc(s["link"], 1)
                for k in range(1, 4):
                    w = cw[:, m, 3 - k:4 - k]
                    dve.wait_ge(s["link"], 3 * m + k)
                    dve.scalar_tensor_tensor(yy[:, TP:T], hist[:, m, :, 3 - k], w, yy[:, TP:T], ALU.mult, ALU.add)
                    o = dve.scalar_tensor_tensor(yy[:, k:TP], zm[:, 0:TP - k], w, yy[:, k:TP], ALU.mult, ALU.add)
                    o.then_inc(s["link" if k < 3 else "y"], 1)

    def silu(self, act, i, j):
        act.wait_ge(self.s["y"], 2 * i + j + 1)
        act.sem_inc(self.s["going"], 1)
        act.activation(self.z[:, 2 * i + j, :], self.y[:, j], ACT.Silu).then_inc(self.s["silu"], 1)

    def store(self, pool):
        pool.dma_start(self.cw[:], self.c.dram["conv_w"]).then_inc(self.s["in"], 16)
        pool.dma_start(self.hist[:], self.c.dram["conv_state"]).then_inc(self.s["in"], 16)
        pool.wait_ge(self.s["y"], self.NT)
        pool.dma_start(self.c.dram["o_conv"], self.st[:]).then_inc(self.s["out"], 16)
        pool.wait_ge(self.s["out"], 16)


def deltanet_scalars(c, small, reset, gcol, bcol, egcol, sel):
    nc, ps, dr = c.nc, c.ps, c.dram
    s = Semaphores(c, "ds")
    with ExitStack() as ctx:
        sb = lambda n, sh: ctx.enter_context(nc.sbuf_tensor(f"ds_{n}", sh, F32))
        par = sb("par", [P, 2])
        tmp = sb("tmp", [P, 2, T])
        one = sb("one", [P, TP])
        block = ctx.enter_context(nc.Block())
        a, A = slice(32, 36), small[32:36, :]

        @block.sync
        def _(sp):
            sp.dma_start(par[a], dr["dn_par"]).then_inc(s["in"], 16)

        @block.scalar
        def _(act):
            act.wait_ge(s["in"], 16)
            act.activation(par[a, 0:1], par[a, 0:1], ACT.Exp).then_inc(s["ea"], 1)
            act.wait_ge(s["x"], 1)
            act.activation(tmp[a, 0], A, ACT.Abs).then_inc(s["alink"], 1)
            act.wait_ge(s["alink"], 1)
            act.activation(tmp[a, 0], tmp[a, 0], ACT.Exp, scale=-1.0).then_inc(s["alink"], 1)
            act.wait_ge(s["alink"], 2)
            act.activation(tmp[a, 0], tmp[a, 0], ACT.Ln, bias=c.ones[a, 0:1]).then_inc(s["l"], 1)
            act.activation(small[64:68, :], small[64:68, :], ACT.Sigmoid).then_inc(s["b"], 1)
            act.wait_ge(s["gc"], 1)
            act.activation(egcol[:], gcol[:], ACT.Exp).then_inc(s["alink"], 1)
            act.activation(small[a, TP:T], small[a, TP:T], ACT.Exp)

        @block.vector
        def _(dve):
            link = Link(dve, s["link"])
            for r in (32, 64):
                dve.tensor_copy(sel[r:r + 4], c.ident[r:r + 4, r:r + 4].unsqueeze(2).to_broadcast([4, 4, P]))
            link(dve.memset(one[a], 1.0))
            dve.wait_ge(s["in"], 16)
            dve.tensor_scalar(A, A, par[a, 1:2], None, ALU.add).then_inc(s["x"], 1)
            link(dve.memset(one[a].rearrange("p (i t) -> p i t", t=BLK)[:, :, 0:1], 0.0))
            dve.wait_ge(s["l"], 1)
            link(dve.tensor_scalar(tmp[a, 1], A, 0.0, None, ALU.max))
            link(dve.tensor_tensor(tmp[a, 1], tmp[a, 1], tmp[a, 0], ALU.add))
            dve.wait_ge(s["ea"], 1)
            link(dve.tensor_scalar(tmp[a, 1], tmp[a, 1], par[a, 0:1], -1.0, ALU.mult, ALU.mult))
            dve.tensor_copy(small[a, TP:T], tmp[a, 1, TP:T])
            dve.tensor_tensor_scan(small[a, 0:TP], one[a], tmp[a, 1, 0:TP], 0.0, ALU.mult, ALU.add).then_inc(s["g"], 1)
            dve.wait_ge(s["t"], 1)
            dve.tensor_copy(gcol[:].rearrange("p i h -> p (i h)"), ps[:, 0, 0:32])
            dve.tensor_copy(bcol[:].rearrange("p i h -> p (i h)"), ps[:, 1, 0:32]).then_inc(s["gc"], 1)
            dve.wait_ge(s["alink"], 3)
            dve.tensor_scalar(egcol[:], egcol[:], -1.0, None, ALU.mult)

        @block.tensor
        def _(pe):
            pe.wait_ge(s["g"], 1)
            pe.wait_ge(s["b"], 1)
            for k, r in enumerate((slice(32, 36), slice(64, 68))):
                for i in range(NBLK):
                    t = pe.transpose(ps[:, k, 4 * i:4 * i + 4], small[r, i * BLK:(i + 1) * BLK], c.ident[r, r])
            t.then_inc(s["t"], 1)


def deltanet_prompt(c, z, small, gcol, bcol, egcol, sel, S, o):
    nc, ps, dr = c.nc, c.ps, c.dram
    s = Semaphores(c, "dp")
    C = H4 * P
    with ExitStack() as ctx:
        sb = lambda n, sh: ctx.enter_context(nc.sbuf_tensor(f"dp_{n}", sh, F32))
        up = sb("up", [P, LEV, P])
        lo = sb("lo", [P, 3, P])
        spare = c.oT[2].rearrange("p h t -> p (h t)")[:, 0:8 * C].rearrange("p (n l x) -> p n l x", n=4, l=2)
        egb, kt, vt, AT = (spare[:, n] for n in range(4))
        A, at, X, Y, qks, dec, qg, kd = (sb(n, [P, 2, C]) for n in ("A", "at", "X", "Y", "qks", "dec", "qg", "kd"))
        Wm = A
        atm = (qks, dec)
        vn, rhs = sb("vn", [P, C]), sb("rhs", [P, C])
        dcol = sb("dcol", [P, 2, 2, H4])
        block = ctx.enter_context(nc.Block())
        hd = lambda h: slice(h * P, (h + 1) * P)
        as4 = lambda t: t.rearrange("p (h x) -> p h x", h=H4)
        R = LEV - 1
        NP = NBLK // 2
        lanes = range(2)
        chunk = lambda i: slice(i * BLK, (i + 1) * BLK)

        @block.sync
        def _(sp):
            sp.dma_start(up[:], dr["up"]).then_inc(s["in"], 16)
            sp.dma_start(lo[:], dr["lo"]).then_inc(s["in"], 16)

        @block.tensor
        def _(pe):
            for p in range(NP):
                if p:
                    pe.wait_ge(s["Su"], 2 * p)
                    pe.wait_ge(s["oc"], 2 * p)
                for L in lanes:
                    t, b = chunk(2 * p + L), 3 * L
                    for h in range(H4):
                        q, k = z[:, h, t], z[:, 4 + h, t]
                        pe.matmul(ps[:, b + 2, hd(h)], sel[32:36, h, :], small[32:36, t], start=True, stop=True)
                        pe.matmul(ps[:, b, hd(h)], k, k, start=True, stop=True)
                        mm = pe.matmul(ps[:, b + 1, hd(h)], q, k, start=True, stop=True)
                    mm.then_inc(s[f"raw{L}"], 1)
                    if L:
                        pe.wait_ge(s["tok0"], p + 1)
                    for h in range(H4):
                        pe.transpose(ps[:, 6, hd(h)], z[:, 4 + h, t], c.ident[:])
                        mm = pe.transpose(ps[:, 7, hd(h)], z[:, 8 + h, t], c.ident[:])
                    mm.then_inc(s[f"kv{L}"], 1)
                for L in lanes:
                    pe.wait_ge(s[f"A{L}"], p + 1)
                    for h in range(H4):
                        pe.transpose(ps[:, 3 * L, hd(h)], A[:, L, hd(h)], c.ident[:])
                        mm = pe.transpose(ps[:, 3 * L + 1, hd(h)], qks[:, L, hd(h)], c.ident[:])
                    mm.then_inc(s[f"turned{L}"], 1)
                for l in range(1, LEV):
                    n = p * R + l
                    for L in lanes:
                        pe.wait_ge(s[f"X0{L}"], p + 1)
                        pe.wait_ge(s[f"atm{L}"], n)
                        if l > 1:
                            pe.wait_ge(s[f"XYs{L}"], n - 1)
                        for h in range(H4):
                            mm = pe.matmul(ps[:, 3 * L, hd(h)], atm[l % 2][:, L, hd(h)], X[:, L, hd(h)], start=True, stop=True)
                        mm.then_inc(s[f"Wm{L}"], 1)
                    for L in lanes:
                        pe.wait_ge(s[f"Wc{L}"], n)
                        for h in range(H4):
                            if l < LEV - 1:
                                pe.matmul(ps[:, 3 * L + 1, hd(h)], Y[:, L, hd(h)], Wm[:, L, hd(h)], start=True, stop=True)
                            mm = pe.matmul(ps[:, 3 * L + 2, hd(h)], Wm[:, L, hd(h)], Y[:, L, hd(h)], start=True, stop=True)
                        mm.then_inc(s[f"XY{L}"], 1)
                for L in lanes:
                    i = 2 * p + L
                    if L:
                        pe.wait_ge(s["Su"], i)
                        pe.wait_ge(s["oc"], i)
                    else:
                        pe.wait_ge(s["tok1"], p + 1)
                    for h in range(H4):
                        mm = pe.matmul(ps[:, 6, hd(h)], z[:, 4 + h, chunk(i)], S[:, hd(h)], start=True, stop=True)
                    mm.then_inc(s["ks"], 1)
                    pe.wait_ge(s["rhs"], i + 1)
                    for h in range(H4):
                        mm = pe.matmul(ps[:, 7, hd(h)], Y[:, L, hd(h)], rhs[:, hd(h)], start=True, stop=True)
                    mm.then_inc(s["vn"], 1)
                    pe.wait_ge(s["vnc"], i + 1)
                    pe.wait_ge(s[f"qg{L}"], p + 1)
                    for h in range(H4):
                        mm = pe.matmul(ps[:, 7, hd(h)], kd[:, L, hd(h)], vn[:, hd(h)], start=True, stop=True)
                    mm.then_inc(s["U"], 1)
                    for h in range(H4):
                        pe.matmul(ps[:, 6, hd(h)], S[:, hd(h)], qg[:, L, hd(h)], start=True, stop=False)
                        mm = pe.matmul(ps[:, 6, hd(h)], vn[:, hd(h)], at[:, L, hd(h)], start=False, stop=True)
                    mm.then_inc(s["ou"], 1)

        @block.scalar
        def _(act):
            for p in range(NP):
                for L in lanes:
                    act.wait_ge(s[f"raw{L}"], p + 1)
                    act.activation(egb[:, L], ps[:, 3 * L + 2, :], ACT.Exp).then_inc(s[f"egb{L}"], 1)
                    act.wait_ge(s[f"kv{L}"], p + 1)
                    act.activation(kt[:, L], ps[:, 6, :], ACT.Copy)
                    act.activation(vt[:, L], ps[:, 7, :], ACT.Copy).then_inc(s[f"tok{L}"], 1)
                    act.wait_ge(s[f"diff{L}"], p + 1)
                    act.activation(dec[:, L], dec[:, L], ACT.Exp, scale=-1.0).then_inc(s[f"dec{L}"], 1)
                    act.activation(dcol[:, L, 1], dcol[:, L, 0], ACT.Exp).then_inc(s[f"dcx{L}"], 1)
                for L in lanes:
                    act.wait_ge(s[f"turned{L}"], p + 1)
                    act.activation(AT[:, L], ps[:, 3 * L, :], ACT.Copy).then_inc(s[f"AT{L}"], 1)
                    act.activation(at[:, L], ps[:, 3 * L + 1, :], ACT.Copy).then_inc(s[f"at{L}"], 1)
                for l in range(1, LEV):
                    for L in lanes:
                        act.wait_ge(s[f"Wm{L}"], p * R + l)
                        act.activation(Wm[:, L], ps[:, 3 * L, :], ACT.Copy).then_inc(s[f"Wc{L}"], 1)
                for L in lanes:
                    i = 2 * p + L
                    act.wait_ge(s["vn"], i + 1)
                    act.activation(vn[:], ps[:, 7, :], ACT.Copy).then_inc(s["vnc"], 1)
                    act.wait_ge(s["ou"], i + 1)
                    act.activation(o[:, :, chunk(i)], as4(ps[:, 6, :]), ACT.Copy).then_inc(s["oc"], 1)

        @block.gpsimd
        def _(pool):
            pool.wait_ge(s["in"], 32)
            for p in range(NP):
                for l in range(1, LEV):
                    for L in lanes:
                        pool.wait_ge(s[f"at{L}"], p + 1)
                        if l >= 3:
                            pool.wait_ge(s[f"Wm{L}"], p * R + l - 2)
                        pool.tensor_tensor(as4(atm[l % 2][:, L]), as4(AT[:, L]), mid(up[:, l, :], H4), ALU.mult).then_inc(s[f"atm{L}"], 1)

        @block.vector
        def _(dve):
            link = Link(dve, s["link"])
            link(dve.memset(S[:], 0.0))
            dve.wait_ge(s["in"], 32)
            for p in range(NP):
                for L in lanes:
                    i, b = 2 * p + L, 3 * L
                    dve.wait_ge(s[f"raw{L}"], p + 1)
                    dve.wait_ge(s[f"egb{L}"], p + 1)
                    for h in range(H4):
                        dve.tensor_scalar(dec[:, L, hd(h)], ps[:, b + 2, hd(h)], gcol[:, i, h:h + 1], 0.0, ALU.subtract, ALU.max)
                    dve.tensor_tensor(dcol[:, L, 0], ps[:, b + 2, P - 1:C:P], gcol[:, i, :], ALU.subtract).then_inc(s[f"diff{L}"], 1)
                for L in lanes:
                    i, b = 2 * p + L, 3 * L
                    dve.wait_ge(s[f"dec{L}"], p + 1)
                    link(dve.tensor_tensor(as4(dec[:, L]), as4(dec[:, L]), mid(lo[:, 0, :], H4), ALU.mult))
                    for h in range(H4):
                        dve.scalar_tensor_tensor(A[:, L, hd(h)], ps[:, b, hd(h)], bcol[:, i, h:h + 1], dec[:, L, hd(h)], ALU.mult, ALU.mult)
                    link(dve.tensor_tensor(qks[:, L], ps[:, b + 1, :], dec[:, L], ALU.mult))
                    dve.tensor_tensor(as4(A[:, L]), as4(A[:, L]), mid(lo[:, 1, :], H4), ALU.mult).then_inc(s[f"A{L}"], 1)
                    dve.wait_ge(s[f"A{L}"], p + 1)
                    link(dve.tensor_tensor(as4(X[:, L]), as4(A[:, L]), mid(lo[:, 2, :], H4), ALU.mult))
                    dve.tensor_tensor(as4(X[:, L]), mid(c.ident[:], H4), as4(X[:, L]), ALU.subtract)
                for L in lanes:
                    i = 2 * p + L
                    dve.wait_ge(s[f"AT{L}"], p + 1)
                    link(dve.tensor_tensor(as4(Y[:, L]), as4(AT[:, L]), mid(up[:, 0, :], H4), ALU.mult))
                    dve.tensor_tensor(as4(Y[:, L]), mid(c.ident[:], H4), as4(Y[:, L]), ALU.subtract).then_inc(s[f"X0{L}"], 1)
                for l in range(1, LEV):
                    for L in lanes:
                        if l <= 1:
                            dve.tensor_tensor(as4(qg[:, L]), z[:, 0:4, chunk(2 * p + L)], as4(egb[:, L]), ALU.mult)
                            dve.wait_ge(s[f"tok{L}"], p + 1)
                            dve.wait_ge(s[f"dcx{L}"], p + 1)
                            dve.tensor_tensor(as4(kd[:, L]), as4(kt[:, L]), last(dcol[:, L, 1], P), ALU.mult).then_inc(s[f"qg{L}"], 1)
                    for L in lanes:
                        dve.wait_ge(s[f"XY{L}"], p * R + l)
                        if l < LEV - 1:
                            dve.tensor_tensor(X[:, L], X[:, L], ps[:, 3 * L + 1, :], ALU.subtract)
                        dve.tensor_tensor(Y[:, L], Y[:, L], ps[:, 3 * L + 2, :], ALU.subtract).then_inc(s[f"XYs{L}"], 1)
                for L in lanes:
                    i = 2 * p + L
                    dve.wait_ge(s["ks"], i + 1)
                    link(dve.tensor_tensor(as4(rhs[:]), as4(ps[:, 6, :]), last(egcol[:, i, :], P), ALU.mult))
                    link(dve.tensor_tensor(rhs[:], rhs[:], vt[:, L], ALU.add))
                    dve.wait_ge(s[f"XYs{L}"], (p + 1) * R)
                    dve.tensor_tensor(as4(rhs[:]), as4(rhs[:]), last(bcol[:, i, :], P), ALU.mult).then_inc(s["rhs"], 1)
                    dve.wait_ge(s["ou"], i + 1)
                    link(dve.tensor_tensor(as4(S[:]), as4(S[:]), last(egb[:, L, P - 1:C:P], P), ALU.mult))
                    dve.tensor_tensor(S[:], S[:], ps[:, 7, :], ALU.add).then_inc(s["Su"], 1)


def store_states(c, name, S, out):
    nc = c.nc
    sem = c.sem(f"{name}_stored")
    with nc.Block() as block:
        @block.sync
        def _(sp):
            sp.dma_start(out, S).then_inc(sem, 16)
            sp.wait_ge(sem, 16)


def recurrent_samples(c, name, state_in, state_out, o, q, k, vT, decay, beta=None):
    nc, ps, dr = c.nc, c.ps, c.dram
    s = Semaphores(c, name)
    NPR = H4 * NB
    N = 4
    with ExitStack() as ctx:
        sb = lambda n, sh: ctx.enter_context(nc.sbuf_tensor(f"{name}_{n}", sh, F32))
        S = sb("S", [P, NPR, P])
        pr = sb("pr", [P, N, P])
        dg = sb("dg", [P, N, P])
        u = sb("u", [P, N, P])
        qc = sb("qc", [P, NPR])
        block = ctx.enter_context(nc.Block())

        @block.sync
        def _(sp):
            sp.dma_start(S[:], state_in).then_inc(s["in"], 16)
            sp.wait_ge(s["u"], NPR // N)
            sp.dma_start(state_out, S[:]).then_inc(s["out"], 16)
            sp.wait_ge(s["out"], 16)

        @block.vector
        def _(dve):
            link = Link(dve, s["link"])
            dve.tensor_copy(qc[:].rearrange("p (h b) -> p h b", b=NB), q).then_inc(s["q"], 1)
            dve.wait_ge(s["in"], 16)
            for n in range(NPR // N):
                h, b0 = n * N // NB, n * N % NB
                sl = slice(n * N, (n + 1) * N)
                kk, vv = k[:, h, b0:b0 + N], vT[:, h, b0:b0 + N]
                d = decay(h, b0, N)
                if beta is not None:
                    dve.tensor_tensor(pr[:], S[:, sl], last(kk, P), ALU.mult)
                dve.tensor_tensor(dg[:], mid(c.ident[:], N), last(vv, P), ALU.mult).then_inc(s["p"], 1)
                link(dve.tensor_tensor(S[:, sl], S[:, sl], last(d, P), ALU.mult))
                dve.wait_ge(s["mm"], n + 1)
                vb = ps[:, 1, :].rearrange("p (n v) -> p n v", n=N)
                if beta is not None:
                    link(dve.tensor_tensor(u[:], ps[:, 0, :].rearrange("p (n v) -> p n v", n=N), last(d, P), ALU.mult))
                    link(dve.tensor_tensor(u[:], vb, u[:], ALU.subtract))
                    link(dve.tensor_tensor(u[:], u[:], last(beta(h, b0, N), P), ALU.mult))
                    link(dve.tensor_tensor(u[:], u[:], last(kk, P), ALU.mult))
                else:
                    link(dve.tensor_tensor(u[:], vb, last(kk, P), ALU.mult))
                dve.tensor_tensor(S[:, sl], S[:, sl], u[:], ALU.add).then_inc(s["u"], 1)
            dve.wait_ge(s["omm"], 1)
            dve.tensor_copy(o[:, :, TP:T], ps[:, 2, 0:NPR].rearrange("p (h b) -> p h b", b=NB))

        @block.tensor
        def _(pe):
            for n in range(NPR // N):
                pe.wait_ge(s["p"], n + 1)
                if n:
                    pe.wait_ge(s["u"], n)
                if beta is not None:
                    pe.matmul(ps[:, 0, :], c.ones[:], pr[:].rearrange("p n v -> p (n v)"), start=True, stop=True)
                pe.matmul(ps[:, 1, :], c.ones[:], dg[:].rearrange("p n v -> p (n v)"), start=True, stop=True).then_inc(s["mm"], 1)
            pe.wait_ge(s["u"], NPR // N)
            pe.wait_ge(s["q"], 1)
            for n in range(NPR):
                mm = pe.matmul(ps[:, 2, n:n + 1], S[:, n, :], qc[:, n:n + 1], start=True, stop=True)
            mm.then_inc(s["omm"], 1)


def spread_rows(c, name, sel, small, rows, dst):
    nc, ps = c.nc, c.ps
    mmd = c.sem(f"{name}_spread")
    with nc.Block() as block:
        @block.tensor
        def _(pe):
            for k, r in enumerate(rows):
                for h in range(H4):
                    mm = pe.matmul(ps[:, k, h * NB:(h + 1) * NB], sel[r:r + 4, h, :], small[r:r + 4, TP:T], start=True, stop=True)
            mm.then_inc(mmd, 1)

        @block.vector
        def _(dve):
            dve.wait_ge(mmd, 1)
            dve.tensor_copy(dst[:].rearrange("p k h b -> p k (h b)"), ps[:, 0:len(rows), 0:H4 * NB])


def deltanet(c, small):
    nc, dr = c.nc, c.dram
    o = c.oT[1]
    with ExitStack() as ctx:
        sb = lambda n, sh: ctx.enter_context(nc.sbuf_tensor(f"dn_{n}", sh, F32))
        z = sb("z", [P, 16, T])
        gcol, bcol, egcol = sb("gcol", [P, NBLK, H4]), sb("bcol", [P, NBLK, H4]), sb("egcol", [P, NBLK, H4])
        sel = sb("sel", [P, H4, P])
        dbs = sb("dbs", [P, 2, H4, NB])
        S = sb("S", [P, H4 * P])
        with ExitStack() as cv:
            conv = Convolution(c, z, lambda n, sh: cv.enter_context(nc.sbuf_tensor(f"cv_{n}", sh, F32)))
            project(c, "dnp", dr["w_dn"], 16, z, conv)
        inverse_norm(c, "l2", z, 8, 1.0,
                     lambda dve, m, r: dve.scalar_tensor_tensor(z[:, m], z[:, m], P ** -0.5 if m < 4 else 1.0, r, ALU.mult, ALU.mult))
        deltanet_scalars(c, small, None, gcol, bcol, egcol, sel)
        spread_rows(c, "dn", sel, small, (32, 64), dbs)
        recurrent_samples(c, "dns", dr["state_dn"], dr["o_dn_s"], o, z[:, 0:4, TP:T], z[:, 4:8, TP:T], z[:, 8:12, TP:T],
                          lambda h, b, n: dbs[:, 0, h, b:b + n], lambda h, b, n: dbs[:, 1, h, b:b + n])
        deltanet_prompt(c, z, small, gcol, bcol, egcol, sel, S, o)
        store_states(c, "dn", S[:], dr["o_dn_p"])
        gated_norm(c, "dng", o, z[:, 12:16], dr["dn_norm"])


def hgrn2(c):
    nc, ps, dr = c.nc, c.ps, c.dram
    o = c.oT[2]
    with ExitStack() as ctx:
        sb = lambda n, sh: ctx.enter_context(nc.sbuf_tensor(f"hg_{n}", sh, F32))
        z = sb("z", [P, 16, T])
        project(c, "hgp", dr["w_hg"], 16, z)
        f = sb("f", [P, H4, NB])
        Gs = sb("Gs", [P, 2, T])
        s = Semaphores(c, "hg")
        with ExitStack() as c2:
            s2 = lambda n, sh: c2.enter_context(nc.sbuf_tensor(f"hg_{n}", sh, F32))
            up = s2("up", [P, LEV, P])
            one = s2("one", [P, TP])
            lf = s2("lf", [P, T])
            E = s2("E", [P, 2, TP])
            Z = s2("Z", [P, 2, TP])
            at = s2("at", [P, NBLK, P])
            vt = s2("vt", [P, NBLK, P])
            qg = s2("qg", [P, TP])
            kd = s2("kd", [P, TP])
            kt = s2("kt", [P, NBLK, P])
            eg = s2("eg", [P, NBLK])
            S = s2("S", [P, H4, P])
            block = c2.enter_context(nc.Block())
            NL = LEV + 1
            bank2 = lambda t: t.rearrange("p (a b) t -> p a (b t)", a=2)

            @block.sync
            def _(sp):
                sp.dma_start(up[:], dr["up"]).then_inc(s["in"], 16)
                sp.wait_ge(s["Su"], H4 * NBLK)
                sp.dma_start(dr["o_hg_p"], S[:]).then_inc(s["out"], 16)
                sp.wait_ge(s["out"], 16)

            @block.scalar
            def _(act):
                def forget(h):
                    k = z[:, 4 + h]
                    if h:
                        act.wait_ge(s["G"], h)
                    act.activation(lf[:], k, ACT.Abs).then_inc(s["alink"], 1)
                    act.wait_ge(s["alink"], 2 * h + 1)
                    act.activation(lf[:], lf[:], ACT.Exp, scale=-1.0).then_inc(s["alink"], 1)
                    act.wait_ge(s["alink"], 2 * h + 2)
                    act.activation(lf[:], lf[:], ACT.Ln, bias=c.ones[:, 0:1]).then_inc(s["l"], 1)
                    act.wait_ge(s["a"], h + 1)
                    act.activation(k, k, ACT.Sigmoid, scale=-1.0).then_inc(s["k"], 1)

                forget(0)
                for h in range(H4):
                    for l in range(LEV):
                        n = h * LEV + l
                        act.wait_ge(s["D"], n + 1)
                        act.activation(E[:, n % 2], E[:, n % 2], ACT.Exp).then_inc(s["E"], 1)
                        if l == 1:
                            act.activation(f[:, h, :], Gs[:, h % 2, TP:T], ACT.Exp)
                            act.activation(qg[:], Gs[:, h % 2, 0:TP], ACT.Exp).then_inc(s["fs"], 1)
                        if l == 2:
                            act.wait_ge(s["kd0"], h + 1)
                            act.activation(kd[:], kd[:], ACT.Exp).then_inc(s["kt"], 1)
                        if l == 3:
                            act.wait_ge(s["vt"], h + 1)
                            act.activation(bank2(vt[:]), ps[:, 4:6, :], ACT.Copy).then_inc(s["vtc"], 1)
                    if h + 1 < H4:
                        forget(h + 1)
                    for i in range(NBLK):
                        n = h * NBLK + i
                        act.wait_ge(s["ou"], n + 1)
                        act.activation(o[:, h, i * BLK:(i + 1) * BLK], ps[:, 6 + n % 2, 0:P], ACT.Copy).then_inc(s["oc"], 1)

            @block.gpsimd
            def _(pool):
                for h in range(H4):
                    G = Gs[:, h % 2, 0:TP]
                    pool.wait_ge(s["G"], h + 1)
                    for l in range(LEV):
                        n = h * LEV + l
                        hs = 1 << l
                        v = lambda t: t.rearrange("p (i u x) -> p i u x", u=2, x=hs)
                        Gv, Ev = v(G), v(E[:, n % 2])
                        anchor = Gv[:, :, 0, hs - 1:hs].to_broadcast([P, TP // (2 * hs), hs])
                        if n >= 2:
                            pool.wait_ge(s["Z"], n - 1)
                        pool.tensor_tensor(Ev[:, :, 1], Gv[:, :, 1], anchor, ALU.subtract)
                        pool.tensor_tensor(Ev[:, :, 0], anchor, Gv[:, :, 0], ALU.subtract).then_inc(s["D"], 1)
                        if l == 1:
                            Gc = G.rearrange("p (i t) -> p i t", t=BLK)
                            if h:
                                pool.wait_ge(s["ktc"], h)
                            pool.tensor_tensor(kd[:].rearrange("p (i t) -> p i t", t=BLK),
                                               Gc[:, :, BLK - 1:BLK].to_broadcast([P, NBLK, BLK]), Gc, ALU.subtract).then_inc(s["kd0"], 1)

            @block.vector
            def _(dve):
                link = Link(dve, s["link"])

                def decay(h):
                    G = Gs[:, h % 2]
                    dve.wait_ge(s["l"], h + 1)
                    dve.tensor_scalar(G, z[:, 4 + h], 0.0, None, ALU.min).then_inc(s["a"], 1)
                    dve.wait_ge(s["a"], h + 1)
                    link(dve.tensor_tensor(lf[:], G, lf[:], ALU.subtract))
                    dve.tensor_copy(G[:, TP:T], lf[:, TP:T])
                    dve.tensor_tensor_scan(G[:, 0:TP], one[:], lf[:, 0:TP], 0.0, ALU.mult, ALU.add).then_inc(s["G"], 1)

                def factors(h, l):
                    n = h * LEV + l
                    v = lambda t: t.rearrange("p (i u x) -> p i u x", u=2, x=1 << l)
                    q, k, Ev, Zv = v(z[:, h, 0:TP]), v(z[:, 4 + h, 0:TP]), v(E[:, n % 2]), v(Z[:, n % 2])
                    dve.wait_ge(s["E"], n + 1)
                    if n >= 2:
                        dve.wait_ge(s["mm"], h * NL + l if l >= 2 else (h - 1) * NL + LEV - 1 + l)
                    dve.tensor_tensor(Zv[:, :, 1], q[:, :, 1], Ev[:, :, 1], ALU.mult)
                    dve.tensor_tensor(Zv[:, :, 0], k[:, :, 0], Ev[:, :, 0], ALU.mult).then_inc(s["Z"], 1)

                def masked(h, l):
                    m = h * NL + l + 1
                    tmp = o[:, h, 0:TP]
                    dve.wait_ge(s["mm"], m + 1)
                    src = ps[:, 2 * (m % 2):2 * (m % 2) + 2, :]
                    as2 = lambda t: t.rearrange("p (a b t) -> p a b t", a=2, t=P)
                    mask = (c.ident[:] if l < 0 else up[:, l, :]).unsqueeze(1).unsqueeze(1).to_broadcast([P, 2, 4, P])
                    src = src.rearrange("p a (b t) -> p a b t", t=P)
                    dst = at[:].rearrange("p (a b) t -> p a b t", a=2)
                    if l < 0:
                        dve.tensor_tensor(dst, src, mask, ALU.mult).then_inc(s["mk"], 1)
                    else:
                        dve.tensor_tensor(as2(tmp), src, mask, ALU.mult).then_inc(s["mk"], 1)
                    dve.wait_ge(s["mk"], m + 1)
                    if l >= 0:
                        link(dve.tensor_tensor(dst, dst, as2(tmp), ALU.add))

                link(dve.memset(one[:], 1.0))
                dve.memset(S[:], 0.0)
                link(dve.memset(one[:].rearrange("p (i t) -> p i t", t=BLK)[:, :, 0:1], 0.0))
                dve.tensor_scalar(z[:, 0:4], z[:, 0:4], P ** -0.5, None, ALU.mult).then_inc(s["q"], 1)
                dve.wait_ge(s["in"], 16)
                dve.wait_ge(s["q"], 1)
                decay(0)
                for h in range(H4):
                    q, k = z[:, h, 0:TP], z[:, 4 + h, 0:TP]
                    dve.wait_ge(s["k"], h + 1)
                    factors(h, 0)
                    masked(h, -1)
                    for l in range(LEV):
                        if l + 1 < LEV:
                            factors(h, l + 1)
                        else:
                            dve.wait_ge(s["kt"], h + 1)
                            dve.tensor_tensor(kd[:], kd[:], k, ALU.mult).then_inc(s["kd"], 1)
                        masked(h, l)
                    dve.wait_ge(s["fs"], h + 1)
                    link(dve.tensor_copy(eg[:], qg[:, BLK - 1:TP:BLK]))
                    dve.tensor_tensor(qg[:], qg[:], q, ALU.mult).then_inc(s["qg"], 1)
                    dve.wait_ge(s["turned"], h + 1)
                    dve.tensor_copy(bank2(kt[:]), ps[:, 6:8, :]).then_inc(s["ktc"], 1)
                    if h + 1 < H4:
                        decay(h + 1)
                    for i in range(NBLK):
                        n = h * NBLK + i
                        dve.wait_ge(s["ou"], n + 1)
                        link(dve.tensor_scalar(S[:, h, :], S[:, h, :], eg[:, i:i + 1], None, ALU.mult))
                        dve.tensor_tensor(S[:, h, :], S[:, h, :], ps[:, 4 + n % 2, 0:P], ALU.add).then_inc(s["Su"], 1)

            @block.tensor
            def _(pe):
                pe.wait_ge(s["q"], 1)
                for h in range(H4):
                    pe.wait_ge(s["k"], h + 1)
                    for l in range(-1, LEV):
                        m, n = h * NL + l + 1, h * LEV + l
                        if l >= 0:
                            pe.wait_ge(s["Z"], n + 1)
                        if m >= 2:
                            pe.wait_ge(s["mk"], m - 1)
                        for i in range(NBLK):
                            t = slice(i * BLK, (i + 1) * BLK)
                            x, y = (Z[:, n % 2, t], Z[:, n % 2, t]) if l >= 0 else (z[:, 4 + h, t], z[:, h, t])
                            mm = pe.matmul(ps[:, 2 * (m % 2) + i // 4, (i % 4) * P:(i % 4 + 1) * P], x, y, start=True, stop=True)
                        mm.then_inc(s["mm"], 1)
                        if l == 1:
                            if h:
                                pe.wait_ge(s["Su"], NBLK * h)
                            for i in range(NBLK):
                                t_ = pe.transpose(ps[:, 4 + i // 4, (i % 4) * P:(i % 4 + 1) * P], z[:, 8 + h, i * BLK:(i + 1) * BLK], c.ident[:])
                            t_.then_inc(s["vt"], 1)
                    pe.wait_ge(s["kd"], h + 1)
                    if h:
                        pe.wait_ge(s["oc"], NBLK * h)
                    for i in range(NBLK):
                        t_ = pe.transpose(ps[:, 6 + i // 4, (i % 4) * P:(i % 4 + 1) * P], kd[:, i * BLK:(i + 1) * BLK], c.ident[:])
                    t_.then_inc(s["turned"], 1)
                    pe.wait_ge(s["ktc"], h + 1)
                    pe.wait_ge(s["vtc"], h + 1)
                    pe.wait_ge(s["qg"], h + 1)
                    for i in range(NBLK):
                        n = h * NBLK + i
                        t = slice(i * BLK, (i + 1) * BLK)
                        if n >= 2:
                            pe.wait_ge(s["oc"], n - 1)
                        if i == 0 and h:
                            pe.wait_ge(s["Su"], n)
                        if i >= 2:
                            pe.wait_ge(s["Su"], n - 1)
                        pe.matmul(ps[:, 4 + n % 2, 0:P], kt[:, i, :], vt[:, i, :], start=True, stop=True)
                        if i:
                            pe.wait_ge(s["Su"], n)
                        pe.matmul(ps[:, 6 + n % 2, 0:P], S[:, h, :], qg[:, t], start=True, stop=False)
                        pe.matmul(ps[:, 6 + n % 2, 0:P], vt[:, i, :], at[:, i, :], start=False, stop=True).then_inc(s["ou"], 1)

        recurrent_samples(c, "hgs", dr["state_hg"], dr["o_hg_s"], o, z[:, 0:4, TP:T], z[:, 4:8, TP:T], z[:, 8:12, TP:T],
                          lambda h, b, n: f[:, h, b:b + n])
        gated_norm(c, "hgg", o, z[:, 12:16], dr["hg_norm"])


def merge(c, mT):
    nc, ps, dr = c.nc, c.ps, c.dram
    wg_here = [c.sem(f"mg_gate_w{b}") for b in range(3)]
    wb_here = [c.sem(f"mg_branch_w{b}") for b in range(3)]
    s = Semaphores(c, "mg")
    with ExitStack() as ctx:
        sb = lambda n, sh: ctx.enter_context(nc.sbuf_tensor(f"mg_{n}", sh, F32))
        wg = sb("wg", [P, 3, KT, P])
        wb = sb("wb", [P, 3, H4, P])
        sg = sb("sg", [P, T])
        tmp = sb("tmp", [P, T])
        block = ctx.enter_context(nc.Block())
        win = lambda t: t.rearrange("p (n w) -> p n w", n=NW)

        @block.sync
        def _(sp):
            with sp.Fori(0, KT) as m:
                for b in range(3):
                    sp.wait_ge(s["wfree"], 3 * m + b + 1)
                    sp.dma_start(wg[:, b], dr["w_mg"][3 * m + b]).then_inc(wg_here[b], 16)
                    sp.dma_start(wb[:, b], dr["w_br"][3 * m + b]).then_inc(wb_here[b], 16)

        @block.tensor
        def _(pe):
            pe.sem_inc(s["wfree"], 3)
            with pe.Fori(0, KT) as m:
                for b in range(3):
                    pe.wait_ge(wg_here[b], 16 * m + 16)
                    pe.wait_ge(s["gate_read"], 3 * m + b + 1)
                    for n in range(NW):
                        for k in range(KT):
                            mm = pe.matmul(ps[:, n, 0:W], wg[:, b, k, :], c.xT[:, k, n * W:(n + 1) * W], start=(k == 0), stop=(k == KT - 1))
                    mm.then_inc(s["gate"], 1)
                    pe.wait_ge(wb_here[b], 16 * m + 16)
                    pe.wait_ge(s["br_read"], 3 * m + b + 1)
                    for n in range(NW):
                        for k in range(H4):
                            mm = pe.matmul(ps[:, 3 + n, 0:W], wb[:, b, k, :], c.oT[b][:, k, n * W:(n + 1) * W], start=(k == 0), stop=(k == H4 - 1))
                    mm.then_inc(s["br"], 1)
                    pe.wait_ge(s["br"], 3 * m + b + 1)
                    pe.sem_inc(s["wfree"], 1)

        @block.scalar
        def _(act):
            act.sem_inc(s["gate_read"], 1)
            with act.Fori(0, KT) as m:
                for b in range(3):
                    act.wait_ge(s["gate"], 3 * m + b + 1)
                    act.wait_ge(s["sg_used"], 3 * m + b + 1)
                    act.activation(win(sg[:]), ps[:, 0:NW, 0:W], ACT.Sigmoid).then_inc(s["gate_read"], 1)

        @block.vector
        def _(dve):
            dve.sem_inc(s["br_read"], 1)
            dve.sem_inc(s["sg_used"], 1)
            with dve.Fori(0, KT) as m:
                for b in range(3):
                    dve.wait_ge(s["br"], 3 * m + b + 1)
                    dve.wait_ge(s["gate_read"], 3 * m + b + 2)
                    if b == 0:
                        dve.tensor_tensor(win(mT[:, m, :]), win(sg[:]), ps[:, 3:3 + NW, 0:W], ALU.mult).then_inc(s["br_read"], 1)
                    else:
                        dve.tensor_tensor(win(tmp[:]), win(sg[:]), ps[:, 3:3 + NW, 0:W], ALU.mult).then_inc(s["br_read"], 1)
                    dve.wait_ge(s["br_read"], 3 * m + b + 2)
                    dve.sem_inc(s["sg_used"], 1)
                    if b:
                        dve.tensor_tensor(mT[:, m, :], mT[:, m, :], tmp[:], ALU.add).then_inc(s["link"], 1)
                        dve.wait_ge(s["link"], 2 * m + b)


def rows(t):
    return BLK if t < NBLK else NB


def norm_rows(dve, act_sems, link, y, r, st, gb, n):
    asked, given = act_sems
    for h in range(2):
        dve.bn_stats(st[0:r, 6 * h:6 * h + 6], y[:, h * 512:(h + 1) * 512])
    link(dve.engine_nop())
    link(dve.bn_aggr(st[0:r, 12:14], st[0:r, 0:12]))
    dve.engine_nop().then_inc(asked, 1)
    dve.wait_ge(given, n + 1)
    link(dve.tensor_scalar(y, y, st[0:r, 12:13], st[0:r, 14:15], ALU.subtract, ALU.mult))
    link(dve.tensor_tensor(y, y, gb[0:r, 0], ALU.mult))
    return dve.tensor_tensor(y, y, gb[0:r, 1], ALU.add)


def inverse_root(act, eps, st, r, asked, given, own, n):
    act.wait_ge(asked, n + 1)
    act.activation(st[0:r, 14:15], st[0:r, 13:14], ACT.Ln, bias=eps[0:r]).then_inc(own, 1)
    act.wait_ge(own, n + 1)
    act.activation(st[0:r, 14:15], st[0:r, 14:15], ACT.Exp, scale=-0.5).then_inc(given, 1)


def mix_out(c, mT, y, x1T):
    nc, ps, dr = c.nc, c.ps, c.dram
    s = Semaphores(c, "mo")
    with ExitStack() as ctx:
        sb = lambda n, sh: ctx.enter_context(nc.sbuf_tensor(f"mo_{n}", sh, F32))
        w = sb("w", [P, KT, D])
        gb = sb("gb", [P, 2, D])
        xt = sb("xt", [P, 2, D])
        st = sb("st", [P, 16])
        block = ctx.enter_context(nc.Block())

        @block.sync
        def _(sp):
            sp.dma_start(w[:], dr["w_out"]).then_inc(s["w"], 16)
            for k in range(2):
                sp.dma_start(gb[:, k, :], dr["ln1"][k:k + 1, :].to_broadcast([P, D])).then_inc(s["gb"], 16)
            for t in range(NTT):
                if t >= 2:
                    sp.wait_ge(s["read"], t - 1)
                sp.dma_start(xt[0:rows(t), t % 2], dr["x"][t * BLK:t * BLK + rows(t)]).then_inc(s["x"], 16)
                sp.wait_ge(s["x"], 16 * (t + 1))
            for t in range(NTT):
                sp.wait_ge(s["y"], t + 1)
                sp.dma_start(dr["s_x1"][t * BLK:t * BLK + rows(t)], y[0:rows(t), t, :]).then_inc(s["stored"], 16)
            sp.wait_ge(s["stored"], 16 * NTT)

        @block.tensor
        def _(pe):
            pe.wait_ge(s["w"], 16)

            def turn(t):
                r = rows(t)
                pe.wait_ge(s["y"], t + 1)
                if t:
                    pe.wait_ge(s["trc"], t)
                for k in range(KT):
                    tr = pe.transpose(ps[:, 4 + k // 4, (k % 4) * P:(k % 4) * P + r], y[0:r, t, k * P:(k + 1) * P], c.ident[0:r, 0:r])
                tr.then_inc(s["tr"], 1)

            for t in range(NTT):
                r = rows(t)
                if t >= 2:
                    pe.wait_ge(s["read"], t - 1)
                for n in range(2):
                    for k in range(KT):
                        mm = pe.matmul(ps[0:r, 2 * (t % 2) + n, :], mT[:, k, t * BLK:t * BLK + r], w[:, k, n * 512:(n + 1) * 512], start=(k == 0), stop=(k == KT - 1))
                mm.then_inc(s["mm"], 1)
                if t:
                    turn(t - 1)
            turn(NTT - 1)

        @block.vector
        def _(dve):
            link = Link(dve, s["link"])
            dve.wait_ge(s["gb"], 32)
            for t in range(NTT):
                r = rows(t)
                dve.wait_ge(s["mm"], t + 1)
                dve.wait_ge(s["x"], 16 * (t + 1))
                yy = y[0:r, t, :]
                dve.scalar_tensor_tensor(yy.rearrange("p (n w) -> p n w", n=2), xt[0:r, t % 2].rearrange("p (n w) -> p n w", n=2), ALPHA,
                                         ps[0:r, 2 * (t % 2):2 * (t % 2) + 2, :], ALU.mult, ALU.add).then_inc(s["read"], 1)
                dve.wait_ge(s["read"], t + 1)
                norm_rows(dve, (s["asked"], s["given"]), link, yy, r, st, gb, t).then_inc(s["y"], 1)

        @block.scalar
        def _(act):
            def copy(t):
                r = rows(t)
                act.wait_ge(s["tr"], t + 1)
                act.activation(x1T[:, :, t * BLK:t * BLK + r].rearrange("p (a b) t -> p a b t", a=2),
                               ps[:, 4:6, :].rearrange("p a (b t) -> p a b t", b=4)[:, :, :, 0:r], ACT.Copy).then_inc(s["trc"], 1)

            for t in range(NTT):
                inverse_root(act, c.eps, st, rows(t), s["asked"], s["given"], s["own"], t)
                if t:
                    copy(t - 1)
            copy(NTT - 1)


def route(c, x1T, rt):
    nc, ps, dr = c.nc, c.ps, c.dram
    s = Semaphores(c, "rt")
    NG = 4
    FAR = 65536.0
    with ExitStack() as ctx:
        sb = lambda n, sh, dt=F32: ctx.enter_context(nc.sbuf_tensor(f"rt_{n}", sh, dt))
        w = sb("w", [P, KT, NE])
        rb = sb("rb", [P, NE])
        tri = sb("tri", [P, P])
        blk = sb("blk", [P, EB])
        tok = sb("tok", [P, NTT], U32)
        zero = sb("zero", [P, EB + 1], U32)
        sc = sb("sc", [P, NTT, NE])
        bi = sb("bi", [P, NTT * NG, 4])
        rank = sb("rank", [P, NTT * NG, 4])
        gs = sb("gs", [P, NTT, NG])
        grank = sb("grank", [P, NTT, NG])
        a = sb("a", [P, NTT * NG])
        b = sb("b", [P, NTT * NG])
        su = sb("su", [P, NTT])
        gw = sb("gw", [P, NTT, NE])
        at = sb("at", [P, NTT, NE])
        far = sb("far", [P, NTT, NE])
        eq = sb("eq", [P, NTT, NE])
        df = sb("df", [P, TOPK, NTT])
        cnt = sb("cnt", [P, NE])
        nb = sb("nb", [P, NE])
        cum = sb("cum", [P, NE])
        t16 = sb("t16", [P, NE])
        past = sb("past", [P, EB, NE])
        be = sb("be", [P, EB + 1])
        block = ctx.enter_context(nc.Block())
        sel = rank[:].rearrange("p (t g) e -> p t (g e)", g=NG)
        fl = lambda t: t.rearrange("p t e -> p (t e)")

        @block.sync
        def _(sp):
            sp.dma_start(w[:], dr["w_router"]).then_inc(s["in"], 16)
            sp.dma_start(rb[:], dr["router_bias"].to_broadcast([P, NE])).then_inc(s["in"], 16)
            sp.dma_start(tri[:], dr["tri"]).then_inc(s["in"], 16)
            sp.dma_start(blk[:], dr["blk"]).then_inc(s["in"], 16)
            sp.dma_start(tok[:], dr["tok"]).then_inc(s["in"], 16)
            sp.wait_ge(s["zero"], 1)
            sp.dma_start(dr["s_row"].rearrange("(p n) o -> p (n o)", p=P), zero[:]).then_inc(s["cleared"], 16)

        @block.gpsimd
        def _(pool):
            pool.wait_ge(s["in"], 80)
            pool.wait_ge(s["cleared"], 16)
            pool.wait_ge(s["dest"], 1)
            for k in range(TOPK):
                for t in range(NTT):
                    r = rows(t)
                    pool.indirect_dma_start(dr["s_row"], bass.IndirectOffsetOnAxis(rt.dest[0:r, k, t:t + 1], 0),
                                            tok[0:r, t:t + 1], None).then_inc(s["scattered"], 16)
            pool.wait_ge(s["scattered"], 16 * TOPK * NTT)

        @block.tensor
        def _(pe):
            pe.wait_ge(s["in"], 80)
            for t in range(NTT):
                r = rows(t)
                for k in range(KT):
                    mm = pe.matmul(ps[0:r, 0, t * NE:(t + 1) * NE], x1T[:, k, t * BLK:t * BLK + r], w[:, k, :], start=(k == 0), stop=(k == KT - 1))
            mm.then_inc(s["mm"], 1)
            pe.wait_ge(s["sel"], 1)
            for t in range(NTT):
                r = rows(t)
                out = ps[0:r, 1, t * NE:(t + 1) * NE]
                pe.matmul(out, tri[0:r, 0:r], sel[0:r, t, :], start=True, stop=(t == 0))
                for u in range(t):
                    pe.matmul(out, c.ones[:, 0:r], sel[:, u, :], start=False, stop=(u == t - 1))
            for t in range(NTT):
                mm = pe.matmul(ps[:, 2, 0:NE], c.ones[0:rows(t), :], sel[0:rows(t), t, :], start=(t == 0), stop=(t == NTT - 1))
            mm.then_inc(s["counts"], 1)

        @block.scalar
        def _(act):
            act.wait_ge(s["z"], 1)
            act.wait_ge(s["mm"], 1)
            act.activation(fl(sc[:, 0:NBLK, :]), ps[:, 0, 0:NBLK * NE], ACT.Sigmoid)
            act.activation(sc[0:NB, NBLK, :], ps[0:NB, 0, NBLK * NE:NTT * NE], ACT.Sigmoid).then_inc(s["sig"], 1)

        @block.vector
        def _(dve):
            link = Link(dve, s["link"])
            dve.memset(zero[:], 0).then_inc(s["zero"], 1)
            dve.memset(sc[:], 0.5).then_inc(s["z"], 1)
            dve.memset(rank[:], 0.0)
            dve.memset(grank[:], 0.0)
            dve.wait_ge(s["sig"], 1)
            dve.wait_ge(s["in"], 80)
            link(dve.tensor_tensor(bi[:].rearrange("p (t g) e -> p t (g e)", g=NG), sc[:], mid(rb[:], NTT), ALU.add))
            gsv = gs[:].rearrange("p t g -> p (t g)")
            pairs = [(i, j) for i in range(4) for j in range(i + 1, 4)]
            for n, (i, j) in enumerate(pairs):
                x, y = bi[:, :, i], bi[:, :, j]
                link(dve.tensor_tensor(a[:], x, y, ALU.add))
                link(dve.tensor_copy(gsv, a[:]) if n == 0 else dve.tensor_tensor(gsv, gsv, a[:], ALU.max))
                dve.tensor_tensor(a[:], y, x, ALU.is_gt)
                link(dve.tensor_tensor(b[:], x, y, ALU.is_ge))
                dve.tensor_tensor(rank[:, :, i], rank[:, :, i], a[:], ALU.add)
                link(dve.tensor_tensor(rank[:, :, j], rank[:, :, j], b[:], ALU.add))
            for i, j in pairs:
                x, y = gs[:, :, i], gs[:, :, j]
                dve.tensor_tensor(a[:, 0:NTT], y, x, ALU.is_gt)
                link(dve.tensor_tensor(b[:, 0:NTT], x, y, ALU.is_ge))
                dve.tensor_tensor(grank[:, :, i], grank[:, :, i], a[:, 0:NTT], ALU.add)
                link(dve.tensor_tensor(grank[:, :, j], grank[:, :, j], b[:, 0:NTT], ALU.add))
            rk, grk = fl(rank[:]), fl(grank[:])
            dve.tensor_scalar(rk, rk, 2.0, None, ALU.is_lt)
            link(dve.tensor_scalar(grk, grk, 1.0, None, ALU.is_lt))
            dve.tensor_tensor(rank[:], rank[:], last(grk, 4), ALU.mult).then_inc(s["sel"], 1)
            dve.wait_ge(s["sel"], 1)
            link(dve.tensor_tensor(fl(gw[:]), rk, fl(sc[:]), ALU.mult))
            link(dve.tensor_reduce(su[:], gw[:], AX.X, ALU.add))
            link(dve.reciprocal(su[:], su[:]))
            link(dve.tensor_tensor(gw[:], gw[:], last(su[:], NE), ALU.mult))
            dve.wait_ge(s["counts"], 1)
            link(dve.tensor_copy(cnt[:], ps[:, 2, 0:NE]))
            link(dve.tensor_scalar(nb[:], cnt[:], 0.0, None, ALU.is_gt))
            for k in range(1, NTT):
                link(dve.tensor_scalar(t16[:], cnt[:], float(k * P), None, ALU.is_gt))
                link(dve.tensor_tensor(nb[:], nb[:], t16[:], ALU.add))
            link(dve.tensor_tensor_scan(cum[:], c.ones[:, 0:NE], nb[:], 0.0, ALU.mult, ALU.add))
            link(dve.tensor_tensor(past[:], last(blk[:], NE), mid(cum[:], EB), ALU.is_ge))
            link(dve.tensor_reduce(be[:, 0:EB], past[:], AX.X, ALU.add))
            dve.tensor_scalar(be[:, 0:EB], be[:, 0:EB], NE - 1.0, None, ALU.min)
            link(dve.tensor_copy(be[:, EB:EB + 1], cum[:, NE - 1:NE]))
            dve.tensor_copy(rt.plan[:], be[0:1, :])
            link(dve.tensor_tensor(nb[:], cum[:], nb[:], ALU.subtract))
            link(dve.tensor_scalar(nb[:], nb[:], float(P), None, ALU.mult))
            dve.memset(at[:, NBLK, :], 0.0)
            link(dve.tensor_tensor(at[:, 0:NBLK, :], ps[:, 1, 0:NBLK * NE].rearrange("p (t e) -> p t e", e=NE), mid(nb[:], NBLK), ALU.add))
            link(dve.tensor_tensor(at[0:NB, NBLK, :], ps[0:NB, 1, NBLK * NE:NTT * NE], nb[0:NB], ALU.add))
            link(dve.tensor_scalar(fl(far[:]), rk, -FAR, FAR, ALU.mult, ALU.add))
            link(dve.tensor_tensor(at[:], at[:], far[:], ALU.add))
            link(dve.tensor_reduce(df[:, 0, :], at[:], AX.X, ALU.min))
            link(dve.tensor_tensor(eq[:], at[:], last(df[:, 0, :], NE), ALU.is_equal))
            link(dve.tensor_tensor(eq[:], eq[:], gw[:], ALU.mult))
            link(dve.tensor_reduce(rt.wt[:, 0, :], eq[:], AX.X, ALU.add))
            link(dve.tensor_scalar(fl(far[:]), fl(far[:]), -2.0, None, ALU.mult))
            link(dve.tensor_tensor(at[:], at[:], far[:], ALU.add))
            link(dve.tensor_reduce(df[:, 1, :], at[:], AX.X, ALU.max))
            link(dve.tensor_tensor(eq[:], at[:], last(df[:, 1, :], NE), ALU.is_equal))
            link(dve.tensor_tensor(eq[:], eq[:], gw[:], ALU.mult))
            link(dve.tensor_reduce(rt.wt[:, 1, :], eq[:], AX.X, ALU.add))
            dve.tensor_copy(rt.dest[:], df[:]).then_inc(s["dest"], 1)


def ple(c, x1T, y):
    nc, ps, dr = c.nc, c.ps, c.dram
    s = Semaphores(c, "pl")
    with ExitStack() as ctx:
        sb = lambda n, sh: ctx.enter_context(nc.sbuf_tensor(f"pl_{n}", sh, F32))
        wg = sb("wg", [P, KT, D])
        wp = sb("wp", [P, 2, D])
        pT = sb("pT", [P, 2, T])
        sg = sb("sg", [P, 2, D])
        block = ctx.enter_context(nc.Block())

        @block.sync
        def _(sp):
            sp.dma_start(pT[:], dr["pT"]).then_inc(s["in"], 16)
            sp.dma_start(wp[:], dr["w_ple"]).then_inc(s["in"], 16)
            sp.dma_start(wg[:], dr["w_ple_gate"]).then_inc(s["in"], 16)

        @block.tensor
        def _(pe):
            pe.wait_ge(s["in"], 48)
            for t in range(NTT):
                r = rows(t)
                tk = slice(t * BLK, t * BLK + r)
                q = 4 * (t % 2)
                if t >= 2:
                    pe.wait_ge(s["read"], t - 1)
                for n in range(2):
                    for k in range(KT):
                        pe.matmul(ps[0:r, q + n, :], x1T[:, k, tk], wg[:, k, n * 512:(n + 1) * 512], start=(k == 0), stop=(k == KT - 1))
                    for k in range(2):
                        mm = pe.matmul(ps[0:r, q + 2 + n, :], pT[:, k, tk], wp[:, k, n * 512:(n + 1) * 512], start=(k == 0), stop=(k == 1))
                mm.then_inc(s["mm"], 1)

        @block.scalar
        def _(act):
            for t in range(NTT):
                r, q = rows(t), 4 * (t % 2)
                act.wait_ge(s["mm"], t + 1)
                if t >= 2:
                    act.wait_ge(s["used"], t - 1)
                act.activation(sg[0:r, t % 2].rearrange("p (n w) -> p n w", n=2), ps[0:r, q:q + 2, :], ACT.Sigmoid).then_inc(s["sig"], 1)

        @block.vector
        def _(dve):
            for t in range(NTT):
                r, q = rows(t), 4 * (t % 2)
                dve.wait_ge(s["sig"], t + 1)
                g = sg[0:r, t % 2].rearrange("p (n w) -> p n w", n=2)
                dve.tensor_tensor(g, g, ps[0:r, q + 2:q + 4, :], ALU.mult).then_inc(s["read"], 1)
                dve.wait_ge(s["read"], t + 1)
                dve.scalar_tensor_tensor(y[0:r, t, :], y[0:r, t, :], ALPHA, sg[0:r, t % 2], ALU.mult, ALU.add).then_inc(s["used"], 1)


def experts(c, rt):
    nc, ps, dr = c.nc, c.ps, c.dram
    HT = DE // P
    w_here = [c.sem(f"ex_w_here{j}") for j in range(2)]
    row_here = [c.sem(f"ex_row_here{j}") for j in range(2)]
    x_here = [c.sem(f"ex_x_here{j}") for j in range(2)]
    stored = [c.sem(f"ex_stored{j}") for j in range(2)]
    s = Semaphores(c, "ex")
    with ExitStack() as ctx:
        sb = lambda n, sh, dt=F32: ctx.enter_context(nc.sbuf_tensor(f"ex_{n}", sh, dt))
        wg = sb("wg", [P, 2, KT, DE])
        wu = sb("wu", [P, 2, KT, DE])
        wd = sb("wd", [P, 2, HT, D])
        row = sb("row", [P, 2], U32)
        xb = sb("xb", [P, 2, D])
        xT = sb("xT", [P, 2, KT, P])
        a = sb("a", [P, DE])
        aT = sb("aT", [P, HT, P])
        ob = sb("ob", [P, 2, D])
        zero = c.outs[:].rearrange("p m t -> p (m t)")[:, NTT * D:(NTT + 1) * D]
        block = ctx.enter_context(nc.Block())

        def blocks(eng):
            n = eng.value_load(rt.plan[0:1, EB:EB + 1], min_val=1, max_val=EB)
            with eng.Fori(0, EB // 2) as i:
                for j in range(2):
                    with eng.If(2 * i + j < n):
                        yield i, j

        @block.sync
        def _(sp):
            def rows_of(i, j):
                sp.dma_start(row[:, j:j + 1], dr["s_row"][bass.ds(i * P, P)]).then_inc(row_here[j], 16)

            rows_of(0, 0)
            for i, j in blocks(sp):
                n = 2 * i + j
                e = sp.value_load(rt.plan[0:1, bass.ds(n, 1)], min_val=0, max_val=NE - 1)
                sp.wait_ge(s["down"], n + 1)
                sp.dma_start(wg[:, j], dr["w_eg"][bass.ds(e, 1)].rearrange("o p k n -> p (o k) n")).then_inc(w_here[j], 16)
                sp.dma_start(wu[:, j], dr["w_eu"][bass.ds(e, 1)].rearrange("o p k n -> p (o k) n")).then_inc(w_here[j], 16)
                sp.dma_start(wd[:, j], dr["w_ed"][bass.ds(e, 1)].rearrange("o p k n -> p (o k) n")).then_inc(w_here[j], 16)
                sp.wait_ge(s["turned"], n + 1)
                rows_of(n + 1, 1 - j)
            sp.wait_ge(s["zero"], 1)
            n = sp.value_load(rt.plan[0:1, EB:EB + 1], min_val=1, max_val=EB)
            with sp.Fori(0, EB) as i:
                with sp.If(i >= n):
                    sp.dma_start(dr["s_rows"][bass.ds(i * P, P)], zero).then_inc(s["cleared"], 16)
                with sp.If(i < n):
                    sp.sem_inc(s["cleared"], 16)
            sp.wait_ge(s["cleared"], 16 * EB)

        @block.gpsimd
        def _(pool):
            def gather(j):
                pool.indirect_dma_start(xb[:, j, :], None, dr["s_x1"], bass.IndirectOffsetOnAxis(row[:, j:j + 1], 0)).then_inc(x_here[j], 16)

            pool.memset(zero, 0.0).then_inc(s["zero"], 1)
            pool.wait_ge(row_here[0], 16)
            gather(0)
            for i, j in blocks(pool):
                n = 2 * i + j
                pool.wait_ge(row_here[1 - j], 16 * i + 16 * (1 + j))
                pool.wait_ge(s["turned"], n + 1)
                pool.sem_inc(s["gathering"], 1)
                gather(1 - j)

        @block.tensor
        def _(pe):
            pe.sem_inc(s["down"], 2)

            def turn(i, j):
                for k in range(KT):
                    t = pe.transpose(ps[:, k // 4, (k % 4) * P:(k % 4 + 1) * P], xb[:, j, k * P:(k + 1) * P], c.ident[:])
                t.then_inc(s["turned"], 1)

            pe.wait_ge(x_here[0], 16)
            turn(0, 0)
            for i, j in blocks(pe):
                n = 2 * i + j
                pe.wait_ge(s["x_copied"], n + 1)
                pe.wait_ge(w_here[j], 48 * i + 48)
                for o, w in ((2, wg), (3, wu)):
                    for k in range(KT):
                        mm = pe.matmul(ps[:, o, :], xT[:, j, k, :], w[:, j, k, :], start=(k == 0), stop=(k == KT - 1))
                    mm.then_inc(s["gate" if o == 2 else "up"], 1)
                pe.wait_ge(x_here[1 - j], 16 * i + 16 * (1 + j))
                turn(n + 1, 1 - j)
                pe.wait_ge(s["a"], n + 1)
                for k in range(HT):
                    t = pe.transpose(ps[:, 4, k * P:(k + 1) * P], a[:, k * P:(k + 1) * P], c.ident[:])
                t.then_inc(s["a_turned"], 1)
                pe.wait_ge(s["a_copied"], n + 1)
                pe.wait_ge(s["o_copied"], 2 * n + 2)
                for o in range(2):
                    for k in range(HT):
                        mm = pe.matmul(ps[:, 5 + o, :], aT[:, k, :], wd[:, j, k, o * 512:(o + 1) * 512], start=(k == 0), stop=(k == HT - 1))
                mm.then_inc(s["down"], 1)

        @block.scalar
        def _(act):
            def x_copy(j):
                act.activation(xT[:, j].rearrange("p (a k) t -> p a (k t)", a=2), ps[:, 0:2, :], ACT.Copy).then_inc(s["x_copied"], 1)

            act.wait_ge(s["turned"], 1)
            x_copy(0)
            for i, j in blocks(act):
                n = 2 * i + j
                act.wait_ge(s["gate"], n + 1)
                act.activation(a[:], ps[:, 2, :], ACT.Silu).then_inc(s["silu"], 1)
                act.wait_ge(s["turned"], n + 2)
                x_copy(1 - j)
                act.wait_ge(s["down"], n + 3)
                act.wait_ge(stored[j], 16 * i + 16)
                act.activation(ob[:, j, 0:512], ps[:, 5, :], ACT.Copy).then_inc(s["o_copied"], 1)
                act.wait_ge(s["o_copied"], 2 * n + 4)
                act.dma_start(dr["s_rows"][bass.ds(n * P, P)], ob[:, j, :]).then_inc(stored[j], 16)
            n = act.value_load(rt.plan[0:1, EB:EB + 1], min_val=1, max_val=EB)
            act.wait_ge(stored[0], 16 * ((n + 1) // 2) + 16)
            act.wait_ge(stored[1], 16 * (n // 2) + 16)
            act.sem_inc(s["all_stored"], 1)

        @block.vector
        def _(dve):
            dve.sem_inc(s["o_copied"], 2)
            dve.sem_inc(stored[0], 16)
            dve.sem_inc(stored[1], 16)
            for i, j in blocks(dve):
                n = 2 * i + j
                dve.wait_ge(s["up"], n + 1)
                dve.wait_ge(s["silu"], n + 1)
                dve.tensor_tensor(a[:], a[:], ps[:, 3, :], ALU.mult).then_inc(s["a"], 1)
                dve.wait_ge(s["a_turned"], n + 1)
                dve.tensor_copy(aT[:].rearrange("p k t -> p (k t)"), ps[:, 4, :]).then_inc(s["a_copied"], 1)
                dve.wait_ge(s["down"], n + 3)
                dve.wait_ge(stored[j], 16 * i + 16)
                dve.tensor_copy(ob[:, j, 512:1024], ps[:, 6, :]).then_inc(s["o_copied"], 1)


def last_norm(c, y, rt):
    nc, dr = c.nc, c.dram
    s = Semaphores(c, "ln")
    with ExitStack() as ctx:
        sb = lambda n, sh: ctx.enter_context(nc.sbuf_tensor(f"ln_{n}", sh, F32))
        gb = sb("gb", [P, 2, D])
        st = sb("st", [P, 16])
        er = sb("er", [P, TOPK, 3, D])
        block = ctx.enter_context(nc.Block())

        @block.gpsimd
        def _(pool):
            for t in range(NTT):
                r = rows(t)
                if t >= 3:
                    pool.wait_ge(s["added"], t - 2)
                for k in range(TOPK):
                    pool.indirect_dma_start(er[0:r, k, t % 3, :], None, dr["s_rows"], bass.IndirectOffsetOnAxis(rt.dest[0:r, k, t:t + 1], 0))\
                        .then_inc(s[f"rows{t % 3}"], 16)

        @block.sync
        def _(sp):
            for k in range(2):
                sp.dma_start(gb[:, k, :], dr["ln2"][k:k + 1, :].to_broadcast([P, D])).then_inc(s["in"], 16)
            for t in range(NTT):
                sp.wait_ge(s["y"], t + 1)
                sp.dma_start(dr["o_y"][t * BLK:t * BLK + rows(t)], y[0:rows(t), t, :]).then_inc(s["out"], 16)
            sp.wait_ge(s["out"], 16 * NTT)

        @block.vector
        def _(dve):
            link = Link(dve, s["link"])
            dve.wait_ge(s["in"], 32)
            for t in range(NTT):
                r = rows(t)
                yy = y[0:r, t, :]
                dve.wait_ge(s[f"rows{t % 3}"], 32 * (t // 3 + 1))
                link(dve.scalar_tensor_tensor(yy, er[0:r, 0, t % 3, :], rt.wt[0:r, 0, t:t + 1], yy, ALU.mult, ALU.add))
                dve.scalar_tensor_tensor(yy, er[0:r, 1, t % 3, :], rt.wt[0:r, 1, t:t + 1], yy, ALU.mult, ALU.add).then_inc(s["added"], 1)
                dve.wait_ge(s["added"], t + 1)
                norm_rows(dve, (s["asked"], s["given"]), link, yy, r, st, gb, t).then_inc(s["y"], 1)

        @block.scalar
        def _(act):
            for t in range(NTT):
                inverse_root(act, c.eps, st, rows(t), s["asked"], s["given"], s["own"], t)


def attention(c):
    nc = c.nc
    with ExitStack() as ctx:
        sb = lambda n, sh: ctx.enter_context(nc.sbuf_tensor(f"at_{n}", sh, F32))
        z = sb("z", [P, 10, T])
        q, kv = z[:, 0:GR, :], z[:, GR:10, :]
        c.gtok = sb("gtok", [P, NBLK, 24])
        kc = sb("kc", [P, NB + 1, NCMP])
        vc = sb("vc", [NCMP, NB + 1, P])
        project(c, "nsa", c.dram["w_nsa"], 10, z)
        nsa_prepare(c, q, kv, c.small)
        with nc.sbuf_tensor("at_Ss", [64, SO_END], F32) as Ss:
            vs = c.xT[:].rearrange("p k t -> p (k t)")[:, 0:NB * PAGES * P].rearrange("p (n v) -> p n v", v=P)
            v_here = c.sem("nsa_v_here")
            nsa_samples_scores(c, q, kv, Ss, kc, vc, vs, v_here)
            nsa_samples_finish(c, kv, Ss, vc, vs, v_here)
        nsa_prompt(c, q, kv, kc, vc)


def layer(nc, dram):
    c = Core(nc, dram)
    c.ident = nc.alloc_sbuf_tensor("ident", [P, P], F32)
    c.ones = nc.alloc_sbuf_tensor("ones", [P, P], F32)
    c.eps = nc.alloc_sbuf_tensor("eps", [P, 1], F32)
    c.xT = nc.alloc_sbuf_tensor("xT", [P, KT, T], F32)
    outs = nc.alloc_sbuf_tensor("outs", [P, 3 * H4, T], F32)
    c.outs = outs
    c.oT = [outs[:, b * H4:(b + 1) * H4, :] for b in range(3)]
    x1T = c.xT
    y = outs[:].rearrange("p m t -> p (m t)")[:, 0:NTT * D].rearrange("p (t d) -> p t d", d=D)
    with nc.sbuf_tensor("small", [96, T], F32) as small:
        c.small = small
        with nc.sbuf_tensor("w_small", [P, KT, 96], F32) as w_small:
            load_shared(c, w_small[:])
            small_projection(c, "small", w_small, small)
        attention(c)
        c.retire()
        deltanet(c, small)
        c.retire()
    hgrn2(c)
    c.retire()
    with nc.sbuf_tensor("mT", [P, KT, T], F32) as mT:
        merge(c, mT)
        mix_out(c, mT, y, x1T)
    rt = Routing(nc)
    route(c, x1T, rt)
    ple(c, x1T, y)
    experts(c, rt)
    last_norm(c, y, rt)



def bucket(dist):
    n = np.maximum(dist, 0)
    exact = NBUCK // 2
    rel = np.log(np.maximum(n, 1).astype(np.float32) / np.float32(exact)) / np.float32(np.log(128 / exact))
    large = np.minimum(exact + (rel * np.float32(NBUCK - exact)).astype(np.int32), NBUCK - 1)
    return np.where(n < exact, n, large)


def constants():
    f = np.float32
    hot = np.zeros((33, LSEL + LWIN), f)
    for off, d, live in ((0, 1151 - np.arange(LSEL), lambda d: d >= 0), (LSEL, 639 - np.arange(LWIN), lambda d: (d >= 0) & (d < WIN))):
        ok = live(d)
        hot[bucket(d)[ok], off + np.where(ok)[0]] = 1
        hot[32, off + np.where(~ok)[0]] = NEG
    i = np.arange(P)
    up = np.zeros((P, LEV, P), f)
    for l in range(LEV):
        h = 1 << l
        same = (i[:, None] // (2 * h)) == (i[None, :] // (2 * h))
        up[:, l, :] = same & (i[:, None] % (2 * h) < h) & (i[None, :] % (2 * h) >= h)
    lo = np.stack([i[None, :] <= i[:, None], i[None, :] < i[:, None], up[:, 0, :].T > 0], 1).astype(f)
    r = np.arange(64)
    own = np.where(r[:, None] // NH == np.arange(NB)[None, :], 0, NEG).astype(f)
    grp = (r[:, None] // GR == r[None, :] // GR).astype(f)
    c0, b0 = np.arange(NCMP) * STR, np.arange(NSB) * SELB
    imap = ((c0[:, None] <= b0[None, :] + SELB - 1) & (c0[:, None] + 2 * STR - 1 >= b0[None, :])).astype(f)
    idx = np.broadcast_to(np.arange(NSB, dtype=f), (64, NSB)).copy()
    return {"ident": np.eye(P, dtype=f), "hot": hot, "up": up, "lo": lo, "own": own, "grp": grp, "imap": imap, "idx": idx,
            "tri": (i[:, None] < i[None, :]).astype(f), "blk": np.broadcast_to(np.arange(EB, dtype=f), (P, EB)).copy(),
            "tok": (np.arange(NTT)[None, :] * P + i[:, None]).astype(np.uint32)}


def tiles(w):
    k = w.shape[0] // P
    return np.ascontiguousarray(w.reshape(k, P, -1, P).transpose(2, 1, 0, 3))


def rows_by_partition(w):
    return np.ascontiguousarray(w.reshape(w.shape[0] // P, P, -1).transpose(1, 0, 2))


def lay_in(a):
    w = a["w_in"][0]
    at = np.cumsum([0, 512, 768, 24, 1536, 4, 4, 512, 512, 512, 512, 512, 3072])
    (nq, nkv, ng, dqkv, da, db, dg, hq, hf, hi, hg, mg) = (w[:, at[i]:at[i + 1]] for i in range(12))
    nq = nq.reshape(D, G, GR, DH).transpose(0, 2, 1, 3).reshape(D, 512)
    small = np.zeros((D, 96), w.dtype)
    small[:, 0:24], small[:, 32:36], small[:, 64:68] = ng, da, db
    x = np.concatenate([a["x_prompt"][0], a["x_sample"][:, 0]], 0)
    pl = np.concatenate([a["p_prompt"][0, 0], a["p_sample"][0, :, 0]], 0)
    wb = a["w_branch"][0].copy()
    wb[0] = wb[0].reshape(G, GR, DH, D).transpose(1, 0, 2, 3).reshape(512, D)
    state = lambda s: np.ascontiguousarray(s[0].transpose(2, 1, 0, 3).reshape(P, H4 * NB, P))
    out = {
        "xT": rows_by_partition(np.ascontiguousarray(x.T)), "x": x,
        "pT": rows_by_partition(np.ascontiguousarray(pl.T)),
        "w_nsa": tiles(np.concatenate([nq, nkv], 1)), "w_small": rows_by_partition(small),
        "w_dn": tiles(np.concatenate([dqkv, dg], 1)), "w_hg": tiles(np.concatenate([hq, hf, hi, hg], 1)),
        "w_mg": np.ascontiguousarray(tiles(mg).reshape(3, KT, P, KT, P).transpose(1, 0, 2, 3, 4).reshape(24, P, KT, P)),
        "w_br": np.ascontiguousarray(np.stack([tiles(wb[b]) for b in range(3)], 1).reshape(24, P, H4, P)),
        "w_out": rows_by_partition(a["w_out"][0]),
        "rb_aug": np.concatenate([a["rel_bias"], np.ones((1, NH), np.float32)], 0),
        "cache": np.ascontiguousarray(a["cache_nsa"][0].reshape(NPOOL, P, 512)),
        "table": np.ascontiguousarray(a["page_table"].reshape(1, NB * PAGES).astype(np.int32)),
        "state_win": np.ascontiguousarray(a["state_win"][0].reshape(NB, WIN, 2 * P)),
        "w_cmp1": np.ascontiguousarray(a["w_cmp1"][0].reshape(2, 32, DH, P).transpose(2, 0, 1, 3)),
        "w_cmp2": np.ascontiguousarray(a["w_cmp2"][0].transpose(1, 0, 2)),
        "pe_cmp": np.ascontiguousarray(a["pe_cmp"][0].transpose(2, 0, 1)),
        "conv_w": np.ascontiguousarray(a["dn_conv_w"][0].reshape(4, 12, P).transpose(2, 1, 0)),
        "conv_state": np.ascontiguousarray(a["state_dn_conv"][0].reshape(NB, 3, 12, P).transpose(3, 2, 0, 1)),
        "dn_par": np.stack([a["dn_a_log"][0], a["dn_dt_bias"][0]], 1),
        "dn_norm": np.ascontiguousarray(a["dn_norm_w"][0].reshape(P, 1)), "hg_norm": np.ascontiguousarray(a["hg_norm_w"][0].reshape(P, 1)),
        "state_dn": state(a["state_dn"]), "state_hg": state(a["state_hg"]),
        "ln1": np.concatenate([a["ln1_g"], a["ln1_b"]], 0), "ln2": np.concatenate([a["ln2_g"], a["ln2_b"]], 0),
        "w_router": rows_by_partition(a["w_router"]), "router_bias": a["router_bias"].reshape(1, NE),
        "w_eg": np.ascontiguousarray(a["w_exp_gate"][0].reshape(NE, KT, P, DE).transpose(0, 2, 1, 3)),
        "w_eu": np.ascontiguousarray(a["w_exp_up"][0].reshape(NE, KT, P, DE).transpose(0, 2, 1, 3)),
        "w_ed": np.ascontiguousarray(a["w_exp_down"][0].reshape(NE, DE // P, P, D).transpose(0, 2, 1, 3)),
        "w_ple": rows_by_partition(a["w_ple"][0]), "w_ple_gate": rows_by_partition(a["w_ple_gate"][0]),
    }
    return {**out, **constants()}


OUTS = {"o_y": (T, D), "o_kvT": (P, 6, T), "o_win": (NB, WIN - 1, 2 * P), "o_conv": (P, 12, 3 + 3 * NB),
        "o_dn_p": (P, H4 * P), "o_dn_s": (P, H4 * NB, P), "o_hg_p": (P, H4, P), "o_hg_s": (P, H4 * NB, P)}
SCRATCH = {"s_gate": ((24, NB), F32), "s_bias": ((NH, P, LSEL + LWIN), F32), "s_x1": ((T, D), F32),
           "s_row": (((EB + 1) * P, 1), U32), "s_rows": ((EB * P, D), F32)}


def lay_out(o):
    kv = np.ascontiguousarray(np.asarray(o["o_kvT"]).transpose(2, 1, 0)).reshape(T, 6, G, DH)
    rows_, win = kv[:, 0:4], kv[:, 4:6]
    st = np.asarray(o["o_conv"])
    cp = st[:, :, 0:3].transpose(2, 1, 0).reshape(3, 1536)
    cs = st[:, :, 3:].reshape(P, 12, NB, 3).transpose(2, 3, 1, 0).reshape(NB, 3, 1536)
    y = np.asarray(o["o_y"])
    ws = np.concatenate([np.asarray(o["o_win"]).reshape(NB, WIN - 1, 2, G, DH), win[TP:, None]], 1)
    state = lambda s: np.ascontiguousarray(np.asarray(s).reshape(P, H4, NB, P).transpose(2, 1, 0, 3))[None]
    pst = lambda s: np.ascontiguousarray(np.asarray(s).reshape(P, H4, P).transpose(1, 0, 2))[None, None]
    return (y[None, 0:TP], y[TP:, None], rows_[None, None, 0:TP], rows_[None, TP:, None],
            win[None, None, TP - WIN:TP], ws[None], cp[None, None], cs[None],
            pst(o["o_dn_p"]), state(o["o_dn_s"]), pst(o["o_hg_p"]), state(o["o_hg_s"]))


def kernel(**inputs):
    import concourse.bacc as bacc
    from concourse.bass_utils import run_bass_kernel_spmd

    nc = bacc.Bacc("TRN2", target_bir_lowering=False, num_devices=1)
    arrays = {f"in_{n}": np.ascontiguousarray(a) for n, a in lay_in({k: np.asarray(v) for k, v in inputs.items()}).items()}
    dram = {n[3:]: nc.dram_tensor(n, a.shape, mybir.dt.from_np(a.dtype), kind="ExternalInput").ap() for n, a in arrays.items()}
    for n, shape in OUTS.items():
        dram[n] = nc.dram_tensor(f"out_{n}", shape, F32, kind="ExternalOutput").ap()
    for n, (shape, dt) in SCRATCH.items():
        dram[n] = nc.dram_tensor(f"scratch_{n}", shape, dt, kind="Internal").ap()
    layer(nc, dram)
    r = run_bass_kernel_spmd(nc, [arrays], core_ids=[0])
    return lay_out({n: r.results[0][f"out_{n}"] for n in OUTS})
```

```python
from contextlib import ExitStack

import concourse.bass as bass
import numpy as np
from concourse import mybir

F32 = mybir.dt.float32
I32 = mybir.dt.int32
U32 = mybir.dt.uint32
FR = mybir.dt.float32r
ALU = mybir.AluOpType
ACT = mybir.ActivationFunctionType
AX = mybir.AxisListType

P = 128
D = 1024
KT = D // P
TP = 1024
NB = 8
T = TP + NB
NW = 3
W = T // NW
BLK = 128
NBLK = TP // BLK
DH = 64
GR = 4
G = 2
NH = G * GR
PAST = 1024
PAGES = PAST // P
NPOOL = 80
WIN = 512
STR = 16
NCMP = TP // STR - 1
SELB = 64
NSB = 17
NBUCK = 32
LSEL = 1280
LWIN = 768
NEG = -1e30
H4 = 4
LEV = 7
NE = 16
TOPK = 2
EB = (TOPK * T + NE * (P - 1)) // P
DE = 512
ALPHA = 2 ** 0.25
EPS = 1e-6
NTT = NBLK + 1


def mid(ap, n):
    return ap.unsqueeze(1).to_broadcast([ap.shape[0], n, ap.shape[1]])


def last(ap, n):
    return ap.unsqueeze(2).to_broadcast([ap.shape[0], ap.shape[1], n])


class Link:

    def __init__(self, eng, sem):
        self.eng, self.sem, self.n = eng, sem, 0

    def __call__(self, ins):
        self.n += 1
        ins.then_inc(self.sem, 1)
        self.eng.wait_ge(self.sem, self.n)


class Semaphores(dict):

    def __init__(self, core, stage):
        self.core, self.stage = core, stage

    def __missing__(self, name):
        self[name] = self.core.sem(f"{self.stage}_{name}")
        return self[name]


class Core:

    def __init__(self, nc, dram):
        self.nc = nc
        self.dram = dram
        self.ps = nc.alloc_psum_tensor("ps", [P, 8, 512], F32)

        self.held = []

    def sem(self, name):
        self.held.append(self.nc.alloc_semaphore(name))
        return self.held[-1]

    def retire(self):
        self.nc.all_engine_barrier()
        self.nc.clear_and_free_semaphores(self.held)
        self.nc.all_engine_barrier()
        self.held = []


class Routing:
    EXPERT, COUNT, ORDINAL, FREE, FIRST, END = 0, EB, EB + 1, 2 * EB + 1, 3 * EB + 1, 4 * EB + 1

    def __init__(self, nc):
        self.dest = nc.alloc_sbuf_tensor("rt_dest", [P, TOPK, NTT], U32)
        self.wt = nc.alloc_sbuf_tensor("rt_wt", [P, TOPK, NTT], F32)
        self.plan = nc.alloc_sbuf_tensor("rt_plan", [1, self.END], I32)


class Tokens:
    PIECES = 4

    def __init__(self, c, name, sb):
        self.c, self.s = c, Semaphores(c, name)
        self.high, self.low = sb("high", [P, KT, T], FR), sb("low", [P, KT, T], FR)

    def pieces(self):
        n = KT // self.PIECES
        return [(q, slice(q * n, (q + 1) * n)) for q in range(self.PIECES)]

    def load(self, sp, stage):
        for q, k in self.pieces():
            sp.dma_start(stage[:, k, :], self.c.dram["xT"][:, k, :]).then_inc(self.s[f"here{q}"], 16)

    def take_high(self, act, stage):
        for q, k in self.pieces():
            act.wait_ge(self.s[f"here{q}"], 16)
            act.activation(self.high[:, k, :], stage[:, k, :], ACT.Copy).then_inc(self.s["high"], 1)

    def take_low(self, dve, stage):
        for q, k in self.pieces():
            dve.wait_ge(self.s["high"], q + 1)
            dve.tensor_tensor(self.low[:, k, :], stage[:, k, :], self.high[:, k, :], ALU.subtract).then_inc(self.s["low"], 1)

    def wait(self, pe):
        pe.wait_ge(self.s["low"], self.PIECES)


def product(pe, out, w, x, k, tokens, first, final):
    pe.matmul(out, w[:, 0, k, :], x.high[:, k, tokens], start=first, stop=False)
    pe.matmul(out, w[:, 1, k, :], x.high[:, k, tokens], start=False, stop=False)
    return pe.matmul(out, w[:, 0, k, :], x.low[:, k, tokens], start=False, stop=final)


def project(c, name, wt, ntiles, dst, x, stage=None, gates=0, conv=None, written=None):
    nc, ps = c.nc, c.ps
    w_here = [c.sem(f"{name}_w_here{j}") for j in range(2)]
    z_ready = c.sem(f"{name}_z_ready")
    z_copied = c.sem(f"{name}_z_copied")
    w_going = c.sem(f"{name}_w_going")
    w_high, w_split = c.sem(f"{name}_w_high"), c.sem(f"{name}_w_split")
    assert ntiles % 2 == 0
    with nc.sbuf_tensor(f"{name}_w", [P, 2, KT, P], F32) as wb, nc.sbuf_tensor(f"{name}_w2", [P, 2, 2, KT, P], FR) as w2, \
            nc.Block() as block:
        @block.sync
        def _(sp):
            with sp.Fori(0, ntiles // 2) as i:
                for j in range(2):
                    sp.wait_ge(w_split, 2 * i + j + 1)
                    sp.dma_start(wb[:, j], wt[2 * i + j]).then_inc(w_here[j], 16)
            if written:
                sp.wait_ge(*written)

        @block.gpsimd
        def _(pool):
            if conv:
                conv.load(pool)
            pool.sem_inc(w_split, 2)
            with pool.Fori(0, ntiles // 2) as i:
                for j in range(2):
                    pool.wait_ge(w_here[j], 16 * i + 16)
                    pool.wait_ge(z_ready, 2 * i + j + 1)
                    pool.sem_inc(w_going, 1)
                    pool.tensor_copy(w2[:, j, 0], wb[:, j]).then_inc(w_high, 1)
                    pool.wait_ge(w_high, 2 * i + j + 1)
                    pool.tensor_tensor(w2[:, j, 1], wb[:, j], w2[:, j, 0], ALU.subtract).then_inc(w_split, 1)
            if conv:
                conv.store(pool)

        @block.tensor
        def _(pe):
            pe.sem_inc(z_ready, 2)
            if stage is not None:
                x.wait(pe)
            with pe.Fori(0, ntiles // 2) as i:
                for j in range(2):
                    pe.wait_ge(w_split, 2 * i + j + 3)
                    pe.wait_ge(z_copied, 2 * i + j + 1)
                    for n in range(NW):
                        out, tk = ps[:, 3 * j + n, 0:W], slice(n * W, (n + 1) * W)
                        for k in range(KT):
                            mm = product(pe, out, w2[:, j], x, k, tk, k == 0, k == KT - 1)
                    mm.then_inc(z_ready, 1)

        @block.scalar
        def _(act):
            act.sem_inc(z_copied, 2)
            if stage is not None:
                x.load(act, stage)
                x.take_high(act, stage)

            with act.Fori(0, (ntiles - gates) // 2) as i:
                for j in range(2):
                    act.wait_ge(z_ready, 2 * i + j + 3)
                    act.activation(dst[:, 2 * i + j, :].rearrange("p (n w) -> p n w", n=NW),
                                   ps[:, 3 * j:3 * j + NW, 0:W], ACT.Copy).then_inc(z_copied, 1)
                    if conv:
                        conv.silu(act, i, j)
            for m in range(ntiles - gates, ntiles):
                act.wait_ge(z_ready, m + 3)
                act.activation(dst[:, m, :].rearrange("p (n w) -> p n w", n=NW),
                               ps[:, 3 * (m % 2):3 * (m % 2) + NW, 0:W], ACT.Silu).then_inc(z_copied, 1)

        @block.vector
        def _(dve):
            if stage is not None:
                x.take_low(dve, stage)
            if conv:
                conv.vector(dve, z_copied)


def load_shared(c, x, stage, ws, ws2, rb, hot, bv, written):
    nc, dr = c.nc, c.dram
    s = Semaphores(c, "sh")
    with nc.Block() as block:
        @block.sync
        def _(sp):
            x.load(sp, stage)
            sp.dma_start(ws[:], dr["w_small"]).then_inc(s["w"], 16)
            sp.dma_start(rb[:], dr["rb_aug"]).then_inc(s["in"], 16)
            sp.dma_start(hot[:], dr["hot"]).then_inc(s["in"], 16)
            sp.dma_start(c.ident[:], dr["ident"]).then_inc(s["ident"], 16)
            sp.wait_ge(s["ident"], 16)
            sp.wait_ge(s["biasc"], 1)
            sp.dma_start(dr["s_bias"], bv[:].unsqueeze(1).to_broadcast([NH, P, LSEL + LWIN])).then_inc(written, 16)

        @block.tensor
        def _(pe):
            pe.wait_ge(s["in"], 32)
            for n in range(4):
                mm = pe.matmul(c.ps[0:NH, n, :], rb[:], hot[:, 512 * n:512 * n + 512], start=True, stop=True)
            mm.then_inc(s["bias"], 1)

        @block.scalar
        def _(act):
            x.take_high(act, stage)

        @block.vector
        def _(dve):
            dve.memset(c.ones[:], 1.0)
            dve.memset(c.eps[:], EPS)
            x.take_low(dve, stage)
            dve.wait_ge(s["w"], 16)
            dve.tensor_copy(ws2[:, 0], ws[:]).then_inc(s["wh"], 1)
            dve.wait_ge(s["wh"], 1)
            dve.tensor_tensor(ws2[:, 1], ws[:], ws2[:, 0], ALU.subtract)
            dve.wait_ge(s["bias"], 1)
            dve.tensor_copy(bv[:].rearrange("p (n w) -> p n w", n=4), c.ps[0:NH, 0:4, :]).then_inc(s["biasc"], 1)


def small_projection(c, name, x, ws2, dst):
    nc, ps = c.nc, c.ps
    z_ready = c.sem(f"{name}_z_ready")
    with nc.Block() as block:
        @block.tensor
        def _(pe):
            for n in range(NW):
                for k in range(KT):
                    mm = product(pe, ps[0:96, n, 0:W], ws2, x, k, slice(n * W, (n + 1) * W), k == 0, k == KT - 1)
            mm.then_inc(z_ready, 1)

        @block.scalar
        def _(act):
            act.wait_ge(z_ready, 1)
            act.activation(dst[:].rearrange("p (n w) -> p n w", n=NW), ps[0:96, 0:NW, 0:W], ACT.Copy)


def nsa_prepare(c, q, kv, small, written):
    nc, ps, dr = c.nc, c.ps, c.dram
    s = Semaphores(c, "prep")
    with nc.Block() as block:
        @block.sync
        def _(sp):
            sp.dma_start(dr["o_kvT"], kv).then_inc(written, 16)
            sp.wait_ge(s["gate"], 1)
            sp.dma_start(dr["s_gate"], small[0:24, TP:T]).then_inc(written, 16)

        @block.tensor
        def _(pe):
            pe.wait_ge(s["gate"], 1)
            for i in range(NBLK):
                t = pe.transpose(ps[:, 4, 32 * i:32 * i + 24], small[0:24, i * BLK:(i + 1) * BLK], c.ident[0:24, 0:24])
            t.then_inc(s["gt"], 1)

        @block.scalar
        def _(act):
            act.activation(small[0:24, :], small[0:24, :], ACT.Sigmoid).then_inc(s["gate"], 1)

        @block.vector
        def _(dve):
            dve.tensor_scalar(q, q, DH ** -0.5, None, ALU.mult)
            dve.wait_ge(s["gt"], 1)
            dve.tensor_copy(c.gtok[:], ps[:, 4, 0:256].rearrange("p (i h) -> p i h", h=32)[:, :, 0:24])


def nsa_samples_scores(c, q, kv, Ss, kc, vc, vs, v_here, rows_written):
    nc, ps, dr = c.nc, c.ps, c.dram
    s = Semaphores(c, "ns")
    HB = NB // 2
    NPG = 4
    PB = 3
    with ExitStack() as ctx:
        sb = lambda n, sh, dt=F32: ctx.enter_context(nc.sbuf_tensor(f"ns_{n}", sh, dt))
        tab = sb("tab", [1, NB * PAGES], I32)
        w1 = sb("w1", [P, 2, 32, P])
        w2 = sb("w2", [P, 2, DH])
        pe_ = sb("pe", [DH, 2, 32])
        peb = sb("peb", [P, 2])
        cmpT = sb("cmpT", [P, 2, HB, PAST])
        pg = sb("pg", [P, NPG, 3 * P])
        kT = sb("kT", [P, 2, PAST])
        hid = sb("hid", [P, 2, HB * NCMP])
        qz = sb("qz", [P, NB * (SELB + NB)])
        block = ctx.enter_context(nc.Block())
        cache = dr["cache"]
        tiles = [(b, p) for b in range(NB) for p in range(PAGES)]

        def page(eng, n):
            if n >= NPG:
                eng.wait_ge(s["turned"], n - NPG + 1)
            v = eng.value_load(tab[0:1, n:n + 1], min_val=0, max_val=NPOOL - 1)
            eng.dma_start(pg[:, n % NPG, :], cache[bass.ds(v, 1), :, 0:3 * P].rearrange("o t f -> t (o f)")).then_inc(s[f"pg{n % NPG}"], 16)

        @block.sync
        def _(sp):
            sp.dma_start(tab[:], dr["table"]).then_inc(s["tab"], 16)
            for h in range(2):
                sp.dma_start(w1[h * DH:(h + 1) * DH], dr["w_cmp1"]).then_inc(s["w"], 16)
            sp.dma_start(w2[:], dr["w_cmp2"]).then_inc(s["w"], 16)
            sp.dma_start(pe_[:], dr["pe_cmp"]).then_inc(s["w"], 16)
            sp.wait_ge(s["tab"], 16)
            for n in range(0, NB * PAGES, 2):
                page(sp, n)
            sp.wait_ge(rows_written, 32)

        @block.tensor
        def _(pe):
            def compress(st, src, nseq):
                for t in range(32):
                    lo = t // STR
                    for g in range(G):
                        r = slice(g * DH, (g + 1) * DH)
                        mv = src[r].rearrange("p b (k s) -> p b k s", s=STR)[:, :, lo:lo + NCMP, t % STR]
                        mm = pe.matmul(ps[:, 4 + g, 0:nseq * NCMP], w1[r, st, t, :], mv, start=(t == 0), stop=(t == 31))
                        if t == 31:
                            mm.then_inc(s["lo"], 1)

            def second(n, st, g, q0, nseq):
                pe.wait_ge(s["hid"], n + 1)
                if n >= 1:
                    pe.wait_ge(s["h2c"], n)
                if st == 0:
                    mm = pe.matmul(ps[g * DH:(g + 1) * DH, 6, 0:nseq * NCMP], w2[:, 0, :], hid[:, n % 2, 0:nseq * NCMP], start=True, stop=True)
                else:
                    for b in range(nseq):
                        mm = pe.matmul(ps[0:NCMP, 6, b * DH:(b + 1) * DH], hid[:, n % 2, b * NCMP:(b + 1) * NCMP], w2[:, 1, :], start=True, stop=True)
                mm.then_inc(s["h2"], 1)

            def prompt():
                pe.wait_ge(s["w"], 64)
                for st in range(2):
                    for t in range(32):
                        mm = pe.matmul(ps[:, 7, st:st + 1], w1[0:DH, st, t, :], pe_[:, st, t:t + 1], start=(t == 0), stop=(t == 31))
                mm.then_inc(s["peb"], 1)
                pe.wait_ge(s["pebc"], 1)
                for st in range(2):
                    if st:
                        pe.wait_ge(s["hid"], 2 * st)
                    compress(st, kv[:, st:st + 1, 0:TP], 1)
                    for g in range(G):
                        second(2 * st + g, st, g, NB, 1)

            n = 4
            tn = 0
            for b in range(NB):
                if b >= 1:
                    pe.wait_ge(s["scored"], b)
                for p in range(PAGES):
                    pe.wait_ge(s[f"pg{tn % NPG}"], 16 * (tn // NPG + 1))
                    if tn >= 2:
                        pe.wait_ge(s["turncopied"], tn - 1)
                    if p == 0 and b % HB == 0 and b > 0:
                        pe.wait_ge(s["h2"], 8)
                    for st in range(3):
                        t = pe.transpose(ps[:, 4 + tn % 2, st * P:(st + 1) * P], pg[:, tn % NPG, st * P:(st + 1) * P], c.ident[:])
                    t.then_inc(s["turned"], 1)
                    tn += 1
                pe.wait_ge(s["qz"], 1)
                pe.wait_ge(s["turncopied"], tn)
                for h in range(2):
                    mm = pe.matmul(ps[0:64, h, :], qz[:, b * 64:(b + 1) * 64], kT[:, b % 2, h * 512:(h + 1) * 512], start=(b == 0), stop=(b == NB - 1))
                mm.then_inc(s["scored"], 1)
                if b == PB - 1:
                    prompt()
                if b % HB == HB - 1:
                    for st in range(2):
                        pe.wait_ge(s["hid"], n)
                        compress(st, cmpT[:, st], HB)
                        for g in range(G):
                            second(n, st, g, b - HB + 1, HB)
                            n += 1

        @block.gpsimd
        def _(pool):
            pool.wait_ge(s["tab"], 16)
            for n in range(NB * PAGES):
                v = pool.value_load(tab[0:1, n:n + 1], min_val=0, max_val=NPOOL - 1)
                pool.dma_start(vs[:, n, :], dr["cache"][bass.ds(v, 1), :, 3 * P:4 * P].rearrange("o t f -> t (o f)")).then_inc(v_here, 16)

        @block.scalar
        def _(act):
            def hidden(n, nseq):
                act.wait_ge(s["lo"], n + 1)
                if n >= 2:
                    act.wait_ge(s["h2"], n - 1)
                st = (n // 2) % 2
                act.activation(hid[:, n % 2, 0:nseq * NCMP], ps[:, 4 + n % 2, 0:nseq * NCMP], ACT.Silu, bias=peb[:, st:st + 1]).then_inc(s["hid"], 1)

            act.wait_ge(s["tab"], 16)
            for n in range(1, NPG, 2):
                page(act, n)
            for b in range(NB):
                for n in range(b * PAGES + 1, (b + 1) * PAGES, 2):
                    if n > NPG:
                        page(act, n)
                if b == PB - 1:
                    act.wait_ge(s["pebc"], 1)
                    for n in range(4):
                        hidden(n, 1)
                if b % HB == HB - 1:
                    for k in range(4):
                        hidden(4 + (b // HB) * 4 + k, HB)

        @block.vector
        def _(dve):
            link = Link(dve, s["link"])
            link(dve.memset(qz[:], 0.0))
            for g in range(G):
                r = slice(g * DH, (g + 1) * DH)
                z = dve.tensor_copy(qz[r].rearrange("p (b x) -> p b x", x=SELB + NB)[:, :, g * GR:(g + 1) * GR],
                                    q[r, :, TP:T].rearrange("p j b -> p b j"))
            z.then_inc(s["qz"], 1)

            def second(n, st, g, q0, nseq):
                dve.wait_ge(s["h2"], n + 1)
                r = slice(g * DH, (g + 1) * DH)
                if st == 0:
                    o = dve.tensor_copy(kc[r, q0:q0 + nseq, :], ps[r, 6, 0:nseq * NCMP].rearrange("p (b k) -> p b k", b=nseq))
                else:
                    o = dve.tensor_copy(vc[:, q0:q0 + nseq, r], ps[0:NCMP, 6, 0:nseq * DH].rearrange("p (b k) -> p b k", b=nseq))
                o.then_inc(s["h2c"], 1)

            n = 4
            tn = 0
            for b in range(NB):
                for p in range(PAGES):
                    dve.wait_ge(s["turned"], tn + 1)
                    if p == 0 and b >= 2:
                        dve.wait_ge(s["scored"], b - 1)
                    dve.tensor_copy(cmpT[:, :, b % HB, p * P:(p + 1) * P], ps[:, 4 + tn % 2, 0:2 * P].rearrange("p (s t) -> p s t", s=2))
                    dve.tensor_copy(kT[:, b % 2, p * P:(p + 1) * P], ps[:, 4 + tn % 2, 2 * P:3 * P]).then_inc(s["turncopied"], 1)
                    tn += 1
                if b == PB - 1:
                    dve.wait_ge(s["peb"], 1)
                    dve.tensor_copy(peb[:], ps[:, 7, 0:2]).then_inc(s["pebc"], 1)
                    for m in range(4):
                        second(m, m // 2, m % 2, NB, 1)
                if b % HB == HB - 1:
                    for st in range(2):
                        for g in range(G):
                            second(n, st, g, b - HB + 1, HB)
                            n += 1
            dve.wait_ge(s["scored"], NB)
            dve.tensor_copy(Ss[:, 0:PAST].rearrange("p (h k) -> p h k", h=2), ps[0:64, 0:2, :])
    
    s2 = Semaphores(c, "nw")
    with ExitStack() as ctx:
        sb = lambda n, sh, dt=F32: ctx.enter_context(nc.sbuf_tensor(f"nw_{n}", sh, dt))
        wk = sb("wk", [P, 2, 4, P])
        wT = sb("wT", [P, 2, WIN])
        qz = sb("qz", [P, NB * (SELB + NB)])
        block = ctx.enter_context(nc.Block())

        @block.sync
        def _(sp):
            for b in range(NB):
                if b >= 2:
                    sp.wait_ge(s2["turned"], b - 1)
                sp.dma_start(wk[:, b % 2], dr["state_win"][b].rearrange("(n p) f -> p n f", p=P)[:, :, 0:P]).then_inc(s2[f"in{b % 2}"], 16)

        @block.tensor
        def _(pe):
            pe.wait_ge(s2["qz"], 1)
            for b in range(NB):
                pe.wait_ge(s2[f"in{b % 2}"], 16 * (b // 2 + 1))
                if b >= 2:
                    pe.wait_ge(s2["copied"], b - 1)
                for n in range(4):
                    t = pe.transpose(ps[:, 4 + b % 2, n * P:(n + 1) * P], wk[:, b % 2, n, :], c.ident[:])
                t.then_inc(s2["turned"], 1)
                pe.wait_ge(s2["copied"], b + 1)
                pe.matmul(ps[0:64, 2, :], qz[:, b * 64:(b + 1) * 64], wT[:, b % 2, :], start=(b == 0), stop=(b == NB - 1)).then_inc(s2["scored"], 1)
            for b in range(NB):
                pe.matmul(ps[0:64, 3, 0:NCMP], qz[:, b * 64:(b + 1) * 64], kc[:, b, :], start=(b == 0), stop=(b == NB - 1))
            for k, st in enumerate((2, 4)):
                for b in range(NB):
                    mm = pe.matmul(ps[0:64, 3, 64 + 8 * k:72 + 8 * k], qz[:, b * 64:(b + 1) * 64], kv[:, st, TP:T], start=(b == 0), stop=(b == NB - 1))
            mm.then_inc(s2["cmp"], 1)

        @block.vector
        def _(dve):
            link = Link(dve, s2["link"])
            link(dve.memset(qz[:], 0.0))
            for g in range(G):
                r = slice(g * DH, (g + 1) * DH)
                z = dve.tensor_copy(qz[r].rearrange("p (b x) -> p b x", x=SELB + NB)[:, :, g * GR:(g + 1) * GR],
                                    q[r, :, TP:T].rearrange("p j b -> p b j"))
            z.then_inc(s2["qz"], 1)
            for b in range(NB):
                dve.wait_ge(s2["turned"], b + 1)
                if b >= 2:
                    dve.wait_ge(s2["scored"], b - 1)
                dve.tensor_copy(wT[:, b % 2, :], ps[:, 4 + b % 2, :]).then_inc(s2["copied"], 1)
            dve.wait_ge(s2["scored"], NB)
            dve.tensor_copy(Ss[:, SO_WIN:SO_WIN + WIN], ps[0:64, 2, :])
            dve.wait_ge(s2["cmp"], 1)
            dve.tensor_copy(Ss[:, SO_NSEL:SO_NSEL + NB], ps[0:64, 3, 64:72])
            dve.tensor_copy(Ss[:, SO_NWIN:SO_NWIN + NB], ps[0:64, 3, 72:80])
            dve.tensor_copy(Ss[:, SO_CMP:SO_CMP + NCMP], ps[0:64, 3, 0:NCMP])


SO_NSEL = PAST
SO_WIN = SO_NSEL + NB
SO_NWIN = SO_WIN + WIN
SO_CMP = SO_NWIN + NB
SO_END = SO_CMP + NCMP + 1


def nsa_samples_finish(c, kv, Ss, vc, vs, v_here):
    nc, ps, dr = c.nc, c.ps, c.dram
    s = Semaphores(c, "nf")
    BR = ((0, SO_WIN), (SO_WIN, SO_CMP), (SO_CMP, SO_CMP + NCMP))
    with ExitStack() as ctx:
        sb = lambda n, sh, dt=F32: ctx.enter_context(nc.sbuf_tensor(f"nf_{n}", sh, dt))
        vw = sb("vw", [P, NB, 4, P])
        vn = sb("vn", [NB, 2, P])
        bs = sb("bs", [64, PAST + 1])
        bw = sb("bw", [64, WIN + 1])
        own = sb("own", [64, NB])
        gs = sb("gs", [64, 3])
        imap = sb("imap", [NCMP, NSB])
        grp = sb("grp", [64, 64])
        idx = sb("idx", [64, NSB])
        sm = sb("sm", [64, 16])
        ec = sb("ec", [64, NCMP])
        ecT = sb("ecT", [NCMP, 64])
        imp = sb("imp", [64, NSB])
        eq = sb("eq", [64, NSB])
        dm = sb("dm", [64, 16])
        pt = sb("pt", [P, 15, 64])
        block = ctx.enter_context(nc.Block())

        @block.sync
        def _(sp):
            for t, src in ((bs, dr["s_bias"][:, 0, P - 1:P + PAST]), (bw, dr["s_bias"][:, 0, LSEL + P - 1:LSEL + P + WIN])):
                sp.dma_start(t[:], src.unsqueeze(0).to_broadcast([NB, *src.shape])).then_inc(s["in"], 16)
            sp.dma_start(gs[:], dr["s_gate"].rearrange("(h r) b -> b h r", r=3), allow_slow_non_contiguous=True).then_inc(s["in"], 16)
            for t, n in ((own, "own"), (imap, "imap"), (grp, "grp"), (idx, "idx")):
                sp.dma_start(t[:], dr[n]).then_inc(s["in"], 16)

        @block.vector
        def _(dve):
            link = Link(dve, s["link"])
            dve.wait_ge(s["in"], 16 * 7)
            dve.tensor_tensor(Ss[:, 0:PAST], Ss[:, 0:PAST], bs[:, 0:PAST], ALU.add)
            dve.tensor_tensor(Ss[:, SO_WIN:SO_NWIN], Ss[:, SO_WIN:SO_NWIN], bw[:, 0:WIN], ALU.add)
            dve.scalar_tensor_tensor(Ss[:, SO_NSEL:SO_WIN], Ss[:, SO_NSEL:SO_WIN], bs[:, PAST:PAST + 1], own[:], ALU.add, ALU.add)
            dve.scalar_tensor_tensor(Ss[:, SO_NWIN:SO_CMP], Ss[:, SO_NWIN:SO_CMP], bw[:, WIN:WIN + 1], own[:], ALU.add, ALU.add)
            cs = slice(*BR[2])
            link(dve.tensor_tensor(Ss[:, cs], Ss[:, cs], bs[:, 31:31 + STR * (NCMP - 1) + 1:STR], ALU.add))
            link(dve.tensor_reduce(sm[:, 0:1], Ss[:, cs], AX.X, ALU.max))
            dve.tensor_scalar(sm[:, 1:2], sm[:, 0:1], -1.0, None, ALU.mult).then_inc(s["zc"], 1)
            dve.wait_ge(s["ec"], 1)
            link(dve.reciprocal(sm[:, 3:4], sm[:, 2:3]))
            dve.tensor_scalar(ec[:], ec[:], sm[:, 3:4], None, ALU.mult).then_inc(s["impt"], 1)
            dve.wait_ge(s["imptc"], 1)
            dve.tensor_copy(ecT[:], ps[0:NCMP, 0, 0:64]).then_inc(s["imp"], 1)
            dve.wait_ge(s["impc"], 1)
            dve.tensor_copy(imp[:], ps[0:64, 1, 0:NSB]).then_inc(s["imp"], 1)
            dve.wait_ge(s["grp"], 1)
            link(dve.tensor_copy(imp[:], ps[0:64, 2, 0:NSB]))
            n = slice(1, NSB - 2)
            link(dve.tensor_reduce(sm[:, 4:5], imp[:, n], AX.X, ALU.min))
            link(dve.tensor_scalar(eq[:, n], imp[:, n], sm[:, 4:5], None, ALU.is_equal))
            link(dve.tensor_tensor(eq[:, n], eq[:, n], idx[:, n], ALU.mult))
            link(dve.tensor_reduce(sm[:, 5:6], eq[:, n], AX.X, ALU.max))
            link(dve.tensor_scalar(dm[:], idx[:, 0:16], sm[:, 5:6], NEG, ALU.is_equal, ALU.mult))
            sel = Ss[:, 0:PAST].rearrange("p (n k) -> p n k", k=SELB)
            link(dve.tensor_tensor(sel, sel, last(dm[:], SELB), ALU.add))
            for k, (a, b) in enumerate(BR):
                link(dve.tensor_reduce(sm[:, 6 + k:7 + k], Ss[:, a:b], AX.X, ALU.max))
            dve.tensor_scalar(sm[:, 6:9], sm[:, 6:9], -1.0, None, ALU.mult).then_inc(s["z3"], 1)
            dve.wait_ge(s["e3"], 1)
            link(dve.reciprocal(sm[:, 12:15], sm[:, 9:12]))
            link(dve.tensor_tensor(sm[:, 12:14], sm[:, 12:14], gs[:, 1:3], ALU.mult))
            link(dve.tensor_tensor(sm[:, 14:15], sm[:, 14:15], gs[:, 0:1], ALU.mult))
            for k, (a, b) in enumerate(BR):
                o = dve.tensor_scalar(Ss[:, a:b], Ss[:, a:b], sm[:, 12 + k:13 + k], None, ALU.mult)
            o.then_inc(s["p3"], 1)
            dve.wait_ge(s["pt"], 1)
            dve.tensor_copy(pt[:, 0:8, :], ps[:, 0, :].rearrange("p (n q) -> p n q", q=64))
            dve.tensor_copy(pt[:, 8:12, :], ps[:, 1, 0:256].rearrange("p (n q) -> p n q", q=64))
            dve.tensor_copy(pt[0:NB, 12:14, :], ps[0:NB, 1, 256:384].rearrange("p (n q) -> p n q", q=64))
            dve.tensor_copy(pt[0:NCMP, 14, :], ps[0:NCMP, 1, 384:448])
            dve.tensor_copy(vn[:], ps[0:NB, 2, 0:2 * P].rearrange("p (n q) -> p n q", q=P)).then_inc(s["ptc"], 1)
            dve.wait_ge(s["pv"], 1)
            for g in range(G):
                r = slice(g * DH, (g + 1) * DH)
                dve.tensor_copy(c.oT[0][r, :, TP:T], ps[r, 3, 0:64].rearrange("p (b g j) -> p g j b", g=G, j=GR)[:, g])

        @block.scalar
        def _(act):
            for b in range(NB):
                act.dma_start(vw[:, b], dr["state_win"][b].rearrange("(n p) f -> p n f", p=P)[:, :, P:2 * P]).then_inc(s["v"], 16)
            act.wait_ge(s["zc"], 1)
            act.activation(ec[:], Ss[:, SO_CMP:SO_CMP + NCMP], ACT.Exp, bias=sm[:, 1:2], accum_out=sm[:, 2:3]).then_inc(s["ec"], 1)
            act.wait_ge(s["z3"], 1)
            for k, (a, b) in enumerate(BR):
                o = act.activation(Ss[:, a:b], Ss[:, a:b], ACT.Exp, bias=sm[:, 6 + k:7 + k], accum_out=sm[:, 9 + k:10 + k])
            o.then_inc(s["e3"], 1)

        @block.tensor
        def _(pe):
            pe.wait_ge(s["impt"], 1)
            pe.transpose(ps[0:NCMP, 0, 0:64], ec[:], c.ident[0:64, 0:64]).then_inc(s["imptc"], 1)
            pe.wait_ge(s["imp"], 1)
            pe.matmul(ps[0:64, 1, 0:NSB], ecT[:], imap[:], start=True, stop=True).then_inc(s["impc"], 1)
            pe.wait_ge(s["imp"], 2)
            pe.matmul(ps[0:64, 2, 0:NSB], grp[:], imp[:], start=True, stop=True).then_inc(s["grp"], 1)
            pe.wait_ge(s["p3"], 1)
            idt = c.ident[0:64, 0:64]
            for n in range(8):
                pe.transpose(ps[:, 0, n * 64:n * 64 + 64], Ss[:, n * P:(n + 1) * P], idt)
            for n in range(4):
                pe.transpose(ps[:, 1, n * 64:n * 64 + 64], Ss[:, SO_WIN + n * P:SO_WIN + (n + 1) * P], idt)
            pe.transpose(ps[0:NB, 1, 256:320], Ss[:, SO_NSEL:SO_NSEL + NB], idt)
            pe.transpose(ps[0:NB, 1, 320:384], Ss[:, SO_NWIN:SO_NWIN + NB], idt)
            pe.transpose(ps[0:NCMP, 1, 384:448], Ss[:, SO_CMP:SO_CMP + NCMP], idt)
            for k in range(2):
                t = pe.transpose(ps[0:NB, 2, k * P:(k + 1) * P], kv[:, 3 + 2 * k, TP:T], c.ident[:])
            t.then_inc(s["pt"], 1)
            pe.wait_ge(s["ptc"], 1)
            pe.wait_ge(v_here, 16 * NB * PAGES)
            pe.wait_ge(s["v"], 16 * NB)
            for b in range(NB):
                q = slice(b * NH, (b + 1) * NH)
                out = ps[:, 3, q]
                for n in range(8):
                    pe.matmul(out, vs[:, b * PAGES + n, :], pt[:, n, q], start=(n == 0), stop=False)
                for n in range(4):
                    pe.matmul(out, vw[:, b, n, :], pt[:, 8 + n, q], start=False, stop=False)
                for n in range(2):
                    pe.matmul(out, vn[:, n, :], pt[0:NB, 12 + n, q], start=False, stop=False)
                mm = pe.matmul(out, vc[:, b, :], pt[0:NCMP, 14, q], start=False, stop=True)
            mm.then_inc(s["pv"], 1)


def nsa_prompt(c, q, kv, kc, vc):
    nc, ps, dr = c.nc, c.ps, c.dram
    s = Semaphores(c, "np")
    NSL = 4
    LAG = 2
    LM = PAST + P
    with ExitStack() as ctx:
        sb = lambda n, sh, dt=F32: ctx.enter_context(nc.sbuf_tensor(f"np_{n}", sh, dt))
        mt = sb("mt", [P, GR, LM])
        mw = sb("mw", [P, GR, 5 * P])
        vt = sb("vt", [P, 2, NBLK, P])
        z = sb("z", [P, LAG + 1, 14 * P])
        sm = sb("sm", [P, LAG + 1, 12])
        ptb = sb("ptb", [P, NSL, 512])
        block = ctx.enter_context(nc.Block())
        steps = [(g, i, j) for g in range(G) for i in range(NBLK) for j in range(GR)]

        def widths(i):
            return (i + 1) * P, min(i + 1, 5) * P, 8 * i + 7

        def blocks(i):
            ws, ww, wc = widths(i)
            out = [(n * P, P, 0, n) for n in range(i + 1)]
            out += [(ws + n * P, P, 1, max(0, i - 4) + n) for n in range(ww // P)]
            return out + [(ws + ww, wc, 2, 0)]

        def groups(i):
            b = blocks(i)
            return [b[k:k + 4] for k in range(0, len(b), 4)]

        @block.sync
        def _(sp):
            for g in range(G):
                if g:
                    sp.wait_ge(s["zdone"], NBLK * GR)
                for j in range(GR):
                    h = g * GR + j
                    v, pitch = dr["s_bias"][h:h + 1, 0:1, :], LSEL + LWIN - 1
                    sp.dma_start(mt[:, j, :], bass.AP(v.tensor, v.offset + P - 1, [[pitch, P], [1, LM]])).then_inc(s[f"in{g}"], 16)
                    sp.dma_start(mw[:, j, :], bass.AP(v.tensor, v.offset + LSEL + P - 1, [[pitch, P], [1, 5 * P]])).then_inc(s[f"in{g}"], 16)
                if not g:
                    sp.dma_start(dr["o_win"], dr["state_win"][:, 1:WIN, :]).then_inc(s["window"], 16)
            sp.wait_ge(s["window"], 16)

        @block.tensor
        def _(pe):
            for k in range(2):
                for i in range(NBLK):
                    t = pe.transpose(ps[:, 2 * k + i // 4, (i % 4) * P:(i % 4 + 1) * P], kv[:, 3 + 2 * k, i * P:(i + 1) * P], c.ident[:])
            t.then_inc(s["vt"], 1)
            pe.wait_ge(s["vtc"], 1)

            def scores(n):
                g, i, j = steps[n]
                r = slice(g * DH, (g + 1) * DH)
                qq = q[r, j, i * P:(i + 1) * P]
                ws, ww, wc = widths(i)
                if n:
                    pe.wait_ge(s["zdone"], n)
                for a in range(0, ws, 512):
                    e = min(ws, a + 512)
                    pe.matmul(ps[:, a // 512, 0:e - a], qq, kv[r, 2, a:e], start=True, stop=True)
                k0 = max(0, i - 4) * P
                a = min(ww, 512)
                pe.matmul(ps[:, 2, 0:a], qq, kv[r, 4, k0:k0 + a], start=True, stop=True)
                if ww > a:
                    pe.matmul(ps[:, 3, 0:ww - a], qq, kv[r, 4, k0 + a:k0 + ww], start=True, stop=True)
                pe.matmul(ps[:, 3, 256:256 + wc], qq, kc[r, NB, 0:wc], start=True, stop=True).then_inc(s["scored"], 1)

            cnt = [0, 0]

            def turn(n, grp):
                k = cnt[0]
                if k >= 2:
                    pe.wait_ge(s["ptc"], k - 1)
                for m, (col, w, _, _) in enumerate(grp):
                    t = pe.transpose(ps[0:w, 4 + k % 2, m * P:(m + 1) * P], z[:, n % (LAG + 1), col:col + w], c.ident[:])
                t.then_inc(s["pt"], 1)
                cnt[0] += 1

            def values(n, grp, first, final):
                g, i, j = steps[n]
                r = slice(g * DH, (g + 1) * DH)
                k = cnt[1]
                pe.wait_ge(s["ptc"], k + 1)
                if first and n >= 2:
                    pe.wait_ge(s["oc"], n - 1)
                for m, (_, w, br, kb) in enumerate(grp):
                    v = vt[:, br, kb, r] if br < 2 else vc[0:w, NB, r]
                    mm = pe.matmul(ps[r, 6 + n % 2, 0:P], v, ptb[0:w, k % NSL, m * P:(m + 1) * P],
                                   start=(first and m == 0), stop=(final and m == len(grp) - 1))
                mm.then_inc(s["pv"], 1)
                cnt[1] += 1

            def finish(n):
                gr = groups(steps[n][1])
                pe.wait_ge(s["p"], n + 1)
                turn(n, gr[0])
                for k in range(len(gr)):
                    if k + 1 < len(gr):
                        turn(n, gr[k + 1])
                    values(n, gr[k], k == 0, k == len(gr) - 1)

            for n in range(len(steps)):
                scores(n)
                if n >= LAG:
                    finish(n - LAG)
            for n in range(len(steps) - LAG, len(steps)):
                finish(n)

        @block.vector
        def _(dve):
            link = Link(dve, s["link"])
            dve.wait_ge(s["vt"], 1)
            dve.tensor_copy(vt[:].rearrange("p k (a b) t -> p (k a) (b t)", a=2), ps[:, 0:4, :]).then_inc(s["vtc"], 1)
            turned = np.cumsum([0] + [len(groups(i)) for _, i, _ in steps]).tolist()

            def bias(n):
                g, i, j = steps[n]
                ws, ww, wc = widths(i)
                if j == 0 and i == 0:
                    dve.wait_ge(s[f"in{g}"], 16 * 2 * GR)
                dve.wait_ge(s["scored"], n + 1)
                if n > LAG:
                    dve.wait_ge(s["pt"], turned[n - LAG])
                zz = z[:, n % (LAG + 1)]
                m0 = PAST - i * P
                mx = sm[:, n % (LAG + 1), 0:4]
                if ws <= 512:
                    dve.tensor_tensor_reduce(zz[:, 0:ws], ps[:, 0, 0:ws], mt[:, j, m0:m0 + ws], 1.0, NEG, ALU.add, ALU.max, mx[:, 0:1])
                else:
                    dve.tensor_tensor_reduce(zz[:, 0:512], ps[:, 0, :], mt[:, j, m0:m0 + 512], 1.0, NEG, ALU.add, ALU.max, mx[:, 3:4])
                    link(dve.tensor_tensor_reduce(zz[:, 512:ws], ps[:, 1, 0:ws - 512], mt[:, j, m0 + 512:m0 + ws], 1.0, NEG, ALU.add, ALU.max, mx[:, 0:1]))
                    dve.tensor_tensor(mx[:, 0:1], mx[:, 0:1], mx[:, 3:4], ALU.max)
                w0 = 5 * P - ww
                a = min(ww, 512)
                dve.tensor_tensor_reduce(zz[:, ws:ws + a], ps[:, 2, 0:a], mw[:, j, w0:w0 + a], 1.0, NEG, ALU.add, ALU.max, mx[:, 1:2])
                if ww > a:
                    link(dve.tensor_tensor_reduce(zz[:, ws + a:ws + ww], ps[:, 3, 0:ww - a], mw[:, j, w0 + a:w0 + ww], 1.0, NEG, ALU.add, ALU.max, sm[:, n % (LAG + 1), 7:8]))
                    dve.tensor_tensor(mx[:, 1:2], mx[:, 1:2], sm[:, n % (LAG + 1), 7:8], ALU.max)
                c0 = m0 + 31
                o = dve.tensor_tensor_reduce(zz[:, ws + ww:ws + ww + wc], ps[:, 3, 256:256 + wc], mt[:, j, c0:c0 + STR * (wc - 1) + 1:STR],
                                             1.0, NEG, ALU.add, ALU.max, mx[:, 2:3])
                link(o)
                dve.tensor_scalar(sm[:, n % (LAG + 1), 4:7], mx[:, 0:3], -1e29, -1.0, ALU.max, ALU.mult).then_inc(s["zdone"], 1)

            def scale(n):
                g, i, j = steps[n]
                ws, ww, wc = widths(i)
                dve.wait_ge(s["exp"], n + 1)
                h = g * GR + j
                su = sm[:, n % (LAG + 1), 8:11]
                link(dve.tensor_scalar(su, su, 0.5, None, ALU.max))
                link(dve.reciprocal(su, su))
                dve.tensor_tensor(su[:, 0:2], su[:, 0:2], c.gtok[:, i, 3 * h + 1:3 * h + 3], ALU.mult)
                link(dve.tensor_tensor(su[:, 2:3], su[:, 2:3], c.gtok[:, i, 3 * h:3 * h + 1], ALU.mult))
                zz = z[:, n % (LAG + 1)]
                for k, (a, e) in enumerate(((0, ws), (ws, ws + ww), (ws + ww, ws + ww + wc))):
                    o = dve.tensor_scalar(zz[:, a:e], zz[:, a:e], su[:, k:k + 1], None, ALU.mult)
                o.then_inc(s["p"], 1)

            def output(n):
                g, i, j = steps[n]
                r = slice(g * DH, (g + 1) * DH)
                dve.wait_ge(s["pv"], turned[n + 1])
                dve.tensor_copy(c.oT[0][r, j, i * P:(i + 1) * P], ps[r, 6 + n % 2, 0:P]).then_inc(s["oc"], 1)

            N = len(steps)
            for n in range(N + LAG + 1):
                if n < N:
                    bias(n)
                if 1 <= n <= N:
                    scale(n - 1)
                if n > LAG:
                    output(n - LAG - 1)

        @block.scalar
        def _(act):
            cnt = [0]

            def exps(n):
                g, i, j = steps[n]
                ws, ww, wc = widths(i)
                act.wait_ge(s["zdone"], n + 1)
                zz = z[:, n % (LAG + 1)]
                for k, (a, e) in enumerate(((0, ws), (ws, ws + ww), (ws + ww, ws + ww + wc))):
                    o = act.activation(zz[:, a:e], zz[:, a:e], ACT.Exp, bias=sm[:, n % (LAG + 1), 4 + k:5 + k], accum_out=sm[:, n % (LAG + 1), 8 + k:9 + k])
                o.then_inc(s["exp"], 1)

            def copies(n):
                for grp in groups(steps[n][1]):
                    k = cnt[0]
                    act.wait_ge(s["pt"], k + 1)
                    if k >= NSL:
                        act.wait_ge(s["pv"], k - NSL + 1)
                    full = [m for m in grp if m[1] == P]
                    o = None
                    if full:
                        o = act.activation(ptb[:, k % NSL, 0:len(full) * P], ps[:, 4 + k % 2, 0:len(full) * P], ACT.Copy)
                    if len(full) < len(grp):
                        w, m = grp[-1][1], len(full) * P
                        o = act.activation(ptb[0:w, k % NSL, m:m + P], ps[0:w, 4 + k % 2, m:m + P], ACT.Copy)
                    o.then_inc(s["ptc"], 1)
                    cnt[0] += 1

            for n in range(len(steps)):
                if n >= LAG:
                    copies(n - LAG)
                exps(n)
            for n in range(len(steps) - LAG, len(steps)):
                copies(n)


def inverse_norm(c, name, x, ntiles, mean, post, load=None, after=None):
    nc, ps = c.nc, c.ps
    s = Semaphores(c, name)
    with nc.sbuf_tensor(f"{name}_sq", [P, 2, T], F32) as sq, nc.sbuf_tensor(f"{name}_r", [P, H4, T], F32) as rr, nc.Block() as block:
        if load:
            @block.sync
            def _(sp):
                load(sp).then_inc(s["in"], 16)

        @block.gpsimd
        def _(pool):
            for m in range(ntiles):
                if m >= 2:
                    pool.wait_ge(s["ss"], m - 1)
                pool.tensor_tensor(sq[:, m % 2], x[:, m], x[:, m], ALU.mult).then_inc(s["sq"], 1)
            if after:
                for m in range(ntiles):
                    pool.wait_ge(s["done"], m + 1)
                    after(pool, m)

        @block.tensor
        def _(pe):
            for m in range(ntiles):
                pe.wait_ge(s["sq"], m + 1)
                if m >= 2:
                    pe.wait_ge(s["ln"], m - 1)
                for n in range(NW):
                    mm = pe.matmul(ps[:, 3 * (m % 2) + n, 0:W], c.ones[:], sq[:, m % 2, n * W:(n + 1) * W], start=True, stop=True)
                mm.then_inc(s["ss"], 1)

        @block.scalar
        def _(act):
            for m0 in range(0, ntiles, H4):
                for m in range(m0, m0 + H4):
                    act.wait_ge(s["ss"], m + 1)
                    if m >= H4:
                        act.wait_ge(s["done"], m - H4 + 1)
                    act.activation(rr[:, m % H4].rearrange("p (n w) -> p n w", n=NW), ps[:, 3 * (m % 2):3 * (m % 2) + NW, 0:W],
                                   ACT.Ln, bias=c.eps[:], scale=mean).then_inc(s["ln"], 1)
                for m in range(m0, m0 + H4):
                    act.wait_ge(s["ln"], m + 1)
                    act.activation(rr[:, m % H4], rr[:, m % H4], ACT.Exp, scale=-0.5).then_inc(s["r"], 1)

        @block.vector
        def _(dve):
            if load:
                dve.wait_ge(s["in"], 16)
            for m in range(ntiles):
                dve.wait_ge(s["r"], m + 1)
                post(dve, m, rr[:, m % H4]).then_inc(s["done"], 1)


def gated_norm(c, name, o, gate, w_in):
    with c.nc.sbuf_tensor(f"{name}_w", [P, 1], F32) as w:
        inverse_norm(c, f"{name}_in", o, H4, 1.0 / P,
                     lambda dve, m, r: dve.scalar_tensor_tensor(o[:, m], o[:, m], w[:], r, ALU.mult, ALU.mult),
                     load=lambda sp: sp.dma_start(w[:], w_in),
                     after=lambda pool, m: pool.tensor_tensor(o[:, m], o[:, m], gate[:, m], ALU.mult))


class Convolution:
    NT = 12

    def __init__(self, c, z, sb):
        self.c, self.z = c, z
        self.cw = sb("cw", [P, self.NT, 4])
        self.hist = sb("hist", [P, self.NT, NB, 3])
        self.y = sb("y", [P, 2, T])
        self.st = sb("st", [P, self.NT, 3 + 3 * NB])
        self.s = Semaphores(c, "cv")

    def vector(self, dve, z_copied):
        s, z, y, cw, hist, st = self.s, self.z, self.y, self.cw, self.hist, self.st
        dve.wait_ge(s["in"], 32)
        dve.sem_inc(s["silu"], 2)
        sv = st[:, :, 3:3 + 3 * NB].rearrange("p m (b t) -> p m b t", t=3)
        dve.tensor_copy(sv[:, :, :, 0:2], hist[:, :, :, 1:3])
        with dve.Fori(0, self.NT // 2) as i:
            for j in range(2):
                m = 2 * i + j
                zm, yy = z[:, m, :], y[:, j]
                dve.wait_ge(z_copied, m + 3)
                dve.tensor_copy(st[:, m, 0:3], zm[:, TP - 3:TP])
                dve.tensor_copy(st[:, m, 5:3 + 3 * NB:3], zm[:, TP:T])
                dve.wait_ge(s["silu"], m + 1)
                dve.tensor_scalar(yy, zm, cw[:, m, 3:4], None, ALU.mult).then_inc(s["link"], 1)
                for k in range(1, 4):
                    w = cw[:, m, 3 - k:4 - k]
                    dve.wait_ge(s["link"], 3 * m + k)
                    dve.scalar_tensor_tensor(yy[:, TP:T], hist[:, m, :, 3 - k], w, yy[:, TP:T], ALU.mult, ALU.add)
                    o = dve.scalar_tensor_tensor(yy[:, k:TP], zm[:, 0:TP - k], w, yy[:, k:TP], ALU.mult, ALU.add)
                    o.then_inc(s["link" if k < 3 else "y"], 1)

    def silu(self, act, i, j):
        act.wait_ge(self.s["y"], 2 * i + j + 1)
        act.sem_inc(self.s["going"], 1)
        act.activation(self.z[:, 2 * i + j, :], self.y[:, j], ACT.Silu).then_inc(self.s["silu"], 1)

    def load(self, pool):
        pool.dma_start(self.cw[:], self.c.dram["conv_w"]).then_inc(self.s["in"], 16)
        pool.dma_start(self.hist[:], self.c.dram["conv_state"]).then_inc(self.s["in"], 16)

    def store(self, pool):
        pool.wait_ge(self.s["y"], self.NT)
        pool.dma_start(self.c.dram["o_conv"], self.st[:]).then_inc(self.s["out"], 16)
        pool.wait_ge(self.s["out"], 16)


def deltanet_scalars(c, small, reset, gcol, bcol, egcol, sel):
    nc, ps, dr = c.nc, c.ps, c.dram
    s = Semaphores(c, "ds")
    with ExitStack() as ctx:
        sb = lambda n, sh: ctx.enter_context(nc.sbuf_tensor(f"ds_{n}", sh, F32))
        par = sb("par", [P, 2])
        tmp = sb("tmp", [P, 2, T])
        one = sb("one", [P, TP])
        block = ctx.enter_context(nc.Block())
        a, A = slice(32, 36), small[32:36, :]

        @block.sync
        def _(sp):
            sp.dma_start(par[a], dr["dn_par"]).then_inc(s["in"], 16)

        @block.scalar
        def _(act):
            act.wait_ge(s["in"], 16)
            act.activation(par[a, 0:1], par[a, 0:1], ACT.Exp).then_inc(s["ea"], 1)
            act.wait_ge(s["x"], 1)
            act.activation(tmp[a, 0], A, ACT.Abs).then_inc(s["alink"], 1)
            act.wait_ge(s["alink"], 1)
            act.activation(tmp[a, 0], tmp[a, 0], ACT.Exp, scale=-1.0).then_inc(s["alink"], 1)
            act.wait_ge(s["alink"], 2)
            act.activation(tmp[a, 0], tmp[a, 0], ACT.Ln, bias=c.ones[a, 0:1]).then_inc(s["l"], 1)
            act.activation(small[64:68, :], small[64:68, :], ACT.Sigmoid).then_inc(s["b"], 1)
            act.wait_ge(s["gc"], 1)
            act.activation(egcol[:], gcol[:], ACT.Exp).then_inc(s["alink"], 1)
            act.activation(small[a, TP:T], small[a, TP:T], ACT.Exp)

        @block.vector
        def _(dve):
            link = Link(dve, s["link"])
            for r in (32, 64):
                dve.tensor_copy(sel[r:r + 4], c.ident[r:r + 4, r:r + 4].unsqueeze(2).to_broadcast([4, 4, P]))
            link(dve.memset(one[a], 1.0))
            dve.wait_ge(s["in"], 16)
            dve.tensor_scalar(A, A, par[a, 1:2], None, ALU.add).then_inc(s["x"], 1)
            link(dve.memset(one[a].rearrange("p (i t) -> p i t", t=BLK)[:, :, 0:1], 0.0))
            dve.wait_ge(s["l"], 1)
            link(dve.tensor_scalar(tmp[a, 1], A, 0.0, None, ALU.max))
            link(dve.tensor_tensor(tmp[a, 1], tmp[a, 1], tmp[a, 0], ALU.add))
            dve.wait_ge(s["ea"], 1)
            link(dve.tensor_scalar(tmp[a, 1], tmp[a, 1], par[a, 0:1], -1.0, ALU.mult, ALU.mult))
            dve.tensor_copy(small[a, TP:T], tmp[a, 1, TP:T])
            dve.tensor_tensor_scan(small[a, 0:TP], one[a], tmp[a, 1, 0:TP], 0.0, ALU.mult, ALU.add).then_inc(s["g"], 1)
            dve.wait_ge(s["t"], 1)
            dve.tensor_copy(gcol[:].rearrange("p i h -> p (i h)"), ps[:, 0, 0:32])
            dve.tensor_copy(bcol[:].rearrange("p i h -> p (i h)"), ps[:, 1, 0:32]).then_inc(s["gc"], 1)
            dve.wait_ge(s["alink"], 3)
            dve.tensor_scalar(egcol[:], egcol[:], -1.0, None, ALU.mult)

        @block.tensor
        def _(pe):
            pe.wait_ge(s["g"], 1)
            pe.wait_ge(s["b"], 1)
            for k, r in enumerate((slice(32, 36), slice(64, 68))):
                for i in range(NBLK):
                    t = pe.transpose(ps[:, k, 4 * i:4 * i + 4], small[r, i * BLK:(i + 1) * BLK], c.ident[r, r])
            t.then_inc(s["t"], 1)


def deltanet_prompt(c, z, small, gcol, bcol, egcol, sel, S, o):
    nc, ps, dr = c.nc, c.ps, c.dram
    s = Semaphores(c, "dp")
    C = H4 * P
    with ExitStack() as ctx:
        sb = lambda n, sh: ctx.enter_context(nc.sbuf_tensor(f"dp_{n}", sh, F32))
        up = sb("up", [P, LEV, P])
        lo = sb("lo", [P, 3, P])
        egb, kt, vt, AT, A, at, X, Y, qks, dec, qg, kd = (sb(n, [P, 2, C]) for n in (
            "egb", "kt", "vt", "AT", "A", "at", "X", "Y", "qks", "dec", "qg", "kd"))
        Wm = A
        atm = (qks, dec)
        vn, rhs = sb("vn", [P, C]), sb("rhs", [P, C])
        dcol = sb("dcol", [P, 2, 2, H4])
        block = ctx.enter_context(nc.Block())
        hd = lambda h: slice(h * P, (h + 1) * P)
        as4 = lambda t: t.rearrange("p (h x) -> p h x", h=H4)
        R = LEV - 1
        NP = NBLK // 2
        lanes = range(2)
        chunk = lambda i: slice(i * BLK, (i + 1) * BLK)

        @block.sync
        def _(sp):
            sp.dma_start(up[:], dr["up"]).then_inc(s["in"], 16)
            sp.dma_start(lo[:], dr["lo"]).then_inc(s["in"], 16)

        @block.tensor
        def _(pe):
            for p in range(NP):
                if p:
                    pe.wait_ge(s["Su"], 2 * p)
                    pe.wait_ge(s["oc"], 2 * p)
                for L in lanes:
                    t, b = chunk(2 * p + L), 3 * L
                    for h in range(H4):
                        q, k = z[:, h, t], z[:, 4 + h, t]
                        pe.matmul(ps[:, b + 2, hd(h)], sel[32:36, h, :], small[32:36, t], start=True, stop=True)
                        pe.matmul(ps[:, b, hd(h)], k, k, start=True, stop=True)
                        mm = pe.matmul(ps[:, b + 1, hd(h)], q, k, start=True, stop=True)
                    mm.then_inc(s[f"raw{L}"], 1)
                    if L:
                        pe.wait_ge(s["tok0"], p + 1)
                    for h in range(H4):
                        pe.transpose(ps[:, 6, hd(h)], z[:, 4 + h, t], c.ident[:])
                        mm = pe.transpose(ps[:, 7, hd(h)], z[:, 8 + h, t], c.ident[:])
                    mm.then_inc(s[f"kv{L}"], 1)
                for L in lanes:
                    pe.wait_ge(s[f"A{L}"], p + 1)
                    for h in range(H4):
                        pe.transpose(ps[:, 3 * L, hd(h)], A[:, L, hd(h)], c.ident[:])
                        mm = pe.transpose(ps[:, 3 * L + 1, hd(h)], qks[:, L, hd(h)], c.ident[:])
                    mm.then_inc(s[f"turned{L}"], 1)
                for l in range(1, LEV):
                    n = p * R + l
                    for L in lanes:
                        pe.wait_ge(s[f"X0{L}"], p + 1)
                        pe.wait_ge(s[f"atm{L}"], n)
                        if l > 1:
                            pe.wait_ge(s[f"XYs{L}"], n - 1)
                        for h in range(H4):
                            mm = pe.matmul(ps[:, 3 * L, hd(h)], atm[l % 2][:, L, hd(h)], X[:, L, hd(h)], start=True, stop=True)
                        mm.then_inc(s[f"Wm{L}"], 1)
                    for L in lanes:
                        pe.wait_ge(s[f"Wc{L}"], n)
                        for h in range(H4):
                            if l < LEV - 1:
                                pe.matmul(ps[:, 3 * L + 1, hd(h)], Y[:, L, hd(h)], Wm[:, L, hd(h)], start=True, stop=True)
                            mm = pe.matmul(ps[:, 3 * L + 2, hd(h)], Wm[:, L, hd(h)], Y[:, L, hd(h)], start=True, stop=True)
                        mm.then_inc(s[f"XY{L}"], 1)
                for L in lanes:
                    i = 2 * p + L
                    if L:
                        pe.wait_ge(s["Su"], i)
                        pe.wait_ge(s["oc"], i)
                    else:
                        pe.wait_ge(s["tok1"], p + 1)
                    for h in range(H4):
                        mm = pe.matmul(ps[:, 6, hd(h)], z[:, 4 + h, chunk(i)], S[:, hd(h)], start=True, stop=True)
                    mm.then_inc(s["ks"], 1)
                    pe.wait_ge(s["rhs"], i + 1)
                    for h in range(H4):
                        mm = pe.matmul(ps[:, 7, hd(h)], Y[:, L, hd(h)], rhs[:, hd(h)], start=True, stop=True)
                    mm.then_inc(s["vn"], 1)
                    pe.wait_ge(s["vnc"], i + 1)
                    pe.wait_ge(s[f"qg{L}"], p + 1)
                    for h in range(H4):
                        mm = pe.matmul(ps[:, 7, hd(h)], kd[:, L, hd(h)], vn[:, hd(h)], start=True, stop=True)
                    mm.then_inc(s["U"], 1)
                    for h in range(H4):
                        pe.matmul(ps[:, 6, hd(h)], S[:, hd(h)], qg[:, L, hd(h)], start=True, stop=False)
                        mm = pe.matmul(ps[:, 6, hd(h)], vn[:, hd(h)], at[:, L, hd(h)], start=False, stop=True)
                    mm.then_inc(s["ou"], 1)

        @block.scalar
        def _(act):
            for p in range(NP):
                for L in lanes:
                    act.wait_ge(s[f"raw{L}"], p + 1)
                    act.activation(egb[:, L], ps[:, 3 * L + 2, :], ACT.Exp).then_inc(s[f"egb{L}"], 1)
                    act.wait_ge(s[f"kv{L}"], p + 1)
                    act.activation(kt[:, L], ps[:, 6, :], ACT.Copy)
                    act.activation(vt[:, L], ps[:, 7, :], ACT.Copy).then_inc(s[f"tok{L}"], 1)
                    act.wait_ge(s[f"diff{L}"], p + 1)
                    act.activation(dec[:, L], dec[:, L], ACT.Exp, scale=-1.0).then_inc(s[f"dec{L}"], 1)
                    act.activation(dcol[:, L, 1], dcol[:, L, 0], ACT.Exp).then_inc(s[f"dcx{L}"], 1)
                for L in lanes:
                    act.wait_ge(s[f"turned{L}"], p + 1)
                    act.activation(AT[:, L], ps[:, 3 * L, :], ACT.Copy).then_inc(s[f"AT{L}"], 1)
                    act.activation(at[:, L], ps[:, 3 * L + 1, :], ACT.Copy).then_inc(s[f"at{L}"], 1)
                for l in range(1, LEV):
                    for L in lanes:
                        act.wait_ge(s[f"Wm{L}"], p * R + l)
                        act.activation(Wm[:, L], ps[:, 3 * L, :], ACT.Copy).then_inc(s[f"Wc{L}"], 1)
                for L in lanes:
                    i = 2 * p + L
                    act.wait_ge(s["vn"], i + 1)
                    act.activation(vn[:], ps[:, 7, :], ACT.Copy).then_inc(s["vnc"], 1)
                    act.wait_ge(s["ou"], i + 1)
                    act.activation(o[:, :, chunk(i)], as4(ps[:, 6, :]), ACT.Copy).then_inc(s["oc"], 1)

        @block.gpsimd
        def _(pool):
            pool.wait_ge(s["in"], 32)
            for p in range(NP):
                for l in range(1, LEV):
                    for L in lanes:
                        pool.wait_ge(s[f"at{L}"], p + 1)
                        if l >= 3:
                            pool.wait_ge(s[f"Wm{L}"], p * R + l - 2)
                        pool.tensor_tensor(as4(atm[l % 2][:, L]), as4(AT[:, L]), mid(up[:, l, :], H4), ALU.mult).then_inc(s[f"atm{L}"], 1)

        @block.vector
        def _(dve):
            link = Link(dve, s["link"])
            link(dve.memset(S[:], 0.0))
            dve.wait_ge(s["in"], 32)
            for p in range(NP):
                for L in lanes:
                    i, b = 2 * p + L, 3 * L
                    dve.wait_ge(s[f"raw{L}"], p + 1)
                    dve.wait_ge(s[f"egb{L}"], p + 1)
                    for h in range(H4):
                        dve.tensor_scalar(dec[:, L, hd(h)], ps[:, b + 2, hd(h)], gcol[:, i, h:h + 1], 0.0, ALU.subtract, ALU.max)
                    dve.tensor_tensor(dcol[:, L, 0], ps[:, b + 2, P - 1:C:P], gcol[:, i, :], ALU.subtract).then_inc(s[f"diff{L}"], 1)
                for L in lanes:
                    i, b = 2 * p + L, 3 * L
                    dve.wait_ge(s[f"dec{L}"], p + 1)
                    link(dve.tensor_tensor(as4(dec[:, L]), as4(dec[:, L]), mid(lo[:, 0, :], H4), ALU.mult))
                    for h in range(H4):
                        dve.scalar_tensor_tensor(A[:, L, hd(h)], ps[:, b, hd(h)], bcol[:, i, h:h + 1], dec[:, L, hd(h)], ALU.mult, ALU.mult)
                    link(dve.tensor_tensor(qks[:, L], ps[:, b + 1, :], dec[:, L], ALU.mult))
                    dve.tensor_tensor(as4(A[:, L]), as4(A[:, L]), mid(lo[:, 1, :], H4), ALU.mult).then_inc(s[f"A{L}"], 1)
                    dve.wait_ge(s[f"A{L}"], p + 1)
                    link(dve.tensor_tensor(as4(X[:, L]), as4(A[:, L]), mid(lo[:, 2, :], H4), ALU.mult))
                    dve.tensor_tensor(as4(X[:, L]), mid(c.ident[:], H4), as4(X[:, L]), ALU.subtract)
                for L in lanes:
                    i = 2 * p + L
                    dve.wait_ge(s[f"AT{L}"], p + 1)
                    link(dve.tensor_tensor(as4(Y[:, L]), as4(AT[:, L]), mid(up[:, 0, :], H4), ALU.mult))
                    dve.tensor_tensor(as4(Y[:, L]), mid(c.ident[:], H4), as4(Y[:, L]), ALU.subtract).then_inc(s[f"X0{L}"], 1)
                for l in range(1, LEV):
                    for L in lanes:
                        if l <= 1:
                            dve.tensor_tensor(as4(qg[:, L]), z[:, 0:4, chunk(2 * p + L)], as4(egb[:, L]), ALU.mult)
                            dve.wait_ge(s[f"tok{L}"], p + 1)
                            dve.wait_ge(s[f"dcx{L}"], p + 1)
                            dve.tensor_tensor(as4(kd[:, L]), as4(kt[:, L]), last(dcol[:, L, 1], P), ALU.mult).then_inc(s[f"qg{L}"], 1)
                    for L in lanes:
                        dve.wait_ge(s[f"XY{L}"], p * R + l)
                        if l < LEV - 1:
                            dve.tensor_tensor(X[:, L], X[:, L], ps[:, 3 * L + 1, :], ALU.subtract)
                        dve.tensor_tensor(Y[:, L], Y[:, L], ps[:, 3 * L + 2, :], ALU.subtract).then_inc(s[f"XYs{L}"], 1)
                for L in lanes:
                    i = 2 * p + L
                    dve.wait_ge(s["ks"], i + 1)
                    link(dve.tensor_tensor(as4(rhs[:]), as4(ps[:, 6, :]), last(egcol[:, i, :], P), ALU.mult))
                    link(dve.tensor_tensor(rhs[:], rhs[:], vt[:, L], ALU.add))
                    dve.wait_ge(s[f"XYs{L}"], (p + 1) * R)
                    dve.tensor_tensor(as4(rhs[:]), as4(rhs[:]), last(bcol[:, i, :], P), ALU.mult).then_inc(s["rhs"], 1)
                    dve.wait_ge(s["ou"], i + 1)
                    link(dve.tensor_tensor(as4(S[:]), as4(S[:]), last(egb[:, L, P - 1:C:P], P), ALU.mult))
                    dve.tensor_tensor(S[:], S[:], ps[:, 7, :], ALU.add).then_inc(s["Su"], 1)


def store_states(c, name, S, out):
    nc = c.nc
    sem = c.sem(f"{name}_stored")
    with nc.Block() as block:
        @block.sync
        def _(sp):
            sp.dma_start(out, S).then_inc(sem, 16)
            sp.wait_ge(sem, 16)


def recurrent_samples(c, name, state_in, state_out, o, q, k, vT, decay, beta=None):
    nc, ps, dr = c.nc, c.ps, c.dram
    s = Semaphores(c, name)
    NPR = H4 * NB
    N = 4
    NS = NPR // N
    with ExitStack() as ctx:
        sb = lambda n, sh: ctx.enter_context(nc.sbuf_tensor(f"{name}_{n}", sh, F32))
        S = sb("S", [P, NPR, P])
        pr = sb("pr", [P, 2, N, P])
        dg = sb("dg", [P, 2, N, P])
        u = sb("u", [P, N, P])
        qc = sb("qc", [P, NPR])
        block = ctx.enter_context(nc.Block())
        head = lambda h: slice(h * NB, (h + 1) * NB)

        @block.sync
        def _(sp):
            for h in range(H4):
                sp.dma_start(S[:, head(h)], state_in[:, head(h)]).then_inc(s[f"in{h}"], 16)
            for h in range(H4):
                sp.wait_ge(s["u"], (h + 1) * NS // H4)
                sp.dma_start(state_out[:, head(h)], S[:, head(h)]).then_inc(s["out"], 16)
            sp.wait_ge(s["out"], 16 * H4)

        @block.vector
        def _(dve):
            link = Link(dve, s["link"])
            dve.tensor_copy(qc[:].rearrange("p (h b) -> p h b", b=NB), q).then_inc(s["q"], 1)

            def place(n):
                return n * N // NB, n * N % NB, slice(n * N, (n + 1) * N), n % 2

            def operands(n):
                h, b0, sl, j = place(n)
                if b0 == 0:
                    dve.wait_ge(s[f"in{h}"], 16)
                if n >= 2:
                    dve.wait_ge(s["mm"], n - 1)
                if beta is not None:
                    dve.tensor_tensor(pr[:, j], S[:, sl], last(k[:, h, b0:b0 + N], P), ALU.mult)
                dve.tensor_tensor(dg[:, j], mid(c.ident[:], N), last(vT[:, h, b0:b0 + N], P), ALU.mult).then_inc(s["p"], 1)

            operands(0)
            for n in range(NS):
                h, b0, sl, j = place(n)
                kk, d = last(k[:, h, b0:b0 + N], P), decay(h, b0, N)
                if n + 1 < NS:
                    operands(n + 1)
                link(dve.tensor_tensor(S[:, sl], S[:, sl], last(d, P), ALU.mult))
                dve.wait_ge(s["mm"], n + 1)
                vb = ps[:, 2 * j + 1, :].rearrange("p (n v) -> p n v", n=N)
                if beta is not None:
                    link(dve.tensor_tensor(u[:], ps[:, 2 * j, :].rearrange("p (n v) -> p n v", n=N), last(d, P), ALU.mult))
                    link(dve.tensor_tensor(u[:], vb, u[:], ALU.subtract))
                    link(dve.tensor_tensor(u[:], u[:], last(beta(h, b0, N), P), ALU.mult))
                    link(dve.tensor_tensor(u[:], u[:], kk, ALU.mult))
                else:
                    link(dve.tensor_tensor(u[:], vb, kk, ALU.mult))
                dve.tensor_tensor(S[:, sl], S[:, sl], u[:], ALU.add).then_inc(s["u"], 1)
            dve.wait_ge(s["omm"], 1)
            dve.tensor_copy(o[:, :, TP:T], ps[:, 4, 0:NPR].rearrange("p (h b) -> p h b", b=NB))

        @block.tensor
        def _(pe):
            def outputs(n):
                pe.wait_ge(s["u"], n + 1)
                for m in range(n * N, (n + 1) * N):
                    mm = pe.matmul(ps[:, 4, m:m + 1], S[:, m, :], qc[:, m:m + 1], start=True, stop=True)
                return mm

            pe.wait_ge(s["q"], 1)
            for n in range(NS):
                j = n % 2
                pe.wait_ge(s["p"], n + 1)
                if n >= 2:
                    pe.wait_ge(s["u"], n - 1)
                if beta is not None:
                    pe.matmul(ps[:, 2 * j, :], c.ones[:], pr[:, j].rearrange("p n v -> p (n v)"), start=True, stop=True)
                pe.matmul(ps[:, 2 * j + 1, :], c.ones[:], dg[:, j].rearrange("p n v -> p (n v)"), start=True, stop=True).then_inc(s["mm"], 1)
                if n >= 2:
                    outputs(n - 2)
            outputs(NS - 2)
            outputs(NS - 1).then_inc(s["omm"], 1)


def spread_rows(c, name, sel, small, rows, dst):
    nc, ps = c.nc, c.ps
    mmd = c.sem(f"{name}_spread")
    with nc.Block() as block:
        @block.tensor
        def _(pe):
            for k, r in enumerate(rows):
                for h in range(H4):
                    mm = pe.matmul(ps[:, k, h * NB:(h + 1) * NB], sel[r:r + 4, h, :], small[r:r + 4, TP:T], start=True, stop=True)
            mm.then_inc(mmd, 1)

        @block.vector
        def _(dve):
            dve.wait_ge(mmd, 1)
            dve.tensor_copy(dst[:].rearrange("p k h b -> p k (h b)"), ps[:, 0:len(rows), 0:H4 * NB])


def deltanet(c, small):
    nc, dr = c.nc, c.dram
    o = c.oT[1]
    with ExitStack() as ctx:
        sb = lambda n, sh, dt=F32: ctx.enter_context(nc.sbuf_tensor(f"dn_{n}", sh, dt))
        z = sb("z", [P, 16, T])
        gcol, bcol, egcol = sb("gcol", [P, NBLK, H4]), sb("bcol", [P, NBLK, H4]), sb("egcol", [P, NBLK, H4])
        sel = sb("sel", [P, H4, P])
        dbs = sb("dbs", [P, 2, H4, NB])
        S = sb("S", [P, H4 * P])
        with ExitStack() as cv:
            sb2 = lambda n, sh, dt=F32: cv.enter_context(nc.sbuf_tensor(f"cv_{n}", sh, dt))
            conv = Convolution(c, z, sb2)
            project(c, "dnp", dr["w_dn"], 16, z, Tokens(c, "dx", sb2), z[:, 8:16], H4, conv)
        inverse_norm(c, "l2", z, 8, 1.0,
                     lambda dve, m, r: dve.scalar_tensor_tensor(z[:, m], z[:, m], P ** -0.5 if m < 4 else 1.0, r, ALU.mult, ALU.mult))
        deltanet_scalars(c, small, None, gcol, bcol, egcol, sel)
        spread_rows(c, "dn", sel, small, (32, 64), dbs)
        recurrent_samples(c, "dns", dr["state_dn"], dr["o_dn_s"], o, z[:, 0:4, TP:T], z[:, 4:8, TP:T], z[:, 8:12, TP:T],
                          lambda h, b, n: dbs[:, 0, h, b:b + n], lambda h, b, n: dbs[:, 1, h, b:b + n])
        deltanet_prompt(c, z, small, gcol, bcol, egcol, sel, S, o)
        store_states(c, "dn", S[:], dr["o_dn_p"])
        gated_norm(c, "dng", o, z[:, 12:16], dr["dn_norm"])


def hgrn2(c):
    nc, ps, dr = c.nc, c.ps, c.dram
    o = c.oT[2]
    with ExitStack() as ctx:
        sb = lambda n, sh: ctx.enter_context(nc.sbuf_tensor(f"hg_{n}", sh, F32))
        z = sb("z", [P, 16, T])
        with ExitStack() as cx:
            x = Tokens(c, "hx", lambda n, sh, dt: cx.enter_context(nc.sbuf_tensor(f"hx_{n}", sh, dt)))
            project(c, "hgp", dr["w_hg"], 16, z, x, z[:, 8:16], H4)
        f = sb("f", [P, H4, NB])
        Gs = sb("Gs", [P, 2, T])
        s = Semaphores(c, "hg")
        with ExitStack() as c2:
            s2 = lambda n, sh: c2.enter_context(nc.sbuf_tensor(f"hg_{n}", sh, F32))
            up = s2("up", [P, LEV, P])
            one = s2("one", [P, TP])
            lf = s2("lf", [P, T])
            E = s2("E", [P, 2, TP])
            Z = s2("Z", [P, 2, TP])
            at = s2("at", [P, NBLK, P])
            vt = s2("vt", [P, NBLK, P])
            qg = s2("qg", [P, TP])
            kd = s2("kd", [P, TP])
            kt = s2("kt", [P, NBLK, P])
            eg = s2("eg", [P, NBLK])
            S = s2("S", [P, H4, P])
            block = c2.enter_context(nc.Block())
            NL = LEV + 1
            bank2 = lambda t: t.rearrange("p (a b) t -> p a (b t)", a=2)

            @block.sync
            def _(sp):
                sp.dma_start(up[:], dr["up"]).then_inc(s["in"], 16)
                sp.wait_ge(s["Su"], H4 * NBLK)
                sp.dma_start(dr["o_hg_p"], S[:]).then_inc(s["out"], 16)
                sp.wait_ge(s["out"], 16)

            @block.scalar
            def _(act):
                def forget(h):
                    k = z[:, 4 + h]
                    if h:
                        act.wait_ge(s["G"], h)
                    act.activation(lf[:], k, ACT.Abs).then_inc(s["alink"], 1)
                    act.wait_ge(s["alink"], 2 * h + 1)
                    act.activation(lf[:], lf[:], ACT.Exp, scale=-1.0).then_inc(s["alink"], 1)
                    act.wait_ge(s["alink"], 2 * h + 2)
                    act.activation(lf[:], lf[:], ACT.Ln, bias=c.ones[:, 0:1]).then_inc(s["l"], 1)
                    act.wait_ge(s["a"], h + 1)
                    act.activation(k, k, ACT.Sigmoid, scale=-1.0).then_inc(s["k"], 1)

                forget(0)
                for h in range(H4):
                    for l in range(LEV):
                        n = h * LEV + l
                        act.wait_ge(s["D"], n + 1)
                        act.activation(E[:, n % 2], E[:, n % 2], ACT.Exp).then_inc(s["E"], 1)
                        if l == 1:
                            act.activation(f[:, h, :], Gs[:, h % 2, TP:T], ACT.Exp)
                            act.activation(qg[:], Gs[:, h % 2, 0:TP], ACT.Exp).then_inc(s["fs"], 1)
                        if l == 2:
                            act.wait_ge(s["kd0"], h + 1)
                            act.activation(kd[:], kd[:], ACT.Exp).then_inc(s["kt"], 1)
                        if l == 3:
                            act.wait_ge(s["vt"], h + 1)
                            act.activation(bank2(vt[:]), ps[:, 4:6, :], ACT.Copy).then_inc(s["vtc"], 1)
                    if h + 1 < H4:
                        forget(h + 1)
                    for i in range(NBLK):
                        n = h * NBLK + i
                        act.wait_ge(s["ou"], n + 1)
                        act.activation(o[:, h, i * BLK:(i + 1) * BLK], ps[:, 6 + n % 2, 0:P], ACT.Copy).then_inc(s["oc"], 1)

            @block.gpsimd
            def _(pool):
                for h in range(H4):
                    G = Gs[:, h % 2, 0:TP]
                    pool.wait_ge(s["G"], h + 1)
                    for l in range(LEV):
                        n = h * LEV + l
                        hs = 1 << l
                        v = lambda t: t.rearrange("p (i u x) -> p i u x", u=2, x=hs)
                        Gv, Ev = v(G), v(E[:, n % 2])
                        anchor = Gv[:, :, 0, hs - 1:hs].to_broadcast([P, TP // (2 * hs), hs])
                        if n >= 2:
                            pool.wait_ge(s["Z"], n - 1)
                        pool.tensor_tensor(Ev[:, :, 1], Gv[:, :, 1], anchor, ALU.subtract)
                        pool.tensor_tensor(Ev[:, :, 0], anchor, Gv[:, :, 0], ALU.subtract).then_inc(s["D"], 1)
                        if l == 1:
                            Gc = G.rearrange("p (i t) -> p i t", t=BLK)
                            if h:
                                pool.wait_ge(s["ktc"], h)
                            pool.tensor_tensor(kd[:].rearrange("p (i t) -> p i t", t=BLK),
                                               Gc[:, :, BLK - 1:BLK].to_broadcast([P, NBLK, BLK]), Gc, ALU.subtract).then_inc(s["kd0"], 1)

            @block.vector
            def _(dve):
                link = Link(dve, s["link"])

                def decay(h):
                    G = Gs[:, h % 2]
                    dve.wait_ge(s["l"], h + 1)
                    dve.tensor_scalar(G, z[:, 4 + h], 0.0, None, ALU.min).then_inc(s["a"], 1)
                    dve.wait_ge(s["a"], h + 1)
                    link(dve.tensor_tensor(lf[:], G, lf[:], ALU.subtract))
                    dve.tensor_copy(G[:, TP:T], lf[:, TP:T])
                    dve.tensor_tensor_scan(G[:, 0:TP], one[:], lf[:, 0:TP], 0.0, ALU.mult, ALU.add).then_inc(s["G"], 1)

                def factors(h, l):
                    n = h * LEV + l
                    v = lambda t: t.rearrange("p (i u x) -> p i u x", u=2, x=1 << l)
                    q, k, Ev, Zv = v(z[:, h, 0:TP]), v(z[:, 4 + h, 0:TP]), v(E[:, n % 2]), v(Z[:, n % 2])
                    dve.wait_ge(s["E"], n + 1)
                    if n >= 2:
                        dve.wait_ge(s["mm"], h * NL + l if l >= 2 else (h - 1) * NL + LEV - 1 + l)
                    dve.tensor_tensor(Zv[:, :, 1], q[:, :, 1], Ev[:, :, 1], ALU.mult)
                    dve.tensor_tensor(Zv[:, :, 0], k[:, :, 0], Ev[:, :, 0], ALU.mult).then_inc(s["Z"], 1)

                def masked(h, l):
                    m = h * NL + l + 1
                    tmp = o[:, h, 0:TP]
                    dve.wait_ge(s["mm"], m + 1)
                    src = ps[:, 2 * (m % 2):2 * (m % 2) + 2, :]
                    as2 = lambda t: t.rearrange("p (a b t) -> p a b t", a=2, t=P)
                    mask = (c.ident[:] if l < 0 else up[:, l, :]).unsqueeze(1).unsqueeze(1).to_broadcast([P, 2, 4, P])
                    src = src.rearrange("p a (b t) -> p a b t", t=P)
                    dst = at[:].rearrange("p (a b) t -> p a b t", a=2)
                    if l < 0:
                        dve.tensor_tensor(dst, src, mask, ALU.mult).then_inc(s["mk"], 1)
                    else:
                        dve.tensor_tensor(as2(tmp), src, mask, ALU.mult).then_inc(s["mk"], 1)
                    dve.wait_ge(s["mk"], m + 1)
                    if l >= 0:
                        link(dve.tensor_tensor(dst, dst, as2(tmp), ALU.add))

                link(dve.memset(one[:], 1.0))
                dve.memset(S[:], 0.0)
                link(dve.memset(one[:].rearrange("p (i t) -> p i t", t=BLK)[:, :, 0:1], 0.0))
                dve.tensor_scalar(z[:, 0:4], z[:, 0:4], P ** -0.5, None, ALU.mult).then_inc(s["q"], 1)
                dve.wait_ge(s["in"], 16)
                dve.wait_ge(s["q"], 1)
                decay(0)
                for h in range(H4):
                    q, k = z[:, h, 0:TP], z[:, 4 + h, 0:TP]
                    dve.wait_ge(s["k"], h + 1)
                    factors(h, 0)
                    masked(h, -1)
                    for l in range(LEV):
                        if l + 1 < LEV:
                            factors(h, l + 1)
                        else:
                            dve.wait_ge(s["kt"], h + 1)
                            dve.tensor_tensor(kd[:], kd[:], k, ALU.mult).then_inc(s["kd"], 1)
                        masked(h, l)
                    dve.wait_ge(s["fs"], h + 1)
                    link(dve.tensor_copy(eg[:], qg[:, BLK - 1:TP:BLK]))
                    dve.tensor_tensor(qg[:], qg[:], q, ALU.mult).then_inc(s["qg"], 1)
                    dve.wait_ge(s["turned"], h + 1)
                    dve.tensor_copy(bank2(kt[:]), ps[:, 6:8, :]).then_inc(s["ktc"], 1)
                    if h + 1 < H4:
                        decay(h + 1)
                    for i in range(NBLK):
                        n = h * NBLK + i
                        dve.wait_ge(s["ou"], n + 1)
                        link(dve.tensor_scalar(S[:, h, :], S[:, h, :], eg[:, i:i + 1], None, ALU.mult))
                        dve.tensor_tensor(S[:, h, :], S[:, h, :], ps[:, 4 + n % 2, 0:P], ALU.add).then_inc(s["Su"], 1)

            @block.tensor
            def _(pe):
                pe.wait_ge(s["q"], 1)
                for h in range(H4):
                    pe.wait_ge(s["k"], h + 1)
                    for l in range(-1, LEV):
                        m, n = h * NL + l + 1, h * LEV + l
                        if l >= 0:
                            pe.wait_ge(s["Z"], n + 1)
                        if m >= 2:
                            pe.wait_ge(s["mk"], m - 1)
                        for i in range(NBLK):
                            t = slice(i * BLK, (i + 1) * BLK)
                            x, y = (Z[:, n % 2, t], Z[:, n % 2, t]) if l >= 0 else (z[:, 4 + h, t], z[:, h, t])
                            mm = pe.matmul(ps[:, 2 * (m % 2) + i // 4, (i % 4) * P:(i % 4 + 1) * P], x, y, start=True, stop=True)
                        mm.then_inc(s["mm"], 1)
                        if l == 1:
                            if h:
                                pe.wait_ge(s["Su"], NBLK * h)
                            for i in range(NBLK):
                                t_ = pe.transpose(ps[:, 4 + i // 4, (i % 4) * P:(i % 4 + 1) * P], z[:, 8 + h, i * BLK:(i + 1) * BLK], c.ident[:])
                            t_.then_inc(s["vt"], 1)
                    pe.wait_ge(s["kd"], h + 1)
                    if h:
                        pe.wait_ge(s["oc"], NBLK * h)
                    for i in range(NBLK):
                        t_ = pe.transpose(ps[:, 6 + i // 4, (i % 4) * P:(i % 4 + 1) * P], kd[:, i * BLK:(i + 1) * BLK], c.ident[:])
                    t_.then_inc(s["turned"], 1)
                    pe.wait_ge(s["ktc"], h + 1)
                    pe.wait_ge(s["vtc"], h + 1)
                    pe.wait_ge(s["qg"], h + 1)
                    for i in range(NBLK):
                        n = h * NBLK + i
                        t = slice(i * BLK, (i + 1) * BLK)
                        if n >= 2:
                            pe.wait_ge(s["oc"], n - 1)
                        if i == 0 and h:
                            pe.wait_ge(s["Su"], n)
                        if i >= 2:
                            pe.wait_ge(s["Su"], n - 1)
                        pe.matmul(ps[:, 4 + n % 2, 0:P], kt[:, i, :], vt[:, i, :], start=True, stop=True)
                        if i:
                            pe.wait_ge(s["Su"], n)
                        pe.matmul(ps[:, 6 + n % 2, 0:P], S[:, h, :], qg[:, t], start=True, stop=False)
                        pe.matmul(ps[:, 6 + n % 2, 0:P], vt[:, i, :], at[:, i, :], start=False, stop=True).then_inc(s["ou"], 1)

        recurrent_samples(c, "hgs", dr["state_hg"], dr["o_hg_s"], o, z[:, 0:4, TP:T], z[:, 4:8, TP:T], z[:, 8:12, TP:T],
                          lambda h, b, n: f[:, h, b:b + n])
        gated_norm(c, "hgg", o, z[:, 12:16], dr["hg_norm"])


def merge(c, mT):
    nc, ps, dr = c.nc, c.ps, c.dram
    s = Semaphores(c, "mg")
    with ExitStack() as ctx:
        sb = lambda n, sh, dt=F32: ctx.enter_context(nc.sbuf_tensor(f"mg_{n}", sh, dt))
        raw = sb("raw", [P, 3, KT, P])
        wg = sb("wg", [P, 3, 2, KT, P], FR)
        wb = sb("wb", [P, 3, H4, P])
        sg = sb("sg", [P, T])
        tmp = sb("tmp", [P, T])
        x = Tokens(c, "mx", sb)
        stage = mT[:]
        block = ctx.enter_context(nc.Block())
        win = lambda t: t.rearrange("p (n w) -> p n w", n=NW)

        def loop(eng):
            with eng.Fori(0, KT) as m:
                for b in range(3):
                    yield m, b, 3 * m + b

        @block.sync
        def _(sp):
            for m, b, n in loop(sp):
                sp.wait_ge(s["wsplit"], n + 1)
                sp.dma_start(raw[:, b], dr["w_mg"][3 * m + b]).then_inc(s[f"wg{b}"], 16)
                sp.wait_ge(s["br"], n + 1)
                sp.dma_start(wb[:, b], dr["w_br"][3 * m + b]).then_inc(s[f"wb{b}"], 16)

        @block.gpsimd
        def _(pool):
            pool.sem_inc(s["wsplit"], 3)
            for m, b, n in loop(pool):
                pool.wait_ge(s["whigh"], n + 1)
                pool.tensor_tensor(wg[:, b, 1], raw[:, b], wg[:, b, 0], ALU.subtract).then_inc(s["wsplit"], 1)

        @block.tensor
        def _(pe):
            pe.sem_inc(s["gate"], 3)
            pe.sem_inc(s["br"], 3)
            x.wait(pe)
            for m, b, n in loop(pe):
                pe.wait_ge(s["wsplit"], n + 4)
                pe.wait_ge(s["gate_read"], n + 1)
                for t in range(NW):
                    for k in range(KT):
                        mm = product(pe, ps[:, t, 0:W], wg[:, b], x, k, slice(t * W, (t + 1) * W), k == 0, k == KT - 1)
                mm.then_inc(s["gate"], 1)
                pe.wait_ge(s[f"wb{b}"], 16 * m + 16)
                pe.wait_ge(s["br_read"], n + 1)
                for t in range(NW):
                    for k in range(H4):
                        mm = pe.matmul(ps[:, 3 + t, 0:W], wb[:, b, k, :], c.oT[b][:, k, t * W:(t + 1) * W], start=(k == 0), stop=(k == H4 - 1))
                mm.then_inc(s["br"], 1)

        @block.scalar
        def _(act):
            act.sem_inc(s["gate_read"], 1)
            x.load(act, stage)
            x.take_high(act, stage)

            def weights(m, b, n):
                act.wait_ge(s[f"wg{b}"], 16 * m + 16)
                act.wait_ge(s["gate"], n + 1)
                act.activation(wg[:, b, 0], raw[:, b], ACT.Copy).then_inc(s["whigh"], 1)

            for b in range(2):
                weights(0, b, b)
            for m, b, n in loop(act):
                if b == 0:
                    weights(m, 2, n + 2)
                else:
                    with act.If(m < KT - 1):
                        weights(m + 1, b - 1, n + 2)
                act.wait_ge(s["gate"], n + 4)
                act.wait_ge(s["sg_used"], n + 1)
                act.activation(win(sg[:]), ps[:, 0:NW, 0:W], ACT.Sigmoid).then_inc(s["gate_read"], 1)

        @block.vector
        def _(dve):
            dve.sem_inc(s["br_read"], 1)
            dve.sem_inc(s["sg_used"], 1)
            x.take_low(dve, stage)
            for m, b, n in loop(dve):
                dve.wait_ge(s["br"], n + 4)
                dve.wait_ge(s["gate_read"], n + 2)
                dst = tmp[:] if b else mT[:, m, :]
                dve.tensor_tensor(win(dst), win(sg[:]), ps[:, 3:3 + NW, 0:W], ALU.mult).then_inc(s["br_read"], 1)
                dve.wait_ge(s["br_read"], n + 2)
                dve.sem_inc(s["sg_used"], 1)
                if b:
                    dve.tensor_tensor(mT[:, m, :], mT[:, m, :], tmp[:], ALU.add).then_inc(s["added"], 1)
                    dve.wait_ge(s["added"], 2 * m + b)


def rows(t):
    return BLK if t < NBLK else NB


def norm_rows(dve, act_sems, link, y, r, st, gb, n):
    asked, given = act_sems
    for h in range(2):
        dve.bn_stats(st[0:r, 6 * h:6 * h + 6], y[:, h * 512:(h + 1) * 512])
    link(dve.engine_nop())
    link(dve.bn_aggr(st[0:r, 12:14], st[0:r, 0:12]))
    dve.engine_nop().then_inc(asked, 1)
    dve.wait_ge(given, n + 1)
    link(dve.reciprocal(st[0:r, 14:15], st[0:r, 14:15]))
    link(dve.tensor_scalar(y, y, st[0:r, 12:13], st[0:r, 14:15], ALU.subtract, ALU.mult))
    return dve.tensor_tensor(y, y, gb[0:r, 0], ALU.mult)


def root(act, eps, st, r, asked, given, n):
    act.wait_ge(asked, n + 1)
    act.activation(st[0:r, 14:15], st[0:r, 13:14], ACT.Sqrt, bias=eps[0:r]).then_inc(given, 1)


def mix_out(c, mT, y, x1T):
    nc, ps, dr = c.nc, c.ps, c.dram
    s = Semaphores(c, "mo")
    with ExitStack() as ctx:
        sb = lambda n, sh: ctx.enter_context(nc.sbuf_tensor(f"mo_{n}", sh, F32))
        w = sb("w", [P, KT, D])
        gb = sb("gb", [P, 2, D])
        xt = sb("xt", [P, 2, D])
        st = sb("st", [P, 16])
        block = ctx.enter_context(nc.Block())

        @block.sync
        def _(sp):
            sp.dma_start(w[:], dr["w_out"]).then_inc(s["w"], 16)
            for k in range(2):
                sp.dma_start(gb[:, k, :], dr["ln1"][k:k + 1, :].to_broadcast([P, D])).then_inc(s["gb"], 16)
            for t in range(NTT):
                if t >= 2:
                    sp.wait_ge(s["read"], t - 1)
                sp.dma_start(xt[0:rows(t), t % 2], dr["x"][t * BLK:t * BLK + rows(t)]).then_inc(s["x"], 16)
                sp.wait_ge(s["x"], 16 * (t + 1))
            for t in range(NTT):
                sp.wait_ge(s["y"], t + 1)
                sp.dma_start(dr["s_x1"][t * BLK:t * BLK + rows(t)], y(t)[0:rows(t)]).then_inc(s["stored"], 16)
            sp.wait_ge(s["stored"], 16 * NTT)

        @block.tensor
        def _(pe):
            pe.wait_ge(s["w"], 16)

            def turn(t):
                r = rows(t)
                pe.wait_ge(s["y"], t + 1)
                if t:
                    pe.wait_ge(s["trc"], t)
                for k in range(KT):
                    tr = pe.transpose(ps[:, 4 + k // 4, (k % 4) * P:(k % 4) * P + r], y(t)[0:r, k * P:(k + 1) * P], c.ident[0:r, 0:r])
                tr.then_inc(s["tr"], 1)

            for t in range(NTT):
                r = rows(t)
                if t >= 2:
                    pe.wait_ge(s["read"], t - 1)
                for n in range(2):
                    for k in range(KT):
                        mm = pe.matmul(ps[0:r, 2 * (t % 2) + n, :], mT[:, k, t * BLK:t * BLK + r], w[:, k, n * 512:(n + 1) * 512], start=(k == 0), stop=(k == KT - 1))
                mm.then_inc(s["mm"], 1)
                if t:
                    turn(t - 1)
            turn(NTT - 1)

        @block.vector
        def _(dve):
            link = Link(dve, s["link"])
            dve.wait_ge(s["gb"], 32)
            for t in range(NTT):
                r = rows(t)
                dve.wait_ge(s["mm"], t + 1)
                dve.wait_ge(s["x"], 16 * (t + 1))
                yy = y(t)[0:r]
                dve.scalar_tensor_tensor(yy.rearrange("p (n w) -> p n w", n=2), xt[0:r, t % 2].rearrange("p (n w) -> p n w", n=2), ALPHA,
                                         ps[0:r, 2 * (t % 2):2 * (t % 2) + 2, :], ALU.mult, ALU.add).then_inc(s["read"], 1)
                dve.wait_ge(s["read"], t + 1)
                link(norm_rows(dve, (s["asked"], s["given"]), link, yy, r, st, gb, t))
                dve.tensor_tensor(yy, yy, gb[0:r, 1], ALU.add).then_inc(s["y"], 1)

        @block.scalar
        def _(act):
            def copy(t):
                r = rows(t)
                act.wait_ge(s["tr"], t + 1)
                act.activation(x1T[:, :, t * BLK:t * BLK + r].rearrange("p (a b) t -> p a b t", a=2),
                               ps[:, 4:6, :].rearrange("p a (b t) -> p a b t", b=4)[:, :, :, 0:r], ACT.Copy).then_inc(s["trc"], 1)

            for t in range(NTT):
                root(act, c.eps, st, rows(t), s["asked"], s["given"], t)
                if t:
                    copy(t - 1)
            copy(NTT - 1)


def route(c, x1T, y, rt):
    nc, ps, dr = c.nc, c.ps, c.dram
    s = Semaphores(c, "rt")
    NG = 4
    FAR = 65536.0
    MID = 9
    with ExitStack() as ctx:
        sb = lambda n, sh, dt=F32: ctx.enter_context(nc.sbuf_tensor(f"rt_{n}", sh, dt))
        w = sb("w", [P, KT, NE])
        rb = sb("rb", [P, NE])
        tri = sb("tri", [P, P])
        blk = sb("blk", [P, EB])
        tok = sb("tok", [P, NTT], U32)
        zero = sb("zero", [P, EB + 2], U32)
        sc = sb("sc", [P, NTT, NE])
        bi = sb("bi", [P, NTT * NG, 4])
        rank = sb("rank", [P, NTT * NG, 4])
        gs = sb("gs", [P, NTT, NG])
        grank = sb("grank", [P, NTT, NG])
        a = sb("a", [P, NTT * NG])
        b = sb("b", [P, NTT * NG])
        su = sb("su", [P, NTT])
        gw = sb("gw", [P, NTT, NE])
        at = sb("at", [P, NTT, NE])
        far = sb("far", [P, NTT, NE])
        eq = sb("eq", [P, NTT, NE])
        df = sb("df", [P, TOPK, NTT])
        cnt = sb("cnt", [P, NE])
        nb = sb("nb", [P, NE])
        cum = sb("cum", [P, NE])
        t16 = sb("t16", [P, NE])
        past = sb("past", [P, EB, NE])
        be = sb("be", [P, rt.END])
        before = sb("before", [P, EB, EB])
        ple = LayerInput(c, x1T, y, lambda n, sh: ctx.enter_context(nc.sbuf_tensor(f"pl_{n}", sh, F32)))
        block = ctx.enter_context(nc.Block())
        sel = rank[:].rearrange("p (t g) e -> p t (g e)", g=NG)
        fl = lambda t: t.rearrange("p t e -> p (t e)")

        @block.sync
        def _(sp):
            sp.dma_start(w[:], dr["w_router"]).then_inc(s["in"], 16)
            sp.dma_start(rb[:], dr["router_bias"].to_broadcast([P, NE])).then_inc(s["in"], 16)
            sp.dma_start(tri[:], dr["tri"]).then_inc(s["in"], 16)
            sp.dma_start(blk[:], dr["blk"]).then_inc(s["in"], 16)
            sp.dma_start(tok[:], dr["tok"]).then_inc(s["in"], 16)
            ple.load(sp)
            sp.wait_ge(s["zero"], 1)
            sp.dma_start(dr["s_row"].rearrange("(p n) o -> p (n o)", p=P), zero[:]).then_inc(s["cleared"], 16)

        @block.gpsimd
        def _(pool):
            ple.gpsimd(pool, range(0, MID))
            pool.wait_ge(s["in"], 80)
            pool.wait_ge(s["cleared"], 16)
            pool.wait_ge(s["dest"], 1)
            for k in range(TOPK):
                for t in range(NTT):
                    r = rows(t)
                    pool.indirect_dma_start(dr["s_row"], bass.IndirectOffsetOnAxis(rt.dest[0:r, k, t:t + 1], 0),
                                            tok[0:r, t:t + 1], None).then_inc(s["scattered"], 16)
            ple.gpsimd(pool, range(MID, ple.UNITS))
            pool.wait_ge(s["scattered"], 16 * TOPK * NTT)

        @block.tensor
        def _(pe):
            pe.wait_ge(s["in"], 80)
            for t in range(NTT):
                r = rows(t)
                for k in range(KT):
                    mm = pe.matmul(ps[0:r, 0, t * NE:(t + 1) * NE], x1T[:, k, t * BLK:t * BLK + r], w[:, k, :], start=(k == 0), stop=(k == KT - 1))
            mm.then_inc(s["mm"], 1)
            ple.tensor(pe, range(0, 4))
            pe.wait_ge(s["sel"], 1)
            for t in range(NTT):
                r = rows(t)
                out = ps[0:r, 1, t * NE:(t + 1) * NE]
                pe.matmul(out, tri[0:r, 0:r], sel[0:r, t, :], start=True, stop=(t == 0))
                for u in range(t):
                    pe.matmul(out, c.ones[:, 0:r], sel[:, u, :], start=False, stop=(u == t - 1))
            for t in range(NTT):
                mm = pe.matmul(ps[:, 2, 0:NE], c.ones[0:rows(t), :], sel[0:rows(t), t, :], start=(t == 0), stop=(t == NTT - 1))
            mm.then_inc(s["counts"], 1)
            ple.tensor(pe, range(4, ple.UNITS))

        @block.scalar
        def _(act):
            act.wait_ge(s["z"], 1)
            act.wait_ge(s["mm"], 1)
            act.activation(fl(sc[:, 0:NBLK, :]), ps[:, 0, 0:NBLK * NE], ACT.Sigmoid)
            act.activation(sc[0:NB, NBLK, :], ps[0:NB, 0, NBLK * NE:NTT * NE], ACT.Sigmoid).then_inc(s["sig"], 1)
            ple.scalar(act)

        @block.vector
        def _(dve):
            link = Link(dve, s["link"])
            dve.memset(zero[:], 0).then_inc(s["zero"], 1)
            dve.memset(sc[:], 0.5).then_inc(s["z"], 1)
            dve.memset(rank[:], 0.0)
            dve.memset(grank[:], 0.0)
            dve.wait_ge(s["sig"], 1)
            dve.wait_ge(s["in"], 80)
            link(dve.tensor_tensor(bi[:].rearrange("p (t g) e -> p t (g e)", g=NG), sc[:], mid(rb[:], NTT), ALU.add))
            gsv = gs[:].rearrange("p t g -> p (t g)")
            pairs = [(i, j) for i in range(4) for j in range(i + 1, 4)]
            for n, (i, j) in enumerate(pairs):
                x, y = bi[:, :, i], bi[:, :, j]
                link(dve.tensor_tensor(a[:], x, y, ALU.add))
                link(dve.tensor_copy(gsv, a[:]) if n == 0 else dve.tensor_tensor(gsv, gsv, a[:], ALU.max))
                dve.tensor_tensor(a[:], y, x, ALU.is_gt)
                link(dve.tensor_tensor(b[:], x, y, ALU.is_ge))
                dve.tensor_tensor(rank[:, :, i], rank[:, :, i], a[:], ALU.add)
                link(dve.tensor_tensor(rank[:, :, j], rank[:, :, j], b[:], ALU.add))
            for i, j in pairs:
                x, y = gs[:, :, i], gs[:, :, j]
                dve.tensor_tensor(a[:, 0:NTT], y, x, ALU.is_gt)
                link(dve.tensor_tensor(b[:, 0:NTT], x, y, ALU.is_ge))
                dve.tensor_tensor(grank[:, :, i], grank[:, :, i], a[:, 0:NTT], ALU.add)
                link(dve.tensor_tensor(grank[:, :, j], grank[:, :, j], b[:, 0:NTT], ALU.add))
            rk, grk = fl(rank[:]), fl(grank[:])
            dve.tensor_scalar(rk, rk, 2.0, None, ALU.is_lt)
            link(dve.tensor_scalar(grk, grk, 1.0, None, ALU.is_lt))
            dve.tensor_tensor(rank[:], rank[:], last(grk, 4), ALU.mult).then_inc(s["sel"], 1)
            dve.wait_ge(s["sel"], 1)
            link(dve.tensor_tensor(fl(gw[:]), rk, fl(sc[:]), ALU.mult))
            link(dve.tensor_reduce(su[:], gw[:], AX.X, ALU.add))
            link(dve.reciprocal(su[:], su[:]))
            link(dve.tensor_tensor(gw[:], gw[:], last(su[:], NE), ALU.mult))
            dve.wait_ge(s["counts"], 1)
            link(dve.tensor_copy(cnt[:], ps[:, 2, 0:NE]))
            link(dve.tensor_scalar(nb[:], cnt[:], 0.0, None, ALU.is_gt))
            for k in range(1, NTT):
                link(dve.tensor_scalar(t16[:], cnt[:], float(k * P), None, ALU.is_gt))
                link(dve.tensor_tensor(nb[:], nb[:], t16[:], ALU.add))
            link(dve.tensor_tensor_scan(cum[:], c.ones[:, 0:NE], nb[:], 0.0, ALU.mult, ALU.add))
            link(dve.tensor_tensor(past[:], last(blk[:], NE), mid(cum[:], EB), ALU.is_ge))
            link(dve.tensor_reduce(be[:, 0:EB], past[:], AX.X, ALU.add))
            dve.tensor_scalar(be[:, 0:EB], be[:, 0:EB], NE - 1.0, None, ALU.min)
            ordinal, free, first = (be[:, k:k + EB] for k in (rt.ORDINAL, rt.FREE, rt.FIRST))
            link(dve.tensor_scalar(t16[:], nb[:], 0.0, None, ALU.is_gt))
            link(dve.tensor_tensor(past[:], past[:], mid(t16[:], EB), ALU.mult))
            link(dve.tensor_reduce(ordinal, past[:], AX.X, ALU.add))
            link(dve.tensor_scalar(free, ordinal, 2.0, None, ALU.add))
            link(dve.tensor_tensor(before[:], last(ordinal, EB), mid(free, EB), ALU.is_ge))
            link(dve.tensor_reduce(free, before[:], AX.X, ALU.add))
            dve.memset(first[:, 0:1], 1.0)
            link(dve.tensor_tensor(first[:, 1:EB], ordinal[:, 1:EB], ordinal[:, 0:EB - 1], ALU.subtract))
            link(dve.tensor_copy(be[:, EB:EB + 1], cum[:, NE - 1:NE]))
            dve.tensor_copy(rt.plan[:], be[0:1, :])
            link(dve.tensor_tensor(nb[:], cum[:], nb[:], ALU.subtract))
            link(dve.tensor_scalar(nb[:], nb[:], float(P), None, ALU.mult))
            dve.memset(at[:, NBLK, :], 0.0)
            link(dve.tensor_tensor(at[:, 0:NBLK, :], ps[:, 1, 0:NBLK * NE].rearrange("p (t e) -> p t e", e=NE), mid(nb[:], NBLK), ALU.add))
            link(dve.tensor_tensor(at[0:NB, NBLK, :], ps[0:NB, 1, NBLK * NE:NTT * NE], nb[0:NB], ALU.add))
            link(dve.tensor_scalar(fl(far[:]), rk, -FAR, FAR, ALU.mult, ALU.add))
            link(dve.tensor_tensor(at[:], at[:], far[:], ALU.add))
            link(dve.tensor_reduce(df[:, 0, :], at[:], AX.X, ALU.min))
            link(dve.tensor_tensor(eq[:], at[:], last(df[:, 0, :], NE), ALU.is_equal))
            link(dve.tensor_tensor(eq[:], eq[:], gw[:], ALU.mult))
            link(dve.tensor_reduce(rt.wt[:, 0, :], eq[:], AX.X, ALU.add))
            link(dve.tensor_scalar(fl(far[:]), fl(far[:]), -2.0, None, ALU.mult))
            link(dve.tensor_tensor(at[:], at[:], far[:], ALU.add))
            link(dve.tensor_reduce(df[:, 1, :], at[:], AX.X, ALU.max))
            link(dve.tensor_tensor(eq[:], at[:], last(df[:, 1, :], NE), ALU.is_equal))
            link(dve.tensor_tensor(eq[:], eq[:], gw[:], ALU.mult))
            link(dve.tensor_reduce(rt.wt[:, 1, :], eq[:], AX.X, ALU.add))
            dve.tensor_copy(rt.dest[:], df[:]).then_inc(s["dest"], 1)


class LayerInput:
    UNITS = 2 * NTT

    def __init__(self, c, x1T, y, sb):
        self.c, self.x1T, self.y, self.s = c, x1T, y, Semaphores(c, "pl")
        self.wg = sb("wg", [P, KT, D])
        self.wp = sb("wp", [P, 2, D])
        self.pT = sb("pT", [P, 2, T])
        self.sg = sb("sg", [P, 2, 512])
        self.pp = sb("pp", [P, 2, 512])

    def unit(self, u):
        t, n = u // 2, u % 2
        return t, rows(t), slice(n * 512, (n + 1) * 512), u % 2, 4 + 2 * (u % 2)

    def load(self, sp):
        dr, s = self.c.dram, self.s
        sp.dma_start(self.wg[:], dr["w_ple_gate"]).then_inc(s["in"], 16)
        sp.dma_start(self.pT[:], dr["pT"]).then_inc(s["in"], 16)
        sp.dma_start(self.wp[:], dr["w_ple"]).then_inc(s["in"], 16)

    def tensor(self, pe, units):
        ps, s = self.c.ps, self.s
        for u in units:
            t, r, cols, j, q = self.unit(u)
            tk = slice(t * BLK, t * BLK + r)
            if u == 0:
                pe.wait_ge(s["in"], 48)
            if u >= 2:
                pe.wait_ge(s["read"], u - 1)
            for k in range(KT):
                pe.matmul(ps[0:r, q, :], self.x1T[:, k, tk], self.wg[:, k, cols], start=(k == 0), stop=(k == KT - 1))
            for k in range(2):
                mm = pe.matmul(ps[0:r, q + 1, :], self.pT[:, k, tk], self.wp[:, k, cols], start=(k == 0), stop=(k == 1))
            mm.then_inc(s["mm"], 1)

    def scalar(self, act):
        ps, s = self.c.ps, self.s
        for u in range(self.UNITS):
            t, r, cols, j, q = self.unit(u)
            act.wait_ge(s["mm"], u + 1)
            if u >= 2:
                act.wait_ge(s["used"], u - 1)
            yv = self.y(t)[0:r, cols]
            act.activation(yv, yv, ACT.Copy, scale=ALPHA)
            act.activation(self.pp[0:r, j], ps[0:r, q + 1, :], ACT.Copy)
            act.activation(self.sg[0:r, j], ps[0:r, q, :], ACT.Sigmoid).then_inc(s["read"], 1)

    def gpsimd(self, pool, units):
        s = self.s
        for u in units:
            t, r, cols, j, q = self.unit(u)
            yv = self.y(t)[0:r, cols]
            pool.wait_ge(s["read"], u + 1)
            pool.tensor_tensor(self.sg[0:r, j], self.sg[0:r, j], self.pp[0:r, j], ALU.mult).then_inc(s["scaled"], 1)
            pool.wait_ge(s["scaled"], u + 1)
            pool.tensor_tensor(yv, yv, self.sg[0:r, j], ALU.add).then_inc(s["used"], 1)


def experts(c, rt):
    nc, ps, dr = c.nc, c.ps, c.dram
    HT = DE // P
    wg_here, wu_here, wd_here = ([c.sem(f"ex_{w}_here{j}") for j in range(2)] for w in ("wg", "wu", "wd"))
    row_here = [c.sem(f"ex_row_here{j}") for j in range(2)]
    x_here = [c.sem(f"ex_x_here{j}") for j in range(2)]
    stored = [c.sem(f"ex_stored{j}") for j in range(2)]
    s = Semaphores(c, "ex")
    with ExitStack() as ctx:
        sb = lambda n, sh, dt=F32: ctx.enter_context(nc.sbuf_tensor(f"ex_{n}", sh, dt))
        wg = sb("wg", [P, 2, KT, DE])
        wu = sb("wu", [P, 2, KT, DE])
        wd = sb("wd", [P, 2, HT, D])
        row = sb("row", [P, 2], U32)
        xb = sb("xb", [P, 2, D])
        xT = sb("xT", [P, 2, KT, P])
        a = sb("a", [P, DE])
        aT = sb("aT", [P, HT, P])
        ob = sb("ob", [P, 2, D])
        zero = c.rest
        block = ctx.enter_context(nc.Block())

        def blocks(eng):
            n = eng.value_load(rt.plan[0:1, EB:EB + 1], min_val=1, max_val=EB)
            with eng.Fori(0, EB // 2) as i:
                for j in range(2):
                    with eng.If(2 * i + j < n):
                        yield i, j

        def planned(eng, what, n, top):
            return eng.value_load(rt.plan[0:1, bass.ds(n + what, 1)], min_val=0, max_val=top)

        def by_buffer(eng, ordinal):
            for v in range(2):
                with eng.If(ordinal - 2 * (ordinal // 2) == v):
                    yield v

        @block.sync
        def _(sp):
            n = sp.value_load(rt.plan[0:1, EB:EB + 1], min_val=1, max_val=EB)
            with sp.Fori(0, EB) as i:
                with sp.If(i < n):
                    first = planned(sp, rt.FIRST, i, 1)
                    with sp.If(first > 0):
                        e = planned(sp, rt.EXPERT, i, NE - 1)
                        ordinal = planned(sp, rt.ORDINAL, i, NE - 1)
                        free = planned(sp, rt.FREE, i, EB)
                        sp.wait_ge(s["down"], free + 2)
                        for v in by_buffer(sp, ordinal):
                            for w, src, here in ((wg, "w_eg", wg_here), (wu, "w_eu", wu_here), (wd, "w_ed", wd_here)):
                                sp.dma_start(w[:, v], dr[src][bass.ds(e, 1)].rearrange("o p k n -> p (o k) n")).then_inc(here[v], 16)
            sp.wait_ge(s["zero"], 1)
            n = sp.value_load(rt.plan[0:1, EB:EB + 1], min_val=1, max_val=EB)
            with sp.Fori(0, EB) as i:
                with sp.If(i >= n):
                    sp.dma_start(dr["s_rows"][bass.ds(i * P, P)], zero).then_inc(s["cleared"], 16)
                with sp.If(i < n):
                    sp.sem_inc(s["cleared"], 16)
            sp.wait_ge(s["cleared"], 16 * EB)

        @block.gpsimd
        def _(pool):
            def gather(j):
                pool.indirect_dma_start(xb[:, j, :], None, dr["s_x1"], bass.IndirectOffsetOnAxis(row[:, j:j + 1], 0)).then_inc(x_here[j], 16)

            pool.memset(zero, 0.0).then_inc(s["zero"], 1)
            pool.wait_ge(row_here[0], 16)
            gather(0)
            for i, j in blocks(pool):
                n = 2 * i + j
                pool.wait_ge(row_here[1 - j], 16 * i + 16 * (1 + j))
                pool.wait_ge(s["turned"], n + 1)
                pool.sem_inc(s["gathering"], 1)
                gather(1 - j)

        @block.tensor
        def _(pe):
            pe.sem_inc(s["down"], 2)

            def turn(i, j):
                for k in range(KT):
                    t = pe.transpose(ps[:, k // 4, (k % 4) * P:(k % 4 + 1) * P], xb[:, j, k * P:(k + 1) * P], c.ident[:])
                t.then_inc(s["turned"], 1)

            pe.wait_ge(x_here[0], 16)
            turn(0, 0)
            for i, j in blocks(pe):
                n = 2 * i + j
                ordinal = planned(pe, rt.ORDINAL, n, NE - 1)
                pe.wait_ge(s["x_copied"], n + 1)
                for v in by_buffer(pe, ordinal):
                    for o, w, here in ((2, wg, wg_here), (3, wu, wu_here)):
                        pe.wait_ge(here[v], 16 * (ordinal // 2) + 16)
                        for k in range(KT):
                            mm = pe.matmul(ps[:, o, :], xT[:, j, k, :], w[:, v, k, :], start=(k == 0), stop=(k == KT - 1))
                        mm.then_inc(s["gate" if o == 2 else "up"], 1)
                pe.wait_ge(x_here[1 - j], 16 * i + 16 * (1 + j))
                turn(n + 1, 1 - j)
                pe.wait_ge(s["a"], n + 1)
                for k in range(HT):
                    t = pe.transpose(ps[:, 4, k * P:(k + 1) * P], a[:, k * P:(k + 1) * P], c.ident[:])
                t.then_inc(s["a_turned"], 1)
                pe.wait_ge(s["a_copied"], n + 1)
                pe.wait_ge(s["o_copied"], 2 * n + 2)
                for v in by_buffer(pe, ordinal):
                    pe.wait_ge(wd_here[v], 16 * (ordinal // 2) + 16)
                    for o in range(2):
                        for k in range(HT):
                            mm = pe.matmul(ps[:, 5 + o, :], aT[:, k, :], wd[:, v, k, o * 512:(o + 1) * 512], start=(k == 0), stop=(k == HT - 1))
                    mm.then_inc(s["down"], 1)

        @block.scalar
        def _(act):
            def x_copy(j):
                act.activation(xT[:, j].rearrange("p (a k) t -> p a (k t)", a=2), ps[:, 0:2, :], ACT.Copy).then_inc(s["x_copied"], 1)

            def rows_of(n, j):
                act.dma_start(row[:, j:j + 1], dr["s_row"][bass.ds(n * P, P)]).then_inc(row_here[j], 16)

            rows_of(0, 0)
            rows_of(1, 1)
            act.wait_ge(s["turned"], 1)
            x_copy(0)
            for i, j in blocks(act):
                n = 2 * i + j
                act.wait_ge(s["gate"], n + 1)
                act.activation(a[:], ps[:, 2, :], ACT.Silu).then_inc(s["silu"], 1)
                act.wait_ge(s["turned"], n + 2)
                x_copy(1 - j)
                rows_of(n + 2, j)
                act.wait_ge(s["down"], n + 3)
                act.wait_ge(stored[j], 16 * i + 16)
                act.activation(ob[:, j, 0:512], ps[:, 5, :], ACT.Copy).then_inc(s["o_copied"], 1)
                act.wait_ge(s["o_copied"], 2 * n + 4)
                act.dma_start(dr["s_rows"][bass.ds(n * P, P)], ob[:, j, :]).then_inc(stored[j], 16)
            n = act.value_load(rt.plan[0:1, EB:EB + 1], min_val=1, max_val=EB)
            act.wait_ge(stored[0], 16 * ((n + 1) // 2) + 16)
            act.wait_ge(stored[1], 16 * (n // 2) + 16)
            act.sem_inc(s["all_stored"], 1)
            act.wait_ge(row_here[0], 16 * ((n + 1) // 2) + 16)
            act.wait_ge(row_here[1], 16 * ((n + 2) // 2))
            act.sem_inc(s["all_stored"], 1)

        @block.vector
        def _(dve):
            dve.sem_inc(s["o_copied"], 2)
            dve.sem_inc(stored[0], 16)
            dve.sem_inc(stored[1], 16)
            for i, j in blocks(dve):
                n = 2 * i + j
                dve.wait_ge(s["up"], n + 1)
                dve.wait_ge(s["silu"], n + 1)
                dve.tensor_tensor(a[:], a[:], ps[:, 3, :], ALU.mult).then_inc(s["a"], 1)
                dve.wait_ge(s["a_turned"], n + 1)
                dve.tensor_copy(aT[:].rearrange("p k t -> p (k t)"), ps[:, 4, :]).then_inc(s["a_copied"], 1)
                dve.wait_ge(s["down"], n + 3)
                dve.wait_ge(stored[j], 16 * i + 16)
                dve.tensor_copy(ob[:, j, 512:1024], ps[:, 6, :]).then_inc(s["o_copied"], 1)


def last_norm(c, y, rt):
    nc, dr = c.nc, c.dram
    s = Semaphores(c, "ln")
    with ExitStack() as ctx:
        sb = lambda n, sh: ctx.enter_context(nc.sbuf_tensor(f"ln_{n}", sh, F32))
        gb = sb("gb", [P, 2, D])
        st = sb("st", [P, 16])
        er = sb("er", [P, TOPK, 3, D])
        block = ctx.enter_context(nc.Block())

        @block.gpsimd
        def _(pool):
            def shift(t):
                yy = y(t)[0:rows(t)]
                if t == 0:
                    pool.wait_ge(s["in"], 32)
                pool.wait_ge(s["scaled"], t + 1)
                pool.tensor_tensor(yy, yy, gb[0:rows(t), 1], ALU.add).then_inc(s["y"], 1)

            for t in range(NTT):
                r = rows(t)
                if t >= 3:
                    pool.wait_ge(s["added"], t - 2)
                for k in range(TOPK):
                    pool.indirect_dma_start(er[0:r, k, t % 3, :], None, dr["s_rows"], bass.IndirectOffsetOnAxis(rt.dest[0:r, k, t:t + 1], 0))\
                        .then_inc(s[f"rows{t % 3}"], 16)
                if t >= 3:
                    shift(t - 3)
            for t in range(NTT - 3, NTT):
                shift(t)

        @block.sync
        def _(sp):
            for k in range(2):
                sp.dma_start(gb[:, k, :], dr["ln2"][k:k + 1, :].to_broadcast([P, D])).then_inc(s["in"], 16)
            for t in range(NTT):
                sp.wait_ge(s["y"], t + 1)
                sp.dma_start(dr["o_y"][t * BLK:t * BLK + rows(t)], y(t)[0:rows(t)]).then_inc(s["out"], 16)
            sp.wait_ge(s["out"], 16 * NTT)

        @block.vector
        def _(dve):
            link = Link(dve, s["link"])
            dve.wait_ge(s["in"], 32)
            for t in range(NTT):
                r = rows(t)
                yy = y(t)[0:r]
                dve.wait_ge(s[f"rows{t % 3}"], 32 * (t // 3 + 1))
                link(dve.scalar_tensor_tensor(yy, er[0:r, 0, t % 3, :], rt.wt[0:r, 0, t:t + 1], yy, ALU.mult, ALU.add))
                dve.scalar_tensor_tensor(yy, er[0:r, 1, t % 3, :], rt.wt[0:r, 1, t:t + 1], yy, ALU.mult, ALU.add).then_inc(s["added"], 1)
                dve.wait_ge(s["added"], t + 1)
                norm_rows(dve, (s["asked"], s["given"]), link, yy, r, st, gb, t).then_inc(s["scaled"], 1)

        @block.scalar
        def _(act):
            for t in range(NTT):
                root(act, c.eps, st, rows(t), s["asked"], s["given"], t)


def attention(c):
    nc = c.nc
    with ExitStack() as ctx:
        sb = lambda n, sh, dt=F32: ctx.enter_context(nc.sbuf_tensor(f"at_{n}", sh, dt))
        z = sb("z", [P, 10, T])
        q, kv = z[:, 0:GR, :], z[:, GR:10, :]
        c.gtok = sb("gtok", [P, NBLK, 24])
        kc = sb("kc", [P, NB + 1, NCMP])
        vc = sb("vc", [NCMP, NB + 1, P])
        with ExitStack() as ctx2:
            sb2 = lambda n, sh, dt=F32: ctx2.enter_context(nc.sbuf_tensor(f"at_{n}", sh, dt))
            x = Tokens(c, "nx", sb2)
            ws, ws2 = sb2("ws", [P, KT, 96]), sb2("ws2", [P, 2, KT, 96], FR)
            rb, hot = sb2("rb", [33, NH]), sb2("hot", [33, LSEL + LWIN])
            bv = sb2("bv", [NH, LSEL + LWIN])
            bias_written, rows_written = c.sem("nsa_bias_written"), c.sem("nsa_rows_written")
            load_shared(c, x, z[:, 2:10], ws, ws2, rb, hot, bv, bias_written)
            small_projection(c, "small", x, ws2, c.small)
            project(c, "nsa", c.dram["w_nsa"], 10, z, x, written=(bias_written, 16))
        nsa_prepare(c, q, kv, c.small, rows_written)
        with nc.sbuf_tensor("at_Ss", [64, SO_END], F32) as Ss, nc.sbuf_tensor("at_vs", [P, NB * PAGES, P], F32) as vs:
            v_here = c.sem("nsa_v_here")
            nsa_samples_scores(c, q, kv, Ss, kc, vc, vs, v_here, rows_written)
            nsa_samples_finish(c, kv, Ss, vc, vs, v_here)
        nsa_prompt(c, q, kv, kc, vc)


def layer(nc, dram):
    c = Core(nc, dram)
    c.ident = nc.alloc_sbuf_tensor("ident", [P, P], F32)
    c.ones = nc.alloc_sbuf_tensor("ones", [P, P], F32)
    c.eps = nc.alloc_sbuf_tensor("eps", [P, 1], F32)
    rt = Routing(nc)
    o01 = nc.alloc_sbuf_tensor("o01", [P, 2 * H4, T], F32)
    c.oT = [o01[:, 0:H4, :], o01[:, H4:2 * H4, :]]
    with nc.sbuf_tensor("small", [96, T], F32) as small:
        c.small = small
        attention(c)
        c.retire()
        deltanet(c, small)
        c.retire()
    o2 = nc.alloc_sbuf_tensor("o2", [P, H4, T], F32)
    c.oT.append(o2[:])
    y01 = o01[:].rearrange("p m t -> p (m t)")[:, 0:NBLK * D].rearrange("p (t d) -> p t d", d=D)
    y2 = o2[:].rearrange("p m t -> p (m t)")
    c.rest = y2[:, D:2 * D]

    def y(t):
        return y01[:, t, :] if t < NBLK else y2[:, 0:D]

    hgrn2(c)
    c.retire()
    with nc.sbuf_tensor("mT", [P, KT, T], F32) as mT:
        merge(c, mT)
        with nc.sbuf_tensor("x1T", [P, KT, T], F32) as x1T:
            mix_out(c, mT, y, x1T)
            route(c, x1T, y, rt)
    experts(c, rt)
    last_norm(c, y, rt)



def bucket(dist):
    n = np.maximum(dist, 0)
    exact = NBUCK // 2
    rel = np.log(np.maximum(n, 1).astype(np.float32) / np.float32(exact)) / np.float32(np.log(128 / exact))
    large = np.minimum(exact + (rel * np.float32(NBUCK - exact)).astype(np.int32), NBUCK - 1)
    return np.where(n < exact, n, large)


def constants():
    f = np.float32
    hot = np.zeros((33, LSEL + LWIN), f)
    for off, d, live in ((0, 1151 - np.arange(LSEL), lambda d: d >= 0), (LSEL, 639 - np.arange(LWIN), lambda d: (d >= 0) & (d < WIN))):
        ok = live(d)
        hot[bucket(d)[ok], off + np.where(ok)[0]] = 1
        hot[32, off + np.where(~ok)[0]] = NEG
    i = np.arange(P)
    up = np.zeros((P, LEV, P), f)
    for l in range(LEV):
        h = 1 << l
        same = (i[:, None] // (2 * h)) == (i[None, :] // (2 * h))
        up[:, l, :] = same & (i[:, None] % (2 * h) < h) & (i[None, :] % (2 * h) >= h)
    lo = np.stack([i[None, :] <= i[:, None], i[None, :] < i[:, None], up[:, 0, :].T > 0], 1).astype(f)
    r = np.arange(64)
    own = np.where(r[:, None] // NH == np.arange(NB)[None, :], 0, NEG).astype(f)
    grp = (r[:, None] // GR == r[None, :] // GR).astype(f)
    c0, b0 = np.arange(NCMP) * STR, np.arange(NSB) * SELB
    imap = ((c0[:, None] <= b0[None, :] + SELB - 1) & (c0[:, None] + 2 * STR - 1 >= b0[None, :])).astype(f)
    idx = np.broadcast_to(np.arange(NSB, dtype=f), (64, NSB)).copy()
    return {"ident": np.eye(P, dtype=f), "hot": hot, "up": up, "lo": lo, "own": own, "grp": grp, "imap": imap, "idx": idx,
            "tri": (i[:, None] < i[None, :]).astype(f), "blk": np.broadcast_to(np.arange(EB, dtype=f), (P, EB)).copy(),
            "tok": (np.arange(NTT)[None, :] * P + i[:, None]).astype(np.uint32)}


def tiles(w):
    k = w.shape[0] // P
    return np.ascontiguousarray(w.reshape(k, P, -1, P).transpose(2, 1, 0, 3))


def rows_by_partition(w):
    return np.ascontiguousarray(w.reshape(w.shape[0] // P, P, -1).transpose(1, 0, 2))


def lay_in(a):
    w = a["w_in"][0]
    at = np.cumsum([0, 512, 768, 24, 1536, 4, 4, 512, 512, 512, 512, 512, 3072])
    (nq, nkv, ng, dqkv, da, db, dg, hq, hf, hi, hg, mg) = (w[:, at[i]:at[i + 1]] for i in range(12))
    nq = nq.reshape(D, G, GR, DH).transpose(0, 2, 1, 3).reshape(D, 512)
    small = np.zeros((D, 96), w.dtype)
    small[:, 0:24], small[:, 32:36], small[:, 64:68] = ng, da, db
    x = np.concatenate([a["x_prompt"][0], a["x_sample"][:, 0]], 0)
    pl = np.concatenate([a["p_prompt"][0, 0], a["p_sample"][0, :, 0]], 0)
    wb = a["w_branch"][0].copy()
    wb[0] = wb[0].reshape(G, GR, DH, D).transpose(1, 0, 2, 3).reshape(512, D)
    state = lambda s: np.ascontiguousarray(s[0].transpose(2, 1, 0, 3).reshape(P, H4 * NB, P))
    out = {
        "xT": rows_by_partition(np.ascontiguousarray(x.T)), "x": x,
        "pT": rows_by_partition(np.ascontiguousarray(pl.T)),
        "w_nsa": tiles(np.concatenate([nq, nkv], 1)), "w_small": rows_by_partition(small),
        "w_dn": tiles(np.concatenate([dqkv, dg], 1)), "w_hg": tiles(np.concatenate([hq, hf, hi, hg], 1)),
        "w_mg": np.ascontiguousarray(tiles(mg).reshape(3, KT, P, KT, P).transpose(1, 0, 2, 3, 4).reshape(24, P, KT, P)),
        "w_br": np.ascontiguousarray(np.stack([tiles(wb[b]) for b in range(3)], 1).reshape(24, P, H4, P)),
        "w_out": rows_by_partition(a["w_out"][0]),
        "rb_aug": np.concatenate([a["rel_bias"], np.ones((1, NH), np.float32)], 0),
        "cache": np.ascontiguousarray(a["cache_nsa"][0].reshape(NPOOL, P, 512)),
        "table": np.ascontiguousarray(a["page_table"].reshape(1, NB * PAGES).astype(np.int32)),
        "state_win": np.ascontiguousarray(a["state_win"][0].reshape(NB, WIN, 2 * P)),
        "w_cmp1": np.ascontiguousarray(a["w_cmp1"][0].reshape(2, 32, DH, P).transpose(2, 0, 1, 3)),
        "w_cmp2": np.ascontiguousarray(a["w_cmp2"][0].transpose(1, 0, 2)),
        "pe_cmp": np.ascontiguousarray(a["pe_cmp"][0].transpose(2, 0, 1)),
        "conv_w": np.ascontiguousarray(a["dn_conv_w"][0].reshape(4, 12, P).transpose(2, 1, 0)),
        "conv_state": np.ascontiguousarray(a["state_dn_conv"][0].reshape(NB, 3, 12, P).transpose(3, 2, 0, 1)),
        "dn_par": np.stack([a["dn_a_log"][0], a["dn_dt_bias"][0]], 1),
        "dn_norm": np.ascontiguousarray(a["dn_norm_w"][0].reshape(P, 1)), "hg_norm": np.ascontiguousarray(a["hg_norm_w"][0].reshape(P, 1)),
        "state_dn": state(a["state_dn"]), "state_hg": state(a["state_hg"]),
        "ln1": np.concatenate([a["ln1_g"], a["ln1_b"]], 0), "ln2": np.concatenate([a["ln2_g"], a["ln2_b"]], 0),
        "w_router": rows_by_partition(a["w_router"]), "router_bias": a["router_bias"].reshape(1, NE),
        "w_eg": np.ascontiguousarray(a["w_exp_gate"][0].reshape(NE, KT, P, DE).transpose(0, 2, 1, 3)),
        "w_eu": np.ascontiguousarray(a["w_exp_up"][0].reshape(NE, KT, P, DE).transpose(0, 2, 1, 3)),
        "w_ed": np.ascontiguousarray(a["w_exp_down"][0].reshape(NE, DE // P, P, D).transpose(0, 2, 1, 3)),
        "w_ple": rows_by_partition(a["w_ple"][0]), "w_ple_gate": rows_by_partition(a["w_ple_gate"][0]),
    }
    return {**out, **constants()}


OUTS = {"o_y": (T, D), "o_kvT": (P, 6, T), "o_win": (NB, WIN - 1, 2 * P), "o_conv": (P, 12, 3 + 3 * NB),
        "o_dn_p": (P, H4 * P), "o_dn_s": (P, H4 * NB, P), "o_hg_p": (P, H4, P), "o_hg_s": (P, H4 * NB, P)}
SCRATCH = {"s_gate": ((24, NB), F32), "s_bias": ((NH, P, LSEL + LWIN), F32), "s_x1": ((T, D), F32),
           "s_row": (((EB + 2) * P, 1), U32), "s_rows": ((EB * P, D), F32)}


def lay_out(o):
    kv = np.ascontiguousarray(np.asarray(o["o_kvT"]).transpose(2, 1, 0)).reshape(T, 6, G, DH)
    rows_, win = kv[:, 0:4], kv[:, 4:6]
    st = np.asarray(o["o_conv"])
    cp = st[:, :, 0:3].transpose(2, 1, 0).reshape(3, 1536)
    cs = st[:, :, 3:].reshape(P, 12, NB, 3).transpose(2, 3, 1, 0).reshape(NB, 3, 1536)
    y = np.asarray(o["o_y"])
    ws = np.concatenate([np.asarray(o["o_win"]).reshape(NB, WIN - 1, 2, G, DH), win[TP:, None]], 1)
    state = lambda s: np.ascontiguousarray(np.asarray(s).reshape(P, H4, NB, P).transpose(2, 1, 0, 3))[None]
    pst = lambda s: np.ascontiguousarray(np.asarray(s).reshape(P, H4, P).transpose(1, 0, 2))[None, None]
    return (y[None, 0:TP], y[TP:, None], rows_[None, None, 0:TP], rows_[None, TP:, None],
            win[None, None, TP - WIN:TP], ws[None], cp[None, None], cs[None],
            pst(o["o_dn_p"]), state(o["o_dn_s"]), pst(o["o_hg_p"]), state(o["o_hg_s"]))


def kernel(**inputs):
    import concourse.bacc as bacc
    from concourse.bass_utils import run_bass_kernel_spmd

    nc = bacc.Bacc("TRN2", target_bir_lowering=False, num_devices=1)
    arrays = {f"in_{n}": np.ascontiguousarray(a) for n, a in lay_in({k: np.asarray(v) for k, v in inputs.items()}).items()}
    dram = {n[3:]: nc.dram_tensor(n, a.shape, mybir.dt.from_np(a.dtype), kind="ExternalInput").ap() for n, a in arrays.items()}
    for n, shape in OUTS.items():
        dram[n] = nc.dram_tensor(f"out_{n}", shape, F32, kind="ExternalOutput").ap()
    for n, (shape, dt) in SCRATCH.items():
        dram[n] = nc.dram_tensor(f"scratch_{n}", shape, dt, kind="Internal").ap()
    layer(nc, dram)
    r = run_bass_kernel_spmd(nc, [arrays], core_ids=[0])
    return lay_out({n: r.results[0][f"out_{n}"] for n in OUTS})
```
